# Optimizing a Trainium2 kernel written in Bass

```python
import math
import jax, jax.numpy as jnp
from jax import lax
import numpy as np

D_MODEL = 1024
BATCH = 1
SEQ = 1024
DEPTH = 1

EPS = 1e-6
NEG_INF = -1e30

A_HEADS = 8
A_HEAD_DIM = 64
A_WIDTH = A_HEADS * A_HEAD_DIM
DILATED_PATTERNS = ((128, 1), (512, 4), (2048, 16))
A_BLOCK = 64

REL_BUCKETS = 32
REL_MAX_DISTANCE = 1024

B_HEADS = 8
B_Q_LORA = 256
B_KV_LORA = 128
B_QK_NOPE = 64
B_QK_ROPE = 32
B_V_DIM = 64
B_WIDTH = B_HEADS * B_V_DIM
ROPE_THETA = 10000.0
B_Q_BLOCK = 128

MIX_WIDTH = A_WIDTH + B_WIDTH
IN_PROJ_WIDTH = 3 * A_WIDTH + B_Q_LORA + B_KV_LORA + B_QK_ROPE

N_GROUPS = 4
EXPERTS_PER_GROUP = 8
N_EXPERTS = N_GROUPS * EXPERTS_PER_GROUP
TOP_K_IN_GROUP = 2
EXPERT_FF = 256
MOE_BLOCK = 128


def rmsnorm(x, g):
    xf = x.astype(jnp.float32)
    y = xf * lax.rsqrt(jnp.mean(xf * xf, axis=-1, keepdims=True) + EPS)
    return (y * g.astype(jnp.float32)).astype(x.dtype)

def t5_relative_bucket(rel):
    half = REL_BUCKETS // 2
    max_exact = half // 2
    n = np.abs(rel)
    large = max_exact + (np.log(np.maximum(n, 1) / max_exact)
                         / math.log(REL_MAX_DISTANCE / max_exact) * (half - max_exact)).astype(np.int32)
    large = np.minimum(large, half - 1)
    return (np.where(rel > 0, half, 0) + np.where(n < max_exact, n, large)).astype(np.int32)

def dilated_window_attention(q, k, v, rel_bias, dilation, half_steps):
    b, h, s, dh = q.shape
    L = s // dilation
    qb = math.gcd(L, A_BLOCK)
    nb = L // qb
    span = qb + 2 * half_steps

    def to_residue(t):
        return t.reshape(b, h, L, dilation, dh).transpose(0, 1, 3, 2, 4)

    qr, kr, vr = to_residue(q), to_residue(k), to_residue(v)
    pad = ((0, 0), (0, 0), (0, 0), (half_steps, half_steps), (0, 0))
    kp, vp = jnp.pad(kr, pad), jnp.pad(vr, pad)
    key_idx = np.arange(nb)[:, None] * qb + np.arange(span)[None, :]
    kb = jnp.take(kp, key_idx, axis=3)
    vb = jnp.take(vp, key_idx, axis=3)
    qblk = qr.reshape(b, h, dilation, nb, qb, dh)
    scores = jnp.einsum('bhrnqd,bhrnkd->bhrnqk', qblk, kb,
                        preferred_element_type=jnp.float32) * (dh ** -0.5)
    rel_steps = np.arange(span)[None, :] - half_steps - np.arange(qb)[:, None]
    buckets = t5_relative_bucket(rel_steps * dilation)
    bias = rel_bias[buckets].astype(jnp.float32).transpose(2, 0, 1)
    key_pos = key_idx - half_steps
    valid = ((np.abs(rel_steps) <= half_steps)[None]
             & (key_pos >= 0)[:, None, :] & (key_pos < L)[:, None, :])
    scores = jnp.where(valid[None, None, None], scores + bias[None, :, None, None], NEG_INF)
    m = jnp.max(scores, axis=-1, keepdims=True)
    p = jnp.exp(scores - m)
    l = jnp.sum(p, axis=-1, keepdims=True)
    o = jnp.einsum('bhrnqk,bhrnkd->bhrnqd', p, vb, preferred_element_type=jnp.float32) / l
    lse = (m + jnp.log(l))[..., 0]
    o = o.reshape(b, h, dilation, L, dh).transpose(0, 1, 3, 2, 4).reshape(b, h, s, dh)
    lse = lse.reshape(b, h, dilation, L).transpose(0, 1, 3, 2).reshape(b, h, s)
    return o, lse

def mixer_dilated(q, k, v, rel_bias):
    outs, lses = [], []
    for window, dilation in DILATED_PATTERNS:
        o, lse = dilated_window_attention(q, k, v, rel_bias, dilation, window // (2 * dilation))
        outs.append(o)
        lses.append(lse)
    w = jax.nn.softmax(jnp.stack(lses, 0), axis=0)
    return jnp.einsum('pbhs,pbhsd->bhsd', w, jnp.stack(outs, 0))

def apply_rope(x):
    s, d = x.shape[1], x.shape[-1]
    half = d // 2
    inv_freq = ROPE_THETA ** (-(jnp.arange(half, dtype=jnp.float32) / half))
    ang = jnp.arange(s, dtype=jnp.float32)[:, None] * inv_freq[None, :]
    cos, sin = jnp.cos(ang)[None, :, None, :], jnp.sin(ang)[None, :, None, :]
    x1, x2 = x[..., :half].astype(jnp.float32), x[..., half:].astype(jnp.float32)
    return jnp.concatenate([x1 * cos - x2 * sin, x1 * sin + x2 * cos], axis=-1).astype(x.dtype)

def mixer_mla(c_q, c_kv, k_rope, g_q_latent, w_q_up, g_kv_latent, w_kv_up):
    b, s, _ = c_q.shape
    q = (rmsnorm(c_q, g_q_latent) @ w_q_up).reshape(b, s, B_HEADS, B_QK_NOPE + B_QK_ROPE)
    q_nope, q_rope = q[..., :B_QK_NOPE], apply_rope(q[..., B_QK_NOPE:])
    kv = (rmsnorm(c_kv, g_kv_latent) @ w_kv_up).reshape(b, s, B_HEADS, B_QK_NOPE + B_V_DIM)
    k_nope, v = kv[..., :B_QK_NOPE], kv[..., B_QK_NOPE:].astype(jnp.float32)
    k_r = apply_rope(k_rope[:, :, None, :])[:, :, 0]
    scale = (B_QK_NOPE + B_QK_ROPE) ** -0.5
    nb = s // B_Q_BLOCK

    def block(args):
        qn, qr = args
        sc = (jnp.einsum('bqhd,bkhd->bhqk', qn, k_nope, preferred_element_type=jnp.float32)
              + jnp.einsum('bqhd,bkd->bhqk', qr, k_r, preferred_element_type=jnp.float32)) * scale
        p = jax.nn.softmax(sc, axis=-1)
        return jnp.einsum('bhqk,bkhd->bqhd', p, v)

    qn_b = q_nope.reshape(b, nb, B_Q_BLOCK, B_HEADS, B_QK_NOPE).transpose(1, 0, 2, 3, 4)
    qr_b = q_rope.reshape(b, nb, B_Q_BLOCK, B_HEADS, B_QK_ROPE).transpose(1, 0, 2, 3, 4)
    o = lax.map(block, (qn_b, qr_b))
    return o.transpose(1, 0, 2, 3, 4).reshape(b, s, B_WIDTH)

def hierarchical_moe(t, w_router_group, b_router_group, w_router_expert, b_router_expert,
                     w_gate, w_up, w_down):
    n_tok, d = t.shape
    group_logits = jnp.dot(t, w_router_group, preferred_element_type=jnp.float32) + b_router_group.astype(jnp.float32)
    group_probs = jax.nn.softmax(group_logits, axis=-1)
    group_idx = jnp.argmax(group_probs, axis=-1)
    group_gate = jnp.take_along_axis(group_probs, group_idx[:, None], axis=-1)
    expert_logits = (jnp.dot(t, w_router_expert, preferred_element_type=jnp.float32)
                     + b_router_expert.astype(jnp.float32)).reshape(n_tok, N_GROUPS, EXPERTS_PER_GROUP)
    in_group = jnp.take_along_axis(expert_logits, group_idx[:, None, None], axis=1)[:, 0]
    top_p, top_i = lax.top_k(jax.nn.softmax(in_group, axis=-1), TOP_K_IN_GROUP)
    gates = group_gate * top_p / jnp.sum(top_p, axis=-1, keepdims=True)
    expert_ids = group_idx[:, None] * EXPERTS_PER_GROUP + top_i

    n_assign = n_tok * TOP_K_IN_GROUP
    flat_expert = expert_ids.reshape(-1)
    flat_token = jnp.repeat(jnp.arange(n_tok), TOP_K_IN_GROUP)
    flat_gate = gates.reshape(-1)
    order = jnp.argsort(flat_expert)
    s_expert, s_token, s_gate = flat_expert[order], flat_token[order], flat_gate[order]
    counts = jnp.bincount(flat_expert, length=N_EXPERTS)
    starts = jnp.cumsum(counts) - counts
    padded = (counts + MOE_BLOCK - 1) // MOE_BLOCK * MOE_BLOCK
    padded_ends = jnp.cumsum(padded)
    padded_starts = padded_ends - padded
    dest = padded_starts[s_expert] + jnp.arange(n_assign) - starts[s_expert]
    n_blocks = -(-n_assign // MOE_BLOCK) + N_EXPERTS
    buf = jnp.zeros((n_blocks * MOE_BLOCK, d), t.dtype).at[dest].set(t[s_token])
    block_expert = jnp.minimum(
        jnp.searchsorted(padded_ends, jnp.arange(n_blocks) * MOE_BLOCK, side='right'), N_EXPERTS - 1)

    def expert_block(args):
        xb, e = args
        hb = jax.nn.silu(xb @ w_gate[e]) * (xb @ w_up[e])
        return hb @ w_down[e]

    out = lax.map(expert_block, (buf.reshape(n_blocks, MOE_BLOCK, d), block_expert))
    contrib = out.reshape(n_blocks * MOE_BLOCK, d)[dest].astype(jnp.float32) * s_gate[:, None]
    return jax.ops.segment_sum(contrib, s_token, num_segments=n_tok)

def first_inputs(seed: int = 0) -> dict:
    key = jax.random.key(seed)
    ks = jax.random.split(key, 24)
    f32 = jnp.float32
    nrm = lambda k, shape, fan_in: jax.random.normal(k, shape, f32) * (fan_in ** -0.5)
    gain = lambda k, shape: 1.0 + 0.02 * jax.random.normal(k, shape, f32)
    return {
        "x": jax.random.normal(ks[0], (BATCH, SEQ, D_MODEL), f32),
        "g_attn_norm": gain(ks[1], (DEPTH, D_MODEL)),
        "w_in": nrm(ks[2], (DEPTH, D_MODEL, IN_PROJ_WIDTH), D_MODEL),
        "rel_bias": 0.5 * jax.random.normal(ks[3], (REL_BUCKETS, A_HEADS), f32),
        "g_q_latent": gain(ks[4], (DEPTH, B_Q_LORA)),
        "w_q_up": nrm(ks[5], (DEPTH, B_Q_LORA, B_HEADS * (B_QK_NOPE + B_QK_ROPE)), B_Q_LORA),
        "g_kv_latent": gain(ks[6], (DEPTH, B_KV_LORA)),
        "w_kv_up": nrm(ks[7], (DEPTH, B_KV_LORA, B_HEADS * (B_QK_NOPE + B_V_DIM)), B_KV_LORA),
        "g_out_a": gain(ks[8], (DEPTH, A_WIDTH)),
        "g_out_b": gain(ks[9], (DEPTH, B_WIDTH)),
        "w_out": nrm(ks[10], (DEPTH, MIX_WIDTH, D_MODEL), MIX_WIDTH),
        "g_ffn_norm": gain(ks[11], (DEPTH, D_MODEL)),
        "w_router_group": nrm(ks[12], (DEPTH, D_MODEL, N_GROUPS), D_MODEL),
        "b_router_group": 0.01 * jax.random.normal(ks[13], (DEPTH, N_GROUPS), f32),
        "w_router_expert": nrm(ks[14], (DEPTH, D_MODEL, N_EXPERTS), D_MODEL),
        "b_router_expert": 0.01 * jax.random.normal(ks[15], (DEPTH, N_EXPERTS), f32),
        "w_gate": nrm(ks[16], (DEPTH, N_EXPERTS, D_MODEL, EXPERT_FF), D_MODEL),
        "w_up": nrm(ks[17], (DEPTH, N_EXPERTS, D_MODEL, EXPERT_FF), D_MODEL),
        "w_down": nrm(ks[18], (DEPTH, N_EXPERTS, EXPERT_FF, D_MODEL), EXPERT_FF),
        "g_final": gain(ks[19], (D_MODEL,)),
    }

def first_block(x, g_attn_norm, w_in, rel_bias, g_q_latent, w_q_up, g_kv_latent, w_kv_up,
              g_out_a, g_out_b, w_out, g_ffn_norm, w_router_group, b_router_group,
              w_router_expert, b_router_expert, w_gate, w_up, w_down, g_final):
    b, s, d = x.shape
    splits = list(np.cumsum([A_WIDTH, A_WIDTH, A_WIDTH, B_Q_LORA, B_KV_LORA]))
    for l in range(DEPTH):
        h = rmsnorm(x, g_attn_norm[l])
        proj = h @ w_in[l]
        q_a, k_a, v_a, c_q, c_kv, k_rope = jnp.split(proj, splits, axis=-1)
        heads = lambda t: t.reshape(b, s, A_HEADS, A_HEAD_DIM).transpose(0, 2, 1, 3)
        out_a = mixer_dilated(heads(q_a), heads(k_a), heads(v_a), rel_bias)
        out_a = out_a.transpose(0, 2, 1, 3).reshape(b, s, A_WIDTH)
        out_b = mixer_mla(c_q, c_kv, k_rope, g_q_latent[l], w_q_up[l], g_kv_latent[l], w_kv_up[l])
        mixed = jnp.concatenate([rmsnorm(out_a, g_out_a[l]), rmsnorm(out_b, g_out_b[l])], axis=-1)
        x = x + (mixed.astype(x.dtype) @ w_out[l])
        h2 = rmsnorm(x, g_ffn_norm[l]).reshape(b * s, d)
        y = hierarchical_moe(h2, w_router_group[l], b_router_group[l], w_router_expert[l],
                             b_router_expert[l], w_gate[l], w_up[l], w_down[l])
        x = x + y.reshape(b, s, d).astype(x.dtype)
    return rmsnorm(x, g_final)


DEPTH_2 = 2

N_EVEN = (DEPTH_2 + 1) // 2
N_ODD = DEPTH_2 // 2

RET_HEADS = 4
RET_DK = 64
RET_DV = 128
RET_CHUNK = 128
ROPE_BASE = 10000.0
SB_HEADS = 8
SB_DH = 64
SB_BLOCK = 128
HG_HEADS = 4
HG_DK = 128
HG_DV = 128
HG_CHUNK = 16
LRU_WIDTH = 512
LRU_BLOCKS = 8
LRU_BW = LRU_WIDTH // LRU_BLOCKS
CONV_W = 4
LRU_C = 8.0

RET_QK = RET_HEADS * RET_DK
RET_V = RET_HEADS * RET_DV
SB_W = SB_HEADS * SB_DH
EVEN_SIZES = (RET_QK, RET_QK, RET_V, RET_V, SB_W, SB_W, SB_W, SB_W)
EVEN_IN = sum(EVEN_SIZES)
EVEN_MIX = RET_V + SB_W
HG_KW = HG_HEADS * HG_DK
HG_VW = HG_HEADS * HG_DV
ODD_SIZES = (HG_KW, HG_KW, HG_VW, HG_VW, LRU_WIDTH, LRU_WIDTH)
ODD_IN = sum(ODD_SIZES)
ODD_MIX = HG_VW + LRU_WIDTH


def split_cols(a, sizes):
    idx = [int(v) for v in np.cumsum(sizes)[:-1]]
    return jnp.split(a, idx, axis=-1)

def rms_norm(x, w=None):
    xf = x.astype(jnp.float32)
    y = xf * lax.rsqrt(jnp.mean(xf * xf, axis=-1, keepdims=True) + EPS)
    if w is not None:
        y = y * w.astype(jnp.float32)
    return y

def rotary(x):
    S, D = x.shape[1], x.shape[-1]
    half = D // 2
    inv = ROPE_BASE ** (-jnp.arange(half, dtype=jnp.float32) / half)
    ang = jnp.arange(S, dtype=jnp.float32)[:, None] * inv[None, :]
    cos = jnp.cos(ang)[None, :, None, :]
    sin = jnp.sin(ang)[None, :, None, :]
    x1, x2 = x[..., :half], x[..., half:]
    return jnp.concatenate([x1 * cos - x2 * sin, x1 * sin + x2 * cos], axis=-1)

def retention(q, k, v):
    B, S, H, dk = q.shape
    dv = v.shape[-1]
    C = RET_CHUNK
    N = S // C
    f32 = jnp.float32
    log_g = jnp.log(1.0 - 2.0 ** (-5.0 - jnp.arange(H, dtype=f32)))
    q = rotary(q.astype(f32))
    k = rotary(k.astype(f32)) * (dk ** -0.5)
    v = v.astype(f32)
    to_chunks = lambda a: a.reshape(B, N, C, H, a.shape[-1]).transpose(0, 3, 1, 2, 4)
    qc, kc, vc = to_chunks(q), to_chunks(k), to_chunks(v)
    pos = jnp.arange(C, dtype=f32)
    dist = pos[:, None] - pos[None, :]
    decay = jnp.where(dist >= 0, jnp.exp(log_g[:, None, None] * jnp.maximum(dist, 0.0)), 0.0)
    scores = jnp.einsum('bhnid,bhnjd->bhnij', qc, kc) * decay[None, :, None]
    o_intra = jnp.einsum('bhnij,bhnje->bhnie', scores, vc)
    k_decay = jnp.exp(log_g[:, None] * (C - 1.0 - pos)[None, :])
    q_decay = jnp.exp(log_g[:, None] * (pos + 1.0)[None, :])
    chunk_kv = jnp.einsum('bhnjd,hj,bhnje->nbhde', kc, k_decay, vc)
    g_chunk = jnp.exp(log_g * C)[None, :, None, None]

    def step(state, kv):
        return state * g_chunk + kv, state

    _, r_prev = lax.scan(step, jnp.zeros((B, H, dk, dv), f32), chunk_kv)
    o_inter = jnp.einsum('bhnid,hi,nbhde->bhnie', qc, q_decay, r_prev)
    return (o_intra + o_inter).transpose(0, 2, 3, 1, 4).reshape(B, S, H, dv)

def stick_breaking(q, k, v):
    B, S, H, d = q.shape
    f32 = jnp.float32
    qf, kf, vf = q.astype(f32), k.astype(f32), v.astype(f32)
    scale = d ** -0.5
    outs = []
    for blk in range(S // SB_BLOCK):
        q0 = blk * SB_BLOCK
        kend = q0 + SB_BLOCK
        z = jnp.einsum('bthd,bshd->bhts', qf[:, q0:kend], kf[:, :kend]) * scale
        t_idx = q0 + jnp.arange(SB_BLOCK)[:, None]
        s_idx = jnp.arange(kend)[None, :]
        strict = s_idx < t_idx
        log_beta = jax.nn.log_sigmoid(z)
        log_one_minus = jnp.where(strict, jax.nn.log_sigmoid(-z), 0.0)
        suffix = lax.cumsum(log_one_minus, axis=3, reverse=True) - log_one_minus
        w = jnp.where(strict, jnp.exp(log_beta + suffix), 0.0)
        outs.append(jnp.einsum('bhts,bshd->bthd', w, vf[:, :kend]))
    return jnp.concatenate(outs, axis=1)

def hgrn2(q, f_logit, i, lb):
    B, S, H, dk = q.shape
    dv = i.shape[-1]
    C = HG_CHUNK
    N = S // C
    f32 = jnp.float32
    lb = lb.reshape(H, dk).astype(f32)
    f_logit = f_logit.astype(f32)
    log_f = jnp.logaddexp(jnp.log(lb), jnp.log1p(-lb) + jax.nn.log_sigmoid(f_logit))
    k = (1.0 - lb) * jax.nn.sigmoid(-f_logit)
    to_chunks = lambda a: a.reshape(B, N, C, H, a.shape[-1]).transpose(1, 0, 3, 2, 4)
    xs = (to_chunks(q.astype(f32)), to_chunks(k), to_chunks(log_f), to_chunks(i.astype(f32)))
    tril = jnp.tril(jnp.ones((C, C), dtype=bool))[:, :, None]

    def step(state, inp):
        qc, kc, lfc, vc = inp
        b = jnp.cumsum(lfc, axis=2)
        diff = b[:, :, :, None, :] - b[:, :, None, :, :]
        decay = jnp.exp(jnp.where(tril, diff, -jnp.inf))
        attn = jnp.einsum('bhtk,bhtsk,bhsk->bhts', qc, decay, kc)
        o = jnp.einsum('bhts,bhsv->bhtv', attn, vc) + jnp.einsum('bhtk,bhkv->bhtv', qc * jnp.exp(b), state)
        b_last = b[:, :, -1:, :]
        state = state * jnp.exp(b_last[:, :, 0, :, None]) + jnp.einsum('bhsk,bhsv->bhkv', kc * jnp.exp(b_last - b), vc)
        return state, o

    _, o = lax.scan(step, jnp.zeros((B, H, dk, dv), f32), xs)
    return o.transpose(1, 0, 3, 2, 4).reshape(B, S, H, dv)

def causal_conv(x, w, b):
    S = x.shape[1]
    xp = jnp.pad(x, ((0, 0), (CONV_W - 1, 0), (0, 0)))
    y = b[None, None, :] + xp[:, 0:S] * w[0]
    for j in range(1, CONV_W):
        y = y + xp[:, j:j + S] * w[j]
    return y

def rg_lru(x, w_a, b_a, w_x, b_x, lam):
    B, S, W = x.shape
    xb = x.reshape(B, S, LRU_BLOCKS, LRU_BW)
    r = jax.nn.sigmoid(jnp.einsum('bsni,nij->bsnj', xb, w_a).reshape(B, S, W) + b_a)
    ig = jax.nn.sigmoid(jnp.einsum('bsni,nij->bsnj', xb, w_x).reshape(B, S, W) + b_x)
    log_a = -LRU_C * r * jax.nn.softplus(-lam)
    a = jnp.exp(log_a)
    mult = jnp.sqrt(-jnp.expm1(2.0 * log_a))
    mult = jnp.where(jnp.arange(S)[None, :, None] == 0, 1.0, mult)
    u = mult * ig * x

    def combine(left, right):
        a1, b1 = left
        a2, b2 = right
        return a1 * a2, a2 * b1 + b2

    _, h = lax.associative_scan(combine, (a, u), axis=1)
    return h

def even_mixer(h, w_in, w_out):
    B, S, _ = h.shape
    proj = jnp.einsum('bsd,de->bse', h.astype(w_in.dtype), w_in).astype(jnp.float32)
    rq, rk, rv, rg, sq, sk, sv, sg = split_cols(proj, EVEN_SIZES)
    ret = retention(rq.reshape(B, S, RET_HEADS, RET_DK), rk.reshape(B, S, RET_HEADS, RET_DK),
                    rv.reshape(B, S, RET_HEADS, RET_DV))
    ret = rms_norm(ret).reshape(B, S, RET_V) * jax.nn.silu(rg)
    sb = stick_breaking(sq.reshape(B, S, SB_HEADS, SB_DH), sk.reshape(B, S, SB_HEADS, SB_DH),
                        sv.reshape(B, S, SB_HEADS, SB_DH))
    sb = sb.reshape(B, S, SB_W) * jax.nn.silu(sg)
    mix = jnp.concatenate([ret, sb], axis=-1)
    return jnp.einsum('bse,ed->bsd', mix.astype(w_out.dtype), w_out)

def odd_mixer(h, w_in, w_out, lb, conv_w, conv_b, w_a, b_a, w_x, b_x, lam):
    B, S, _ = h.shape
    f32 = jnp.float32
    proj = jnp.einsum('bsd,de->bse', h.astype(w_in.dtype), w_in).astype(f32)
    hq, hf, hi, hg, lx, lg = split_cols(proj, ODD_SIZES)
    hc = hgrn2(hq.reshape(B, S, HG_HEADS, HG_DK), hf.reshape(B, S, HG_HEADS, HG_DK),
               hi.reshape(B, S, HG_HEADS, HG_DV), lb)
    hc = rms_norm(hc).reshape(B, S, HG_VW) * jax.nn.silu(hg)
    xc = causal_conv(lx, conv_w.astype(f32), conv_b.astype(f32))
    hl = rg_lru(xc, w_a.astype(f32), b_a.astype(f32), w_x.astype(f32), b_x.astype(f32), lam.astype(f32))
    hl = hl * jax.nn.silu(lg)
    mix = jnp.concatenate([hc, hl], axis=-1)
    return jnp.einsum('bse,ed->bsd', mix.astype(w_out.dtype), w_out)

def second_inputs(seed: int = 0) -> dict:
    key = jax.random.key(seed)
    ks = jax.random.split(key, 16)
    f32 = jnp.float32
    nrm = lambda k, shape, s: jax.random.normal(k, shape, f32) * s
    u = jax.random.uniform(ks[15], (N_ODD, LRU_WIDTH), f32, 0.9, 0.999)
    a0 = u ** (1.0 / LRU_C)
    return {
        'x': nrm(ks[0], (BATCH, SEQ, D_MODEL), 1.0),
        'pre_norm_w': 1.0 + nrm(ks[1], (DEPTH_2, D_MODEL), 0.02),
        'post_norm_w': 1.0 + nrm(ks[2], (DEPTH_2, D_MODEL), 0.02),
        'even_w_in': nrm(ks[3], (N_EVEN, D_MODEL, EVEN_IN), D_MODEL ** -0.5),
        'even_w_out': nrm(ks[4], (N_EVEN, EVEN_MIX, D_MODEL), EVEN_MIX ** -0.5),
        'odd_w_in': nrm(ks[5], (N_ODD, D_MODEL, ODD_IN), D_MODEL ** -0.5),
        'odd_w_out': nrm(ks[6], (N_ODD, ODD_MIX, D_MODEL), ODD_MIX ** -0.5),
        'hgrn_lb_logits': nrm(ks[7], (N_ODD, HG_KW), 1.0),
        'conv_w': nrm(ks[8], (N_ODD, CONV_W, LRU_WIDTH), CONV_W ** -0.5),
        'conv_b': nrm(ks[9], (N_ODD, LRU_WIDTH), 0.01),
        'lru_w_a': nrm(ks[10], (N_ODD, LRU_BLOCKS, LRU_BW, LRU_BW), LRU_BW ** -0.5),
        'lru_b_a': nrm(ks[11], (N_ODD, LRU_WIDTH), 0.01),
        'lru_w_x': nrm(ks[12], (N_ODD, LRU_BLOCKS, LRU_BW, LRU_BW), LRU_BW ** -0.5),
        'lru_b_x': nrm(ks[13], (N_ODD, LRU_WIDTH), 0.01),
        'lru_lambda': jnp.log(a0) - jnp.log1p(-a0),
    }

def second_block(x, pre_norm_w, post_norm_w, even_w_in, even_w_out, odd_w_in, odd_w_out,
              hgrn_lb_logits, conv_w, conv_b, lru_w_a, lru_b_a, lru_w_x, lru_b_x, lru_lambda):
    cum = jnp.cumsum(jax.nn.softmax(hgrn_lb_logits.astype(jnp.float32), axis=0), axis=0)
    lower_bounds = cum - cum[0:1]
    for layer in range(DEPTH_2):
        h = rms_norm(x, pre_norm_w[layer])
        if layer % 2 == 0:
            e = layer // 2
            y = even_mixer(h, even_w_in[e], even_w_out[e])
        else:
            o = layer // 2
            y = odd_mixer(h, odd_w_in[o], odd_w_out[o], lower_bounds[o], conv_w[o], conv_b[o],
                          lru_w_a[o], lru_b_a[o], lru_w_x[o], lru_b_x[o], lru_lambda[o])
        x = x + rms_norm(y, post_norm_w[layer]).astype(x.dtype)
    return x


def setup_inputs(seed=0):
    out = dict(first_inputs(seed))
    for name, value in second_inputs(seed + 1).items():
        if name != "x":
            out[name + "_2"] = value
    return out


def reference(
    x, g_attn_norm, w_in, rel_bias, g_q_latent, w_q_up, g_kv_latent, w_kv_up, g_out_a, g_out_b,
    w_out, g_ffn_norm, w_router_group, b_router_group, w_router_expert, b_router_expert, w_gate,
    w_up, w_down, g_final, pre_norm_w_2, post_norm_w_2, even_w_in_2, even_w_out_2, odd_w_in_2,
    odd_w_out_2, hgrn_lb_logits_2, conv_w_2, conv_b_2, lru_w_a_2, lru_b_a_2, lru_w_x_2,
    lru_b_x_2, lru_lambda_2,
):
    x = first_block(
        x, g_attn_norm, w_in, rel_bias, g_q_latent, w_q_up, g_kv_latent, w_kv_up, g_out_a,
        g_out_b, w_out, g_ffn_norm, w_router_group, b_router_group, w_router_expert,
        b_router_expert, w_gate, w_up, w_down, g_final,
    )
    return second_block(
        x, pre_norm_w_2, post_norm_w_2, even_w_in_2, even_w_out_2, odd_w_in_2, odd_w_out_2,
        hgrn_lb_logits_2, conv_w_2, conv_b_2, lru_w_a_2, lru_b_a_2, lru_w_x_2, lru_b_x_2,
        lru_lambda_2,
    )


_drawn_inputs = setup_inputs


def setup_inputs(seed=0):
    import zlib

    import numpy as np

    out = dict(_drawn_inputs(seed))
    spreads = {}
    factors = {'b_router_group': 4.819,
     'b_router_expert': 5.334,
     'conv_b_2': 3.436,
     'lru_b_a_2': 61.721,
     'lru_b_x_2': 33.888,
     'post_norm_w_2': 2.67}
    for name, (base, spread) in spreads.items():
        noise = np.random.default_rng([zlib.crc32(name.encode()), seed]).standard_normal(out[name].shape)
        drawn = base * np.exp(spread * noise) if base else spread * noise
        out[name] = __import__('jax').numpy.asarray(drawn.astype(out[name].dtype))
    for name, factor in factors.items():
        out[name] = (out[name] * factor).astype(out[name].dtype)
    return out
```

```python
import math
from contextlib import ExitStack, contextmanager

import numpy as np
import concourse.bass as bass
from concourse import mybir

F32 = mybir.dt.float32
U32 = mybir.dt.uint32
ALU = mybir.AluOpType
ACT = mybir.ActivationFunctionType
AX = mybir.AxisListType

P = 128
D = 1024
S = 1024
NT = S // P
BANK = 512
EPS = 1e-6
NEG = -1e30


class Stage:

    def __init__(self, nc):
        self.nc, self.ctx, self.sems = nc, ExitStack(), []

    def sb(self, name, shape, dt=F32):
        return self.ctx.enter_context(self.nc.sbuf_tensor(name, shape, dt))

    def ps(self, name, shape, dt=F32):
        return self.ctx.enter_context(self.nc.psum_tensor(name, shape, dt))

    def sem(self, name):
        s = self.nc.alloc_semaphore(name)
        self.sems.append(s)
        return s


@contextmanager
def stage(nc):
    st = Stage(nc)
    yield st
    nc.clear_and_free_semaphores(st.sems)
    nc.all_engine_barrier()
    st.ctx.close()


def tiled(ap):
    return ap.rearrange("(k p) n -> p k n", p=P)


def rows(ap, t):
    return ap[bass.ds(t * P, P), :]


def along(eng, count, step, body):
    if count == step:
        for i in range(count):
            body(i, i)
        return
    with eng.Fori(0, count // step) as r:
        for u in range(step):
            body(r * step + u, u)



def project(nc, name, hT, nk, segs):

    def groups(seg):
        return NT if seg["kind"] == "row" else 2 * max(1, seg["width"] // P)

    def chunks(eng, emit):
        g, loaded, uses = 0, [0, 0], [0] * NT
        for seg in segs:
            nd, G, n = seg.get("nd", 1), groups(seg), seg["n"]
            pairs = n // 2 if n >= 4 else 0
            if pairs:
                with eng.Fori(0, pairs) as r:
                    for u in range(2):
                        slot = (g + u) % 2
                        emit(seg, r * 2 + u, r * 2 + (g + u), slot,
                             r * (16 * nd) + (loaded[slot] + 16 * nd), [r * 2 + (uses[j] + u) for j in range(G)])
                g += 2 * pairs
                loaded = [v + 16 * nd * pairs for v in loaded]
                uses = [v + 2 * pairs * (j < G) for j, v in enumerate(uses)]
            for i in range(2 * pairs, n):
                slot = g % 2
                loaded[slot] += 16 * nd
                emit(seg, i, g, slot, loaded[slot], uses[:G])
                g += 1
                uses = [v + (j < G) for j, v in enumerate(uses)]
        return uses

    with stage(nc) as st:
        wbuf = st.sb(name + "_w", [P, 2, nk, BANK])
        obuf = st.sb(name + "_o", [P, NT, BANK])
        acc = [st.ps(f"{name}_acc{j}", [P, BANK]) for j in range(NT)]
        w_in = [st.sem(f"{name}_w_in{s}") for s in range(2)]
        w_used = st.sem(name + "_w_used")
        mm_done = [st.sem(f"{name}_mm{j}") for j in range(NT)]
        copied = [st.sem(f"{name}_copied{j}") for j in range(NT)]
        stored = [st.sem(f"{name}_stored{j}") for j in range(NT)]

        def size(seg):
            return (P, seg["width"]) if seg["kind"] == "row" else (min(P, seg["width"]), BANK)

        with nc.Block() as block:
            @block.sync
            def _(sp):
                def emit(seg, i, g, slot, loaded, uses):
                    sp.wait_ge(w_used, g + 1)
                    for dst, src in seg["load"](i):
                        sp.dma_start(wbuf[:, slot, :, dst], src).then_inc(w_in[slot], 16)
                chunks(sp, emit)

            @block.tensor
            def _(pe):
                pe.sem_inc(w_used, 2)

                def emit(seg, i, g, slot, loaded, uses):
                    pe.wait_ge(w_in[slot], loaded)
                    m, n = size(seg)
                    G = groups(seg)
                    for j in range(G):
                        pe.wait_ge(copied[j], uses[j] + 1)
                        for k in range(nk):
                            if seg["kind"] == "row":
                                a, b = hT[:, k, j * P:(j + 1) * P], wbuf[:, slot, k, 0:n]
                            else:
                                a = wbuf[:, slot, k, (j // 2) * P:(j // 2) * P + m]
                                b = hT[:, k, (j % 2) * BANK:(j % 2 + 1) * BANK]
                            mm = pe.matmul(acc[j][0:m, 0:n], a, b, start=(k == 0), stop=(k == nk - 1))
                        mm.then_inc(mm_done[j], 1)
                    pe.wait_ge(mm_done[G - 1], uses[G - 1] + 1)
                    pe.sem_inc(w_used, 1)
                chunks(pe, emit)

            @block.scalar
            def _(act):
                for j in range(NT):
                    act.sem_inc(stored[j], 16)
                for j in range(0, NT, 2):
                    act.sem_inc(copied[j], 1)

                def emit(seg, i, g, slot, loaded, uses):
                    m, n = size(seg)
                    for j in range(groups(seg)):
                        if j % 2 == 0:
                            act.wait_ge(mm_done[j], uses[j] + 1)
                            act.wait_ge(stored[j], uses[j] * 16 + 16)
                            act.activation(obuf[0:m, j, 0:n], acc[j][0:m, 0:n], ACT.Copy).then_inc(copied[j], 1)
                        act.wait_ge(copied[j], uses[j] + 2)
                        act.dma_start(seg["dst"](i, j), obuf[0:m, j, 0:n]).then_inc(stored[j], 16)
                uses = chunks(act, emit)
                for j in range(NT):
                    act.wait_ge(stored[j], 16 * uses[j] + 16)

            @block.vector
            def _(dve):
                for j in range(1, NT, 2):
                    dve.sem_inc(copied[j], 1)

                def emit(seg, i, g, slot, loaded, uses):
                    m, n = size(seg)
                    for j in range(1, groups(seg), 2):
                        dve.wait_ge(mm_done[j], uses[j] + 1)
                        dve.wait_ge(stored[j], uses[j] * 16 + 16)
                        dve.tensor_copy(obuf[0:m, j, 0:n], acc[j][0:m, 0:n]).then_inc(copied[j], 1)
                chunks(dve, emit)


def columns(w, c0, width):
    v = tiled(w)
    return lambda i: [(slice(0, width), v[:, :, bass.ds(i * width + c0, width)])]


def to_rows(dst, c0, width):
    return lambda i, j: dst[j * P:(j + 1) * P, bass.ds(i * width + c0, width)]


def to_T(dst, r0, width):
    m = min(P, width)
    return lambda i, j: dst[bass.ds(i * width + (r0 + (j // 2) * P), m), (j % 2) * BANK:(j % 2 + 1) * BANK]



def norm_rows(nc, name, ident, width, loads, groups, hT=None, gain=None, add=None, post=None, gate=None,
              keep=None, keep_normed=None, row_gain=None):
    nk = width // P
    nl = len(loads) + (add is not None) + len(gate or [])
    ng = len(groups)
    with stage(nc) as st:
        x = st.sb(name + "_x", [P, 2, width])
        junk = st.sb(name + "_junk", [P, 2, width])
        y = st.sb(name + "_y", [P, 2, width])
        a = st.sb(name + "_a", [P, 2, width]) if add is not None else None
        a2 = st.sb(name + "_a2", [P, 2, width]) if post is not None else None
        x2 = st.sb(name + "_x2", [P, 2, width]) if add is not None else x
        gt = st.sb(name + "_gt", [P, 2, width]) if gate is not None else None
        sg = st.sb(name + "_sg", [P, 2, width]) if gate is not None else None
        y2 = st.sb(name + "_y2", [P, 2, width]) if gate is not None else y
        ss = st.sb(name + "_ss", [P, 2, 8])
        ms = st.sb(name + "_ms", [P, 2, 8])
        rt = st.sb(name + "_rt", [P, 2, 8])
        rs = st.sb(name + "_rs", [P, 2, 8])
        gcol = st.sb(name + "_gcol", [P, 8])
        prow = st.sb(name + "_prow", [P, width]) if post is not None else None
        tp = [st.ps(f"{name}_tp{s}", [P, 2 * BANK]) for s in range(2)]
        consts_in = st.sem(name + "_consts_in")
        tile_in = [st.sem(f"{name}_tile_in{s}") for s in range(2)]
        x_free = st.sem(name + "_x_free")
        add_sq, add_ms, add_rt, add_rs, add_scaled = (st.sem(name + n) for n in ("_asq", "_ams", "_art", "_ars", "_ascaled"))
        x_ready, sq, msr, rtr, rsr, normed, gated, sig, g2 = (
            st.sem(name + n) for n in ("_x_ready", "_sq", "_ms_ready", "_rt_ready", "_rs_ready", "_normed", "_gated", "_sig", "_g2"))
        turned, copied = st.sem(name + "_turned"), st.sem(name + "_copied")
        kept = [st.sem(f"{name}_kept{s}") for s in range(2)]
        nconst = (gain is not None) + (post is not None)
        n_keep = (keep is not None) + (keep_normed is not None)
        out_sem = gated if gate is not None else normed
        n_out = 1 if gate is not None else ng + (len(pass_cols(groups, width)) > 0)

        with nc.Block() as block:
            @block.sync
            def _(sp):
                if gain is not None:
                    for dst, src in gain(gcol):
                        sp.dma_start(dst, src, allow_slow_non_contiguous=True).then_inc(consts_in, 16)
                if post is not None:
                    sp.dma_start(prow[:, :], post.partition_broadcast(P)).then_inc(consts_in, 16)

                def tile(t, u):
                    sp.wait_ge(x_free, t + 1)
                    if n_keep:
                        sp.wait_ge(kept[u], (t - u) * (8 * n_keep) + 16 * n_keep)
                    for c0, w, src in loads:
                        sp.dma_start(x[:, u, c0:c0 + w], src(t)).then_inc(tile_in[u], 16)
                    if add is not None:
                        sp.dma_start(a[:, u, :], rows(add, t)).then_inc(tile_in[u], 16)
                    for c0, w, src in gate or []:
                        sp.dma_start(gt[:, u, c0:c0 + w], src(t)).then_inc(tile_in[u], 16)
                along(sp, NT, 2, tile)

            @block.scalar
            def _(act):
                if n_keep:
                    act.sem_inc(kept[0], 16 * n_keep)
                    act.sem_inc(kept[1], 16 * n_keep)

                def tile(t, u):
                    act.wait_ge(tile_in[u], (t - u) * (8 * nl) + 16 * nl)
                    if post is not None:
                        act.activation(junk[:, u, :], a[:, u, :], ACT.Square, accum_out=ss[:, u, 7:8]).then_inc(add_sq, 1)
                        act.wait_ge(add_ms, t + 1)
                        act.activation(rt[:, u, 7:8], ms[:, u, 7:8], ACT.Sqrt).then_inc(add_rt, 1)
                        act.wait_ge(add_rt, t + 1)
                    if gate is not None:
                        act.activation(sg[:, u, :], gt[:, u, :], ACT.Sigmoid).then_inc(sig, 1)
                    if add is not None:
                        act.wait_ge(x_ready, t + 1)
                    if keep is not None:
                        act.dma_start(rows(keep, t), x2[:, u, :]).then_inc(kept[u], 16)
                    for n, (c0, w) in enumerate(groups):
                        act.activation(junk[:, u, c0:c0 + w], x2[:, u, c0:c0 + w], ACT.Square,
                                       accum_out=ss[:, u, n:n + 1]).then_inc(sq, 1)
                    if ng:
                        act.wait_ge(msr, (t + 1) * len({w for _, w in groups}))
                        act.activation(rt[:, u, 0:ng], ms[:, u, 0:ng], ACT.Sqrt).then_inc(rtr, 1)
                    if keep_normed is not None:
                        act.wait_ge(normed, (t + 1) * n_out)
                        act.dma_start(rows(keep_normed, t), y[:, u, :]).then_inc(kept[u], 16)
                along(act, NT, 2, tile)
                if n_keep:
                    for u in range(2):
                        act.wait_ge(kept[u], 16 * n_keep * (NT // 2 + 1))

            @block.vector
            def _(dve):
                dve.sem_inc(x_free, 2)
                dve.sem_inc(copied, 2)
                if nconst:
                    dve.wait_ge(consts_in, 16 * (len(gain(gcol)) if gain is not None else 0) + 16 * (post is not None))

                def tile(t, u):
                    dve.wait_ge(tile_in[u], (t - u) * (8 * nl) + 16 * nl)
                    if post is not None:
                        dve.wait_ge(add_sq, t + 1)
                        dve.tensor_scalar(ms[:, u, 7:8], ss[:, u, 7:8], 1.0 / width, EPS, ALU.mult, ALU.add).then_inc(add_ms, 1)
                        dve.wait_ge(add_rt, t + 1)
                        dve.reciprocal(rs[:, u, 7:8], rt[:, u, 7:8]).then_inc(add_rs, 1)
                        dve.wait_ge(add_rs, t + 1)
                        dve.scalar_tensor_tensor(out=(a2 if loads else x2)[:, u, :], in0=a[:, u, :], scalar=rs[:, u, 7:8],
                                                 in1=prow[:, :], op0=ALU.mult, op1=ALU.mult
                                                 ).then_inc(add_scaled if loads else x_ready, 1)
                        if loads:
                            dve.wait_ge(add_scaled, t + 1)
                            dve.tensor_tensor(x2[:, u, :], x[:, u, :], a2[:, u, :], ALU.add).then_inc(x_ready, 1)
                    elif add is not None:
                        dve.tensor_tensor(x2[:, u, :], x[:, u, :], a[:, u, :], ALU.add).then_inc(x_ready, 1)
                    if gate is not None:
                        dve.wait_ge(sig, t + 1)
                        dve.tensor_tensor(sg[:, u, :], sg[:, u, :], gt[:, u, :], ALU.mult).then_inc(g2, 1)
                    if ng:
                        dve.wait_ge(sq, (t + 1) * ng)
                        sizes = sorted({w for _, w in groups}, reverse=True)
                        for w in sizes:
                            idx = [n for n, g in enumerate(groups) if g[1] == w]
                            dve.tensor_scalar(ms[:, u, idx[0]:idx[-1] + 1], ss[:, u, idx[0]:idx[-1] + 1], 1.0 / w, EPS,
                                              ALU.mult, ALU.add).then_inc(msr, 1)
                        dve.wait_ge(rtr, t + 1)
                        dve.reciprocal(rs[:, u, 0:ng], rt[:, u, 0:ng]).then_inc(rsr, 1)
                        dve.wait_ge(rsr, t + 1)
                    if hT is not None:
                        dve.wait_ge(turned, t + 1)
                    for n, (c0, w) in enumerate(groups):
                        dve.tensor_scalar(y[:, u, c0:c0 + w], x2[:, u, c0:c0 + w], rs[:, u, n:n + 1], None,
                                          ALU.mult).then_inc(normed, 1)
                    for c0, w in pass_cols(groups, width)[:1] if (hT is not None) else []:
                        dve.tensor_copy(y[:, u, c0:c0 + w], x2[:, u, c0:c0 + w]).then_inc(normed, 1)
                    if gate is not None:
                        dve.wait_ge(normed, (t + 1) * (ng + (len(pass_cols(groups, width)) > 0)))
                        dve.wait_ge(g2, t + 1)
                        dve.tensor_tensor(y2[:, u, :], y[:, u, :], sg[:, u, :], ALU.mult).then_inc(gated, 1)
                        dve.wait_ge(gated, t + 1)
                    elif hT is not None:
                        dve.wait_ge(normed, (t + 1) * n_out)
                    else:
                        dve.wait_ge(x_ready, t + 1)
                    dve.sem_inc(x_free, 1)
                    if hT is not None:
                        dve.wait_ge(turned, t + 3)
                        src = tp[u][:, 0:width].rearrange("p (k n) -> p k n", k=nk)
                        dst = hT[:, 0:nk, bass.ds(t * P, P)]
                        if gain is not None:
                            dve.tensor_tensor(dst, src, gcol[:, 0:nk].unsqueeze(2).to_broadcast([P, nk, P]),
                                              ALU.mult).then_inc(copied, 1)
                        else:
                            dve.tensor_copy(dst, src).then_inc(copied, 1)
                along(dve, NT, 2, tile)

            if hT is not None:
                @block.tensor
                def _(pe):
                    pe.sem_inc(turned, 2)

                    def tile(t, u):
                        pe.wait_ge(out_sem, (t + 1) * n_out)
                        pe.wait_ge(copied, t + 1)
                        for k in range(nk):
                            mm = pe.transpose(tp[u][:, k * P:(k + 1) * P], y2[:, u, k * P:(k + 1) * P], ident[:, :])
                        mm.then_inc(turned, 1)
                    along(pe, NT, 2, tile)


def pass_cols(groups, width):
    end = max([c0 + w for c0, w in groups], default=0)
    return [(end, width - end)] if end < width else []


def gain_of(parts):
    def loads(gcol):
        out, k = [], 0
        for v in parts:
            n = v.shape[0] // P
            out.append((gcol[:, k:k + n], v.rearrange("(k p) -> p k", p=P)))
            k += n
        return out
    return loads



def bias_table(nc, rel_bias, onehot, log_count, table):
    W = 2 * S
    with stage(nc) as st:
        oh = st.sb("bt_oh", [32, W])
        rb = st.sb("bt_rb", [32, 8])
        lc = st.sb("bt_lc", [8, W])
        out = st.sb("bt_out", [8, W])
        out8 = st.sb("bt_out8", [8, W])
        ps = st.ps("bt_ps", [P, W])
        consts_in, mm, added, scaled, stored = (st.sem("bt_" + n) for n in ("in", "mm", "added", "scaled", "stored"))
        with nc.Block() as block:
            @block.sync
            def _(sp):
                sp.dma_start(oh[:, :], onehot).then_inc(consts_in, 16)
                sp.dma_start(rb[:, :], rel_bias).then_inc(consts_in, 16)
                sp.dma_start(lc[:, :], log_count.partition_broadcast(8)).then_inc(consts_in, 16)
                sp.wait_ge(scaled, 1)
                sp.dma_start(table, out8[:, :]).then_inc(stored, 16)
                sp.wait_ge(stored, 16)

            @block.tensor
            def _(pe):
                pe.wait_ge(consts_in, 48)
                for c in range(W // BANK):
                    m = pe.matmul(ps[0:8, c * BANK:(c + 1) * BANK], rb[:, :], oh[:, c * BANK:(c + 1) * BANK],
                                  start=True, stop=True)
                m.then_inc(mm, 1)

            @block.vector
            def _(dve):
                dve.wait_ge(consts_in, 48)
                dve.wait_ge(mm, 1)
                dve.tensor_tensor(out[:, :], ps[0:8, :], lc[:, :], ALU.add).then_inc(added, 1)
                dve.wait_ge(added, 1)
                dve.tensor_scalar(out8[:, :], out[:, :], 8.0, None, ALU.mult).then_inc(scaled, 1)


def softmax_attention(nc, name, ident, heads, K, DV, scale, loads, v_src, out, table=None):
    nl = len(loads) + 1 + (table is not None)
    WB = 2 * S - P
    T8 = NT

    with stage(nc) as st:
        qT = st.sb(name + "_qT", [K, 2, S])
        kT = st.sb(name + "_kT", [K, 2, S])
        v = st.sb(name + "_v", [P, 2, NT, DV])
        wb = st.sb(name + "_wb", [P, 2, WB]) if table is not None else None
        sc = st.sb(name + "_sc", [P, 2, S]) if table is not None else None
        p = st.sb(name + "_p", [P, 2, S])
        pT = st.sb(name + "_pT", [P, 2, S])
        mx, nm, rs, ri = (st.sb(name + n, [P, 16]) for n in ("_mx", "_nm", "_rs", "_ri"))
        o = st.sb(name + "_ob", [P, 2, NT, DV])
        sps = [st.ps(f"{name}_s{s}", [P, S]) for s in range(2)]
        tps = st.ps(name + "_t", [P, S])
        ops = [st.ps(f"{name}_op{s}", [P, BANK]) for s in range(2)]
        head_in = [st.sem(f"{name}_head_in{s}") for s in range(2)]
        s_done, s_free, max_done, nm_done, p_done = (st.sem(name + n) for n in ("_s_done", "_s_free", "_max", "_nm_done", "_p_done"))
        turned_a, turned_b, pT_a, pT_b = (st.sem(name + n) for n in ("_turned_a", "_turned_b", "_pT_a", "_pT_b"))
        pv_done, ri_done, o_done = (st.sem(name + n) for n in ("_pv_done", "_ri_done", "_o_done"))
        passed = st.sem(name + "_passed")
        stored = [st.sem(f"{name}_stored{s}") for s in range(2)]

        def steps(eng, body):
            with eng.Fori(0, heads // 2) as r:
                for l in range(2 * T8 + 2):
                    body(l, r)

        H = T8 // 2 * P

        with nc.Block() as block:
            @block.sync
            def _(sp):
                def load(h, u):
                    for buf, p0, n, src in loads:
                        dst = (qT, kT)[buf]
                        sp.dma_start(dst[p0:p0 + n, u, :], src(h)).then_inc(head_in[u], 16)
                    sp.dma_start(v[:, u, :, :], v_src(h)).then_inc(head_in[u], 16)
                    if table is not None:
                        src = bass.AP(table.tensor, h * (2 * S), [[1, P], [1, WB]])
                        sp.dma_start(wb[:, u, :], src).then_inc(head_in[u], 16)

                def store(h, u):
                    sp.wait_ge(o_done, h * T8 + (T8 + 2))
                    sp.dma_start(out[:, bass.ds(h * DV, DV)].rearrange("(t p) d -> p t d", p=P),
                                 o[:, u, :, :]).then_inc(stored[u], 16)

                sp.sem_inc(stored[0], 16)
                sp.sem_inc(stored[1], 16)
                for u in range(2):
                    load(u, u)
                with sp.Fori(0, heads // 2 - 1) as r:
                    for u in range(2):
                        h = r * 2 + u
                        store(h, u)
                        sp.wait_ge(pv_done, h * T8 + (T8 + 16))
                        load(h + 2, u)
                for u in range(2):
                    store(heads - 2 + u, u)
                for u in range(2):
                    sp.wait_ge(stored[u], 16 * (heads // 2 + 1))

            @block.tensor
            def _(pe):
                pe.sem_inc(turned_a, 2)
                pe.sem_inc(turned_b, 2)
                pe.sem_inc(pv_done, 16)

                def body(l, r):
                    T = r * 16 + l
                    if l < 16:
                        u, i = l // T8, l % T8
                        if i == 0:
                            pe.wait_ge(head_in[u], r * (16 * nl) + 16 * nl)
                        pe.wait_ge(s_free, T + 1)
                        for c in range(2):
                            mm = pe.matmul(sps[l % 2][:, c * BANK:(c + 1) * BANK], qT[:, u, i * P:(i + 1) * P],
                                           kT[:, u, c * BANK:(c + 1) * BANK], start=True, stop=True)
                        mm.then_inc(s_done, 1)
                    m = l - 1
                    if 0 <= m < 16:
                        pe.wait_ge(p_done, T + 2)
                        pe.wait_ge(pT_a, T)
                        for k in range(NT):
                            if k == NT // 2:
                                pe.wait_ge(pT_b, T)
                            mm = pe.transpose(tps[:, k * P:(k + 1) * P], p[:, m % 2, k * P:(k + 1) * P], ident[:, :])
                            if k == NT // 2 - 1:
                                mm.then_inc(turned_a, 1)
                        mm.then_inc(turned_b, 1)
                    m = l - 2
                    if 0 <= m < 16:
                        u, i = m // T8, m % T8
                        pe.wait_ge(o_done, T - 1)
                        pe.wait_ge(pT_a, T)
                        pe.wait_ge(pT_b, T)
                        for k in range(NT):
                            mm = pe.matmul(ops[m % 2][:, 0:DV], pT[:, m % 2, k * P:(k + 1) * P], v[:, u, k, :],
                                           start=(k == 0), stop=(k == NT - 1))
                        mm.then_inc(pv_done, 1)
                steps(pe, body)

            @block.vector
            def _(dve):
                if table is not None:
                    dve.sem_inc(s_free, 2)
                dve.sem_inc(pT_a, 1)
                dve.sem_inc(o_done, 2)

                def body(l, r):
                    T = r * 16 + l
                    if l < 16:
                        u, i = l // T8, l % T8
                        dve.wait_ge(s_done, T + 1)
                        if table is not None:
                            if i == 0:
                                dve.wait_ge(head_in[u], r * (16 * nl) + 16 * nl)
                            dve.wait_ge(p_done, T + 1)
                            dve.sem_inc(passed, 1)
                            dve.tensor_tensor_reduce(out=sc[:, l % 2, :], in0=sps[l % 2][:, :], in1=wb[:, u, i * P:i * P + S][:, ::-1],
                                                     scale=1.0, scalar=-3e38, op0=ALU.add, op1=ALU.max,
                                                     accum_out=mx[:, l:l + 1]).then_inc(s_free, 1)
                            dve.wait_ge(s_free, T + 3)
                        else:
                            dve.reduce_max(mx[:, l:l + 1], sps[l % 2][:, :], AX.X).then_inc(max_done, 1)
                            dve.wait_ge(max_done, T + 1)
                        dve.tensor_scalar(nm[:, l:l + 1], mx[:, l:l + 1], -scale, None, ALU.mult).then_inc(nm_done, 1)
                    m = l - 1
                    if 0 <= m < 16:
                        dve.wait_ge(turned_a, T + 2)
                        dve.wait_ge(pv_done, T + 14)
                        dve.tensor_copy(pT[:, m % 2, 0:H], tps[:, 0:H]).then_inc(pT_a, 1)
                    m = l - 2
                    if 0 <= m < 16:
                        u, i = m // T8, m % T8
                        dve.wait_ge(p_done, T + 1)
                        dve.reciprocal(ri[:, m:m + 1], rs[:, m:m + 1]).then_inc(ri_done, 1)
                        dve.wait_ge(pv_done, T + 15)
                        dve.wait_ge(ri_done, T - 1)
                        if i == 0:
                            dve.wait_ge(stored[u], r * 16 + 16)
                        dve.tensor_scalar(o[:, u, i, :], ops[m % 2][:, 0:DV], ri[:, m:m + 1], None,
                                          ALU.mult).then_inc(o_done, 1)
                steps(dve, body)

            @block.scalar
            def _(act):
                if table is None:
                    act.sem_inc(s_free, 2)
                act.sem_inc(p_done, 2)
                act.sem_inc(pT_b, 1)

                def body(l, r):
                    T = r * 16 + l
                    if l < 16:
                        act.wait_ge(nm_done, T + 1)
                        act.wait_ge(turned_b, T + 1)
                        src = sc[:, l % 2, :] if table is not None else sps[l % 2][:, :]
                        act.activation(p[:, l % 2, :], src, ACT.Exp, bias=nm[:, l:l + 1], scale=scale,
                                       accum_out=rs[:, l:l + 1]).then_inc(p_done, 1)
                        if table is None:
                            act.wait_ge(p_done, T + 3)
                            act.sem_inc(s_free, 1)
                    m = l - 1
                    if 0 <= m < 16:
                        act.wait_ge(turned_b, T + 2)
                        act.wait_ge(pv_done, T + 14)
                        act.activation(pT[:, m % 2, H:S], tps[:, H:S], ACT.Copy).then_inc(pT_b, 1)
                steps(act, body)


def rope_keys_queries(nc, qlT, cosT, sinT, qrT_out, krT_src, krT_out):
    with stage(nc) as st:
        c = st.sb("rk_c", [P, S])
        s = st.sb("rk_s", [P, S])
        a = st.sb("rk_a", [P, 3, S])
        b = st.sb("rk_b", [P, 3, S])
        o = st.sb("rk_o", [P, 3, S])
        loaded, ma, mb, added, stored = (st.sem("rk_" + n) for n in ("in", "ma", "mb", "added", "stored"))
        n = [P, P, 32]
        with nc.Block() as block:
            @block.sync
            def _(sp):
                sp.dma_start(c[:, :], cosT).then_inc(loaded, 16)
                sp.dma_start(s[:, :], sinT).then_inc(loaded, 16)
                for j in range(2):
                    sp.dma_start(a[:, j, :], qlT[512 + j * P:512 + (j + 1) * P, :]).then_inc(loaded, 16)
                    sp.dma_start(b[:, j, :], qlT[768 + j * P:768 + (j + 1) * P, :]).then_inc(loaded, 16)
                sp.dma_start(a[0:32, 2, :], krT_src[0:32, :]).then_inc(loaded, 16)
                sp.dma_start(b[0:32, 2, :], krT_src[32:64, :]).then_inc(loaded, 16)
                for j in range(3):
                    sp.wait_ge(added, j + 1)
                    dst = qrT_out[j * P:(j + 1) * P, :] if j < 2 else krT_out
                    sp.dma_start(dst, o[0:n[j], j, :]).then_inc(stored, 16)
                sp.wait_ge(stored, 48)

            @block.gpsimd
            def _(pool):
                pool.wait_ge(loaded, 128)
                for j in range(3):
                    pool.tensor_tensor(b[0:n[j], j, :], b[0:n[j], j, :], s[0:n[j], :], ALU.mult).then_inc(mb, 1)

            @block.vector
            def _(dve):
                dve.wait_ge(loaded, 128)
                for j in range(3):
                    dve.tensor_tensor(a[0:n[j], j, :], a[0:n[j], j, :], c[0:n[j], :], ALU.mult).then_inc(ma, 1)
                    dve.wait_ge(ma, j + 1)
                    dve.wait_ge(mb, j + 1)
                    dve.tensor_tensor(o[0:n[j], j, :], a[0:n[j], j, :], b[0:n[j], j, :], ALU.add).then_inc(added, 1)


def first_attention(nc, A, C, scr, ident, hT):
    x0 = A["x"].rearrange("b s d -> (b s) d")
    norm_rows(nc, "n0", ident, D, [(0, D, lambda t: rows(x0, t))], [(0, D)], hT=hT,
              gain=gain_of([A["g_attn_norm"][0]]))
    w_in = A["w_in"][0]
    kr0 = 3 * 512 + 384
    krv = tiled(w_in)
    project(nc, "pa", hT, 8, [
        dict(kind="T", n=2, width=512, load=columns(w_in, 0, 512), dst=to_T(scr["qkT"], 0, 512)),
        dict(kind="row", n=1, width=512, load=columns(w_in, 1024, 512), dst=to_rows(scr["va"], 0, 512)),
        dict(kind="row", n=1, width=384, load=columns(w_in, 1536, 384), dst=to_rows(scr["lat"], 0, 384)),
        dict(kind="T", n=1, width=64, nd=3, dst=to_T(scr["krT"], 0, 64),
             load=lambda i: [(slice(0, 32), krv[:, :, kr0:kr0 + 32]), (slice(32, 48), krv[:, :, kr0 + 16:kr0 + 32]),
                             (slice(48, 64), krv[:, :, kr0:kr0 + 16])]),
    ])
    bias_table(nc, A["rel_bias"], C["onehot"], C["log_count"], scr["table"])
    qk = scr["qkT"]
    softmax_attention(nc, "aa", ident, 8, 64, 64, 64 ** -0.5,
                      [(0, 0, 64, lambda h: qk[bass.ds(h * 64, 64), :]),
                       (1, 0, 64, lambda h: qk[bass.ds(h * 64 + 512, 64), :])],
                      lambda h: scr["va"][:, bass.ds(h * 64, 64)].rearrange("(t p) d -> p t d", p=P),
                      scr["oa"], table=scr["table"])
    norm_rows(nc, "nl", ident, 384, [(0, 384, lambda t: rows(scr["lat"], t))], [(0, 256), (256, 128)], hT=hT,
              gain=gain_of([A["g_q_latent"][0], A["g_kv_latent"][0]]))
    wq = A["w_q_up"][0].rearrange("(k p) (h c) -> k p h c", p=P, c=96)

    def q_nope(i):
        return [(slice(64 * h, 64 * h + 64), A["w_q_up"][0].rearrange("(k p) n -> p k n", p=P)[:, :, 96 * h:96 * h + 64])
                for h in range(8)]

    def q_rope(i):
        w = A["w_q_up"][0].rearrange("(k p) n -> p k n", p=P)
        out = []
        for h in range(8):
            r0 = 96 * h + 64
            out += [(slice(32 * h, 32 * h + 32), w[:, :, r0:r0 + 32]),
                    (slice(256 + 32 * h, 256 + 32 * h + 16), w[:, :, r0 + 16:r0 + 32]),
                    (slice(256 + 32 * h + 16, 256 + 32 * h + 32), w[:, :, r0:r0 + 16])]
        return out
    project(nc, "pq", hT, 2, [
        dict(kind="T", n=1, width=512, nd=8, load=q_nope, dst=to_T(scr["qlT"], 0, 512)),
        dict(kind="T", n=1, width=512, nd=24, load=q_rope, dst=to_T(scr["qlT"], 512, 512)),
    ])
    kvw = A["w_kv_up"][0].rearrange("(k p) n -> p k n", p=P)
    project(nc, "pk", hT[:, 2:3, :], 1, [
        dict(kind="T", n=1, width=512, nd=8, dst=to_T(scr["knT"], 0, 512),
             load=lambda i: [(slice(64 * h, 64 * h + 64), kvw[:, :, 128 * h:128 * h + 64]) for h in range(8)]),
        dict(kind="row", n=1, width=512, nd=8, dst=to_rows(scr["vb"], 0, 512),
             load=lambda i: [(slice(64 * h, 64 * h + 64), kvw[:, :, 128 * h + 64:128 * h + 128]) for h in range(8)]),
    ])
    rope_keys_queries(nc, scr["qlT"], C["mla_cosT"], C["mla_sinT"], scr["qrT"], scr["krT"], scr["krT2"])
    softmax_attention(nc, "ab", ident, 8, 96, 64, 96 ** -0.5,
                      [(0, 0, 64, lambda h: scr["qlT"][bass.ds(h * 64, 64), :]),
                       (0, 64, 32, lambda h: scr["qrT"][bass.ds(h * 32, 32), :]),
                       (1, 0, 64, lambda h: scr["knT"][bass.ds(h * 64, 64), :]),
                       (1, 64, 32, lambda h: scr["krT2"])],
                      lambda h: scr["vb"][:, bass.ds(h * 64, 64)].rearrange("(t p) d -> p t d", p=P),
                      scr["ob"])
    norm_rows(nc, "nm", ident, D, [(0, 512, lambda t: rows(scr["oa"], t)), (512, 512, lambda t: rows(scr["ob"], t))],
              [(0, 512), (512, 512)], hT=hT, gain=gain_of([A["g_out_a"][0], A["g_out_b"][0]]))
    project(nc, "po", hT, 8, [dict(kind="row", n=2, width=512, load=columns(A["w_out"][0], 0, 512),
                                   dst=to_rows(scr["y"], 0, 512))])


def identity(nc, ident, diag=1):
    with stage(nc) as st:
        zero, done = st.sem("id_zero"), st.sem("id_done")
        with nc.Block() as block:
            @block.gpsimd
            def _(pool):
                pool.memset(ident[:, :], 0.0).then_inc(zero, 1)
                pool.wait_ge(zero, 1)
                pool.affine_select(out=ident[:, :], in_=ident[:, :], compare_op=ALU.not_equal, fill=1.0, base=0,
                                   pattern=[[-1, P]], channel_multiplier=1).then_inc(done, 1)
                pool.wait_ge(done, 1)


SCRATCH = dict(
    qkT=(1024, S), va=(S, 512), lat=(S, 384), krT=(64, S), krT2=(32, S), table=(8, 2 * S), oa=(S, 512),
    qlT=(1024, S), qrT=(256, S), knT=(512, S), vb=(S, 512), ob=(S, 512), y=(S, D),
)


def constants():
    rel = (S - 1) - np.arange(2 * S)
    half, exact = 16, 8
    n = np.abs(rel)
    large = exact + (np.log(np.maximum(n, 1) / exact) / math.log(1024 / exact) * (half - exact)).astype(np.int32)
    bucket = np.where(rel > 0, half, 0) + np.where(n < exact, n, np.minimum(large, half - 1))
    count = np.zeros(2 * S)
    for window, dilation in ((128, 1), (512, 4), (2048, 16)):
        steps = window // (2 * dilation)
        count += (rel % dilation == 0) & (n <= steps * dilation)
    c = {
        "onehot": (bucket[None, :] == np.arange(32)[:, None]).astype(np.float32),
        "log_count": np.where(count > 0, np.log(np.maximum(count, 1)), NEG).astype(np.float32),
    }
    inv = (10000.0 ** (-(np.arange(16, dtype=np.float32) / np.float32(16)))).astype(np.float32)
    ang = (np.arange(S, dtype=np.float32)[:, None] * inv[None, :]).astype(np.float32)
    c["mla_cosT"] = np.tile(np.cos(ang).T, (8, 1)).astype(np.float32)
    c["mla_sinT"] = np.tile(np.concatenate([-np.sin(ang).T, np.sin(ang).T], 0), (4, 1)).astype(np.float32)
    e = np.arange(32)
    c["router"] = np.concatenate([e, 32 - e, np.arange(15)]).astype(np.float32)
    c["before"] = np.triu(np.ones((P, P)), 1).astype(np.float32)
    pos = np.arange(P, dtype=np.float64)
    inv = (10000.0 ** (-(np.arange(32, dtype=np.float32) / np.float32(32)))).astype(np.float32)
    ang = (np.arange(S, dtype=np.float32)[:, None] * inv[None, :]).astype(np.float32)
    c["ret_cs"] = np.concatenate([np.cos(ang), np.sin(ang)], 1).astype(np.float32)
    g = np.log(1.0 - 2.0 ** (-5.0 - np.arange(4)))
    scale = 64 ** -0.5
    dist = pos[None, :] - pos[:, None]
    c["ret_decay"] = np.concatenate([np.where(dist >= 0, np.exp(gh * np.maximum(dist, 0)), 0) * scale for gh in g],
                                    1).astype(np.float32)
    c["ret_rowdec"] = np.concatenate([np.exp(g[None, :] * (pos + 1)[:, None]),
                                      np.exp(g[None, :] * (P - 1 - pos)[:, None]) * scale], 1).astype(np.float32)
    c["ret_gchunk"] = np.exp(P * np.stack([np.repeat(g[2 * j:2 * j + 2], 64) for j in range(2)], 1)).astype(np.float32)
    strict = pos[None, :] < pos[:, None]
    c["strict"] = np.stack([strict, np.where(strict, 0, NEG)], 1).astype(np.float32)
    s, t = np.arange(P)[:, None], np.arange(P)[None, :]
    c["levels"] = np.stack([(s // (2 * m) == t // (2 * m)) & (s % (2 * m) < m) & (t % (2 * m) >= m)
                            for m in (64, 32, 16, 8, 4, 2, 1)] + [s == t], 1).astype(np.float32)
    return c



NG, NE, FF = 4, 32, 256
EG = NE // NG
NOV = 2 * S // P - 1
NB = 48


def route(nc, hT, A, C, tok_of_slot, slot_out, gates, slots, over):
    with stage(nc) as st:
        wr = st.sb("ro_wr", [P, 8, NG + NE])
        br = st.sb("ro_br", [P, NG + NE])
        cst = st.sb("ro_cst", [P, 2 * NE + NOV])
        ltm = st.sb("ro_lt", [P, P])
        ones = st.sb("ro_ones", [P, P])
        L = st.sb("ro_L", [P, NT, NG + NE])
        g4 = [st.sb(f"ro_g4{i}", [P, NT, NG]) for i in range(6)]
        c1 = [st.sb(f"ro_c1{i}", [P, NT]) for i in range(14)]
        e32 = [st.sb(f"ro_e{i}", [P, NT, NE]) for i in range(14)]
        M = st.sb("ro_M", [P, NT, NE])
        cum = st.sb("ro_cum", [P, NT + 1, NE])
        rank = st.sb("ro_rank", [P, NT, NE])
        kk = st.sb("ro_kk", [P, 8, NT, NE])
        cnt = st.sb("ro_cnt", [P, 12, NE])
        ovb = st.sb("ro_ovb", [P, NOV, NE])
        ovs = st.sb("ro_ovs", [P, 2 * NB])
        posf = st.sb("ro_posf", [P, NT, 2])
        zero = st.sb("ro_zero", [P, NB], U32)
        tok = st.sb("ro_tok", [P, NT], U32)
        blank = st.sb("ro_blank", [P, D])
        blanked = st.sem("ro_blanked")
        pl = st.ps("ro_pl", [P, BANK])
        pr = st.ps("ro_pr", [P, BANK])
        pc = st.ps("ro_pc", [P, BANK])
        ins, cleared, lg, exps, e_ready, m_ready, ranks, d, tok_ready, slots_ready, scattered, e2_ready, e2s = (
            st.sem("ro_" + n) for n in ("in", "cleared", "logits", "exps", "e_ready", "m_ready", "ranks", "step", "tok", "slots",
                                        "scattered", "e2_ready", "e2"))
        G8, E8 = [P, NT, NG], [P, NT, NE]
        with nc.Block() as block:
            @block.sync
            def _(sp):
                sp.dma_start(wr[:, :, 0:NG], tiled(A["w_router_group"][0])).then_inc(ins, 16)
                sp.dma_start(wr[:, :, NG:], tiled(A["w_router_expert"][0])).then_inc(ins, 16)
                sp.dma_start(br[:, 0:NG], A["b_router_group"][0].partition_broadcast(P)).then_inc(ins, 16)
                sp.dma_start(br[:, NG:], A["b_router_expert"][0].partition_broadcast(P)).then_inc(ins, 16)
                sp.dma_start(cst[:, :], C["router"].partition_broadcast(P)).then_inc(ins, 16)
                sp.dma_start(ltm[:, :], C["before"]).then_inc(ins, 16)

            @block.tensor
            def _(pe):
                pe.wait_ge(ins, 96)
                for t in range(NT):
                    for k in range(8):
                        mm = pe.matmul(pl[:, t * 36:(t + 1) * 36], hT[:, k, t * P:(t + 1) * P], wr[:, k, :],
                                       start=(k == 0), stop=(k == 7))
                mm.then_inc(lg, 1)
                pe.wait_ge(m_ready, 1)
                pe.matmul(pr[:, 0:NT * NE], ltm[:, :], M[:, :, :].rearrange("p t e -> p (t e)"), start=True, stop=False)
                pe.matmul(pr[:, 0:NT * NE], ones[:, :], cum[:, 0:NT, :].rearrange("p t e -> p (t e)"), start=False, stop=True)
                pe.matmul(pc[:, 0:NE], ones[:, :], cum[:, NT, :], start=True, stop=True).then_inc(ranks, 1)

            @block.scalar
            def _(act):
                act.wait_ge(tok_ready, 3)
                act.dma_start(slot_out.rearrange("(p b) n -> p b n", b=NB)[:, NE:, :],
                              blank[:, :].unsqueeze(1).to_broadcast([P, NB - NE, D])).then_inc(blanked, 16)
                act.wait_ge(e_ready, 1)
                act.activation(g4[3][:, :, :], g4[2][:, :, :], ACT.Exp).then_inc(exps, 1)
                act.wait_ge(e2_ready, 1)
                act.activation(c1[7][:, :], c1[6][:, :], ACT.Exp).then_inc(e2s, 1)
                act.wait_ge(blanked, 16)

            @block.vector
            def _(dve):
                n = [0]

                def step(ins_):
                    n[0] += 1
                    ins_.then_inc(d, 1)
                    dve.wait_ge(d, n[0])

                step(dve.memset(ones[:, :], 1.0))
                dve.wait_ge(ins, 96)
                dve.wait_ge(lg, 1)
                step(dve.tensor_tensor(L[:, :, :], pl[:, 0:NT * 36].rearrange("p (t n) -> p t n", t=NT),
                                       br[:, :].unsqueeze(1).to_broadcast([P, NT, 36]), ALU.add))
                Lg, Le = L[:, :, 0:NG], L[:, :, NG:]
                step(dve.reduce_max(c1[0][:, :], Lg, AX.X))
                gm = c1[0][:, :].unsqueeze(2).to_broadcast(G8)
                dve.tensor_tensor(g4[2][:, :, :], Lg, gm, ALU.subtract).then_inc(e_ready, 1)
                step(dve.tensor_tensor(g4[0][:, :, :], Lg, gm, ALU.is_equal))
                step(dve.tensor_tensor(g4[1][:, :, :], g4[0][:, :, :],
                                       cst[:, 2 * NE - NG:2 * NE].unsqueeze(1).to_broadcast(G8), ALU.mult))
                step(dve.reduce_max(c1[1][:, :], g4[1][:, :, :], AX.X))
                step(dve.tensor_tensor(g4[4][:, :, :], g4[1][:, :, :], c1[1][:, :].unsqueeze(2).to_broadcast(G8), ALU.is_equal))
                step(dve.tensor_scalar(g4[5][:, :, :], g4[4][:, :, :], -1.0, 1e30, ALU.add, ALU.mult))
                E4 = [P, NT, NG, EG]
                v4 = lambda x: x.rearrange("p t (g e) -> p t g e", g=NG)
                step(dve.tensor_tensor(v4(e32[0][:, :, :]), v4(Le), g4[4][:, :, :].unsqueeze(3).to_broadcast(E4), ALU.mult))
                step(dve.tensor_tensor(v4(e32[1][:, :, :]), v4(e32[0][:, :, :]), g4[5][:, :, :].unsqueeze(3).to_broadcast(E4), ALU.add))
                prio = cst[:, NE:2 * NE].unsqueeze(1).to_broadcast(E8)

                def pick(src, mx, pm, eq, pri, oh):
                    step(dve.reduce_max(mx[:, :], src[:, :, :], AX.X))
                    step(dve.tensor_tensor(eq[:, :, :], src[:, :, :], mx[:, :].unsqueeze(2).to_broadcast(E8), ALU.is_equal))
                    step(dve.tensor_tensor(pri[:, :, :], eq[:, :, :], prio, ALU.mult))
                    step(dve.reduce_max(pm[:, :], pri[:, :, :], AX.X))
                    step(dve.tensor_tensor(oh[:, :, :], pri[:, :, :], pm[:, :].unsqueeze(2).to_broadcast(E8), ALU.is_equal))

                oh1, oh2 = e32[4], e32[8]
                pick(e32[1], c1[2], c1[3], e32[2], e32[3], oh1)
                step(dve.scalar_tensor_tensor(out=e32[5][:, :, :], in0=oh1[:, :, :], scalar=-4e30, in1=e32[1][:, :, :],
                                              op0=ALU.mult, op1=ALU.add))
                pick(e32[5], c1[4], c1[5], e32[6], e32[7], oh2)
                dve.tensor_tensor(c1[6][:, :], c1[4][:, :], c1[2][:, :], ALU.subtract).then_inc(e2_ready, 1)
                step(dve.tensor_tensor(M[:, :, :], oh1[:, :, :], oh2[:, :, :], ALU.add))
                step(dve.memset(cum[:, 0, :], 0.0))
                for t in range(NT):
                    ins_ = dve.tensor_tensor(cum[:, t + 1, :], cum[:, t, :], M[:, t, :], ALU.add)
                    if t == NT - 1:
                        dve_last = ins_
                        ins_.then_inc(m_ready, 1)
                        dve.wait_ge(m_ready, 1)
                    else:
                        step(ins_)
                dve.wait_ge(exps, 1)
                step(dve.reduce_sum(c1[8][:, :], g4[3][:, :, :], AX.X))
                dve.wait_ge(e2s, 1)
                step(dve.tensor_scalar(c1[9][:, :], c1[7][:, :], 1.0, None, ALU.add))
                step(dve.tensor_tensor(c1[10][:, :], c1[9][:, :], c1[8][:, :], ALU.mult))
                step(dve.reciprocal(gates[:, :, 0], c1[10][:, :]))
                step(dve.tensor_tensor(gates[:, :, 1], gates[:, :, 0], c1[7][:, :], ALU.mult))
                dve.wait_ge(ranks, 1)
                step(dve.tensor_copy(cnt[:, 0, :], pc[:, 0:NE]))
                step(dve.memset(cnt[:, 1, :], 0.0))
                for j in range(1, 8):
                    step(dve.scalar_tensor_tensor(out=cnt[:, 1 + j, :], in0=cnt[:, 0, :], scalar=float(P * j), in1=cnt[:, j, :],
                                                  op0=ALU.is_gt, op1=ALU.add))
                nov, oend, obase = cnt[:, 8, :], cnt[:, 9, :], cnt[:, 10, :]
                step(dve.tensor_tensor_scan(oend, ones[:, 0:NE], nov, 0.0, ALU.mult, ALU.add))
                step(dve.tensor_tensor(cnt[:, 11, :], oend, nov, ALU.subtract))
                step(dve.tensor_tensor(obase, cnt[:, 11, :], cst[:, 0:NE], ALU.subtract))
                step(dve.tensor_tensor(ovb[:, :, :], oend.unsqueeze(1).to_broadcast([P, NOV, NE]),
                                       cst[:, 2 * NE:].unsqueeze(2).to_broadcast([P, NOV, NE]), ALU.is_le))
                step(dve.reduce_sum(ovs[:, 0:NOV], ovb[:, :, :], AX.X))
                step(dve.tensor_scalar(ovs[:, NB:NB + NOV], ovs[:, 0:NOV], float(NE - 1), None, ALU.min))
                step(dve.tensor_copy(over[:, 0:NOV], ovs[:, NB:NB + NOV]))
                step(dve.tensor_copy(over[:, NOV:NOV + 1], cnt[:, 9, NE - 1:NE]))
                step(dve.tensor_copy(rank[:, :, :], pr[:, 0:NT * NE].rearrange("p (t e) -> p t e", t=NT)))
                step(dve.tensor_scalar(kk[:, 1, :, :], rank[:, :, :], float(P), None, ALU.is_ge))
                for j in range(2, 8):
                    step(dve.scalar_tensor_tensor(out=kk[:, j, :, :], in0=rank[:, :, :], scalar=float(P * j), in1=kk[:, j - 1, :, :],
                                                  op0=ALU.is_ge, op1=ALU.add))
                step(dve.tensor_scalar(e32[9][:, :, :], rank[:, :, :], float(NB), None, ALU.mult))
                step(dve.scalar_tensor_tensor(out=e32[10][:, :, :], in0=kk[:, 7, :, :], scalar=float(1 - NB * P), in1=e32[9][:, :, :],
                                              op0=ALU.mult, op1=ALU.add))
                step(dve.tensor_scalar(cnt[:, 1, :], obase, float(NE - 1), None, ALU.add))
                step(dve.tensor_tensor(e32[11][:, :, :], kk[:, 1, :, :], cnt[:, 1, :].unsqueeze(1).to_broadcast(E8), ALU.mult))
                step(dve.tensor_tensor(e32[12][:, :, :], e32[10][:, :, :], e32[11][:, :, :], ALU.add))
                step(dve.tensor_tensor(e32[13][:, :, :], e32[12][:, :, :], cst[:, 0:NE].unsqueeze(1).to_broadcast(E8), ALU.add))
                step(dve.tensor_tensor(e32[9][:, :, :], e32[13][:, :, :], oh1[:, :, :], ALU.mult))
                step(dve.tensor_tensor(e32[10][:, :, :], e32[13][:, :, :], oh2[:, :, :], ALU.mult))
                step(dve.reduce_sum(posf[:, :, 0], e32[9][:, :, :], AX.X))
                step(dve.reduce_sum(posf[:, :, 1], e32[10][:, :, :], AX.X))
                dve.tensor_copy(slots[:, :, :], posf[:, :, :]).then_inc(slots_ready, 1)

            @block.gpsimd
            def _(pool):
                pool.memset(zero[:, :], 0).then_inc(tok_ready, 1)
                pool.iota(tok[:, :], pattern=[[P, NT]], base=0, channel_multiplier=1).then_inc(tok_ready, 1)
                pool.memset(blank[:, :], 0.0).then_inc(tok_ready, 1)
                pool.wait_ge(tok_ready, 3)
                pool.dma_start(tok_of_slot.rearrange("(p b) n -> p (b n)", p=P), zero[:, :]).then_inc(cleared, 16)
                pool.wait_ge(cleared, 16)
                pool.wait_ge(slots_ready, 1)
                for t in range(NT):
                    for c in range(2):
                        pool.indirect_dma_start(tok_of_slot, bass.IndirectOffsetOnAxis(ap=slots[:, t, c:c + 1], axis=0),
                                                tok[:, t:t + 1], None).then_inc(scattered, 16)
                pool.wait_ge(scattered, 16 * 2 * NT)


def experts(nc, ident, xn, A, tok_of_slot, slot_out, over):
    out_v = slot_out.rearrange("(p b) n -> p b n", b=NB)
    wg_d = A["w_gate"][0].rearrange("e (k p) n -> p e k n", p=P)
    wu_d = A["w_up"][0].rearrange("e (k p) n -> p e k n", p=P)
    wd_d = A["w_down"][0].rearrange("e (k p) n -> p e k n", p=P)
    NW = 3
    with stage(nc) as st:
        idx = st.sb("ex_idx", [P, NB], U32)
        idc = st.sb("ex_idc", [P, 2], U32)
        gain = st.sb("ex_gain", [P, 8])
        wgu = st.sb("ex_wgu", [P, NW, 8, 2 * FF])
        wd = st.sb("ex_wd", [P, NW, 2, D])
        xg = st.sb("ex_xg", [P, 2, D])
        xT = st.sb("ex_xT", [P, 2, 8, P])
        sg = st.sb("ex_sg", [P, 2, FF])
        hh = st.sb("ex_hh", [P, 2, FF])
        h2 = st.sb("ex_h2", [P, 2, FF])
        hTs = st.sb("ex_hT", [P, 2, 2, P])
        ob = st.sb("ex_ob", [P, 2, D])
        tp = st.ps("ex_tp", [P, D])
        gu = [st.ps(f"ex_gu{s}", [P, BANK]) for s in range(2)]
        tph = st.ps("ex_tph", [P, BANK])
        dn = st.ps("ex_dn", [P, D])
        consts_in, idx_in = st.sem("ex_consts"), st.sem("ex_idx_in")
        w_in = [st.sem(f"ex_w_in{s}") for s in range(NW)]
        w_used = st.sem("ex_w_used")
        idx_ok, passed = st.sem("ex_idx_ok"), st.sem("ex_passed")
        x_in = [st.sem(f"ex_x_in{s}") for s in range(2)]
        turned, xT_ok, gu_ok, sig_ok, hh_ok, h2_ok, hturned, hT_ok, dn_ok, ob_a, ob_b = (
            st.sem("ex_" + n) for n in ("turned", "xT_ok", "gu_ok", "sig_ok", "hh_ok", "h2_ok", "hturned", "hT_ok", "dn_ok", "ob_a", "ob_b"))
        stored = [st.sem(f"ex_stored{s}") for s in range(2)]

        def steps(eng, lags, body):
            first, loops = 8, 3
            for s in range(first):
                body(s, s, True)
            with eng.Fori(0, loops) as r:
                for v in range(6):
                    body(r * 6 + (first + v), first + v, False)
            for s in range(first + 6 * loops, NE + lags):
                body(s, s, True)

        def load_weights(sp, e, slot):
            sp.dma_start(wgu[:, slot, :, 0:FF], wg_d[:, e]).then_inc(w_in[slot], 16)
            sp.dma_start(wgu[:, slot, :, FF:], wu_d[:, e]).then_inc(w_in[slot], 16)
            sp.dma_start(wd[:, slot, :, :], wd_d[:, e]).then_inc(w_in[slot], 16)

        def gather(pool, b, slot):
            pool.indirect_dma_start(xg[:, slot, :], None, xn, bass.IndirectOffsetOnAxis(ap=idc[:, slot:slot + 1], axis=0)
                                    ).then_inc(x_in[slot], 16)

        with nc.Block() as block:
            @block.sync
            def _(sp):
                sp.dma_start(idx[:, :], tok_of_slot.rearrange("(p b) n -> p (b n)", p=P)).then_inc(idx_in, 16)
                sp.dma_start(gain[:, :], A["g_ffn_norm"][0].rearrange("(k p) -> p k", p=P),
                             allow_slow_non_contiguous=True).then_inc(consts_in, 16)

                def body(b, c, fixed):
                    if fixed and c >= NE:
                        return
                    if c >= NW:
                        sp.wait_ge(w_used, b - (NW - 1))
                    e = b
                    load_weights(sp, slice(e, e + 1) if fixed else bass.ds(e, 1), c % NW)
                steps(sp, 0, body)

            @block.gpsimd
            def _(pool):
                pool.wait_ge(idx_in, 16)

                def body(b, c, fixed):
                    if fixed and c >= NE:
                        return
                    if c >= 2:
                        pool.wait_ge(turned, b - 1)
                    pool.tensor_copy(idc[:, c % 2:c % 2 + 1], idx[:, bass.ds(b, 1)]).then_inc(idx_ok, 1)
                    pool.wait_ge(idx_ok, b + 1)
                    pool.sem_inc(passed, 1)
                    gather(pool, b, c % 2)
                steps(pool, 0, body)

            @block.tensor
            def _(pe):
                def body(s, c, fixed):
                    if not fixed or c < NE:
                        pe.wait_ge(x_in[c % 2], (s - c % 2) * 8 + 16)
                        if c >= 1:
                            pe.wait_ge(xT_ok, s)
                        for k in range(8):
                            mm = pe.transpose(tp[:, k * P:(k + 1) * P], xg[:, c % 2, k * P:(k + 1) * P], ident[:, :])
                        mm.then_inc(turned, 1)
                    b, c1 = s - 1, c - 1
                    if c1 >= 0 and (not fixed or c1 < NE):
                        pe.wait_ge(w_in[c1 % NW], (b - c1 % NW) * 16 + 48)
                        pe.wait_ge(xT_ok, b + 1)
                        if c1 >= 2:
                            pe.wait_ge(h2_ok, b - 1)
                        for k in range(8):
                            mm = pe.matmul(gu[c1 % 2][:, :], xT[:, c1 % 2, k, :], wgu[:, c1 % NW, k, :], start=(k == 0), stop=(k == 7))
                        mm.then_inc(gu_ok, 1)
                    b, c2 = s - 2, c - 2
                    if c2 >= 0 and (not fixed or c2 < NE):
                        pe.wait_ge(h2_ok, b + 1)
                        if c2 >= 1:
                            pe.wait_ge(hT_ok, b)
                        for k in range(2):
                            mm = pe.transpose(tph[:, k * P:(k + 1) * P], h2[:, c2 % 2, k * P:(k + 1) * P], ident[:, :])
                        mm.then_inc(hturned, 1)
                        pe.wait_ge(hT_ok, b + 1)
                        if c2 >= 1:
                            pe.wait_ge(ob_a, b)
                            pe.wait_ge(ob_b, b)
                        for n in range(2):
                            for k in range(2):
                                mm = pe.matmul(dn[:, n * BANK:(n + 1) * BANK], hTs[:, c2 % 2, k, :],
                                               wd[:, c2 % NW, k, n * BANK:(n + 1) * BANK], start=(k == 0), stop=(k == 1))
                        mm.then_inc(dn_ok, 1)
                        pe.wait_ge(dn_ok, b + 1)
                        pe.sem_inc(w_used, 1)
                steps(pe, 2, body)

            @block.scalar
            def _(act):
                def body(s, c, fixed):
                    b, c1 = s - 1, c - 1
                    if c1 >= 0 and (not fixed or c1 < NE):
                        act.wait_ge(gu_ok, b + 1)
                        act.activation(sg[:, c1 % 2, :], gu[c1 % 2][:, 0:FF], ACT.Sigmoid).then_inc(sig_ok, 1)
                    b, c2 = s - 2, c - 2
                    if c2 >= 0 and (not fixed or c2 < NE):
                        act.wait_ge(hturned, b + 1)
                        act.activation(hTs[:, c2 % 2, :, :].rearrange("p k n -> p (k n)"), tph[:, 0:2 * P], ACT.Copy).then_inc(hT_ok, 1)
                        act.wait_ge(dn_ok, b + 1)
                        if c2 >= 2:
                            act.wait_ge(stored[c2 % 2], (b - c2 % 2) * 8)
                        act.activation(ob[:, c2 % 2, 0:BANK], dn[:, 0:BANK], ACT.Copy).then_inc(ob_a, 1)
                        act.wait_ge(ob_a, b + 1)
                        act.wait_ge(ob_b, b + 1)
                        act.dma_start(out_v[:, bass.ds(b, 1), :].rearrange("p b n -> p (b n)"), ob[:, c2 % 2, :]).then_inc(stored[c2 % 2], 16)
                steps(act, 2, body)
                act.wait_ge(stored[0], 8 * NE)
                act.wait_ge(stored[1], 8 * NE)

            @block.vector
            def _(dve):
                dve.wait_ge(consts_in, 16)

                def body(s, c, fixed):
                    if not fixed or c < NE:
                        dve.wait_ge(turned, s + 1)
                        if c >= 2:
                            dve.wait_ge(gu_ok, s - 1)
                        dve.tensor_tensor(xT[:, c % 2, :, :], tp[:, :].rearrange("p (k n) -> p k n", k=8),
                                          gain[:, :].unsqueeze(2).to_broadcast([P, 8, P]), ALU.mult).then_inc(xT_ok, 1)
                    b, c1 = s - 1, c - 1
                    if c1 >= 0 and (not fixed or c1 < NE):
                        dve.wait_ge(sig_ok, b + 1)
                        dve.tensor_tensor(hh[:, c1 % 2, :], gu[c1 % 2][:, 0:FF], sg[:, c1 % 2, :], ALU.mult).then_inc(hh_ok, 1)
                        dve.wait_ge(hh_ok, b + 1)
                        if c1 >= 2:
                            dve.wait_ge(hturned, b - 1)
                        dve.tensor_tensor(h2[:, c1 % 2, :], hh[:, c1 % 2, :], gu[c1 % 2][:, FF:], ALU.mult).then_inc(h2_ok, 1)
                    b, c2 = s - 2, c - 2
                    if c2 >= 0 and (not fixed or c2 < NE):
                        dve.wait_ge(dn_ok, b + 1)
                        if c2 >= 2:
                            dve.wait_ge(stored[c2 % 2], (b - c2 % 2) * 8)
                        dve.tensor_copy(ob[:, c2 % 2, BANK:], dn[:, BANK:]).then_inc(ob_b, 1)
                steps(dve, 2, body)

    with stage(nc) as st:
        idx = st.sb("fx_idx", [P, NB], U32)
        idc = st.sb("fx_idc", [P, 1], U32)
        gain = st.sb("fx_gain", [P, 8])
        wgu = st.sb("fx_wgu", [P, 8, 2 * FF])
        wd = st.sb("fx_wd", [P, 2, D])
        xg = st.sb("fx_xg", [P, D])
        xT = st.sb("fx_xT", [P, 8, P])
        sg, hh, h2 = (st.sb("fx_" + n, [P, FF]) for n in ("sg", "hh", "h2"))
        hTs = st.sb("fx_hT", [P, 2 * P])
        ob = st.sb("fx_ob", [P, D])
        tp, dn = st.ps("fx_tp", [P, D]), st.ps("fx_dn", [P, D])
        gu, tph = st.ps("fx_gu", [P, BANK]), st.ps("fx_tph", [P, BANK])
        consts_in, w_in, idx_ok, x_in, turned, xT_ok, gu_ok, sig_ok, hh_ok, h2_ok, hturned, hT_ok, dn_ok, ob_ok, stored = (
            st.sem("fx_" + n) for n in ("consts", "w_in", "idx_ok", "x_in", "turned", "xT_ok", "gu_ok", "sig_ok", "hh_ok",
                                        "h2_ok", "hturned", "hT_ok", "dn_ok", "ob_ok", "stored"))

        passed = st.sem("fx_passed")

        def each(eng, body):
            n = eng.value_load(over[0:1, NOV:NOV + 1], min_val=0, max_val=NOV)
            with eng.Fori(0, NOV) as j:
                with eng.If(n > j):
                    body(j)

        with nc.Block() as block:
            @block.sync
            def _(sp):
                sp.dma_start(idx[:, :], tok_of_slot.rearrange("(p b) n -> p (b n)", p=P)).then_inc(consts_in, 16)
                sp.dma_start(gain[:, :], A["g_ffn_norm"][0].rearrange("(k p) -> p k", p=P),
                             allow_slow_non_contiguous=True).then_inc(consts_in, 16)
                sp.wait_ge(consts_in, 32)
                sp.sem_inc(stored, 16)

                def body(j):
                    e = sp.value_load(over[0:1, bass.ds(j, 1)], min_val=0, max_val=NE - 1)
                    sp.wait_ge(stored, j * 16 + 16)
                    sp.dma_start(wgu[:, :, 0:FF], wg_d[:, bass.ds(e, 1)]).then_inc(w_in, 16)
                    sp.dma_start(wgu[:, :, FF:], wu_d[:, bass.ds(e, 1)]).then_inc(w_in, 16)
                    sp.dma_start(wd[:, :, :], wd_d[:, bass.ds(e, 1)]).then_inc(w_in, 16)
                    sp.wait_ge(ob_ok, j + 1)
                    sp.dma_start(out_v[:, bass.ds(j + NE, 1), :].rearrange("p b n -> p (b n)"), ob[:, :]).then_inc(stored, 16)
                    sp.wait_ge(stored, j * 16 + 32)
                    sp.sem_inc(passed, 1)
                each(sp, body)

            @block.gpsimd
            def _(pool):
                pool.wait_ge(consts_in, 32)

                def body(j):
                    pool.wait_ge(stored, j * 16 + 16)
                    pool.tensor_copy(idc[:, :], idx[:, bass.ds(j + NE, 1)]).then_inc(idx_ok, 1)
                    pool.wait_ge(idx_ok, j + 1)
                    pool.sem_inc(passed, 1)
                    pool.indirect_dma_start(xg[:, :], None, xn, bass.IndirectOffsetOnAxis(ap=idc[:, :], axis=0)).then_inc(x_in, 16)
                each(pool, body)

            @block.tensor
            def _(pe):
                def body(j):
                    pe.wait_ge(x_in, j * 16 + 16)
                    for k in range(8):
                        mm = pe.transpose(tp[:, k * P:(k + 1) * P], xg[:, k * P:(k + 1) * P], ident[:, :])
                    mm.then_inc(turned, 1)
                    pe.wait_ge(w_in, j * 48 + 48)
                    pe.wait_ge(xT_ok, j + 1)
                    for k in range(8):
                        mm = pe.matmul(gu[:, :], xT[:, k, :], wgu[:, k, :], start=(k == 0), stop=(k == 7))
                    mm.then_inc(gu_ok, 1)
                    pe.wait_ge(h2_ok, j + 1)
                    for k in range(2):
                        mm = pe.transpose(tph[:, k * P:(k + 1) * P], h2[:, k * P:(k + 1) * P], ident[:, :])
                    mm.then_inc(hturned, 1)
                    pe.wait_ge(hT_ok, j + 1)
                    for n in range(2):
                        for k in range(2):
                            mm = pe.matmul(dn[:, n * BANK:(n + 1) * BANK], hTs[:, k * P:(k + 1) * P],
                                           wd[:, k, n * BANK:(n + 1) * BANK], start=(k == 0), stop=(k == 1))
                    mm.then_inc(dn_ok, 1)
                each(pe, body)

            @block.scalar
            def _(act):
                def body(j):
                    act.wait_ge(gu_ok, j + 1)
                    act.activation(sg[:, :], gu[:, 0:FF], ACT.Sigmoid).then_inc(sig_ok, 1)
                    act.wait_ge(hturned, j + 1)
                    act.activation(hTs[:, :], tph[:, 0:2 * P], ACT.Copy).then_inc(hT_ok, 1)
                each(act, body)

            @block.vector
            def _(dve):
                dve.wait_ge(consts_in, 32)

                def body(j):
                    dve.wait_ge(turned, j + 1)
                    dve.tensor_tensor(xT[:, :, :], tp[:, :].rearrange("p (k n) -> p k n", k=8),
                                      gain[:, :].unsqueeze(2).to_broadcast([P, 8, P]), ALU.mult).then_inc(xT_ok, 1)
                    dve.wait_ge(sig_ok, j + 1)
                    dve.tensor_tensor(hh[:, :], gu[:, 0:FF], sg[:, :], ALU.mult).then_inc(hh_ok, 1)
                    dve.wait_ge(hh_ok, j + 1)
                    dve.tensor_tensor(h2[:, :], hh[:, :], gu[:, FF:], ALU.mult).then_inc(h2_ok, 1)
                    dve.wait_ge(dn_ok, j + 1)
                    dve.tensor_copy(ob[:, :], dn[:, :]).then_inc(ob_ok, 1)
                each(dve, body)


def combine(nc, x1, slot_out, gates, slots, out):
    with stage(nc) as st:
        x = st.sb("co_x", [P, 2, D])
        a, b = st.sb("co_a", [P, 2, D]), st.sb("co_b", [P, 2, D])
        s1, s2 = st.sb("co_s1", [P, 2, D]), st.sb("co_s2", [P, 2, D])
        x_in = [st.sem(f"co_x_in{u}") for u in range(2)]
        g_in = [st.sem(f"co_g_in{u}") for u in range(2)]
        first, both = st.sem("co_first"), st.sem("co_both")
        stored = [st.sem(f"co_stored{u}") for u in range(2)]
        with nc.Block() as block:
            @block.sync
            def _(sp):
                for t in range(NT):
                    if t >= 2:
                        sp.wait_ge(first, t - 1)
                    sp.dma_start(x[:, t % 2, :], rows(x1, t)).then_inc(x_in[t % 2], 16)

            @block.gpsimd
            def _(pool):
                for t in range(NT):
                    if t >= 2:
                        pool.wait_ge(both, t - 1)
                    for c, buf in enumerate((a, b)):
                        pool.indirect_dma_start(buf[:, t % 2, :], None, slot_out,
                                                bass.IndirectOffsetOnAxis(ap=slots[:, t, c:c + 1], axis=0)).then_inc(g_in[t % 2], 16)

            @block.vector
            def _(dve):
                for t in range(NT):
                    u, n = t % 2, t // 2 + 1
                    dve.wait_ge(x_in[u], 16 * n)
                    dve.wait_ge(g_in[u], 32 * n)
                    dve.scalar_tensor_tensor(out=s1[:, u, :], in0=a[:, u, :], scalar=gates[:, t, 0:1], in1=x[:, u, :],
                                             op0=ALU.mult, op1=ALU.add).then_inc(first, 1)
                    dve.wait_ge(first, t + 1)
                    if t >= 2:
                        dve.wait_ge(stored[u], 16 * (n - 1))
                    dve.scalar_tensor_tensor(out=s2[:, u, :], in0=b[:, u, :], scalar=gates[:, t, 1:2], in1=s1[:, u, :],
                                             op0=ALU.mult, op1=ALU.add).then_inc(both, 1)

            @block.scalar
            def _(act):
                for t in range(NT):
                    act.wait_ge(both, t + 1)
                    act.dma_start(rows(out, t), s2[:, t % 2, :]).then_inc(stored[t % 2], 16)
                act.wait_ge(stored[0], 64)
                act.wait_ge(stored[1], 64)


def moe(nc, A, C, scr, ident, hT):
    x0 = A["x"].rearrange("b s d -> (b s) d")
    norm_rows(nc, "n1", ident, D, [(0, D, lambda t: rows(x0, t))], [(0, D)], hT=hT, add=scr["y"], keep=scr["x1"],
              keep_normed=scr["xn"], gain=gain_of([A["g_ffn_norm"][0]]))
    with ExitStack() as ctx:
        gates = ctx.enter_context(nc.sbuf_tensor("gates", [P, NT, 2], F32))
        slots = ctx.enter_context(nc.sbuf_tensor("slots", [P, NT, 2], U32))
        over = ctx.enter_context(nc.sbuf_tensor("over", [P, NOV + 1], U32))
        tok_of_slot = nc.dram_tensor("tok_of_slot", (P * NB, 1), U32, kind="Internal").ap()
        route(nc, hT, A, C, tok_of_slot, scr["slot_out"], gates, slots, over)
        experts(nc, ident, scr["xn"], A, tok_of_slot, scr["slot_out"], over)
        combine(nc, scr["x1"], scr["slot_out"], gates, slots, scr["xm"])


SCRATCH.update(x1=(S, D), xn=(S, D), slot_out=(P * NB, D), xm=(S, D))



RH, RDK, RDV = 4, 64, 128


def retention(nc, ident, rows_in, C, out):
    QK = 2 * RH

    def by_parity(ap, q):
        return ap.rearrange("p (j q n) -> p j q n", q=2, n=P)[:, :, q, :]

    with stage(nc) as st:
        x = st.sb("re_x", [P, 2, 1024])
        cs = st.sb("re_cs", [P, NT, 64])
        t1, t2, t3, t4 = (st.sb(f"re_t{i}", [P, 2, QK, 32]) for i in range(4))
        rot = st.sb("re_rot", [P, 2, QK, 64])
        dec = st.sb("re_dec", [P, 2, QK, 64])
        rowdec = st.sb("re_rowdec", [P, QK])
        dmat = st.sb("re_dmat", [P, RH * P])
        gch = st.sb("re_gch", [P, 2])
        qkT = st.sb("re_qkT", [P, 2, 6, P])
        sc = st.sb("re_sc", [P, 2, RH * P])
        state = st.sb("re_state", [P, 2, 2, RDV])
        ob = st.sb("re_ob", [P, 2, RH * RDV])
        tp = [st.ps(f"re_tp{i}", [P, BANK]) for i in range(2)]
        sps = [st.ps(f"re_s{i}", [P, BANK]) for i in range(2)]
        ops = [st.ps(f"re_o{i}", [P, BANK]) for i in range(2)]
        kv = st.ps("re_kv", [P, BANK])
        consts_in, m1, rotated, decayed, turned, T_ok, s_ok, sc_ok, o_ok, kv_ok, state_ok, ob_ok = (
            st.sem("re_" + n) for n in ("consts", "m1", "rotated", "decayed", "turned", "T_ok", "s_ok", "sc_ok", "o_ok", "kv_ok",
                                        "state_ok", "ob_ok"))
        x_in = [st.sem(f"re_x_in{u}") for u in range(2)]
        stored = [st.sem(f"re_stored{u}") for u in range(2)]
        with nc.Block() as block:
            @block.sync
            def _(sp):
                sp.dma_start(cs[:, :, :], C["ret_cs"].rearrange("(t p) n -> p t n", p=P)).then_inc(consts_in, 16)
                sp.dma_start(rowdec[:, :], C["ret_rowdec"]).then_inc(consts_in, 16)
                sp.dma_start(dmat[:, :], C["ret_decay"]).then_inc(consts_in, 16)
                sp.dma_start(gch[:, :], C["ret_gchunk"]).then_inc(consts_in, 16)
                for t in range(NT):
                    u = t % 2
                    if t >= 2:
                        sp.wait_ge(kv_ok, t - 1)
                        sp.wait_ge(o_ok, t - 1)
                        sp.wait_ge(m1, 4 * (t - 1))
                    sp.dma_start(x[:, u, :], rows_in[t * P:(t + 1) * P, 0:1024]).then_inc(x_in[u], 16)

            @block.gpsimd
            def _(pool):
                pool.wait_ge(consts_in, 64)
                for t in range(NT):
                    u = t % 2
                    pool.wait_ge(x_in[u], 16 * (t // 2 + 1))
                    if t >= 2:
                        pool.wait_ge(turned, t - 1)
                        pool.wait_ge(kv_ok, t - 1)
                    xv = x[:, u, 0:512].rearrange("p (h d) -> p h d", d=64)
                    c = cs[:, t, 0:32].unsqueeze(1).to_broadcast([P, QK, 32])
                    s = cs[:, t, 32:64].unsqueeze(1).to_broadcast([P, QK, 32])
                    for o, a, b in ((t1, 0, c), (t2, 1, s), (t3, 0, s), (t4, 1, c)):
                        pool.tensor_tensor(o[:, u, :, :], xv[:, :, 32 * a:32 * a + 32], b, ALU.mult).then_inc(m1, 1)
                    pool.wait_ge(m1, 4 * (t + 1))
                    pool.tensor_tensor(rot[:, u, :, 0:32], t1[:, u, :, :], t2[:, u, :, :], ALU.subtract).then_inc(rotated, 1)
                    pool.tensor_tensor(rot[:, u, :, 32:64], t3[:, u, :, :], t4[:, u, :, :], ALU.add).then_inc(rotated, 1)
                    pool.wait_ge(rotated, 2 * (t + 1))
                    pool.tensor_tensor(dec[:, u, :, :], rot[:, u, :, :], rowdec[:, :].unsqueeze(2).to_broadcast([P, QK, 64]),
                                       ALU.mult).then_inc(decayed, 1)

            @block.tensor
            def _(pe):
                for t in range(NT):
                    u = t % 2
                    pe.wait_ge(decayed, t + 1)
                    if t >= 1:
                        pe.wait_ge(T_ok, 2 * t)
                    r = rot[:, u, :, :].rearrange("p h d -> p (h d)")
                    d = dec[:, u, :, :].rearrange("p h d -> p (h d)")
                    for j in range(4):
                        pe.transpose(tp[0][:, j * P:(j + 1) * P], r[:, j * P:(j + 1) * P], ident[:, :])
                    for j in range(2):
                        mm = pe.transpose(tp[1][:, j * P:(j + 1) * P], d[:, j * P:(j + 1) * P], ident[:, :])
                    mm.then_inc(turned, 1)
                    pe.wait_ge(T_ok, 2 * (t + 1))
                    if t >= 1:
                        pe.wait_ge(sc_ok, 2 * t)
                    for h in range(RH):
                        p0, j = 64 * (h % 2), h // 2
                        mm = pe.matmul(sps[h % 2][:, j * P:(j + 1) * P], qkT[p0:p0 + 64, u, 2 + j, :], qkT[p0:p0 + 64, u, j, :],
                                       start=True, stop=True)
                    mm.then_inc(s_ok, 1)
                    if t >= 1:
                        pe.wait_ge(state_ok, 2 * t + 1)
                    for h in range(RH):
                        p0, j = 64 * (h % 2), h // 2
                        mm = pe.matmul(kv[p0:p0 + 64, j * RDV:(j + 1) * RDV], dec[:, u, RH + h, :],
                                       x[:, u, 512 + h * RDV:512 + (h + 1) * RDV], start=True, stop=True, skip_group_check=True)
                    mm.then_inc(kv_ok, 1)
                    pe.wait_ge(sc_ok, 2 * (t + 1))
                    pe.wait_ge(state_ok, 2 * t + 1)
                    if t >= 1:
                        pe.wait_ge(ob_ok, 2 * t)
                    for h in range(RH):
                        p0, j = 64 * (h % 2), h // 2
                        o = ops[h % 2][:, j * RDV:(j + 1) * RDV]
                        pe.matmul(o, sc[:, u, h * P:(h + 1) * P], x[:, u, 512 + h * RDV:512 + (h + 1) * RDV], start=True, stop=False)
                        mm = pe.matmul(o, qkT[p0:p0 + 64, u, 4 + j, :], state[p0:p0 + 64, u, j, :], start=False, stop=True)
                    mm.then_inc(o_ok, 1)

            @block.vector
            def _(dve):
                dve.memset(state[:, 0, :, :], 0.0).then_inc(state_ok, 1)
                dve.wait_ge(consts_in, 64)
                for t in range(NT):
                    u = t % 2
                    dve.wait_ge(turned, t + 1)
                    if t >= 2:
                        dve.wait_ge(o_ok, t - 1)
                    dve.tensor_copy(qkT[:, u, 0:4, :].rearrange("p j n -> p (j n)"), tp[0][:, :]).then_inc(T_ok, 1)
                    dve.tensor_copy(qkT[:, u, 4:6, :].rearrange("p j n -> p (j n)"), tp[1][:, 0:2 * P]).then_inc(T_ok, 1)
                    dve.wait_ge(s_ok, t + 1)
                    for q in range(2):
                        dve.tensor_tensor(by_parity(sc[:, u, :], q), sps[q][:, 0:2 * P].rearrange("p (j n) -> p j n", j=2),
                                          by_parity(dmat[:, :], q), ALU.mult).then_inc(sc_ok, 1)
                    dve.wait_ge(kv_ok, t + 1)
                    dve.wait_ge(state_ok, 2 * t + 1)
                    if t >= 1:
                        dve.wait_ge(o_ok, t)
                    for j in range(2):
                        dve.scalar_tensor_tensor(out=state[:, 1 - u, j, :], in0=state[:, u, j, :], scalar=gch[:, j:j + 1],
                                                 in1=kv[:, j * RDV:(j + 1) * RDV], op0=ALU.mult, op1=ALU.add).then_inc(state_ok, 1)

            @block.scalar
            def _(act):
                for t in range(NT):
                    u = t % 2
                    act.wait_ge(o_ok, t + 1)
                    if t >= 2:
                        act.wait_ge(stored[u], 16 * (t // 2))
                    for q in range(2):
                        act.activation(by_parity(ob[:, u, :], q), ops[q][:, 0:2 * P].rearrange("p (j n) -> p j n", j=2),
                                       ACT.Copy).then_inc(ob_ok, 1)
                    act.wait_ge(ob_ok, 2 * (t + 1))
                    act.dma_start(rows(out, t), ob[:, u, :]).then_inc(stored[u], 16)
                act.wait_ge(stored[0], 64)
                act.wait_ge(stored[1], 64)



def stick_breaking(nc, ident, heads, qkT_in, v_in, C, out):
    T8, DV = NT, 64
    widths = [(i + 1) * P for i in range(T8)]
    with stage(nc) as st:
        qraw = st.sb("sb_qraw", [64, 2, S])
        qT = st.sb("sb_qT", [64, 2, S])
        kT = st.sb("sb_kT", [64, 2, S])
        v = st.sb("sb_v", [P, 2, NT, DV])
        az = st.sb("sb_az", [P, S])
        ez = st.sb("sb_ez", [P, S])
        lg = st.sb("sb_lg", [P, 2, S])
        sp_ = st.sb("sb_sp", [P, S])
        cu = st.sb("sb_cu", [P, S])
        un = st.sb("sb_un", [P, 2, S])
        w = st.sb("sb_w", [P, 2, S])
        wT = st.sb("sb_wT", [P, 2, S])
        ones = st.sb("sb_ones", [P, S])
        masks = st.sb("sb_masks", [P, 2, P])
        o = st.sb("sb_ob", [P, 2, NT, DV])
        sps = [st.ps(f"sb_s{s}", [P, S]) for s in range(2)]
        tps = st.ps("sb_t", [P, S])
        ops = [st.ps(f"sb_op{s}", [P, BANK]) for s in range(2)]
        head_in = [st.sem(f"sb_head_in{s}") for s in range(2)]
        stored = [st.sem(f"sb_stored{s}") for s in range(2)]
        (consts_in, ones_ok, q_ok, z_ok, az_ok, ez_ok, lg_ok, sp_ok, spm_ok, cu_ok, un_ok, unm_ok, w_ok, turned_a, turned_b,
         wT_a, wT_b, pv_done, o_done) = (
            st.sem("sb_" + n) for n in ("consts", "ones_ok", "q_ok", "z_ok", "az_ok", "ez_ok", "lg_ok", "sp_ok", "spm_ok", "cu_ok",
                                        "un_ok", "unm_ok", "w_ok", "turned_a", "turned_b", "wT_a", "wT_b", "pv_done", "o_done"))
        passed = st.sem("sb_passed")

        def steps(eng, body):
            with eng.Fori(0, heads // 2) as r:
                for l in range(2 * T8 + 3):
                    body(l, r)

        def halves(i):
            return min(i + 1, BANK // P), i + 1

        with nc.Block() as block:
            @block.sync
            def _(sp):
                def load(h, u):
                    sp.dma_start(qraw[:, u, :], qkT_in[bass.ds(h * 64, 64), :]).then_inc(head_in[u], 16)
                    sp.dma_start(kT[:, u, :], qkT_in[bass.ds(h * 64 + 512, 64), :]).then_inc(head_in[u], 16)
                    sp.dma_start(v[:, u, :, :], v_in[:, bass.ds(h * 64, 64)].rearrange("(t p) d -> p t d", p=P)).then_inc(head_in[u], 16)

                def store(h, u):
                    sp.wait_ge(o_done, h * T8 + (T8 + 3))
                    sp.dma_start(out[:, bass.ds(h * DV, DV)].rearrange("(t p) d -> p t d", p=P),
                                 o[:, u, :, :]).then_inc(stored[u], 16)

                sp.sem_inc(stored[0], 16)
                sp.sem_inc(stored[1], 16)
                sp.dma_start(masks[:, :, :], C["strict"]).then_inc(consts_in, 16)
                for u in range(2):
                    load(u, u)
                with sp.Fori(0, heads // 2 - 1) as r:
                    for u in range(2):
                        h = r * 2 + u
                        store(h, u)
                        sp.wait_ge(pv_done, h * T8 + (T8 + 16))
                        load(h + 2, u)
                for u in range(2):
                    store(heads - 2 + u, u)
                for u in range(2):
                    sp.wait_ge(stored[u], 16 * (heads // 2 + 1))

            @block.gpsimd
            def _(pool):
                pool.wait_ge(consts_in, 16)

                def body(l, r):
                    T = r * 16 + l
                    if l in (0, T8):
                        u = l // T8
                        pool.wait_ge(head_in[u], r * 48 + 48)
                        pool.wait_ge(pv_done, T + 1 if u == 0 else T - 7 + 8)
                        pool.sem_inc(passed, 1)
                        pool.tensor_scalar(qT[:, u, :], qraw[:, u, :], 0.125, None, ALU.mult).then_inc(q_ok, 1)
                    if l < 16:
                        i = l % T8
                        pool.wait_ge(un_ok, T + 3)
                        un_d = un[:, l % 2, i * P:(i + 1) * P]
                        pool.tensor_tensor(un_d, un_d, masks[:, 1, :], ALU.add).then_inc(unm_ok, 1)
                steps(pool, body)

            @block.tensor
            def _(pe):
                pe.sem_inc(turned_a, 2)
                pe.sem_inc(turned_b, 2)
                pe.sem_inc(pv_done, 16)

                def body(l, r):
                    T = r * 16 + l
                    if l < 16:
                        u, i = l // T8, l % T8
                        if i == 0:
                            pe.wait_ge(q_ok, r * 2 + (u + 1))
                            pe.wait_ge(head_in[u], r * 48 + 48)
                        pe.wait_ge(un_ok, T + 1)
                        for c0 in range(0, widths[i], BANK):
                            c1 = min(widths[i], c0 + BANK)
                            mm = pe.matmul(sps[l % 2][:, c0:c1], qT[:, u, i * P:(i + 1) * P], kT[:, u, c0:c1], start=True, stop=True)
                        mm.then_inc(z_ok, 1)
                    m = l - 2
                    if 0 <= m < 16:
                        i = m % T8
                        a, b = halves(i)
                        pe.wait_ge(w_ok, T + 1)
                        pe.wait_ge(wT_a, T)
                        pe.wait_ge(wT_b, T)
                        for k in range(b):
                            mm = pe.transpose(tps[:, k * P:(k + 1) * P], w[:, m % 2, k * P:(k + 1) * P], ident[:, :])
                            if k == a - 1 and b > a:
                                mm.then_inc(turned_a, 1)
                        if b > a:
                            mm.then_inc(turned_b, 1)
                        else:
                            mm.then_inc(turned_a, 1)
                            pe.wait_ge(turned_a, T + 1)
                            pe.sem_inc(turned_b, 1)
                    m = l - 3
                    if 0 <= m < 16:
                        u, i = m // T8, m % T8
                        pe.wait_ge(o_done, T - 1)
                        pe.wait_ge(wT_a, T)
                        pe.wait_ge(wT_b, T)
                        for k in range(i + 1):
                            mm = pe.matmul(ops[m % 2][:, 0:DV], wT[:, m % 2, k * P:(k + 1) * P], v[:, u, k, :],
                                           start=(k == 0), stop=(k == i))
                        mm.then_inc(pv_done, 1)
                steps(pe, body)

            @block.vector
            def _(dve):
                dve.sem_inc(un_ok, 2)
                dve.sem_inc(wT_a, 2)
                dve.sem_inc(o_done, 3)
                dve.memset(ones[:, :], 1.0).then_inc(ones_ok, 1)
                dve.wait_ge(ones_ok, 1)
                dve.wait_ge(consts_in, 16)

                def body(l, r):
                    T = r * 16 + l
                    if l < 16:
                        i = l % T8
                        n = widths[i]
                        dve.wait_ge(lg_ok, T + 1)
                        dve.scalar_tensor_tensor(out=sp_[:, 0:n], in0=sps[l % 2][:, 0:n], scalar=0.0, in1=lg[:, l % 2, 0:n],
                                                 op0=ALU.max, op1=ALU.add).then_inc(sp_ok, 1)
                        dve.wait_ge(sp_ok, T + 1)
                        dve.tensor_tensor(sp_[:, n - P:n], sp_[:, n - P:n], masks[:, 0, :], ALU.mult).then_inc(spm_ok, 1)
                        dve.wait_ge(spm_ok, T + 1)
                        dve.tensor_tensor_scan(cu[:, 0:n][:, ::-1], ones[:, 0:n], sp_[:, 0:n][:, ::-1], 0.0,
                                               ALU.mult, ALU.subtract).then_inc(cu_ok, 1)
                        dve.wait_ge(cu_ok, T + 1)
                        dve.wait_ge(w_ok, T + 1)
                        dve.tensor_tensor(un[:, l % 2, 0:n], sps[l % 2][:, 0:n], cu[:, 0:n], ALU.add).then_inc(un_ok, 1)
                    m = l - 2
                    if 0 <= m < 16:
                        a, _ = halves(m % T8)
                        dve.wait_ge(turned_a, T + 1)
                        dve.wait_ge(pv_done, T + 13)
                        dve.tensor_copy(wT[:, m % 2, 0:a * P], tps[:, 0:a * P]).then_inc(wT_a, 1)
                    m = l - 3
                    if 0 <= m < 16:
                        u, i = m // T8, m % T8
                        dve.wait_ge(pv_done, T + 14)
                        if i == 0:
                            dve.wait_ge(stored[u], r * 16 + 16)
                        dve.tensor_copy(o[:, u, i, :], ops[m % 2][:, 0:DV]).then_inc(o_done, 1)
                steps(dve, body)

            @block.scalar
            def _(act):
                act.sem_inc(w_ok, 2)
                act.sem_inc(wT_b, 2)

                def body(l, r):
                    T = r * 16 + l
                    if l < 16:
                        i = l % T8
                        n = widths[i]
                        act.wait_ge(z_ok, T + 1)
                        act.activation(az[:, 0:n], sps[l % 2][:, 0:n], ACT.Abs).then_inc(az_ok, 1)
                        act.wait_ge(az_ok, T + 1)
                        act.activation(ez[:, 0:n], az[:, 0:n], ACT.Exp, scale=-1.0).then_inc(ez_ok, 1)
                        act.wait_ge(ez_ok, T + 1)
                        act.wait_ge(un_ok, T + 1)
                        act.activation(lg[:, l % 2, 0:n], ez[:, 0:n], ACT.Ln, bias=1.0).then_inc(lg_ok, 1)
                    m = l - 1
                    if 0 <= m < 16:
                        n = widths[m % T8]
                        act.wait_ge(unm_ok, T)
                        act.wait_ge(un_ok, T + 2)
                        act.wait_ge(turned_b, T)
                        act.activation(w[:, m % 2, 0:n], un[:, m % 2, 0:n], ACT.Exp).then_inc(w_ok, 1)
                    m = l - 2
                    if 0 <= m < 16:
                        a, b = halves(m % T8)
                        act.wait_ge(turned_b, T + 1)
                        if b > a:
                            act.wait_ge(pv_done, T + 13)
                            act.activation(wT[:, m % 2, a * P:b * P], tps[:, a * P:b * P], ACT.Copy).then_inc(wT_b, 1)
                        else:
                            act.sem_inc(wT_b, 1)
                steps(act, body)



HH = 4
LEVELS = [64, 32, 16, 8, 4, 2, 1]


def hgrn2(nc, ident, fT_in, v_in, C, out):
    NL = len(LEVELS)
    with stage(nc) as st:
        q = st.sb("hg_q", [P, 2, S])
        f = st.sb("hg_f", [P, 2, S])
        vv = st.sb("hg_v", [P, 2, NT, P])
        kk = st.sb("hg_k", [P, S])
        az, ez, lf = (st.sb("hg_" + n, [P, S]) for n in ("az", "ez", "lf"))
        b = st.sb("hg_b", [P, S])
        df = st.sb("hg_df", [P, 2, S])
        ex = st.sb("hg_ex", [P, 2, S])
        eb, el, qb, kb = (st.sb("hg_" + n, [P, S]) for n in ("eb", "el", "qb", "kb"))
        dl = st.sb("hg_dl", [P, S])
        qk = st.sb("hg_qk", [P, NL, S])
        ones = st.sb("hg_ones", [P, P])
        mask = st.sb("hg_mask", [P, NL + 1, P])
        ms = st.sb("hg_ms", [P, 2, NL + 1, P])
        sT = st.sb("hg_sT", [P, 2, P])
        kr = st.sb("hg_kr", [P, 2, P])
        state = st.sb("hg_state", [P, 2, P])
        ob = st.sb("hg_ob", [P, 2, NT, P])
        sps = [st.ps(f"hg_s{i}", [P, 2 * BANK]) for i in range(2)]
        tps, ops, kvs = st.ps("hg_t", [P, BANK]), st.ps("hg_o", [P, BANK]), st.ps("hg_kv", [P, BANK])
        head_in = [st.sem(f"hg_in{u}") for u in range(2)]
        stored = [st.sem(f"hg_stored{u}") for u in range(2)]
        (consts_in, ones_ok, k_ok, az_ok, ez_ok, lg_ok, lf_ok, b_ok, df_ok, ex_ok, qk_ok, dl_ok, eb_ok, el_ok, qb_ok, kb_ok,
         s_ok, ms_ok, sT_ok, turned, kr_ok, o_ok, kv_ok, state_ok, ob_ok, state0) = (
            st.sem("hg_" + n) for n in ("consts", "ones_ok", "k_ok", "az_ok", "ez_ok", "lg_ok", "lf_ok", "b_ok", "df_ok", "ex_ok",
                                        "qk_ok", "dl_ok", "eb_ok", "el_ok", "qb_ok", "kb_ok", "s_ok", "ms_ok", "sT_ok", "turned",
                                        "kr_ok", "o_ok", "kv_ok", "state_ok", "ob_ok", "state0"))

        def split(x, m):
            return x.rearrange("p (n h m) -> p n h m", h=2, m=m)

        with nc.Block() as block:
            @block.sync
            def _(sp):
                sp.dma_start(mask[:, :, :], C["levels"]).then_inc(consts_in, 16)

                for h in range(HH):
                    u = h % 2
                    if h >= 2:
                        sp.wait_ge(o_ok, NT * (h - 1))
                        sp.wait_ge(kv_ok, NT * (h - 1))
                    sp.dma_start(f[:, u, :], fT_in[512 + h * P:512 + (h + 1) * P, :]).then_inc(head_in[u], 16)
                    sp.dma_start(q[:, u, :], fT_in[h * P:(h + 1) * P, :]).then_inc(head_in[u], 16)
                    sp.dma_start(vv[:, u, :, :], v_in[:, h * P:(h + 1) * P].rearrange("(t p) d -> p t d", p=P)).then_inc(head_in[u], 16)
                    if h >= 1:
                        sp.wait_ge(ob_ok, NT * h)
                        sp.dma_start(out[:, (h - 1) * P:h * P].rearrange("(t p) d -> p t d", p=P), ob[:, 1 - u, :, :]).then_inc(stored[1 - u], 16)
                sp.wait_ge(ob_ok, NT * HH)
                sp.dma_start(out[:, (HH - 1) * P:HH * P].rearrange("(t p) d -> p t d", p=P), ob[:, 1, :, :]).then_inc(stored[1], 16)
                sp.wait_ge(stored[0], 32)
                sp.wait_ge(stored[1], 32)

            @block.scalar
            def _(act):
                for h in range(HH):
                    u = h % 2
                    act.wait_ge(head_in[u], 48 * (h // 2 + 1))
                    if h >= 1:
                        act.wait_ge(qk_ok, 2 * NL * h)
                        act.wait_ge(kb_ok, h)
                        act.wait_ge(s_ok, NT * h)
                    act.activation(kk[:, :], f[:, u, :], ACT.Sigmoid, scale=-1.0).then_inc(k_ok, 1)
                    act.activation(az[:, :], f[:, u, :], ACT.Abs).then_inc(az_ok, 1)
                    act.wait_ge(az_ok, h + 1)
                    act.activation(ez[:, :], az[:, :], ACT.Exp, scale=-1.0).then_inc(ez_ok, 1)
                    act.wait_ge(ez_ok, h + 1)
                    if h >= 1:
                        act.wait_ge(b_ok, NT * h)
                    act.activation(az[:, :], ez[:, :], ACT.Ln, bias=1.0).then_inc(lg_ok, 1)
                    for n in range(NL):
                        g = h * NL + n
                        act.wait_ge(df_ok, 2 * (g + 1))
                        if g >= 2:
                            act.wait_ge(qk_ok, 2 * (g - 1))
                        act.activation(ex[:, n % 2 if h % 2 == 0 else (n + 1) % 2, :], df[:, g % 2, :], ACT.Exp).then_inc(ex_ok, 1)
                    act.wait_ge(b_ok, NT * (h + 1))
                    if h >= 1:
                        act.wait_ge(state_ok, NT * h)
                    act.activation(eb[:, :], b[:, :], ACT.Exp).then_inc(eb_ok, 1)
                    act.wait_ge(dl_ok, h + 1)
                    act.activation(el[:, :], dl[:, :], ACT.Exp).then_inc(el_ok, 1)
                    for c in range(NT):
                        g = h * NT + c
                        act.wait_ge(turned, g + 1)
                        if g >= 2:
                            act.wait_ge(kv_ok, g - 1)
                        act.activation(kr[:, g % 2, :], tps[:, 0:P], ACT.Copy).then_inc(kr_ok, 1)
                        if c == 0 and h >= 2:
                            act.wait_ge(stored[u], 16 * (h // 2))
                        act.wait_ge(o_ok, g + 1)
                        act.activation(ob[:, u, c, :], ops[:, 0:P], ACT.Copy).then_inc(ob_ok, 1)

            @block.gpsimd
            def _(pool):
                for h in range(HH):
                    u = h % 2
                    if h >= 1:
                        pool.wait_ge(s_ok, NT * h)
                        pool.wait_ge(turned, NT * h)
                        pool.wait_ge(o_ok, NT * h)
                    for n, m in enumerate(LEVELS):
                        g = h * NL + n
                        pool.wait_ge(ex_ok, g + 1)
                        pool.wait_ge(k_ok, h + 1)
                        pool.tensor_tensor(split(qk[:, n, :], m)[:, :, 0, :], split(kk[:, :], m)[:, :, 0, :],
                                           split(ex[:, g % 2, :], m)[:, :, 0, :], ALU.mult).then_inc(qk_ok, 1)
                        pool.tensor_tensor(split(qk[:, n, :], m)[:, :, 1, :], split(q[:, u, :], m)[:, :, 1, :],
                                           split(ex[:, g % 2, :], m)[:, :, 1, :], ALU.mult).then_inc(qk_ok, 1)
                    pool.wait_ge(eb_ok, h + 1)
                    pool.tensor_tensor(qb[:, :], q[:, u, :], eb[:, :], ALU.mult).then_inc(qb_ok, 1)
                    pool.wait_ge(el_ok, h + 1)
                    pool.tensor_tensor(kb[:, :], kk[:, :], el[:, :], ALU.mult).then_inc(kb_ok, 1)

            @block.vector
            def _(dve):
                dve.memset(ones[:, :], 1.0).then_inc(ones_ok, 1)
                dve.wait_ge(ones_ok, 1)
                dve.wait_ge(consts_in, 16)
                for h in range(HH):
                    u = h % 2
                    dve.wait_ge(lg_ok, h + 1)
                    dve.scalar_tensor_tensor(out=lf[:, :], in0=f[:, u, :], scalar=0.0, in1=az[:, :], op0=ALU.min,
                                             op1=ALU.subtract).then_inc(lf_ok, 1)
                    dve.wait_ge(lf_ok, h + 1)
                    if h >= 1:
                        dve.wait_ge(eb_ok, h)
                    for c in range(NT):
                        dve.tensor_tensor_scan(b[:, c * P:(c + 1) * P], ones[:, :], lf[:, c * P:(c + 1) * P], 0.0,
                                               ALU.mult, ALU.add).then_inc(b_ok, 1)
                    dve.wait_ge(b_ok, NT * (h + 1))
                    for n, m in enumerate(LEVELS):
                        g = h * NL + n
                        if g >= 2:
                            dve.wait_ge(ex_ok, g - 1)
                        bv, dv = split(b[:, :], m), split(df[:, g % 2, :], m)
                        mid = bv[:, :, 0, m - 1:m].to_broadcast([P, S // (2 * m), m])
                        dve.tensor_tensor(dv[:, :, 0, :], mid, bv[:, :, 0, :], ALU.subtract).then_inc(df_ok, 1)
                        dve.tensor_tensor(dv[:, :, 1, :], bv[:, :, 1, :], mid, ALU.subtract).then_inc(df_ok, 1)
                    bc = b[:, :].rearrange("p (n m) -> p n m", m=P)
                    if h >= 1:
                        dve.wait_ge(el_ok, h)
                    dve.tensor_tensor(dl[:, :].rearrange("p (n m) -> p n m", m=P), bc[:, :, P - 1:P].to_broadcast([P, NT, P]), bc,
                                      ALU.subtract).then_inc(dl_ok, 1)
                    if h >= 1:
                        dve.wait_ge(o_ok, NT * h)
                    dve.memset(state[:, 0, :], 0.0).then_inc(state0, 1)
                    for c in range(NT):
                        g = h * NT + c
                        dve.wait_ge(s_ok, g + 1)
                        dve.tensor_tensor(ms[:, g % 2, :, :].rearrange("p l n -> p (l n)"), sps[g % 2][:, :],
                                          mask[:, :, :].rearrange("p l n -> p (l n)"), ALU.mult).then_inc(ms_ok, 1)
                        dve.wait_ge(ms_ok, g + 1)
                        if g >= 2:
                            dve.wait_ge(o_ok, g - 1)
                        dve.reduce_sum(sT[:, g % 2, :], ms[:, g % 2, :, :].rearrange("p l n -> p n l"), AX.X).then_inc(sT_ok, 1)
                        dve.wait_ge(kv_ok, g + 1)
                        if c == 0:
                            dve.wait_ge(state0, h + 1)
                        else:
                            dve.wait_ge(state_ok, g)
                            dve.wait_ge(o_ok, g)
                        dve.wait_ge(eb_ok, h + 1)
                        dve.scalar_tensor_tensor(out=state[:, (c + 1) % 2, :], in0=state[:, c % 2, :],
                                                 scalar=eb[:, c * P + P - 1:c * P + P], in1=kvs[:, 0:P],
                                                 op0=ALU.mult, op1=ALU.add).then_inc(state_ok, 1)

            @block.tensor
            def _(pe):
                for h in range(HH):
                    u = h % 2
                    pe.wait_ge(qk_ok, 2 * NL * (h + 1))
                    pe.wait_ge(kb_ok, h + 1)
                    pe.wait_ge(qb_ok, h + 1)
                    for c in range(NT):
                        g = h * NT + c
                        cc = slice(c * P, (c + 1) * P)
                        if g >= 2:
                            pe.wait_ge(ms_ok, g - 1)
                        for n in range(NL):
                            pe.matmul(sps[g % 2][:, n * P:(n + 1) * P], qk[:, n, cc], qk[:, n, cc], start=True, stop=True)
                        pe.matmul(sps[g % 2][:, NL * P:(NL + 1) * P], kk[:, cc], q[:, u, cc], start=True, stop=True).then_inc(s_ok, 1)
                        if g >= 1:
                            pe.wait_ge(kr_ok, g)
                        pe.transpose(tps[:, 0:P], kb[:, cc], ident[:, :]).then_inc(turned, 1)
                        pe.wait_ge(kr_ok, g + 1)
                        if g >= 1:
                            pe.wait_ge(state_ok, g)
                        pe.matmul(kvs[:, 0:P], kr[:, g % 2, :], vv[:, u, c, :], start=True, stop=True).then_inc(kv_ok, 1)
                        pe.wait_ge(sT_ok, g + 1)
                        if c == 0:
                            pe.wait_ge(state0, h + 1)
                        if g >= 1:
                            pe.wait_ge(ob_ok, g)
                        pe.matmul(ops[:, 0:P], sT[:, g % 2, :], vv[:, u, c, :], start=True, stop=False)
                        pe.matmul(ops[:, 0:P], qb[:, cc], state[:, c % 2, :], start=False, stop=True).then_inc(o_ok, 1)



def rg_lru(nc, xT_in, A, hT):
    NTI = 4
    with stage(nc) as st:
        x = st.sb("lr_x", [P, 2, S + 4])
        gt = st.sb("lr_gt", [P, 2, S])
        cva, cvb = st.sb("lr_cva", [P, 2, S]), st.sb("lr_cvb", [P, 2, S])
        wa, wx = st.sb("lr_wa", [P, NTI, P]), st.sb("lr_wx", [P, NTI, P])
        cw, cb = st.sb("lr_cw", [P, NTI, 4]), st.sb("lr_cb", [P, NTI])
        ba, bx, lam = st.sb("lr_ba", [P, NTI]), st.sb("lr_bx", [P, NTI]), st.sb("lr_lam", [P, NTI])
        sm = [st.sb(f"lr_sm{i}", [P, NTI]) for i in range(12)]
        r, ig, y, a, th, a2, m2, mu, u1, u2, hs, sg, gs = (
            st.sb("lr_" + n, [P, S]) for n in ("r", "ig", "y", "a", "th", "a2", "m2", "mu", "u1", "u2", "hs", "sg", "gs"))
        pa, px = st.ps("lr_pa", [P, S]), st.ps("lr_px", [P, S])
        consts_in, cleared, e_ok, c8_ok, d, conv, mm, r_ok, ig_ok, y_ok, a_ok, th_ok, m2_ok, mu_ok, sg_ok, h_ok, lam_ok, pads = (
            st.sem("lr_" + n) for n in ("consts", "cleared", "e_ok", "c8_ok", "step", "conv", "mm", "r_ok", "ig_ok", "y_ok", "a_ok",
                                        "th_ok", "m2_ok", "mu_ok", "sg_ok", "h_ok", "lam_ok", "pads"))
        wab_in = st.sem("lr_wab_in")
        x_in = [st.sem(f"lr_x_in{u}") for u in range(2)]
        with nc.Block() as block:
            @block.sync
            def _(sp):
                slow = dict(allow_slow_non_contiguous=True)
                for j in range(4):
                    sp.dma_start(cw[:, :, j], A["conv_w_2"][0, j, :].rearrange("(t p) -> p t", p=P), **slow).then_inc(consts_in, 16)
                for dst, name in ((cb, "conv_b_2"), (ba, "lru_b_a_2"), (bx, "lru_b_x_2"), (lam, "lru_lambda_2")):
                    sp.dma_start(dst[:, :], A[name][0].rearrange("(t p) -> p t", p=P), **slow).then_inc(consts_in, 16)
                sp.wait_ge(cleared, 2)
                for dst, name in ((wa, "lru_w_a_2"), (wx, "lru_w_x_2")):
                    for b in range(2):
                        sp.dma_start(dst[64 * b:64 * b + 64, :, 64 * b:64 * b + 64],
                                     A[name][0].rearrange("(t b) i j -> b i t j", b=2)[b]).then_inc(wab_in, 16)
                sp.wait_ge(pads, 1)
                for t in range(NTI):
                    if t >= 2:
                        sp.wait_ge(h_ok, t - 1)
                    sp.dma_start(x[:, t % 2, 4:S + 4], xT_in[t * P:(t + 1) * P, :]).then_inc(x_in[t % 2], 16)
                    sp.dma_start(gt[:, t % 2, :], xT_in[512 + t * P:512 + (t + 1) * P, :]).then_inc(x_in[t % 2], 16)

            @block.gpsimd
            def _(pool):
                pool.memset(wa[:, :, :], 0.0).then_inc(cleared, 1)
                pool.memset(wx[:, :, :], 0.0).then_inc(cleared, 1)
                for t in range(NTI):
                    u = t % 2
                    pool.wait_ge(sg_ok, t + 1)
                    if t >= 1:
                        pool.wait_ge(h_ok, t)
                    pool.tensor_tensor(gs[:, :], gt[:, u, :], sg[:, :], ALU.mult).then_inc(lam_ok, 1)

            @block.tensor
            def _(pe):
                pe.wait_ge(wab_in, 16 * 4)
                for t in range(NTI):
                    pe.wait_ge(conv, 4 * (t + 1))
                    if t >= 1:
                        pe.wait_ge(ig_ok, t)
                        pe.wait_ge(r_ok, t)
                    for dst, w in ((pa, wa), (px, wx)):
                        for n in range(2):
                            m = pe.matmul(dst[:, n * BANK:(n + 1) * BANK], w[:, t, :], cvb[:, t % 2, n * BANK:(n + 1) * BANK],
                                          start=True, stop=True)
                    m.then_inc(mm, 1)

            @block.scalar
            def _(act):
                act.wait_ge(e_ok, 1)
                act.activation(sm[1][:, :], sm[0][:, :], ACT.Exp, scale=-1.0).then_inc(e_ok, 1)
                act.wait_ge(consts_in, 16 * 8)
                for t in range(NTI):
                    u = t % 2
                    act.wait_ge(x_in[u], 32 * (t // 2 + 1))
                    if t >= 1:
                        act.wait_ge(lam_ok, t)
                        act.wait_ge(h_ok, t)
                    act.activation(sg[:, :], gt[:, u, :], ACT.Sigmoid).then_inc(sg_ok, 1)
                    act.wait_ge(mm, t + 1)
                    act.activation(r[:, :], pa[:, :], ACT.Sigmoid, bias=ba[:, t:t + 1]).then_inc(r_ok, 1)
                    act.activation(ig[:, :], px[:, :], ACT.Sigmoid, bias=bx[:, t:t + 1]).then_inc(ig_ok, 1)
                    act.wait_ge(y_ok, t + 1)
                    act.activation(a[:, :], y[:, :], ACT.Exp, scale=-1.0).then_inc(a_ok, 1)
                    act.activation(th[:, :], y[:, :], ACT.Tanh).then_inc(th_ok, 1)
                    act.wait_ge(m2_ok, t + 1)
                    act.activation(mu[:, :], m2[:, :], ACT.Sqrt).then_inc(mu_ok, 1)

            @block.vector
            def _(dve):
                n = [0]

                def step(ins):
                    n[0] += 1
                    ins.then_inc(d, 1)
                    dve.wait_ge(d, n[0])

                dve.memset(x[:, :, 0:4], 0.0).then_inc(pads, 1)
                dve.wait_ge(consts_in, 16 * 8)
                step(dve.scalar_tensor_tensor(out=sm[0][:, :], in0=lam[:, :], scalar=-1.0, in1=lam[:, :], op0=ALU.mult, op1=ALU.max))
                dve.sem_inc(e_ok, 1)
                dve.wait_ge(e_ok, 2)
                step(dve.tensor_scalar(sm[2][:, :], sm[1][:, :], 2.0, None, ALU.add))
                step(dve.reciprocal(sm[3][:, :], sm[2][:, :]))
                step(dve.tensor_tensor(sm[4][:, :], sm[1][:, :], sm[3][:, :], ALU.mult))
                step(dve.tensor_tensor(sm[5][:, :], sm[4][:, :], sm[4][:, :], ALU.mult))
                step(dve.tensor_scalar(sm[6][:, :], sm[5][:, :], 1.0 / 17, 1.0 / 15, ALU.mult, ALU.add))
                for k in (13, 11, 9, 7, 5, 3, 1):
                    step(dve.tensor_tensor(sm[7][:, :], sm[6][:, :], sm[5][:, :], ALU.mult))
                    step(dve.tensor_scalar(sm[6][:, :], sm[7][:, :], 1.0 / k, None, ALU.add))
                step(dve.tensor_tensor(sm[8][:, :], sm[6][:, :], sm[4][:, :], ALU.mult))
                step(dve.tensor_scalar(sm[9][:, :], lam[:, :], -1.0, 0.0, ALU.mult, ALU.max))
                step(dve.scalar_tensor_tensor(out=sm[10][:, :], in0=sm[8][:, :], scalar=2.0, in1=sm[9][:, :], op0=ALU.mult, op1=ALU.add))
                step(dve.tensor_scalar(sm[11][:, :], sm[10][:, :], 8.0, None, ALU.mult))
                for t in range(NTI):
                    u = t % 2
                    dve.wait_ge(x_in[u], 32 * (t // 2 + 1))
                    if t == 0:
                        dve.wait_ge(pads, 1)
                    src = [x[:, u, 1 + j:1 + j + S] for j in range(4)]
                    if t >= 2:
                        dve.wait_ge(mm, t - 1)
                    dve.tensor_scalar(cva[:, u, :], src[0], cw[:, t, 0:1], cb[:, t:t + 1], ALU.mult, ALU.add).then_inc(conv, 1)
                    for j, (o, i) in enumerate(((cvb, cva), (cva, cvb), (cvb, cva)), 1):
                        dve.wait_ge(conv, 4 * t + j)
                        dve.scalar_tensor_tensor(out=o[:, u, :], in0=src[j], scalar=cw[:, t, j:j + 1], in1=i[:, u, :],
                                                 op0=ALU.mult, op1=ALU.add).then_inc(conv, 1)
                    xc = cvb[:, u, :]
                    dve.wait_ge(r_ok, t + 1)
                    step(dve.tensor_scalar(y[:, :], r[:, :], sm[11][:, t:t + 1], None, ALU.mult))
                    dve.sem_inc(y_ok, 1)
                    dve.wait_ge(ig_ok, t + 1)
                    dve.wait_ge(conv, 4 * t + 4)
                    step(dve.tensor_tensor(u1[:, :], ig[:, :], xc, ALU.mult))
                    dve.wait_ge(a_ok, t + 1)
                    step(dve.tensor_tensor(a2[:, :], a[:, :], a[:, :], ALU.mult))
                    dve.wait_ge(th_ok, t + 1)
                    dve.scalar_tensor_tensor(out=m2[:, :], in0=a2[:, :], scalar=1.0, in1=th[:, :], op0=ALU.add,
                                             op1=ALU.mult).then_inc(m2_ok, 1)
                    dve.wait_ge(mu_ok, t + 1)
                    step(dve.memset(mu[:, 0:1], 1.0))
                    step(dve.tensor_tensor(u2[:, :], mu[:, :], u1[:, :], ALU.mult))
                    step(dve.tensor_tensor_scan(hs[:, :], a[:, :], u2[:, :], 0.0, ALU.mult, ALU.add))
                    dve.wait_ge(lam_ok, t + 1)
                    dve.tensor_tensor(hT[:, 4 + t, :], hs[:, :], gs[:, :], ALU.mult).then_inc(h_ok, 1)


def second(nc, A, C, scr, ident, hT, out):
    norm_rows(nc, "e0", ident, D, [], [(0, D)], hT=hT, add=scr["xm"], post=A["g_final"], keep=scr["x2"],
              gain=gain_of([A["pre_norm_w_2"][0]]))
    we = A["even_w_in_2"][0]
    project(nc, "pe", hT, 8, [
        dict(kind="row", n=3, width=512, load=columns(we, 0, 512), dst=to_rows(scr["erows"], 0, 512)),
        dict(kind="T", n=2, width=512, load=columns(we, 1536, 512), dst=to_T(scr["sqkT"], 0, 512)),
        dict(kind="row", n=2, width=512, load=columns(we, 2560, 512), dst=to_rows(scr["srows"], 0, 512)),
    ])
    retention(nc, ident, scr["erows"], C, scr["ret"])
    stick_breaking(nc, ident, 8, scr["sqkT"], scr["srows"], C, scr["stick"])
    norm_rows(nc, "e1", ident, D, [(0, 512, lambda t: rows(scr["ret"], t)), (512, 512, lambda t: rows(scr["stick"], t))],
              [(128 * h, 128) for h in range(4)], hT=hT,
              gate=[(0, 512, lambda t: rows(scr["erows"][:, 1024:1536], t)), (512, 512, lambda t: rows(scr["srows"][:, 512:1024], t))])
    project(nc, "pf", hT, 8, [dict(kind="row", n=2, width=512, load=columns(A["even_w_out_2"][0], 0, 512),
                                   dst=to_rows(scr["y2"], 0, 512))])
    norm_rows(nc, "o0", ident, D, [(0, D, lambda t: rows(scr["x2"], t))], [(0, D)], hT=hT, add=scr["y2"],
              post=A["post_norm_w_2"][0], keep=scr["x3"], gain=gain_of([A["pre_norm_w_2"][1]]))
    wo = A["odd_w_in_2"][0]
    project(nc, "pg", hT, 8, [
        dict(kind="T", n=2, width=512, load=columns(wo, 0, 512), dst=to_T(scr["oT"], 0, 512)),
        dict(kind="row", n=2, width=512, load=columns(wo, 1024, 512), dst=to_rows(scr["orows"], 0, 512)),
        dict(kind="T", n=2, width=512, load=columns(wo, 2048, 512), dst=to_T(scr["oT"], 1024, 512)),
    ])
    hgrn2(nc, ident, scr["oT"], scr["orows"], C, scr["hc"])
    rg_lru(nc, scr["oT"][1024:2048, :], A, hT)
    norm_rows(nc, "o1", ident, 512, [(0, 512, lambda t: rows(scr["hc"], t))], [(128 * h, 128) for h in range(4)], hT=hT,
              gate=[(0, 512, lambda t: rows(scr["orows"][:, 512:1024], t))])
    project(nc, "ph", hT, 8, [dict(kind="row", n=2, width=512, load=columns(A["odd_w_out_2"][0], 0, 512),
                                   dst=to_rows(scr["y3"], 0, 512))])
    norm_rows(nc, "o2", ident, D, [(0, D, lambda t: rows(scr["x3"], t))], [], add=scr["y3"], post=A["post_norm_w_2"][1], keep=out)


SCRATCH.update(x2=(S, D), erows=(S, 1536), sqkT=(1024, S), srows=(S, 1024), ret=(S, 512), stick=(S, 512), y2=(S, D), x3=(S, D),
               oT=(2048, S), orows=(S, 1024), hc=(S, 512), y3=(S, D))


def build(nc, A, C, out):
    scr = {n: nc.dram_tensor("scr_" + n, s, F32, kind="Internal").ap() for n, s in SCRATCH.items()}
    with ExitStack() as ctx:
        ident = ctx.enter_context(nc.sbuf_tensor("ident", [P, P], F32))
        hT = ctx.enter_context(nc.sbuf_tensor("hT", [P, 8, S], F32))
        identity(nc, ident)
        first_attention(nc, A, C, scr, ident, hT)
        moe(nc, A, C, scr, ident, hT)
        second(nc, A, C, scr, ident, hT, out.rearrange("b s d -> (b s) d"))


def kernel(**inputs):
    import concourse.bacc as _bacc
    from concourse.bass_utils import run_bass_kernel_spmd as _run
    nc = _bacc.Bacc("TRN2", target_bir_lowering=False, num_devices=1)
    arrays, A, C = {}, {}, {}
    for name, v in inputs.items():
        if name == "hgrn_lb_logits_2":
            continue
        v = np.ascontiguousarray(v)
        arrays["in_" + name] = v
        A[name] = nc.dram_tensor("in_" + name, v.shape, F32, kind="ExternalInput").ap()
    for name, v in constants().items():
        arrays["const_" + name] = v
        C[name] = nc.dram_tensor("const_" + name, v.shape, F32, kind="ExternalInput").ap()
    out = nc.dram_tensor("out", (1, S, D), F32, kind="ExternalOutput").ap()
    build(nc, A, C, out)
    r = _run(nc, [arrays], core_ids=[0])
    return r.results[0]["out"]
```

```python
import math
from contextlib import ExitStack, contextmanager

import numpy as np
import concourse.bass as bass
from concourse import mybir

F32 = mybir.dt.float32
F32R = mybir.dt.float32r
U32 = mybir.dt.uint32
ALU = mybir.AluOpType
ACT = mybir.ActivationFunctionType
AX = mybir.AxisListType

P = 128
D = 1024
S = 1024
NT = S // P
BANK = 512
EPS = 1e-6
NEG = -1e30


class Stage:

    def __init__(self, nc):
        self.nc, self.ctx, self.sems = nc, ExitStack(), []

    def sb(self, name, shape, dt=F32):
        return self.ctx.enter_context(self.nc.sbuf_tensor(name, shape, dt))

    def ps(self, name, shape, dt=F32):
        return self.ctx.enter_context(self.nc.psum_tensor(name, shape, dt))

    def sem(self, name):
        s = self.nc.alloc_semaphore(name)
        self.sems.append(s)
        return s


@contextmanager
def stage(nc):
    st = Stage(nc)
    yield st
    nc.clear_and_free_semaphores(st.sems)
    nc.all_engine_barrier()
    st.ctx.close()


def tiled(ap):
    return ap.rearrange("(k p) n -> p k n", p=P)


def rows(ap, t):
    return ap[bass.ds(t * P, P), :]


def along(eng, count, step, body):
    if count == step:
        for i in range(count):
            body(i, i)
        return
    with eng.Fori(0, count // step) as r:
        for u in range(step):
            body(r * step + u, u)



HI, LO = 0, 1
PARTS = ((HI, HI), (HI, LO), (LO, HI))


def product(pe, out, n, a, b):
    for k in range(n):
        for i, (p, q) in enumerate(PARTS):
            mm = pe.matmul(out, a(p, k), b(q, k), start=(k == 0 and i == 0), stop=(k == n - 1 and i == 2))
    return mm


def project(nc, name, hT, nk, chunks, gain=None):
    N = len(chunks)

    def groups(ch):
        return NT if ch["kind"] == "row" else 2 * max(1, ch["width"] // P)

    def size(ch):
        return (P, ch["width"]) if ch["kind"] == "row" else (min(P, ch["width"]), BANK)

    uses = [[sum(groups(c) > j for c in chunks[:g]) for j in range(groups(ch))] for g, ch in enumerate(chunks)]
    loads = [len(ch["load"]) for ch in chunks]
    nst = [[16 * uses[g][j] for j in range(groups(ch))] for g, ch in enumerate(chunks)]

    with stage(nc) as st:
        raw = st.sb(name + "_raw", [P, 2, nk, BANK])
        w = st.sb(name + "_w", [P, 2, 2, nk, BANK], F32R)
        obuf = st.sb(name + "_o", [P, NT, BANK])
        gcol = st.sb(name + "_g", [P, nk]) if gain is not None else None
        acc = [st.ps(f"{name}_acc{j}", [P, BANK]) for j in range(NT)]
        gain_in = st.sem(name + "_gain_in")
        raw_in = [st.sem(f"{name}_raw_in{s}") for s in range(2)]
        hi_ok, lo_ok = st.sem(name + "_hi_ok"), st.sem(name + "_lo_ok")
        mm_done = [st.sem(f"{name}_mm{j}") for j in range(NT)]
        copied = [st.sem(f"{name}_copied{j}") for j in range(NT)]
        stored = [st.sem(f"{name}_stored{j}") for j in range(NT)]

        with nc.Block() as block:
            @block.sync
            def _(sp):
                if gain is not None:
                    for k0, v in gain:
                        sp.dma_start(gcol[:, k0:k0 + v.shape[0] // P], v.rearrange("(k p) -> p k", p=P),
                                     allow_slow_non_contiguous=True).then_inc(gain_in, 16)
                for g, ch in enumerate(chunks):
                    if g >= 2:
                        sp.wait_ge(lo_ok, nk * (g - 1))
                    for dst, src in ch["load"]:
                        sp.dma_start(raw[:, g % 2, :, dst], src).then_inc(raw_in[g % 2], 16)

            @block.tensor
            def _(pe):
                for g, ch in enumerate(chunks):
                    m, n = size(ch)
                    s = g % 2
                    pe.wait_ge(lo_ok, nk * (g + 1))
                    for j in range(groups(ch)):
                        if uses[g][j]:
                            pe.wait_ge(copied[j], uses[g][j])
                        if ch["kind"] == "row":
                            mm = product(pe, acc[j][0:m, 0:n], nk, lambda p, k: hT[:, p, k, j * P:(j + 1) * P],
                                         lambda q, k: w[:, s, q, k, 0:n])
                        else:
                            c0 = (j // 2) * P
                            mm = product(pe, acc[j][0:m, 0:n], nk, lambda p, k: w[:, s, p, k, c0:c0 + m],
                                         lambda q, k: hT[:, q, k, (j % 2) * BANK:(j % 2 + 1) * BANK])
                        mm.then_inc(mm_done[j], 1)

            def split_hi(act, g):
                n = chunks[g]["width"]
                act.wait_ge(raw_in[g % 2], 16 * sum(loads[g % 2:g + 1:2]))
                if g >= 2:
                    last = groups(chunks[g - 2]) - 1
                    act.wait_ge(mm_done[last], uses[g - 2][last] + 1)
                for k in range(nk):
                    act.activation(w[:, g % 2, HI, k, 0:n], raw[:, g % 2, k, 0:n], ACT.Copy,
                                   scale=1.0 if gain is None else gcol[:, k:k + 1]).then_inc(hi_ok, 1)

            def split_lo(dve, g):
                n = chunks[g]["width"]
                dve.wait_ge(raw_in[g % 2], 16 * sum(loads[g % 2:g + 1:2]))
                for k in range(nk):
                    dve.wait_ge(hi_ok, nk * g + k + 1)
                    dve.scalar_tensor_tensor(out=w[:, g % 2, LO, k, 0:n], in0=raw[:, g % 2, k, 0:n],
                                             scalar=1.0 if gain is None else gcol[:, k:k + 1],
                                             in1=w[:, g % 2, HI, k, 0:n].bitcast(F32), op0=ALU.mult,
                                             op1=ALU.subtract).then_inc(lo_ok, 1)

            @block.scalar
            def _(act):
                if gain is not None:
                    act.wait_ge(gain_in, 16 * len(gain))
                split_hi(act, 0)
                for g, ch in enumerate(chunks):
                    m, n = size(ch)
                    if g + 1 < N:
                        split_hi(act, g + 1)
                    for j in range(groups(ch)):
                        dst = ch["dst"]
                        if j % 2 == 0:
                            act.wait_ge(mm_done[j], uses[g][j] + 1)
                            if nst[g][j]:
                                act.wait_ge(stored[j], nst[g][j])
                            act.activation(obuf[0:m, j, 0:n], acc[j][0:m, 0:n], ACT.Copy).then_inc(copied[j], 1)
                        act.wait_ge(copied[j], uses[g][j] + 1)
                        act.dma_start(dst(j), obuf[0:m, j, 0:n]).then_inc(stored[j], 16)
                for j in range(NT):
                    total = 16 * sum(groups(c) > j for c in chunks)
                    if total:
                        act.wait_ge(stored[j], total)

            @block.vector
            def _(dve):
                if gain is not None:
                    dve.wait_ge(gain_in, 16 * len(gain))
                split_lo(dve, 0)
                for g, ch in enumerate(chunks):
                    m, n = size(ch)
                    if g + 1 < N:
                        split_lo(dve, g + 1)
                    for j in range(groups(ch)):
                        if j % 2 == 1:
                            dve.wait_ge(mm_done[j], uses[g][j] + 1)
                            if nst[g][j]:
                                dve.wait_ge(stored[j], nst[g][j])
                            dve.tensor_copy(obuf[0:m, j, 0:n], acc[j][0:m, 0:n]).then_inc(copied[j], 1)


def columns(w, c0, width):
    return [(slice(0, width), tiled(w)[:, :, c0:c0 + width])]


def to_rows(dst, c0, width):
    return lambda j: dst[j * P:(j + 1) * P, c0:c0 + width]


def to_T(dst, r0, width):
    m = min(P, width)

    return lambda j: dst[r0 + (j // 2) * P:r0 + (j // 2) * P + m, (j % 2) * BANK:(j % 2 + 1) * BANK]



class Rows:

    def __init__(self, nc, st, name, ident, width, loads, groups, hT=None, y_psum=None, post=None,
                 gate=None, expert_rows=None, keep=None, keep_normed=None, ns=2):
        self.ident, self.width, self.loads, self.groups, self.hT, self.ns = ident, width, loads, groups, hT, ns
        self.y_psum, self.post, self.gate, self.expert_rows = y_psum, post, gate, expert_rows
        self.keep, self.keep_normed = keep, keep_normed
        self.nk, self.ng = width // P, len(groups)
        self.nl = len(loads) + len(gate or [])
        self.has_y = y_psum is not None or expert_rows is not None
        sb = lambda n, shape=(P, ns, width), dt=F32: st.sb(name + n, list(shape), dt)
        self.x = sb("_x")
        self.junk = sb("_junk", (P, width))
        self.y = sb("_y") if expert_rows else None
        self.e = [sb(f"_e{c}", (P, 2, width)) for c in range(2)] if expert_rows else None
        self.xe = sb("_xe", (P, width)) if expert_rows else None
        self.xs = sb("_xs") if self.has_y else self.x
        self.z = sb("_z", (P, 1 if gate else 2, width)) if self.ng else None
        self.gt = sb("_gt") if gate else None
        self.sg = sb("_sg", (P, width)) if gate else None
        self.zg = sb("_zg", (P, 2, width)) if gate else self.z
        self.ss, self.ms, self.rs = (sb(n, (P, ns, 8)) for n in ("_ss", "_ms", "_rs"))
        self.half = sb("_half", (P, 1))
        self.prow = sb("_prow", (P, width)) if post is not None else None
        self.tp = st.ps(name + "_tp", [P, width]) if hT is not None else None
        sem = lambda n: st.sem(name + n)
        self.post_in, self.half_ok = sem("_post_in"), sem("_half_ok")
        self.tile_in = [sem(f"_tile_in{u}") for u in range(ns)]
        self.rows_in = [sem(f"_rows_in{u}") for u in range(2)] if expert_rows else None
        self.summed1, self.summed, self.x_ok, self.y_sq, self.y_ms, self.y_rs, self.yn_ok = (
            sem(n) for n in ("_summed1", "_summed", "_x_ok", "_y_sq", "_y_ms", "_y_rs", "_yn_ok"))
        self.sq, self.ms_ok, self.rs_ok, self.z_ok, self.sig, self.silu, self.zg_ok = (
            sem(n) for n in ("_sq", "_ms_ok", "_rs_ok", "_z_ok", "_sig", "_silu", "_zg_ok"))
        self.turned, self.hi_ok, self.lo_ok = sem("_turned"), sem("_hi_ok"), sem("_lo_ok")
        self.kept = [sem(f"_kept{u}") for u in range(ns)]
        self.kept_z = [sem(f"_kept_z{u}") for u in range(2)]
        end = max([c0 + w for c0, w in groups], default=0)
        self.rest = (end, width) if self.ng and end < width else None
        self.nz = self.ng + (self.rest is not None)

    def loaded(self, eng, t):
        if self.nl:
            eng.wait_ge(self.tile_in[t % self.ns], 16 * self.nl * (t // self.ns + 1))

    def x_done(self, eng, t):
        if self.xs is not self.x:
            eng.wait_ge(self.x_ok, t + 1)
        else:
            self.loaded(eng, t)

    def z_done(self, eng, t):
        if self.gate:
            eng.wait_ge(self.zg_ok, t + 1)
        else:
            eng.wait_ge(self.z_ok, self.nz * (t + 1))

    def load(self, sp, t):
        u = t % self.ns
        if t == 0 and self.post is not None:
            sp.dma_start(self.prow[:, :], self.post.partition_broadcast(P)).then_inc(self.post_in, 16)
        if t >= self.ns:
            if self.expert_rows:
                sp.wait_ge(self.summed, t - self.ns + 1)
            elif self.xs is not self.x:
                sp.wait_ge(self.x_ok, t - self.ns + 1)
            else:
                self.z_done(sp, t - self.ns)
        for c0, w, src in self.loads:
            sp.dma_start(self.x[:, u, c0:c0 + w], src(t)).then_inc(self.tile_in[u], 16)
        for c0, w, src in self.gate or []:
            sp.dma_start(self.gt[:, u, c0:c0 + w], src(t)).then_inc(self.tile_in[u], 16)


    def pool_gather(self, pool, t):
        slot_out, gates, slots = self.expert_rows
        if t >= 2:
            pool.wait_ge(self.summed, t - 1)
        for c in range(2):
            pool.indirect_dma_start(self.e[c][:, t % 2, :], None, slot_out,
                                    bass.IndirectOffsetOnAxis(ap=slots[:, t, c:c + 1], axis=0)).then_inc(self.rows_in[t % 2], 16)

    def pool_begin(self, pool):
        pool.memset(self.half[:, :], -0.5).then_inc(self.half_ok, 1)
        pool.wait_ge(self.half_ok, 1)

    def pool_y(self, pool, t):
        u = t % self.ns
        if self.post is not None:
            pool.wait_ge(self.y_sq, t + 1)
            pool.tensor_scalar(self.ms[:, u, 7:8], self.ss[:, u, 7:8], 1.0 / self.width, EPS, ALU.mult, ALU.add).then_inc(self.y_ms, 1)
            pool.wait_ge(self.y_ms, t + 1)
            pool.tensor_tensor(self.rs[:, u, 7:8], self.ms[:, u, 7:8], self.half[:, :], ALU.pow).then_inc(self.y_rs, 1)

    def pool_x(self, pool, t):
        u = t % self.ns
        if self.ng:
            pool.wait_ge(self.sq, self.ng * (t + 1))
            for n, (c0, w) in enumerate(self.groups):
                pool.tensor_scalar(self.ms[:, u, n:n + 1], self.ss[:, u, n:n + 1], 1.0 / w, EPS, ALU.mult,
                                   ALU.add).then_inc(self.ms_ok, 1)
            pool.wait_ge(self.ms_ok, self.ng * (t + 1))
            if t >= self.ns:
                pool.wait_ge(self.z_ok, self.nz * (t - self.ns + 1))
            pool.tensor_tensor(self.rs[:, u, 0:self.ng], self.ms[:, u, 0:self.ng], self.half[:, :].to_broadcast([P, self.ng]),
                               ALU.pow).then_inc(self.rs_ok, 1)


    def act_y(self, act, t):
        if self.post is not None:
            if self.y_psum is not None:
                src, done, _ = self.y_psum
                act.wait_ge(done, t + 1)
                src = src(t)
            else:
                act.wait_ge(self.summed, t + 1)
                src = self.y[:, t % self.ns, :]
            if t >= 1:
                act.wait_ge(self.sq if self.ng else self.y_sq, max(1, self.ng) * t)
            act.activation(self.junk[:, :], src, ACT.Square, accum_out=self.ss[:, t % self.ns, 7:8]).then_inc(self.y_sq, 1)

    def act_x(self, act, t):
        u = t % self.ns
        if self.gate:
            self.loaded(act, t)
            if t >= 1:
                act.wait_ge(self.zg_ok, t)
            act.activation(self.sg[:, :], self.gt[:, u, :], ACT.Sigmoid).then_inc(self.sig, 1)
        if self.ng or self.keep is not None:
            self.x_done(act, t)
        if self.keep is not None:
            act.dma_start(rows(self.keep, t), self.xs[:, u, :]).then_inc(self.kept[u], 16)
        if self.ng and self.post is not None:
            act.wait_ge(self.y_sq, t + 1)
        elif self.ng and t >= 1:
            act.wait_ge(self.sq, self.ng * t)
        for n, (c0, w) in enumerate(self.groups):
            act.activation(self.junk[:, c0:c0 + w], self.xs[:, u, c0:c0 + w], ACT.Square,
                           accum_out=self.ss[:, u, n:n + 1]).then_inc(self.sq, 1)

    def act_turn(self, act, t):
        if self.keep_normed is not None:
            self.z_done(act, t)
            act.dma_start(rows(self.keep_normed, t), self.zg[:, t % 2, :]).then_inc(self.kept_z[t % 2], 16)
        if self.hT is not None:
            act.wait_ge(self.turned, t + 1)
            act.activation(self.hT[:, HI, 0:self.nk, t * P:(t + 1) * P], self.tp[:, :].rearrange("p (k n) -> p k n", n=P),
                           ACT.Copy).then_inc(self.hi_ok, 1)

    def act_end(self, act):
        for u in range(self.ns):
            if self.keep is not None:
                act.wait_ge(self.kept[u], 16 * NT // self.ns)
        for u in range(2):
            if self.keep_normed is not None:
                act.wait_ge(self.kept_z[u], 16 * NT // 2)


    def dve_y(self, dve, t):
        if self.expert_rows:
            u = t % self.ns
            _, gates, _ = self.expert_rows
            self.loaded(dve, t)
            dve.wait_ge(self.rows_in[t % 2], 32 * (t // 2 + 1))
            dve.scalar_tensor_tensor(out=self.xe[:, :], in0=self.e[0][:, t % 2, :], scalar=gates[:, t, 0:1], in1=self.x[:, u, :],
                                     op0=ALU.mult, op1=ALU.add).then_inc(self.summed1, 1)
            dve.wait_ge(self.summed1, t + 1)
            dve.scalar_tensor_tensor(out=self.y[:, u, :], in0=self.e[1][:, t % 2, :], scalar=gates[:, t, 1:2], in1=self.xe[:, :],
                                     op0=ALU.mult, op1=ALU.add).then_inc(self.summed, 1)

    def dve_x(self, dve, t):
        if not self.has_y:
            return
        u = t % self.ns
        if t == 0 and self.post is not None:
            dve.wait_ge(self.post_in, 16)
        self.loaded(dve, t)
        if self.keep is not None and t >= self.ns:
            dve.wait_ge(self.kept[u], 16 * (t // self.ns))
        if self.y_psum is not None:
            y, done, free = self.y_psum
            dve.wait_ge(done, t + 1)
            y = y(t)
        else:
            y, free = self.y[:, u, :], None
        if self.post is not None:
            dve.wait_ge(self.y_rs, t + 1)
            add_x = self.loads and not self.expert_rows
            ok = self.yn_ok if add_x else self.x_ok
            dve.scalar_tensor_tensor(out=self.xs[:, u, :], in0=y, scalar=self.rs[:, u, 7:8], in1=self.prow[:, :],
                                     op0=ALU.mult, op1=ALU.mult).then_inc(ok, 1)
            dve.wait_ge(ok, t + 1)
            if free is not None:
                dve.sem_inc(free, 1)
            if add_x:
                dve.tensor_tensor(self.xs[:, u, :], self.x[:, u, :], self.xs[:, u, :], ALU.add).then_inc(self.x_ok, 1)
        else:
            dve.tensor_tensor(self.xs[:, u, :], y, self.x[:, u, :], ALU.add).then_inc(self.x_ok, 1)
            if free is not None:
                dve.wait_ge(self.x_ok, t + 1)
                dve.sem_inc(free, 1)

    def dve_z(self, dve, t):
        u, zu = t % self.ns, 0 if self.gate else t % 2
        if self.gate:
            dve.wait_ge(self.sig, t + 1)
            dve.tensor_tensor(self.sg[:, :], self.sg[:, :], self.gt[:, u, :], ALU.mult).then_inc(self.silu, 1)
        if self.ng:
            dve.wait_ge(self.rs_ok, t + 1)
            self.x_done(dve, t)
            if t >= 2 and not self.gate:
                if self.hT is not None:
                    dve.wait_ge(self.turned, t - 1)
                if self.keep_normed is not None:
                    dve.wait_ge(self.kept_z[t % 2], 16 * (t // 2))
            for n, (c0, w) in enumerate(self.groups):
                dve.tensor_scalar(self.z[:, zu, c0:c0 + w], self.xs[:, u, c0:c0 + w], self.rs[:, u, n:n + 1], None,
                                  ALU.mult).then_inc(self.z_ok, 1)
            if self.rest:
                a, b = self.rest
                dve.tensor_copy(self.z[:, zu, a:b], self.xs[:, u, a:b]).then_inc(self.z_ok, 1)
        if self.gate:
            dve.wait_ge(self.z_ok, self.nz * (t + 1))
            dve.wait_ge(self.silu, t + 1)
            if t >= 2:
                dve.wait_ge(self.turned, t - 1)
            dve.tensor_tensor(self.zg[:, t % 2, :], self.z[:, 0, :], self.sg[:, :], ALU.mult).then_inc(self.zg_ok, 1)

    def dve_turn(self, dve, t):
        if self.hT is not None:
            dve.wait_ge(self.hi_ok, t + 1)
            at = (slice(0, self.nk), slice(t * P, (t + 1) * P))
            dve.tensor_tensor(self.hT[:, LO, at[0], at[1]], self.tp[:, :].rearrange("p (k n) -> p k n", n=P),
                              self.hT[:, HI, at[0], at[1]].bitcast(F32), ALU.subtract).then_inc(self.lo_ok, 1)


    def pe_turn(self, pe, t):
        if self.hT is not None:
            self.z_done(pe, t)
            if t >= 1:
                pe.wait_ge(self.lo_ok, t)
            for k in range(self.nk):
                mm = pe.transpose(self.tp[:, k * P:(k + 1) * P], self.zg[:, t % 2, k * P:(k + 1) * P], self.ident[:, :])
            mm.then_inc(self.turned, 1)


def at_step(s, *calls):
    for f, lag, eng in calls:
        if 0 <= s - lag < NT:
            f(eng, s - lag)


def norm_rows(nc, name, ident, width, loads, groups, **options):
    with stage(nc) as st:
        r = Rows(nc, st, name, ident, width, loads, groups, ns=4, **options)
        lx = 1 if r.has_y else 0
        with nc.Block() as block:
            @block.sync
            def _(sp):
                for t in range(NT):
                    r.load(sp, t)

            @block.gpsimd
            def _(pool):
                r.pool_begin(pool)
                if r.expert_rows:
                    r.pool_gather(pool, 0)
                for s in range(NT + lx):
                    if r.expert_rows:
                        at_step(s, (r.pool_gather, -1, pool))
                    at_step(s, (r.pool_x, lx, pool), (r.pool_y, 0, pool))

            @block.scalar
            def _(act):
                for s in range(NT + lx + 2):
                    at_step(s, (r.act_turn, lx + 2, act), (r.act_x, lx, act), (r.act_y, 0, act))
                r.act_end(act)

            @block.vector
            def _(dve):
                for s in range(NT + lx + 2):
                    at_step(s, (r.dve_z, lx + 1, dve), (r.dve_turn, lx + 2, dve), (r.dve_x, lx, dve), (r.dve_y, 0, dve))

            @block.tensor
            def _(pe):
                for t in range(NT):
                    r.pe_turn(pe, t)


def mix_out(nc, name, ident, hT, w_out, gain, front, back):
    with stage(nc) as st:
        raw = st.sb(name + "_raw", [P, 2, D])
        w = st.sb(name + "_w", [P, 2, 8, D], F32R)
        gcol = st.sb(name + "_g", [P, 8]) if gain is not None else None
        acc = [st.ps(f"{name}_acc{u}", [P, D]) for u in range(2)]
        gain_in, hi_ok, lo_ok, y_done, y_free = (st.sem(name + n) for n in ("_gain_in", "_whi_ok", "_wlo_ok", "_y_done", "_y_free"))
        raw_in = [st.sem(f"{name}_raw_in{u}") for u in range(2)]
        f = Rows(nc, st, name + "f", ident, **front)
        b = Rows(nc, st, name + "b", ident, y_psum=(lambda t: acc[t % 2][:, :], y_done, y_free), **back)
        wv = tiled(w_out)
        STEPS = NT + 5

        with nc.Block() as block:
            @block.sync
            def _(sp):
                f.load(sp, 0)
                f.load(sp, 1)
                if gain is not None:
                    for k0, v in gain:
                        sp.dma_start(gcol[:, k0:k0 + v.shape[0] // P], v.rearrange("(k p) -> p k", p=P),
                                     allow_slow_non_contiguous=True).then_inc(gain_in, 16)
                for k in range(8):
                    if k >= 2:
                        sp.wait_ge(lo_ok, k - 1)
                    sp.dma_start(raw[:, k % 2, :], wv[:, k, :]).then_inc(raw_in[k % 2], 16)
                b.load(sp, 0)
                b.load(sp, 1)
                for t in range(2, NT + 2):
                    if t < NT:
                        f.load(sp, t)
                    if t >= 4:
                        b.load(sp, t - 2)

            @block.gpsimd
            def _(pool):
                f.pool_begin(pool)
                b.pool_begin(pool)
                for s in range(STEPS):
                    at_step(s, (b.pool_y, 3, pool), (f.pool_x, 0, pool), (b.pool_x, 3, pool))

            def scale(k):
                return 1.0 if gain is None else gcol[:, k:k + 1]

            @block.scalar
            def _(act):
                for s in range(STEPS):
                    at_step(s, (b.act_y, 3, act), (f.act_turn, 1, act), (b.act_turn, 5, act), (f.act_x, 0, act), (b.act_x, 3, act))
                    if s == 0:
                        if gain is not None:
                            act.wait_ge(gain_in, 16 * len(gain))
                        for k in range(8):
                            act.wait_ge(raw_in[k % 2], 16 * (k // 2 + 1))
                            act.activation(w[:, HI, k, :], raw[:, k % 2, :], ACT.Copy, scale=scale(k)).then_inc(hi_ok, 1)
                b.act_end(act)

            @block.vector
            def _(dve):
                for s in range(STEPS):
                    at_step(s, (f.dve_z, 1, dve))
                    if s == 1:
                        if gain is not None:
                            dve.wait_ge(gain_in, 16 * len(gain))
                        for k in range(8):
                            dve.wait_ge(hi_ok, k + 1)
                            dve.scalar_tensor_tensor(out=w[:, LO, k, :], in0=raw[:, k % 2, :], scalar=scale(k),
                                                     in1=w[:, HI, k, :].bitcast(F32), op0=ALU.mult, op1=ALU.subtract).then_inc(lo_ok, 1)
                    at_step(s, (b.dve_z, 4, dve), (b.dve_x, 3, dve), (f.dve_turn, 1, dve), (b.dve_turn, 5, dve))

            @block.tensor
            def _(pe):
                def multiply(pe, t):
                    pe.wait_ge(f.lo_ok, t + 1)
                    if t >= 2:
                        pe.wait_ge(y_free, t - 1)
                    for n in range(2):
                        nn = slice(n * BANK, (n + 1) * BANK)
                        for k in range(8):
                            if t == 0 and n == 0:
                                pe.wait_ge(lo_ok, k + 1)
                            for i, (p, q) in enumerate(PARTS):
                                mm = pe.matmul(acc[t % 2][:, nn], hT[:, p, k, t * P:(t + 1) * P], w[:, q, k, nn],
                                               start=(k == 0 and i == 0), stop=(k == 7 and i == 2))
                    mm.then_inc(y_done, 1)

                for s in range(STEPS):
                    at_step(s, (f.pe_turn, 1, pe), (b.pe_turn, 5, pe), (multiply, 2, pe))



def bias_table(nc, rel_bias, onehot, log_count, table):
    W = 2 * S
    with stage(nc) as st:
        oh = st.sb("bt_oh", [32, W])
        rb = st.sb("bt_rb", [32, 8])
        lc = st.sb("bt_lc", [8, W])
        out = st.sb("bt_out", [8, W])
        out8 = st.sb("bt_out8", [8, W])
        ps = st.ps("bt_ps", [P, W])
        consts_in, mm, added, scaled, stored = (st.sem("bt_" + n) for n in ("in", "mm", "added", "scaled", "stored"))
        with nc.Block() as block:
            @block.sync
            def _(sp):
                sp.dma_start(oh[:, :], onehot).then_inc(consts_in, 16)
                sp.dma_start(rb[:, :], rel_bias).then_inc(consts_in, 16)
                sp.dma_start(lc[:, :], log_count.partition_broadcast(8)).then_inc(consts_in, 16)
                sp.wait_ge(scaled, 1)
                sp.dma_start(table, out8[:, :]).then_inc(stored, 16)
                sp.wait_ge(stored, 16)

            @block.tensor
            def _(pe):
                pe.wait_ge(consts_in, 48)
                for c in range(W // BANK):
                    m = pe.matmul(ps[0:8, c * BANK:(c + 1) * BANK], rb[:, :], oh[:, c * BANK:(c + 1) * BANK],
                                  start=True, stop=True)
                m.then_inc(mm, 1)

            @block.vector
            def _(dve):
                dve.wait_ge(consts_in, 48)
                dve.wait_ge(mm, 1)
                dve.tensor_tensor(out[:, :], ps[0:8, :], lc[:, :], ALU.add).then_inc(added, 1)
                dve.wait_ge(added, 1)
                dve.tensor_scalar(out8[:, :], out[:, :], 8.0, None, ALU.mult).then_inc(scaled, 1)


TURN = 16


def tiles(eng, total, peel, lag, body):
    for T in range(peel):
        body(T % TURN, T)
    with eng.Fori(0, total // TURN - 1) as r:
        for l in range(peel, peel + TURN):
            body(l % TURN, r * TURN + l)
    for T in range(total - TURN + peel, total + lag):
        body(T % TURN, T)


def active(T, k, total):
    return not isinstance(T, int) or 0 <= T - k < total


def reached(eng, sem, n):
    if not isinstance(n, int) or n > 0:
        eng.wait_ge(sem, n)



def softmax_attention(nc, name, ident, heads, scale, q_src, k_src, v_src, out, table=None, rope=None):
    DV, T8 = 64, NT
    total = heads * T8
    WB = 2 * S - P
    nraw = 4 + (4 if rope else 0)
    nv = 1 + (table is not None)
    H = T8 // 2 * P

    with stage(nc) as st:
        qraw, kraw = (st.sb(name + n, [P, 2, S]) for n in ("_qraw", "_kraw"))
        qs, kh, kl = (st.sb(name + n, [P, 2, S], F32R) for n in ("_qs", "_kh", "_kl"))
        if rope:
            rqraw, krraw = st.sb(name + "_rqraw", [P, 2, S]), st.sb(name + "_krraw", [P, S])
            rqs, krs = st.sb(name + "_rqs", [P, 2, S], F32R), st.sb(name + "_krs", [P, S], F32R)
        v = st.sb(name + "_v", [P, 2, NT, DV])
        wb = st.sb(name + "_wb", [P, 2, WB]) if table is not None else None
        sc = st.sb(name + "_sc", [P, 2, S]) if table is not None else None
        p = st.sb(name + "_p", [P, 4, S])
        pT = st.sb(name + "_pT", [P, 2, S])
        mx, nm, rs, ri = (st.sb(name + n, [P, TURN]) for n in ("_mx", "_nm", "_rs", "_ri"))
        o = st.sb(name + "_ob", [P, 2, NT, DV])
        sps = [st.ps(f"{name}_s{s}", [P, S]) for s in range(2)]
        tps = st.ps(name + "_t", [P, S])
        ops = [st.ps(f"{name}_op{s}", [P, BANK]) for s in range(2)]
        raw_in = [st.sem(f"{name}_raw_in{s}") for s in range(2)]
        v_in = [st.sem(f"{name}_v_in{s}") for s in range(2)]
        kr_in, kr_ok, hi_ok, lo_ok, s_done, s_free, max_done, nm_done, p_done = (
            st.sem(name + n) for n in ("_kr_in", "_kr_ok", "_hi_ok", "_lo_ok", "_s_done", "_s_free", "_max", "_nm_done", "_p_done"))
        turned_a, turned_b, pT_a, pT_b = (st.sem(name + n) for n in ("_turned_a", "_turned_b", "_pT_a", "_pT_b"))
        pv_done, ri_done, o_done = (st.sem(name + n) for n in ("_pv_done", "_ri_done", "_o_done"))
        passed = st.sem(name + "_passed")
        stored = [st.sem(f"{name}_stored{s}") for s in range(2)]

        with nc.Block() as block:
            @block.sync
            def _(sp):
                def load_raw(h, u):
                    for b in range(2):
                        sp.dma_start(qraw[64 * b:64 * b + 64, u, :], q_src(h)).then_inc(raw_in[u], 16)
                        sp.dma_start(kraw[64 * b:64 * b + 64, u, :], k_src(h)).then_inc(raw_in[u], 16)
                    if rope:
                        for b in range(4):
                            sp.dma_start(rqraw[32 * b:32 * b + 32, u, :], rope(h)).then_inc(raw_in[u], 16)

                def load_v(h, u):
                    sp.dma_start(v[:, u, :, :], v_src(h)).then_inc(v_in[u], 16)
                    if table is not None:
                        src = bass.AP(table.tensor, h * (2 * S), [[1, P], [1, WB]])
                        sp.dma_start(wb[:, u, :], src).then_inc(v_in[u], 16)

                def store(h, u):
                    sp.wait_ge(o_done, h * T8 + T8)
                    sp.sem_inc(passed, 1)
                    sp.dma_start(out[:, bass.ds(h * DV, DV)].rearrange("(t p) d -> p t d", p=P),
                                 o[:, u, :, :]).then_inc(stored[u], 16)

                sp.sem_inc(stored[0], 16)
                sp.sem_inc(stored[1], 16)
                load_raw(0, 0)
                if rope:
                    for b in range(4):
                        sp.dma_start(krraw[32 * b:32 * b + 32, :], rope(None)).then_inc(kr_in, 16)
                load_v(0, 0)
                load_raw(1, 1)
                load_v(1, 1)
                with sp.Fori(0, heads // 2 - 1) as r:
                    for u in range(2):
                        h = r * 2 + u
                        sp.wait_ge(lo_ok, h * 8 + 8)
                        sp.sem_inc(passed, 1)
                        load_raw(h + 2, u)
                        store(h, u)
                        sp.wait_ge(pv_done, h * T8 + T8)
                        sp.sem_inc(passed, 1)
                        load_v(h + 2, u)
                for u in range(2):
                    store(heads - 2 + u, u)
                for u in range(2):
                    sp.wait_ge(stored[u], 16 * (heads // 2 + 1))

            @block.gpsimd
            def _(pool):
                def lo(dst, raw, n):
                    pool.tensor_tensor(dst, raw, dst.bitcast(F32), ALU.subtract).then_inc(lo_ok, n)

                if rope:
                    pool.wait_ge(kr_ok, 1)
                    for b in (1, 3):
                        s = slice(32 * b, 32 * b + 32)
                        pool.tensor_tensor(krs[s, :], krraw[s, :], krs[s, :].bitcast(F32), ALU.subtract).then_inc(kr_ok, 1)
                        pool.wait_ge(kr_ok, 2 if b == 1 else 3)
                nhi = 3 if rope else 2
                with pool.Fori(0, heads // 2) as r:
                    for u in range(2):
                        done = lambda n: pool.wait_ge(lo_ok, r * 16 + (8 * u + n))
                        pool.wait_ge(hi_ok, r * (2 * nhi) + nhi * (u + 1))
                        lo(qs[64:P, u, :], qraw[64:P, u, :], 4)
                        done(4)
                        pool.tensor_tensor(kl[:, u, :], kraw[:, u, :], kh[:, u, :].bitcast(F32),
                                           ALU.subtract).then_inc(lo_ok, 2 if rope else 4)
                        if rope:
                            done(6)
                            lo(rqs[64:P, u, :], rqraw[64:P, u, :], 2)
                        done(8)

            @block.tensor
            def _(pe):
                if rope:
                    pe.wait_ge(kr_ok, 3)

                def body(l, T):
                    if active(T, 0, total):
                        u, i = l // T8, l % T8
                        if i == 0:
                            pe.wait_ge(lo_ok, T + 8)
                        reached(pe, s_free if table is not None else p_done, T - 1)
                        ii = slice(i * P, (i + 1) * P)
                        for c in range(2):
                            cc = slice(c * BANK, (c + 1) * BANK)
                            pe.matmul(sps[l % 2][:, cc], qs[:, u, ii], kh[:, u, cc], start=True, stop=False)
                            mm = pe.matmul(sps[l % 2][:, cc], qs[:, u, ii], kl[:, u, cc], start=False, stop=not rope)
                            if rope:
                                mm = pe.matmul(sps[l % 2][:, cc], rqs[:, u, ii], krs[:, cc], start=False, stop=True)
                        mm.then_inc(s_done, 1)
                    if active(T, 2, total):
                        m = (l - 2) % TURN
                        reached(pe, p_done, T - 1)
                        reached(pe, pT_a, T - 2)
                        for k in range(NT):
                            if k == NT // 2:
                                reached(pe, pT_b, T - 2)
                            mm = pe.transpose(tps[:, k * P:(k + 1) * P], p[:, m % 4, k * P:(k + 1) * P], ident[:, :])
                            if k == NT // 2 - 1:
                                mm.then_inc(turned_a, 1)
                        mm.then_inc(turned_b, 1)
                    if active(T, 3, total):
                        m = (l - 3) % TURN
                        u, i = m // T8, m % T8
                        if i == 0:
                            pe.wait_ge(v_in[u], (T - 3 - 8 * u) * nv + 16 * nv)
                        reached(pe, o_done, T - 4)
                        reached(pe, pT_a, T - 2)
                        reached(pe, pT_b, T - 2)
                        for k in range(NT):
                            mm = pe.matmul(ops[m % 2][:, 0:DV], pT[:, m % 2, k * P:(k + 1) * P], v[:, u, k, :],
                                           start=(k == 0), stop=(k == NT - 1))
                        mm.then_inc(pv_done, 1)
                tiles(pe, total, 5, 3, body)

            @block.vector
            def _(dve):
                def body(l, T):
                    if active(T, 0, total):
                        u, i = l // T8, l % T8
                        dve.wait_ge(s_done, T + 1)
                        if table is not None:
                            if i == 0:
                                dve.wait_ge(v_in[u], (T - 8 * u) * nv + 16 * nv)
                            reached(dve, p_done, T - 1)
                            dve.sem_inc(passed, 1)
                            dve.tensor_tensor_reduce(out=sc[:, l % 2, :], in0=sps[l % 2][:, :], in1=wb[:, u, i * P:i * P + S][:, ::-1],
                                                     scale=1.0, scalar=-3e38, op0=ALU.add, op1=ALU.max,
                                                     accum_out=mx[:, l:l + 1]).then_inc(s_free, 1)
                            dve.wait_ge(s_free, T + 1)
                        else:
                            dve.reduce_max(mx[:, l:l + 1], sps[l % 2][:, :], AX.X).then_inc(max_done, 1)
                            dve.wait_ge(max_done, T + 1)
                        dve.tensor_scalar(nm[:, l:l + 1], mx[:, l:l + 1], -scale, None, ALU.mult).then_inc(nm_done, 1)
                    if active(T, 2, total):
                        m = (l - 2) % TURN
                        reached(dve, turned_a, T - 1)
                        reached(dve, pv_done, T - 3)
                        dve.tensor_copy(pT[:, m % 2, 0:H], tps[:, 0:H]).then_inc(pT_a, 1)
                    if active(T, 3, total):
                        m = (l - 3) % TURN
                        u, i = m // T8, m % T8
                        reached(dve, p_done, T - 2)
                        dve.reciprocal(ri[:, m:m + 1], rs[:, m:m + 1]).then_inc(ri_done, 1)
                        reached(dve, pv_done, T - 2)
                        reached(dve, ri_done, T - 2)
                        if i == 0:
                            dve.wait_ge(stored[u], T - 3 - 8 * u + 16)
                        dve.tensor_scalar(o[:, u, i, :], ops[m % 2][:, 0:DV], ri[:, m:m + 1], None,
                                          ALU.mult).then_inc(o_done, 1)
                tiles(dve, total, 5, 3, body)

            @block.scalar
            def _(act):
                def split_hi(u, n_in):
                    act.wait_ge(raw_in[u], n_in)
                    act.activation(qs[:, u, :], qraw[:, u, :], ACT.Copy).then_inc(hi_ok, 1)
                    act.activation(kh[:, u, :], kraw[:, u, :], ACT.Copy).then_inc(hi_ok, 1)
                    if rope:
                        act.activation(rqs[:, u, :], rqraw[:, u, :], ACT.Copy).then_inc(hi_ok, 1)

                split_hi(0, 16 * nraw)
                if rope:
                    act.wait_ge(kr_in, 64)
                    act.activation(krs[:, :], krraw[:, :], ACT.Copy).then_inc(kr_ok, 1)

                def body(l, T):
                    if active(T, 2, total):
                        m = (l - 2) % TURN
                        reached(act, turned_b, T - 1)
                        reached(act, pv_done, T - 3)
                        act.activation(pT[:, m % 2, H:S], tps[:, H:S], ACT.Copy).then_inc(pT_b, 1)
                    if active(T, 0, total):
                        act.wait_ge(nm_done, T + 1)
                        reached(act, turned_b, T - 3)
                        src = sc[:, l % 2, :] if table is not None else sps[l % 2][:, :]
                        act.activation(p[:, l % 4, :], src, ACT.Exp, bias=nm[:, l:l + 1], scale=scale,
                                       accum_out=rs[:, l:l + 1]).then_inc(p_done, 1)
                        if l % T8 == 3 and active(T + 5, 0, total):
                            u = 1 - l // T8
                            act.wait_ge(s_done, T + 1)
                            split_hi(u, (T + 5 - 8 * u) * nraw + 16 * nraw)
                tiles(act, total, 5, 3, body)


def rope_keys_queries(nc, qlT, cosT, sinT, qrT_out, krT_src, krT_out):
    with stage(nc) as st:
        c = st.sb("rk_c", [P, S])
        s = st.sb("rk_s", [P, S])
        a = st.sb("rk_a", [P, 3, S])
        b = st.sb("rk_b", [P, 3, S])
        o = st.sb("rk_o", [P, 3, S])
        loaded, ma, mb, added, stored = (st.sem("rk_" + n) for n in ("in", "ma", "mb", "added", "stored"))
        n = [P, P, 32]
        with nc.Block() as block:
            @block.sync
            def _(sp):
                sp.dma_start(c[:, :], cosT).then_inc(loaded, 16)
                sp.dma_start(s[:, :], sinT).then_inc(loaded, 16)
                for j in range(2):
                    sp.dma_start(a[:, j, :], qlT[512 + j * P:512 + (j + 1) * P, :]).then_inc(loaded, 16)
                    sp.dma_start(b[:, j, :], qlT[768 + j * P:768 + (j + 1) * P, :]).then_inc(loaded, 16)
                sp.dma_start(a[0:32, 2, :], krT_src[0:32, :]).then_inc(loaded, 16)
                sp.dma_start(b[0:32, 2, :], krT_src[32:64, :]).then_inc(loaded, 16)
                for j in range(3):
                    sp.wait_ge(added, j + 1)
                    dst = qrT_out[j * P:(j + 1) * P, :] if j < 2 else krT_out
                    sp.dma_start(dst, o[0:n[j], j, :]).then_inc(stored, 16)
                sp.wait_ge(stored, 48)

            @block.gpsimd
            def _(pool):
                pool.wait_ge(loaded, 128)
                for j in range(3):
                    pool.tensor_tensor(b[0:n[j], j, :], b[0:n[j], j, :], s[0:n[j], :], ALU.mult).then_inc(mb, 1)

            @block.vector
            def _(dve):
                dve.wait_ge(loaded, 128)
                for j in range(3):
                    dve.tensor_tensor(a[0:n[j], j, :], a[0:n[j], j, :], c[0:n[j], :], ALU.mult).then_inc(ma, 1)
                    dve.wait_ge(ma, j + 1)
                    dve.wait_ge(mb, j + 1)
                    dve.tensor_tensor(o[0:n[j], j, :], a[0:n[j], j, :], b[0:n[j], j, :], ALU.add).then_inc(added, 1)


def first_attention(nc, A, C, scr, ident, hT):
    x0 = A["x"].rearrange("b s d -> (b s) d")
    norm_rows(nc, "n0", ident, D, [(0, D, lambda t: rows(x0, t))], [(0, D)], hT=hT)
    w_in = A["w_in"][0]
    kr0 = 3 * 512 + 384
    krv = tiled(w_in)
    project(nc, "pa", hT, 8, [
        *(dict(kind="T", width=512, load=columns(w_in, c, 512), dst=to_T(scr["qkT"], c, 512)) for c in (0, 512)),
        dict(kind="row", width=512, load=columns(w_in, 1024, 512), dst=to_rows(scr["va"], 0, 512)),
        dict(kind="row", width=384, load=columns(w_in, 1536, 384), dst=to_rows(scr["lat"], 0, 384)),
        dict(kind="T", width=64, dst=to_T(scr["krT"], 0, 64),
             load=[(slice(0, 32), krv[:, :, kr0:kr0 + 32]), (slice(32, 48), krv[:, :, kr0 + 16:kr0 + 32]),
                             (slice(48, 64), krv[:, :, kr0:kr0 + 16])]),
    ], gain=[(0, A["g_attn_norm"][0])])
    bias_table(nc, A["rel_bias"], C["onehot"], C["log_count"], scr["table"])
    qk = scr["qkT"]
    heads_of = lambda src, h0=0: lambda h: src[bass.ds(h * 64 + h0, 64), :]
    values_of = lambda src: lambda h: src[:, bass.ds(h * 64, 64)].rearrange("(t p) d -> p t d", p=P)
    softmax_attention(nc, "aa", ident, 8, 64 ** -0.5, heads_of(qk), heads_of(qk, 512), values_of(scr["va"]), scr["oa"],
                      table=scr["table"])
    norm_rows(nc, "nl", ident, 384, [(0, 384, lambda t: rows(scr["lat"], t))], [(0, 256), (256, 128)], hT=hT)
    wq = tiled(A["w_q_up"][0])
    q_nope = [(slice(64 * h, 64 * h + 64), wq[:, :, 96 * h:96 * h + 64]) for h in range(8)]
    q_rope = []
    for h in range(8):
        r0 = 96 * h + 64
        q_rope += [(slice(32 * h, 32 * h + 32), wq[:, :, r0:r0 + 32]),
                   (slice(256 + 32 * h, 256 + 32 * h + 16), wq[:, :, r0 + 16:r0 + 32]),
                   (slice(256 + 32 * h + 16, 256 + 32 * h + 32), wq[:, :, r0:r0 + 16])]
    project(nc, "pq", hT[:, :, 0:2, :], 2, [
        dict(kind="T", width=512, load=q_nope, dst=to_T(scr["qlT"], 0, 512)),
        dict(kind="T", width=512, load=q_rope, dst=to_T(scr["qlT"], 512, 512)),
    ], gain=[(0, A["g_q_latent"][0])])
    kvw = tiled(A["w_kv_up"][0])
    project(nc, "pk", hT[:, :, 2:3, :], 1, [
        dict(kind="T", width=512, dst=to_T(scr["knT"], 0, 512),
             load=[(slice(64 * h, 64 * h + 64), kvw[:, :, 128 * h:128 * h + 64]) for h in range(8)]),
        dict(kind="row", width=512, dst=to_rows(scr["vb"], 0, 512),
             load=[(slice(64 * h, 64 * h + 64), kvw[:, :, 128 * h + 64:128 * h + 128]) for h in range(8)]),
    ], gain=[(0, A["g_kv_latent"][0])])
    rope_keys_queries(nc, scr["qlT"], C["mla_cosT"], C["mla_sinT"], scr["qrT"], scr["krT"], scr["krT2"])
    softmax_attention(nc, "ab", ident, 8, 96 ** -0.5, heads_of(scr["qlT"]), heads_of(scr["knT"]), values_of(scr["vb"]), scr["ob"],
                      rope=lambda h: scr["krT2"] if h is None else scr["qrT"][bass.ds(h * 32, 32), :])
    mix_out(nc, "am", ident, hT, A["w_out"][0], [(0, A["g_out_a"][0]), (4, A["g_out_b"][0])],
            dict(width=D, loads=[(0, 512, lambda t: rows(scr["oa"], t)), (512, 512, lambda t: rows(scr["ob"], t))],
                 groups=[(0, 512), (512, 512)], hT=hT),
            dict(width=D, loads=[(0, D, lambda t: rows(x0, t))], groups=[(0, D)], hT=hT, keep=scr["x1"], keep_normed=scr["xn"]))


def identity(nc, ident, diag=1):
    with stage(nc) as st:
        zero, done = st.sem("id_zero"), st.sem("id_done")
        with nc.Block() as block:
            @block.gpsimd
            def _(pool):
                pool.memset(ident[:, :], 0.0).then_inc(zero, 1)
                pool.wait_ge(zero, 1)
                pool.affine_select(out=ident[:, :], in_=ident[:, :], compare_op=ALU.not_equal, fill=1.0, base=0,
                                   pattern=[[-1, P]], channel_multiplier=1).then_inc(done, 1)
                pool.wait_ge(done, 1)


SCRATCH = dict(
    qkT=(1024, S), va=(S, 512), lat=(S, 384), krT=(64, S), krT2=(32, S), table=(8, 2 * S), oa=(S, 512),
    qlT=(1024, S), qrT=(256, S), knT=(512, S), vb=(S, 512), ob=(S, 512),
)


def constants():
    rel = (S - 1) - np.arange(2 * S)
    half, exact = 16, 8
    n = np.abs(rel)
    large = exact + (np.log(np.maximum(n, 1) / exact) / math.log(1024 / exact) * (half - exact)).astype(np.int32)
    bucket = np.where(rel > 0, half, 0) + np.where(n < exact, n, np.minimum(large, half - 1))
    count = np.zeros(2 * S)
    for window, dilation in ((128, 1), (512, 4), (2048, 16)):
        steps = window // (2 * dilation)
        count += (rel % dilation == 0) & (n <= steps * dilation)
    c = {
        "onehot": (bucket[None, :] == np.arange(32)[:, None]).astype(np.float32),
        "log_count": np.where(count > 0, np.log(np.maximum(count, 1)), NEG).astype(np.float32),
    }
    inv = (10000.0 ** (-(np.arange(16, dtype=np.float32) / np.float32(16)))).astype(np.float32)
    ang = (np.arange(S, dtype=np.float32)[:, None] * inv[None, :]).astype(np.float32)
    c["mla_cosT"] = np.tile(np.cos(ang).T, (8, 1)).astype(np.float32)
    c["mla_sinT"] = np.tile(np.concatenate([-np.sin(ang).T, np.sin(ang).T], 0), (4, 1)).astype(np.float32)
    e = np.arange(32)
    c["router"] = np.concatenate([e, 32 - e, np.arange(15)]).astype(np.float32)
    c["before"] = np.triu(np.ones((P, P)), 1).astype(np.float32)
    pos = np.arange(P, dtype=np.float64)
    inv = (10000.0 ** (-(np.arange(32, dtype=np.float32) / np.float32(32)))).astype(np.float32)
    ang = (np.arange(S, dtype=np.float32)[:, None] * inv[None, :]).astype(np.float32)
    c["ret_cs"] = np.concatenate([np.cos(ang), np.sin(ang)], 1).astype(np.float32)
    g = np.log(1.0 - 2.0 ** (-5.0 - np.arange(4)))
    scale = 64 ** -0.5
    dist = pos[None, :] - pos[:, None]
    c["ret_decay"] = np.concatenate([np.where(dist >= 0, np.exp(gh * np.maximum(dist, 0)), 0) * scale for gh in g],
                                    1).astype(np.float32)
    c["ret_rowdec"] = np.concatenate([np.exp(g[None, :] * (pos + 1)[:, None]),
                                      np.exp(g[None, :] * (P - 1 - pos)[:, None]) * scale], 1).astype(np.float32)
    c["ret_gchunk"] = np.exp(P * np.stack([np.repeat(g[2 * j:2 * j + 2], 64) for j in range(2)], 1)).astype(np.float32)
    strict = pos[None, :] < pos[:, None]
    c["strict"] = np.stack([strict, ~strict], 1).astype(np.float32)
    s, t = np.arange(P)[:, None], np.arange(P)[None, :]
    c["levels"] = np.stack([(s // (2 * m) == t // (2 * m)) & (s % (2 * m) < m) & (t % (2 * m) >= m)
                            for m in (64, 32, 16, 8, 4, 2, 1)] + [s == t], 1).astype(np.float32)
    return c



NG, NE, FF = 4, 32, 256
EG = NE // NG
NOV = 2 * S // P - 1
NB = 48


def route(nc, hT, A, C, tok_of_slot, slot_out, gates, slots, over):
    with stage(nc) as st:
        wr = st.sb("ro_wr", [P, 8, NG + NE])
        wg = st.sb("ro_wg", [P, 8, NG + NE])
        ws = st.sb("ro_ws", [P, 2, 8, NG + NE], F32R)
        gcol = st.sb("ro_g", [P, 8])
        br = st.sb("ro_br", [P, NG + NE])
        cst = st.sb("ro_cst", [P, 2 * NE + NOV])
        ltm = st.sb("ro_lt", [P, P])
        ones = st.sb("ro_ones", [P, P])
        L = st.sb("ro_L", [P, NT, NG + NE])
        g4 = [st.sb(f"ro_g4{i}", [P, NT, NG]) for i in range(6)]
        c1 = [st.sb(f"ro_c1{i}", [P, NT]) for i in range(14)]
        e32 = [st.sb(f"ro_e{i}", [P, NT, NE]) for i in range(14)]
        M = st.sb("ro_M", [P, NT, NE])
        cum = st.sb("ro_cum", [P, NT + 1, NE])
        rank = st.sb("ro_rank", [P, NT, NE])
        kk = st.sb("ro_kk", [P, 8, NT, NE])
        cnt = st.sb("ro_cnt", [P, 12, NE])
        ovb = st.sb("ro_ovb", [P, NOV, NE])
        ovs = st.sb("ro_ovs", [P, 2 * NB])
        posf = st.sb("ro_posf", [P, NT, 2])
        zero = st.sb("ro_zero", [P, NB], U32)
        tok = st.sb("ro_tok", [P, NT], U32)
        blank = st.sb("ro_blank", [P, D])
        blanked = st.sem("ro_blanked")
        pl = st.ps("ro_pl", [P, BANK])
        pr = st.ps("ro_pr", [P, BANK])
        pc = st.ps("ro_pc", [P, BANK])
        ins, cleared, lg, exps, e_ready, m_ready, ranks, d, tok_ready, slots_ready, scattered, e2_ready, e2s, split_ok = (
            st.sem("ro_" + n) for n in ("in", "cleared", "logits", "exps", "e_ready", "m_ready", "ranks", "step", "tok", "slots",
                                        "scattered", "e2_ready", "e2", "split_ok"))
        G8, E8 = [P, NT, NG], [P, NT, NE]
        with nc.Block() as block:
            @block.sync
            def _(sp):
                sp.dma_start(wr[:, :, 0:NG], tiled(A["w_router_group"][0])).then_inc(ins, 16)
                sp.dma_start(wr[:, :, NG:], tiled(A["w_router_expert"][0])).then_inc(ins, 16)
                sp.dma_start(br[:, 0:NG], A["b_router_group"][0].partition_broadcast(P)).then_inc(ins, 16)
                sp.dma_start(br[:, NG:], A["b_router_expert"][0].partition_broadcast(P)).then_inc(ins, 16)
                sp.dma_start(cst[:, :], C["router"].partition_broadcast(P)).then_inc(ins, 16)
                sp.dma_start(ltm[:, :], C["before"]).then_inc(ins, 16)
                sp.dma_start(gcol[:, :], A["g_ffn_norm"][0].rearrange("(k p) -> p k", p=P),
                             allow_slow_non_contiguous=True).then_inc(ins, 16)

            @block.tensor
            def _(pe):
                pe.wait_ge(ins, 112)
                pe.wait_ge(split_ok, 1)
                for t in range(NT):
                    mm = product(pe, pl[:, t * 36:(t + 1) * 36], 8, lambda p, k: hT[:, p, k, t * P:(t + 1) * P],
                                 lambda q, k: ws[:, q, k, :])
                mm.then_inc(lg, 1)
                pe.wait_ge(m_ready, 1)
                pe.matmul(pr[:, 0:NT * NE], ltm[:, :], M[:, :, :].rearrange("p t e -> p (t e)"), start=True, stop=False)
                pe.matmul(pr[:, 0:NT * NE], ones[:, :], cum[:, 0:NT, :].rearrange("p t e -> p (t e)"), start=False, stop=True)
                pe.matmul(pc[:, 0:NE], ones[:, :], cum[:, NT, :], start=True, stop=True).then_inc(ranks, 1)

            @block.scalar
            def _(act):
                act.wait_ge(tok_ready, 3)
                act.dma_start(slot_out.rearrange("(p b) n -> p b n", b=NB)[:, NE:, :],
                              blank[:, :].unsqueeze(1).to_broadcast([P, NB - NE, D])).then_inc(blanked, 16)
                act.wait_ge(e_ready, 1)
                act.activation(g4[3][:, :, :], g4[2][:, :, :], ACT.Exp).then_inc(exps, 1)
                act.wait_ge(e2_ready, 1)
                act.activation(c1[7][:, :], c1[6][:, :], ACT.Exp).then_inc(e2s, 1)
                act.wait_ge(blanked, 16)

            @block.vector
            def _(dve):
                n = [0]

                def step(ins_):
                    n[0] += 1
                    ins_.then_inc(d, 1)
                    dve.wait_ge(d, n[0])

                step(dve.memset(ones[:, :], 1.0))
                dve.wait_ge(ins, 112)
                step(dve.tensor_tensor(wg[:, :, :], wr[:, :, :], gcol[:, :].unsqueeze(2).to_broadcast([P, 8, NG + NE]), ALU.mult))
                step(dve.tensor_copy(ws[:, HI, :, :], wg[:, :, :]))
                dve.tensor_tensor(ws[:, LO, :, :], wg[:, :, :], ws[:, HI, :, :].bitcast(F32), ALU.subtract).then_inc(split_ok, 1)
                dve.wait_ge(lg, 1)
                step(dve.tensor_tensor(L[:, :, :], pl[:, 0:NT * 36].rearrange("p (t n) -> p t n", t=NT),
                                       br[:, :].unsqueeze(1).to_broadcast([P, NT, 36]), ALU.add))
                Lg, Le = L[:, :, 0:NG], L[:, :, NG:]
                step(dve.reduce_max(c1[0][:, :], Lg, AX.X))
                gm = c1[0][:, :].unsqueeze(2).to_broadcast(G8)
                dve.tensor_tensor(g4[2][:, :, :], Lg, gm, ALU.subtract).then_inc(e_ready, 1)
                step(dve.tensor_tensor(g4[0][:, :, :], Lg, gm, ALU.is_equal))
                step(dve.tensor_tensor(g4[1][:, :, :], g4[0][:, :, :],
                                       cst[:, 2 * NE - NG:2 * NE].unsqueeze(1).to_broadcast(G8), ALU.mult))
                step(dve.reduce_max(c1[1][:, :], g4[1][:, :, :], AX.X))
                step(dve.tensor_tensor(g4[4][:, :, :], g4[1][:, :, :], c1[1][:, :].unsqueeze(2).to_broadcast(G8), ALU.is_equal))
                step(dve.tensor_scalar(g4[5][:, :, :], g4[4][:, :, :], -1.0, 1e30, ALU.add, ALU.mult))
                E4 = [P, NT, NG, EG]
                v4 = lambda x: x.rearrange("p t (g e) -> p t g e", g=NG)
                step(dve.tensor_tensor(v4(e32[0][:, :, :]), v4(Le), g4[4][:, :, :].unsqueeze(3).to_broadcast(E4), ALU.mult))
                step(dve.tensor_tensor(v4(e32[1][:, :, :]), v4(e32[0][:, :, :]), g4[5][:, :, :].unsqueeze(3).to_broadcast(E4), ALU.add))
                prio = cst[:, NE:2 * NE].unsqueeze(1).to_broadcast(E8)

                def pick(src, mx, pm, eq, pri, oh):
                    step(dve.reduce_max(mx[:, :], src[:, :, :], AX.X))
                    step(dve.tensor_tensor(eq[:, :, :], src[:, :, :], mx[:, :].unsqueeze(2).to_broadcast(E8), ALU.is_equal))
                    step(dve.tensor_tensor(pri[:, :, :], eq[:, :, :], prio, ALU.mult))
                    step(dve.reduce_max(pm[:, :], pri[:, :, :], AX.X))
                    step(dve.tensor_tensor(oh[:, :, :], pri[:, :, :], pm[:, :].unsqueeze(2).to_broadcast(E8), ALU.is_equal))

                oh1, oh2 = e32[4], e32[8]
                pick(e32[1], c1[2], c1[3], e32[2], e32[3], oh1)
                step(dve.scalar_tensor_tensor(out=e32[5][:, :, :], in0=oh1[:, :, :], scalar=-4e30, in1=e32[1][:, :, :],
                                              op0=ALU.mult, op1=ALU.add))
                pick(e32[5], c1[4], c1[5], e32[6], e32[7], oh2)
                dve.tensor_tensor(c1[6][:, :], c1[4][:, :], c1[2][:, :], ALU.subtract).then_inc(e2_ready, 1)
                step(dve.tensor_tensor(M[:, :, :], oh1[:, :, :], oh2[:, :, :], ALU.add))
                step(dve.memset(cum[:, 0, :], 0.0))
                for t in range(NT):
                    ins_ = dve.tensor_tensor(cum[:, t + 1, :], cum[:, t, :], M[:, t, :], ALU.add)
                    if t == NT - 1:
                        dve_last = ins_
                        ins_.then_inc(m_ready, 1)
                        dve.wait_ge(m_ready, 1)
                    else:
                        step(ins_)
                dve.wait_ge(exps, 1)
                step(dve.reduce_sum(c1[8][:, :], g4[3][:, :, :], AX.X))
                dve.wait_ge(e2s, 1)
                step(dve.tensor_scalar(c1[9][:, :], c1[7][:, :], 1.0, None, ALU.add))
                step(dve.tensor_tensor(c1[10][:, :], c1[9][:, :], c1[8][:, :], ALU.mult))
                step(dve.reciprocal(gates[:, :, 0], c1[10][:, :]))
                step(dve.tensor_tensor(gates[:, :, 1], gates[:, :, 0], c1[7][:, :], ALU.mult))
                dve.wait_ge(ranks, 1)
                step(dve.tensor_copy(cnt[:, 0, :], pc[:, 0:NE]))
                step(dve.memset(cnt[:, 1, :], 0.0))
                for j in range(1, 8):
                    step(dve.scalar_tensor_tensor(out=cnt[:, 1 + j, :], in0=cnt[:, 0, :], scalar=float(P * j), in1=cnt[:, j, :],
                                                  op0=ALU.is_gt, op1=ALU.add))
                nov, oend, obase = cnt[:, 8, :], cnt[:, 9, :], cnt[:, 10, :]
                step(dve.tensor_tensor_scan(oend, ones[:, 0:NE], nov, 0.0, ALU.mult, ALU.add))
                step(dve.tensor_tensor(cnt[:, 11, :], oend, nov, ALU.subtract))
                step(dve.tensor_tensor(obase, cnt[:, 11, :], cst[:, 0:NE], ALU.subtract))
                step(dve.tensor_tensor(ovb[:, :, :], oend.unsqueeze(1).to_broadcast([P, NOV, NE]),
                                       cst[:, 2 * NE:].unsqueeze(2).to_broadcast([P, NOV, NE]), ALU.is_le))
                step(dve.reduce_sum(ovs[:, 0:NOV], ovb[:, :, :], AX.X))
                step(dve.tensor_scalar(ovs[:, NB:NB + NOV], ovs[:, 0:NOV], float(NE - 1), None, ALU.min))
                step(dve.tensor_copy(over[:, 0:NOV], ovs[:, NB:NB + NOV]))
                step(dve.tensor_copy(over[:, NOV:NOV + 1], cnt[:, 9, NE - 1:NE]))
                step(dve.tensor_copy(rank[:, :, :], pr[:, 0:NT * NE].rearrange("p (t e) -> p t e", t=NT)))
                step(dve.tensor_scalar(kk[:, 1, :, :], rank[:, :, :], float(P), None, ALU.is_ge))
                for j in range(2, 8):
                    step(dve.scalar_tensor_tensor(out=kk[:, j, :, :], in0=rank[:, :, :], scalar=float(P * j), in1=kk[:, j - 1, :, :],
                                                  op0=ALU.is_ge, op1=ALU.add))
                step(dve.tensor_scalar(e32[9][:, :, :], rank[:, :, :], float(NB), None, ALU.mult))
                step(dve.scalar_tensor_tensor(out=e32[10][:, :, :], in0=kk[:, 7, :, :], scalar=float(1 - NB * P), in1=e32[9][:, :, :],
                                              op0=ALU.mult, op1=ALU.add))
                step(dve.tensor_scalar(cnt[:, 1, :], obase, float(NE - 1), None, ALU.add))
                step(dve.tensor_tensor(e32[11][:, :, :], kk[:, 1, :, :], cnt[:, 1, :].unsqueeze(1).to_broadcast(E8), ALU.mult))
                step(dve.tensor_tensor(e32[12][:, :, :], e32[10][:, :, :], e32[11][:, :, :], ALU.add))
                step(dve.tensor_tensor(e32[13][:, :, :], e32[12][:, :, :], cst[:, 0:NE].unsqueeze(1).to_broadcast(E8), ALU.add))
                step(dve.tensor_tensor(e32[9][:, :, :], e32[13][:, :, :], oh1[:, :, :], ALU.mult))
                step(dve.tensor_tensor(e32[10][:, :, :], e32[13][:, :, :], oh2[:, :, :], ALU.mult))
                step(dve.reduce_sum(posf[:, :, 0], e32[9][:, :, :], AX.X))
                step(dve.reduce_sum(posf[:, :, 1], e32[10][:, :, :], AX.X))
                dve.tensor_copy(slots[:, :, :], posf[:, :, :]).then_inc(slots_ready, 1)

            @block.gpsimd
            def _(pool):
                pool.memset(zero[:, :], 0).then_inc(tok_ready, 1)
                pool.iota(tok[:, :], pattern=[[P, NT]], base=0, channel_multiplier=1).then_inc(tok_ready, 1)
                pool.memset(blank[:, :], 0.0).then_inc(tok_ready, 1)
                pool.wait_ge(tok_ready, 3)
                pool.dma_start(tok_of_slot.rearrange("(p b) n -> p (b n)", p=P), zero[:, :]).then_inc(cleared, 16)
                pool.wait_ge(cleared, 16)
                pool.wait_ge(slots_ready, 1)
                for t in range(NT):
                    for c in range(2):
                        pool.indirect_dma_start(tok_of_slot, bass.IndirectOffsetOnAxis(ap=slots[:, t, c:c + 1], axis=0),
                                                tok[:, t:t + 1], None).then_inc(scattered, 16)
                pool.wait_ge(scattered, 16 * 2 * NT)


def experts(nc, ident, xn, A, tok_of_slot, slot_out, over):
    out_v = slot_out.rearrange("(p b) n -> p b n", b=NB)
    wg_d = A["w_gate"][0].rearrange("e (k p) n -> p e k n", p=P)
    wu_d = A["w_up"][0].rearrange("e (k p) n -> p e k n", p=P)
    wd_d = A["w_down"][0].rearrange("e (k p) n -> p e k n", p=P)
    NW = 3
    with stage(nc) as st:
        idx = st.sb("ex_idx", [P, NB], U32)
        idc = st.sb("ex_idc", [P, 2], U32)
        gain = st.sb("ex_gain", [P, 8])
        wgu = st.sb("ex_wgu", [P, NW, 8, 2 * FF])
        wd = st.sb("ex_wd", [P, NW, 2, D])
        xg = st.sb("ex_xg", [P, 2, D])
        xT = st.sb("ex_xT", [P, 2, 8, P])
        sg = st.sb("ex_sg", [P, 2, FF])
        hh = st.sb("ex_hh", [P, 2, FF])
        h2 = st.sb("ex_h2", [P, 2, FF])
        hTs = st.sb("ex_hT", [P, 2, 2, P])
        ob = st.sb("ex_ob", [P, 2, D])
        tp = st.ps("ex_tp", [P, D])
        gu = [st.ps(f"ex_gu{s}", [P, BANK]) for s in range(2)]
        tph = st.ps("ex_tph", [P, BANK])
        dn = st.ps("ex_dn", [P, D])
        consts_in, idx_in = st.sem("ex_consts"), st.sem("ex_idx_in")
        w_in = [st.sem(f"ex_w_in{s}") for s in range(NW)]
        w_used = st.sem("ex_w_used")
        idx_ok, passed = st.sem("ex_idx_ok"), st.sem("ex_passed")
        x_in = [st.sem(f"ex_x_in{s}") for s in range(2)]
        turned, xT_ok, gu_ok, sig_ok, hh_ok, h2_ok, hturned, hT_ok, dn_ok, ob_a, ob_b = (
            st.sem("ex_" + n) for n in ("turned", "xT_ok", "gu_ok", "sig_ok", "hh_ok", "h2_ok", "hturned", "hT_ok", "dn_ok", "ob_a", "ob_b"))
        stored = [st.sem(f"ex_stored{s}") for s in range(2)]

        def steps(eng, lags, body):
            first, loops = 8, 3
            for s in range(first):
                body(s, s, True)
            with eng.Fori(0, loops) as r:
                for v in range(6):
                    body(r * 6 + (first + v), first + v, False)
            for s in range(first + 6 * loops, NE + lags):
                body(s, s, True)

        def load_weights(sp, e, slot):
            sp.dma_start(wgu[:, slot, :, 0:FF], wg_d[:, e]).then_inc(w_in[slot], 16)
            sp.dma_start(wgu[:, slot, :, FF:], wu_d[:, e]).then_inc(w_in[slot], 16)
            sp.dma_start(wd[:, slot, :, :], wd_d[:, e]).then_inc(w_in[slot], 16)

        def gather(pool, b, slot):
            pool.indirect_dma_start(xg[:, slot, :], None, xn, bass.IndirectOffsetOnAxis(ap=idc[:, slot:slot + 1], axis=0)
                                    ).then_inc(x_in[slot], 16)

        with nc.Block() as block:
            @block.sync
            def _(sp):
                sp.dma_start(idx[:, :], tok_of_slot.rearrange("(p b) n -> p (b n)", p=P)).then_inc(idx_in, 16)
                sp.dma_start(gain[:, :], A["g_ffn_norm"][0].rearrange("(k p) -> p k", p=P),
                             allow_slow_non_contiguous=True).then_inc(consts_in, 16)

                def body(b, c, fixed):
                    if fixed and c >= NE:
                        return
                    if c >= NW:
                        sp.wait_ge(w_used, b - (NW - 1))
                    e = b
                    load_weights(sp, slice(e, e + 1) if fixed else bass.ds(e, 1), c % NW)
                steps(sp, 0, body)

            @block.gpsimd
            def _(pool):
                pool.wait_ge(idx_in, 16)

                def body(b, c, fixed):
                    if fixed and c >= NE:
                        return
                    if c >= 2:
                        pool.wait_ge(turned, b - 1)
                    pool.tensor_copy(idc[:, c % 2:c % 2 + 1], idx[:, bass.ds(b, 1)]).then_inc(idx_ok, 1)
                    pool.wait_ge(idx_ok, b + 1)
                    pool.sem_inc(passed, 1)
                    gather(pool, b, c % 2)
                steps(pool, 0, body)

            @block.tensor
            def _(pe):
                def body(s, c, fixed):
                    if not fixed or c < NE:
                        pe.wait_ge(x_in[c % 2], (s - c % 2) * 8 + 16)
                        if c >= 1:
                            pe.wait_ge(xT_ok, s)
                        for k in range(8):
                            mm = pe.transpose(tp[:, k * P:(k + 1) * P], xg[:, c % 2, k * P:(k + 1) * P], ident[:, :])
                        mm.then_inc(turned, 1)
                    b, c1 = s - 1, c - 1
                    if c1 >= 0 and (not fixed or c1 < NE):
                        pe.wait_ge(w_in[c1 % NW], (b - c1 % NW) * 16 + 48)
                        pe.wait_ge(xT_ok, b + 1)
                        if c1 >= 2:
                            pe.wait_ge(h2_ok, b - 1)
                        for k in range(8):
                            mm = pe.matmul(gu[c1 % 2][:, :], xT[:, c1 % 2, k, :], wgu[:, c1 % NW, k, :], start=(k == 0), stop=(k == 7))
                        mm.then_inc(gu_ok, 1)
                    b, c2 = s - 2, c - 2
                    if c2 >= 0 and (not fixed or c2 < NE):
                        pe.wait_ge(h2_ok, b + 1)
                        if c2 >= 1:
                            pe.wait_ge(hT_ok, b)
                        for k in range(2):
                            mm = pe.transpose(tph[:, k * P:(k + 1) * P], h2[:, c2 % 2, k * P:(k + 1) * P], ident[:, :])
                        mm.then_inc(hturned, 1)
                        pe.wait_ge(hT_ok, b + 1)
                        if c2 >= 1:
                            pe.wait_ge(ob_a, b)
                            pe.wait_ge(ob_b, b)
                        for n in range(2):
                            for k in range(2):
                                mm = pe.matmul(dn[:, n * BANK:(n + 1) * BANK], hTs[:, c2 % 2, k, :],
                                               wd[:, c2 % NW, k, n * BANK:(n + 1) * BANK], start=(k == 0), stop=(k == 1))
                        mm.then_inc(dn_ok, 1)
                        pe.wait_ge(dn_ok, b + 1)
                        pe.sem_inc(w_used, 1)
                steps(pe, 2, body)

            @block.scalar
            def _(act):
                def body(s, c, fixed):
                    b, c1 = s - 1, c - 1
                    if c1 >= 0 and (not fixed or c1 < NE):
                        act.wait_ge(gu_ok, b + 1)
                        act.activation(sg[:, c1 % 2, :], gu[c1 % 2][:, 0:FF], ACT.Sigmoid).then_inc(sig_ok, 1)
                    b, c2 = s - 2, c - 2
                    if c2 >= 0 and (not fixed or c2 < NE):
                        act.wait_ge(hturned, b + 1)
                        act.activation(hTs[:, c2 % 2, :, :].rearrange("p k n -> p (k n)"), tph[:, 0:2 * P], ACT.Copy).then_inc(hT_ok, 1)
                        act.wait_ge(dn_ok, b + 1)
                        if c2 >= 2:
                            act.wait_ge(stored[c2 % 2], (b - c2 % 2) * 8)
                        act.activation(ob[:, c2 % 2, 0:BANK], dn[:, 0:BANK], ACT.Copy).then_inc(ob_a, 1)
                        act.wait_ge(ob_a, b + 1)
                        act.wait_ge(ob_b, b + 1)
                        act.dma_start(out_v[:, bass.ds(b, 1), :].rearrange("p b n -> p (b n)"), ob[:, c2 % 2, :]).then_inc(stored[c2 % 2], 16)
                steps(act, 2, body)
                act.wait_ge(stored[0], 8 * NE)
                act.wait_ge(stored[1], 8 * NE)

            @block.vector
            def _(dve):
                dve.wait_ge(consts_in, 16)

                def body(s, c, fixed):
                    if not fixed or c < NE:
                        dve.wait_ge(turned, s + 1)
                        if c >= 2:
                            dve.wait_ge(gu_ok, s - 1)
                        dve.tensor_tensor(xT[:, c % 2, :, :], tp[:, :].rearrange("p (k n) -> p k n", k=8),
                                          gain[:, :].unsqueeze(2).to_broadcast([P, 8, P]), ALU.mult).then_inc(xT_ok, 1)
                    b, c1 = s - 1, c - 1
                    if c1 >= 0 and (not fixed or c1 < NE):
                        dve.wait_ge(sig_ok, b + 1)
                        dve.tensor_tensor(hh[:, c1 % 2, :], gu[c1 % 2][:, 0:FF], sg[:, c1 % 2, :], ALU.mult).then_inc(hh_ok, 1)
                        dve.wait_ge(hh_ok, b + 1)
                        if c1 >= 2:
                            dve.wait_ge(hturned, b - 1)
                        dve.tensor_tensor(h2[:, c1 % 2, :], hh[:, c1 % 2, :], gu[c1 % 2][:, FF:], ALU.mult).then_inc(h2_ok, 1)
                    b, c2 = s - 2, c - 2
                    if c2 >= 0 and (not fixed or c2 < NE):
                        dve.wait_ge(dn_ok, b + 1)
                        if c2 >= 2:
                            dve.wait_ge(stored[c2 % 2], (b - c2 % 2) * 8)
                        dve.tensor_copy(ob[:, c2 % 2, BANK:], dn[:, BANK:]).then_inc(ob_b, 1)
                steps(dve, 2, body)

    with stage(nc) as st:
        idx = st.sb("fx_idx", [P, NB], U32)
        idc = st.sb("fx_idc", [P, 1], U32)
        gain = st.sb("fx_gain", [P, 8])
        wgu = st.sb("fx_wgu", [P, 8, 2 * FF])
        wd = st.sb("fx_wd", [P, 2, D])
        xg = st.sb("fx_xg", [P, D])
        xT = st.sb("fx_xT", [P, 8, P])
        sg, hh, h2 = (st.sb("fx_" + n, [P, FF]) for n in ("sg", "hh", "h2"))
        hTs = st.sb("fx_hT", [P, 2 * P])
        ob = st.sb("fx_ob", [P, D])
        tp, dn = st.ps("fx_tp", [P, D]), st.ps("fx_dn", [P, D])
        gu, tph = st.ps("fx_gu", [P, BANK]), st.ps("fx_tph", [P, BANK])
        consts_in, w_in, idx_ok, x_in, turned, xT_ok, gu_ok, sig_ok, hh_ok, h2_ok, hturned, hT_ok, dn_ok, ob_ok, stored = (
            st.sem("fx_" + n) for n in ("consts", "w_in", "idx_ok", "x_in", "turned", "xT_ok", "gu_ok", "sig_ok", "hh_ok",
                                        "h2_ok", "hturned", "hT_ok", "dn_ok", "ob_ok", "stored"))

        passed = st.sem("fx_passed")

        def each(eng, body):
            n = eng.value_load(over[0:1, NOV:NOV + 1], min_val=0, max_val=NOV)
            with eng.Fori(0, NOV) as j:
                with eng.If(n > j):
                    body(j)

        with nc.Block() as block:
            @block.sync
            def _(sp):
                sp.dma_start(idx[:, :], tok_of_slot.rearrange("(p b) n -> p (b n)", p=P)).then_inc(consts_in, 16)
                sp.dma_start(gain[:, :], A["g_ffn_norm"][0].rearrange("(k p) -> p k", p=P),
                             allow_slow_non_contiguous=True).then_inc(consts_in, 16)
                sp.wait_ge(consts_in, 32)
                sp.sem_inc(stored, 16)

                def body(j):
                    e = sp.value_load(over[0:1, bass.ds(j, 1)], min_val=0, max_val=NE - 1)
                    sp.wait_ge(stored, j * 16 + 16)
                    sp.dma_start(wgu[:, :, 0:FF], wg_d[:, bass.ds(e, 1)]).then_inc(w_in, 16)
                    sp.dma_start(wgu[:, :, FF:], wu_d[:, bass.ds(e, 1)]).then_inc(w_in, 16)
                    sp.dma_start(wd[:, :, :], wd_d[:, bass.ds(e, 1)]).then_inc(w_in, 16)
                    sp.wait_ge(ob_ok, j + 1)
                    sp.dma_start(out_v[:, bass.ds(j + NE, 1), :].rearrange("p b n -> p (b n)"), ob[:, :]).then_inc(stored, 16)
                    sp.wait_ge(stored, j * 16 + 32)
                    sp.sem_inc(passed, 1)
                each(sp, body)

            @block.gpsimd
            def _(pool):
                pool.wait_ge(consts_in, 32)

                def body(j):
                    pool.wait_ge(stored, j * 16 + 16)
                    pool.tensor_copy(idc[:, :], idx[:, bass.ds(j + NE, 1)]).then_inc(idx_ok, 1)
                    pool.wait_ge(idx_ok, j + 1)
                    pool.sem_inc(passed, 1)
                    pool.indirect_dma_start(xg[:, :], None, xn, bass.IndirectOffsetOnAxis(ap=idc[:, :], axis=0)).then_inc(x_in, 16)
                each(pool, body)

            @block.tensor
            def _(pe):
                def body(j):
                    pe.wait_ge(x_in, j * 16 + 16)
                    for k in range(8):
                        mm = pe.transpose(tp[:, k * P:(k + 1) * P], xg[:, k * P:(k + 1) * P], ident[:, :])
                    mm.then_inc(turned, 1)
                    pe.wait_ge(w_in, j * 48 + 48)
                    pe.wait_ge(xT_ok, j + 1)
                    for k in range(8):
                        mm = pe.matmul(gu[:, :], xT[:, k, :], wgu[:, k, :], start=(k == 0), stop=(k == 7))
                    mm.then_inc(gu_ok, 1)
                    pe.wait_ge(h2_ok, j + 1)
                    for k in range(2):
                        mm = pe.transpose(tph[:, k * P:(k + 1) * P], h2[:, k * P:(k + 1) * P], ident[:, :])
                    mm.then_inc(hturned, 1)
                    pe.wait_ge(hT_ok, j + 1)
                    for n in range(2):
                        for k in range(2):
                            mm = pe.matmul(dn[:, n * BANK:(n + 1) * BANK], hTs[:, k * P:(k + 1) * P],
                                           wd[:, k, n * BANK:(n + 1) * BANK], start=(k == 0), stop=(k == 1))
                    mm.then_inc(dn_ok, 1)
                each(pe, body)

            @block.scalar
            def _(act):
                def body(j):
                    act.wait_ge(gu_ok, j + 1)
                    act.activation(sg[:, :], gu[:, 0:FF], ACT.Sigmoid).then_inc(sig_ok, 1)
                    act.wait_ge(hturned, j + 1)
                    act.activation(hTs[:, :], tph[:, 0:2 * P], ACT.Copy).then_inc(hT_ok, 1)
                each(act, body)

            @block.vector
            def _(dve):
                dve.wait_ge(consts_in, 32)

                def body(j):
                    dve.wait_ge(turned, j + 1)
                    dve.tensor_tensor(xT[:, :, :], tp[:, :].rearrange("p (k n) -> p k n", k=8),
                                      gain[:, :].unsqueeze(2).to_broadcast([P, 8, P]), ALU.mult).then_inc(xT_ok, 1)
                    dve.wait_ge(sig_ok, j + 1)
                    dve.tensor_tensor(hh[:, :], gu[:, 0:FF], sg[:, :], ALU.mult).then_inc(hh_ok, 1)
                    dve.wait_ge(hh_ok, j + 1)
                    dve.tensor_tensor(h2[:, :], hh[:, :], gu[:, FF:], ALU.mult).then_inc(h2_ok, 1)
                    dve.wait_ge(dn_ok, j + 1)
                    dve.tensor_copy(ob[:, :], dn[:, :]).then_inc(ob_ok, 1)
                each(dve, body)


def moe(nc, A, C, scr, ident, hT):
    with ExitStack() as ctx:
        gates = ctx.enter_context(nc.sbuf_tensor("gates", [P, NT, 2], F32))
        slots = ctx.enter_context(nc.sbuf_tensor("slots", [P, NT, 2], U32))
        over = ctx.enter_context(nc.sbuf_tensor("over", [P, NOV + 1], U32))
        tok_of_slot = nc.dram_tensor("tok_of_slot", (P * NB, 1), U32, kind="Internal").ap()
        route(nc, hT, A, C, tok_of_slot, scr["slot_out"], gates, slots, over)
        experts(nc, ident, scr["xn"], A, tok_of_slot, scr["slot_out"], over)
        norm_rows(nc, "e0", ident, D, [(0, D, lambda t: rows(scr["x1"], t))], [(0, D)], hT=hT,
                  expert_rows=(scr["slot_out"], gates, slots), post=A["g_final"], keep=scr["x2"])


SCRATCH.update(x1=(S, D), xn=(S, D), slot_out=(P * NB, D), x2=(S, D))



RH, RDK, RDV = 4, 64, 128


def retention(nc, ident, rows_in, C, out):
    QK = 2 * RH

    def by_parity(ap, q):
        return ap.rearrange("p (j q n) -> p j q n", q=2, n=P)[:, :, q, :]

    with stage(nc) as st:
        x = st.sb("re_x", [P, 2, 1024])
        cs = st.sb("re_cs", [P, NT, 64])
        t1, t2, t3, t4 = (st.sb(f"re_t{i}", [P, 2, QK, 32]) for i in range(4))
        rot = st.sb("re_rot", [P, 2, QK, 64])
        dec = st.sb("re_dec", [P, 2, QK, 64])
        rowdec = st.sb("re_rowdec", [P, QK])
        dmat = st.sb("re_dmat", [P, RH * P])
        gch = st.sb("re_gch", [P, 2])
        qkT = st.sb("re_qkT", [P, 2, 6, P])
        sc = st.sb("re_sc", [P, 2, RH * P])
        state = st.sb("re_state", [P, 2, 2, RDV])
        ob = st.sb("re_ob", [P, 2, RH * RDV])
        tp = [st.ps(f"re_tp{i}", [P, BANK]) for i in range(2)]
        sps = [st.ps(f"re_s{i}", [P, BANK]) for i in range(2)]
        ops = [st.ps(f"re_o{i}", [P, BANK]) for i in range(2)]
        kv = st.ps("re_kv", [P, BANK])
        consts_in, m1, rotated, decayed, turned, T_ok, s_ok, sc_ok, o_ok, kv_ok, state_ok, ob_ok = (
            st.sem("re_" + n) for n in ("consts", "m1", "rotated", "decayed", "turned", "T_ok", "s_ok", "sc_ok", "o_ok", "kv_ok",
                                        "state_ok", "ob_ok"))
        x_in = [st.sem(f"re_x_in{u}") for u in range(2)]
        stored = [st.sem(f"re_stored{u}") for u in range(2)]
        with nc.Block() as block:
            @block.sync
            def _(sp):
                sp.dma_start(cs[:, :, :], C["ret_cs"].rearrange("(t p) n -> p t n", p=P)).then_inc(consts_in, 16)
                sp.dma_start(rowdec[:, :], C["ret_rowdec"]).then_inc(consts_in, 16)
                sp.dma_start(dmat[:, :], C["ret_decay"]).then_inc(consts_in, 16)
                sp.dma_start(gch[:, :], C["ret_gchunk"]).then_inc(consts_in, 16)
                for t in range(NT):
                    u = t % 2
                    if t >= 2:
                        sp.wait_ge(kv_ok, t - 1)
                        sp.wait_ge(o_ok, t - 1)
                        sp.wait_ge(m1, 4 * (t - 1))
                    sp.dma_start(x[:, u, :], rows_in[t * P:(t + 1) * P, 0:1024]).then_inc(x_in[u], 16)

            @block.gpsimd
            def _(pool):
                pool.wait_ge(consts_in, 64)
                for t in range(NT):
                    u = t % 2
                    pool.wait_ge(x_in[u], 16 * (t // 2 + 1))
                    if t >= 2:
                        pool.wait_ge(turned, t - 1)
                        pool.wait_ge(kv_ok, t - 1)
                    xv = x[:, u, 0:512].rearrange("p (h d) -> p h d", d=64)
                    c = cs[:, t, 0:32].unsqueeze(1).to_broadcast([P, QK, 32])
                    s = cs[:, t, 32:64].unsqueeze(1).to_broadcast([P, QK, 32])
                    for o, a, b in ((t1, 0, c), (t2, 1, s), (t3, 0, s), (t4, 1, c)):
                        pool.tensor_tensor(o[:, u, :, :], xv[:, :, 32 * a:32 * a + 32], b, ALU.mult).then_inc(m1, 1)
                    pool.wait_ge(m1, 4 * (t + 1))
                    pool.tensor_tensor(rot[:, u, :, 0:32], t1[:, u, :, :], t2[:, u, :, :], ALU.subtract).then_inc(rotated, 1)
                    pool.tensor_tensor(rot[:, u, :, 32:64], t3[:, u, :, :], t4[:, u, :, :], ALU.add).then_inc(rotated, 1)
                    pool.wait_ge(rotated, 2 * (t + 1))
                    pool.tensor_tensor(dec[:, u, :, :], rot[:, u, :, :], rowdec[:, :].unsqueeze(2).to_broadcast([P, QK, 64]),
                                       ALU.mult).then_inc(decayed, 1)

            @block.tensor
            def _(pe):
                for t in range(NT):
                    u = t % 2
                    pe.wait_ge(decayed, t + 1)
                    if t >= 1:
                        pe.wait_ge(T_ok, 2 * t)
                    r = rot[:, u, :, :].rearrange("p h d -> p (h d)")
                    d = dec[:, u, :, :].rearrange("p h d -> p (h d)")
                    for j in range(4):
                        pe.transpose(tp[0][:, j * P:(j + 1) * P], r[:, j * P:(j + 1) * P], ident[:, :])
                    for j in range(2):
                        mm = pe.transpose(tp[1][:, j * P:(j + 1) * P], d[:, j * P:(j + 1) * P], ident[:, :])
                    mm.then_inc(turned, 1)
                    pe.wait_ge(T_ok, 2 * (t + 1))
                    if t >= 1:
                        pe.wait_ge(sc_ok, 2 * t)
                    for h in range(RH):
                        p0, j = 64 * (h % 2), h // 2
                        mm = pe.matmul(sps[h % 2][:, j * P:(j + 1) * P], qkT[p0:p0 + 64, u, 2 + j, :], qkT[p0:p0 + 64, u, j, :],
                                       start=True, stop=True)
                    mm.then_inc(s_ok, 1)
                    if t >= 1:
                        pe.wait_ge(state_ok, 2 * t + 1)
                    for h in range(RH):
                        p0, j = 64 * (h % 2), h // 2
                        mm = pe.matmul(kv[p0:p0 + 64, j * RDV:(j + 1) * RDV], dec[:, u, RH + h, :],
                                       x[:, u, 512 + h * RDV:512 + (h + 1) * RDV], start=True, stop=True, skip_group_check=True)
                    mm.then_inc(kv_ok, 1)
                    pe.wait_ge(sc_ok, 2 * (t + 1))
                    pe.wait_ge(state_ok, 2 * t + 1)
                    if t >= 1:
                        pe.wait_ge(ob_ok, 2 * t)
                    for h in range(RH):
                        p0, j = 64 * (h % 2), h // 2
                        o = ops[h % 2][:, j * RDV:(j + 1) * RDV]
                        pe.matmul(o, sc[:, u, h * P:(h + 1) * P], x[:, u, 512 + h * RDV:512 + (h + 1) * RDV], start=True, stop=False)
                        mm = pe.matmul(o, qkT[p0:p0 + 64, u, 4 + j, :], state[p0:p0 + 64, u, j, :], start=False, stop=True)
                    mm.then_inc(o_ok, 1)

            @block.vector
            def _(dve):
                dve.memset(state[:, 0, :, :], 0.0).then_inc(state_ok, 1)
                dve.wait_ge(consts_in, 64)
                for t in range(NT):
                    u = t % 2
                    dve.wait_ge(turned, t + 1)
                    if t >= 2:
                        dve.wait_ge(o_ok, t - 1)
                    dve.tensor_copy(qkT[:, u, 0:4, :].rearrange("p j n -> p (j n)"), tp[0][:, :]).then_inc(T_ok, 1)
                    dve.tensor_copy(qkT[:, u, 4:6, :].rearrange("p j n -> p (j n)"), tp[1][:, 0:2 * P]).then_inc(T_ok, 1)
                    dve.wait_ge(s_ok, t + 1)
                    for q in range(2):
                        dve.tensor_tensor(by_parity(sc[:, u, :], q), sps[q][:, 0:2 * P].rearrange("p (j n) -> p j n", j=2),
                                          by_parity(dmat[:, :], q), ALU.mult).then_inc(sc_ok, 1)
                    dve.wait_ge(kv_ok, t + 1)
                    dve.wait_ge(state_ok, 2 * t + 1)
                    if t >= 1:
                        dve.wait_ge(o_ok, t)
                    for j in range(2):
                        dve.scalar_tensor_tensor(out=state[:, 1 - u, j, :], in0=state[:, u, j, :], scalar=gch[:, j:j + 1],
                                                 in1=kv[:, j * RDV:(j + 1) * RDV], op0=ALU.mult, op1=ALU.add).then_inc(state_ok, 1)

            @block.scalar
            def _(act):
                for t in range(NT):
                    u = t % 2
                    act.wait_ge(o_ok, t + 1)
                    if t >= 2:
                        act.wait_ge(stored[u], 16 * (t // 2))
                    for q in range(2):
                        act.activation(by_parity(ob[:, u, :], q), ops[q][:, 0:2 * P].rearrange("p (j n) -> p j n", j=2),
                                       ACT.Copy).then_inc(ob_ok, 1)
                    act.wait_ge(ob_ok, 2 * (t + 1))
                    act.dma_start(rows(out, t), ob[:, u, :]).then_inc(stored[u], 16)
                act.wait_ge(stored[0], 64)
                act.wait_ge(stored[1], 64)



def stick_breaking(nc, ident, heads, qkT_in, v_in_d, C, out):
    T8, DV = NT, 64
    total = heads * T8
    widths = [(i + 1) * P for i in range(T8)]
    with stage(nc) as st:
        qraw, kraw = (st.sb("sb_" + n, [P, 2, S]) for n in ("qraw", "kraw"))
        qs, kh, kl = (st.sb("sb_" + n, [P, 2, S], F32R) for n in ("qs", "kh", "kl"))
        v = st.sb("sb_v", [P, 2, NT, DV])
        om = st.sb("sb_om", [P, 2, S])
        be = st.sb("sb_be", [P, 4, S])
        pr = st.sb("sb_pr", [P, 2, S + 1])
        w = st.sb("sb_w", [P, 4, S])
        wT = st.sb("sb_wT", [P, 2, S])
        ones = st.sb("sb_ones", [P, S])
        masks = st.sb("sb_masks", [P, 2, P])
        o = st.sb("sb_ob", [P, 2, NT, DV])
        sps = [st.ps(f"sb_s{s}", [P, S]) for s in range(2)]
        tps = st.ps("sb_t", [P, S])
        ops = [st.ps(f"sb_op{s}", [P, BANK]) for s in range(2)]
        raw_in = [st.sem(f"sb_raw_in{s}") for s in range(2)]
        v_in = [st.sem(f"sb_v_in{s}") for s in range(2)]
        stored = [st.sem(f"sb_stored{s}") for s in range(2)]
        (consts_in, ones_ok, hi_ok, lo_ok, z_ok, om_ok, be_ok, om_masked, be_masked, pr_ok, w_ok, turned_a, turned_b,
         wT_a, wT_b, pv_done, o_done) = (
            st.sem("sb_" + n) for n in ("consts", "ones_ok", "hi_ok", "lo_ok", "z_ok", "om_ok", "be_ok", "om_masked", "be_masked",
                                        "pr_ok", "w_ok", "turned_a", "turned_b", "wT_a", "wT_b", "pv_done", "o_done"))

        passed = st.sem("sb_passed")

        def halves(i):
            return min(i + 1, BANK // P), i + 1

        with nc.Block() as block:
            @block.sync
            def _(sp):
                def load_raw(h, u):
                    for b in range(2):
                        sp.dma_start(qraw[64 * b:64 * b + 64, u, :], qkT_in[bass.ds(h * 64, 64), :]).then_inc(raw_in[u], 16)
                        sp.dma_start(kraw[64 * b:64 * b + 64, u, :], qkT_in[bass.ds(h * 64 + 512, 64), :]).then_inc(raw_in[u], 16)

                def load_v(h, u):
                    sp.dma_start(v[:, u, :, :], v_in_d[:, bass.ds(h * 64, 64)].rearrange("(t p) d -> p t d", p=P)).then_inc(v_in[u], 16)

                def store(h, u):
                    sp.wait_ge(o_done, h * T8 + T8)
                    sp.sem_inc(passed, 1)
                    sp.dma_start(out[:, bass.ds(h * DV, DV)].rearrange("(t p) d -> p t d", p=P),
                                 o[:, u, :, :]).then_inc(stored[u], 16)

                sp.sem_inc(stored[0], 16)
                sp.sem_inc(stored[1], 16)
                load_raw(0, 0)
                sp.dma_start(masks[:, :, :], C["strict"]).then_inc(consts_in, 16)
                load_v(0, 0)
                load_raw(1, 1)
                load_v(1, 1)
                with sp.Fori(0, heads // 2 - 1) as r:
                    for u in range(2):
                        h = r * 2 + u
                        sp.wait_ge(lo_ok, h * 8 + 8)
                        sp.sem_inc(passed, 1)
                        load_raw(h + 2, u)
                        store(h, u)
                        sp.wait_ge(pv_done, h * T8 + T8)
                        sp.sem_inc(passed, 1)
                        load_v(h + 2, u)
                for u in range(2):
                    store(heads - 2 + u, u)
                for u in range(2):
                    sp.wait_ge(stored[u], 16 * (heads // 2 + 1))

            @block.tensor
            def _(pe):
                def body(l, T):
                    if active(T, 0, total):
                        u, i = l // T8, l % T8
                        if i == 0:
                            pe.wait_ge(lo_ok, T + 8)
                        reached(pe, be_ok, T - 1)
                        for c0 in range(0, widths[i], BANK):
                            cc = slice(c0, min(widths[i], c0 + BANK))
                            pe.matmul(sps[l % 2][:, cc], qs[:, u, i * P:(i + 1) * P], kh[:, u, cc], start=True, stop=False)
                            mm = pe.matmul(sps[l % 2][:, cc], qs[:, u, i * P:(i + 1) * P], kl[:, u, cc], start=False, stop=True)
                        mm.then_inc(z_ok, 1)
                    if active(T, 3, total):
                        m = (l - 3) % TURN
                        a, b = halves(m % T8)
                        reached(pe, w_ok, T - 2)
                        reached(pe, wT_a, T - 3)
                        reached(pe, wT_b, T - 3)
                        for k in range(b):
                            mm = pe.transpose(tps[:, k * P:(k + 1) * P], w[:, m % 4, k * P:(k + 1) * P], ident[:, :])
                            if k == a - 1 and b > a:
                                mm.then_inc(turned_a, 1)
                        if b > a:
                            mm.then_inc(turned_b, 1)
                        else:
                            mm.then_inc(turned_a, 1)
                            pe.wait_ge(turned_a, T - 2)
                            pe.sem_inc(turned_b, 1)
                    if active(T, 4, total):
                        m = (l - 4) % TURN
                        u, i = m // T8, m % T8
                        if i == 0:
                            pe.wait_ge(v_in[u], T - 4 - 8 * u + 16)
                        reached(pe, o_done, T - 5)
                        reached(pe, wT_a, T - 3)
                        reached(pe, wT_b, T - 3)
                        for k in range(i + 1):
                            mm = pe.matmul(ops[m % 2][:, 0:DV], wT[:, m % 2, k * P:(k + 1) * P], v[:, u, k, :],
                                           start=(k == 0), stop=(k == i))
                        mm.then_inc(pv_done, 1)
                tiles(pe, total, 8, 4, body)

            @block.scalar
            def _(act):
                def split_hi(u, n_in):
                    act.wait_ge(raw_in[u], n_in)
                    act.activation(qs[:, u, :], qraw[:, u, :], ACT.Copy).then_inc(hi_ok, 4)
                    act.activation(kh[:, u, :], kraw[:, u, :], ACT.Copy).then_inc(hi_ok, 4)

                split_hi(0, 64)

                def body(l, T):
                    if active(T, 0, total):
                        n = widths[l % T8]
                        act.wait_ge(z_ok, T + 1)
                        reached(act, pr_ok, T - 1)
                        act.activation(om[:, l % 2, 0:n], sps[l % 2][:, 0:n], ACT.Sigmoid, scale=-0.125).then_inc(om_ok, 1)
                    if active(T, 3, total):
                        m = (l - 3) % TURN
                        a, b = halves(m % T8)
                        reached(act, turned_b, T - 2)
                        if b > a:
                            reached(act, pv_done, T - 4)
                            act.activation(wT[:, m % 2, a * P:b * P], tps[:, a * P:b * P], ACT.Copy).then_inc(wT_b, 1)
                        else:
                            act.sem_inc(wT_b, 1)
                    if active(T, 0, total):
                        n = widths[l % T8]
                        reached(act, w_ok, T - 3)
                        act.activation(be[:, l % 4, 0:n], sps[l % 2][:, 0:n], ACT.Sigmoid, scale=0.125).then_inc(be_ok, 1)
                        if l % T8 == 3 and active(T + 5, 0, total):
                            u = 1 - l // T8
                            split_hi(u, (T + 5 - 8 * u) * 4 + 64)
                tiles(act, total, 8, 4, body)

            @block.vector
            def _(dve):
                def split_lo(u, n_hi):
                    dve.wait_ge(hi_ok, n_hi)
                    dve.tensor_tensor(qs[64:P, u, :], qraw[64:P, u, :], qs[64:P, u, :].bitcast(F32), ALU.subtract).then_inc(lo_ok, 4)
                    dve.tensor_tensor(kl[:, u, :], kraw[:, u, :], kh[:, u, :].bitcast(F32), ALU.subtract).then_inc(lo_ok, 4)

                dve.memset(ones[:, :], 1.0).then_inc(ones_ok, 1)
                dve.memset(pr[:, :, S:S + 1], 1.0).then_inc(ones_ok, 1)
                split_lo(0, 8)
                dve.wait_ge(ones_ok, 2)
                dve.wait_ge(consts_in, 16)

                def body(l, T):
                    if active(T, 3, total):
                        m = (l - 3) % TURN
                        a, _ = halves(m % T8)
                        reached(dve, turned_a, T - 2)
                        reached(dve, pv_done, T - 4)
                        dve.tensor_copy(wT[:, m % 2, 0:a * P], tps[:, 0:a * P]).then_inc(wT_a, 1)
                    if active(T, 0, total):
                        n = widths[l % T8]
                        dve.wait_ge(om_ok, T + 1)
                        d = om[:, l % 2, n - P:n]
                        dve.tensor_tensor(d, d, masks[:, 1, :], ALU.max).then_inc(om_masked, 1)
                        dve.wait_ge(om_masked, T + 1)
                        reached(dve, w_ok, T - 1)
                        dve.tensor_tensor_scan(pr[:, l % 2, S - n:S][:, ::-1], om[:, l % 2, 0:n][:, ::-1], ones[:, 0:n], 1.0,
                                               ALU.mult, ALU.mult).then_inc(pr_ok, 1)
                        dve.wait_ge(be_ok, T + 1)
                        d = be[:, l % 4, n - P:n]
                        dve.tensor_tensor(d, d, masks[:, 0, :], ALU.mult).then_inc(be_masked, 1)
                        if l % T8 == 4 and active(T + 4, 0, total):
                            split_lo(1 - l // T8, T + 4 + 8)
                    if active(T, 4, total):
                        m = (l - 4) % TURN
                        u, i = m // T8, m % T8
                        reached(dve, pv_done, T - 3)
                        if i == 0:
                            dve.wait_ge(stored[u], T - 4 - 8 * u + 16)
                        dve.tensor_copy(o[:, u, i, :], ops[m % 2][:, 0:DV]).then_inc(o_done, 1)
                tiles(dve, total, 8, 4, body)

            @block.gpsimd
            def _(pool):
                def body(l, T):
                    if active(T, 0, total):
                        n = widths[l % T8]
                        pool.wait_ge(be_masked, T + 1)
                        pool.wait_ge(pr_ok, T + 1)
                        reached(pool, turned_b, T - 3)
                        pool.tensor_tensor(w[:, l % 4, 0:n], be[:, l % 4, 0:n], pr[:, l % 2, S - n + 1:S + 1],
                                           ALU.mult).then_inc(w_ok, 1)
                tiles(pool, total, 8, 0, body)



HH = 4
LEVELS = [64, 32, 16, 8, 4, 2, 1]


def hgrn2(nc, ident, fT_in, v_in, C, out):
    NL = len(LEVELS)
    with stage(nc) as st:
        q = st.sb("hg_q", [P, 2, S])
        f = st.sb("hg_f", [P, 2, S])
        vv = st.sb("hg_v", [P, 2, NT, P])
        kk = st.sb("hg_k", [P, S])
        az, ez, lf = (st.sb("hg_" + n, [P, S]) for n in ("az", "ez", "lf"))
        b = st.sb("hg_b", [P, S])
        df = st.sb("hg_df", [P, 2, S])
        ex = st.sb("hg_ex", [P, 2, S])
        eb, el, qb, kb = (st.sb("hg_" + n, [P, S]) for n in ("eb", "el", "qb", "kb"))
        dl = st.sb("hg_dl", [P, S])
        qk = st.sb("hg_qk", [P, NL, S])
        ones = st.sb("hg_ones", [P, P])
        mask = st.sb("hg_mask", [P, NL + 1, P])
        ms = st.sb("hg_ms", [P, 2, NL + 1, P])
        sT = st.sb("hg_sT", [P, 2, P])
        kr = st.sb("hg_kr", [P, 2, P])
        state = st.sb("hg_state", [P, 2, P])
        ob = st.sb("hg_ob", [P, 2, NT, P])
        sps = [st.ps(f"hg_s{i}", [P, 2 * BANK]) for i in range(2)]
        tps, ops, kvs = st.ps("hg_t", [P, BANK]), st.ps("hg_o", [P, BANK]), st.ps("hg_kv", [P, BANK])
        head_in = [st.sem(f"hg_in{u}") for u in range(2)]
        stored = [st.sem(f"hg_stored{u}") for u in range(2)]
        (consts_in, ones_ok, k_ok, az_ok, ez_ok, lg_ok, lf_ok, b_ok, df_ok, ex_ok, qk_ok, dl_ok, eb_ok, el_ok, qb_ok, kb_ok,
         s_ok, ms_ok, sT_ok, turned, kr_ok, o_ok, kv_ok, state_ok, ob_ok, state0) = (
            st.sem("hg_" + n) for n in ("consts", "ones_ok", "k_ok", "az_ok", "ez_ok", "lg_ok", "lf_ok", "b_ok", "df_ok", "ex_ok",
                                        "qk_ok", "dl_ok", "eb_ok", "el_ok", "qb_ok", "kb_ok", "s_ok", "ms_ok", "sT_ok", "turned",
                                        "kr_ok", "o_ok", "kv_ok", "state_ok", "ob_ok", "state0"))

        def split(x, m):
            return x.rearrange("p (n h m) -> p n h m", h=2, m=m)

        with nc.Block() as block:
            @block.sync
            def _(sp):
                sp.dma_start(mask[:, :, :], C["levels"]).then_inc(consts_in, 16)

                for h in range(HH):
                    u = h % 2
                    if h >= 2:
                        sp.wait_ge(o_ok, NT * (h - 1))
                        sp.wait_ge(kv_ok, NT * (h - 1))
                    sp.dma_start(f[:, u, :], fT_in[512 + h * P:512 + (h + 1) * P, :]).then_inc(head_in[u], 16)
                    sp.dma_start(q[:, u, :], fT_in[h * P:(h + 1) * P, :]).then_inc(head_in[u], 16)
                    sp.dma_start(vv[:, u, :, :], v_in[:, h * P:(h + 1) * P].rearrange("(t p) d -> p t d", p=P)).then_inc(head_in[u], 16)
                    if h >= 1:
                        sp.wait_ge(ob_ok, NT * h)
                        sp.dma_start(out[:, (h - 1) * P:h * P].rearrange("(t p) d -> p t d", p=P), ob[:, 1 - u, :, :]).then_inc(stored[1 - u], 16)
                sp.wait_ge(ob_ok, NT * HH)
                sp.dma_start(out[:, (HH - 1) * P:HH * P].rearrange("(t p) d -> p t d", p=P), ob[:, 1, :, :]).then_inc(stored[1], 16)
                sp.wait_ge(stored[0], 32)
                sp.wait_ge(stored[1], 32)

            @block.scalar
            def _(act):
                for h in range(HH):
                    u = h % 2
                    act.wait_ge(head_in[u], 48 * (h // 2 + 1))
                    if h >= 1:
                        act.wait_ge(qk_ok, 2 * NL * h)
                        act.wait_ge(kb_ok, h)
                        act.wait_ge(s_ok, NT * h)
                    act.activation(kk[:, :], f[:, u, :], ACT.Sigmoid, scale=-1.0).then_inc(k_ok, 1)
                    act.activation(az[:, :], f[:, u, :], ACT.Abs).then_inc(az_ok, 1)
                    act.wait_ge(az_ok, h + 1)
                    act.activation(ez[:, :], az[:, :], ACT.Exp, scale=-1.0).then_inc(ez_ok, 1)
                    act.wait_ge(ez_ok, h + 1)
                    if h >= 1:
                        act.wait_ge(b_ok, NT * h)
                    act.activation(az[:, :], ez[:, :], ACT.Ln, bias=1.0).then_inc(lg_ok, 1)
                    for n in range(NL):
                        g = h * NL + n
                        act.wait_ge(df_ok, 2 * (g + 1))
                        if g >= 2:
                            act.wait_ge(qk_ok, 2 * (g - 1))
                        act.activation(ex[:, n % 2 if h % 2 == 0 else (n + 1) % 2, :], df[:, g % 2, :], ACT.Exp).then_inc(ex_ok, 1)
                    act.wait_ge(b_ok, NT * (h + 1))
                    if h >= 1:
                        act.wait_ge(state_ok, NT * h)
                    act.activation(eb[:, :], b[:, :], ACT.Exp).then_inc(eb_ok, 1)
                    act.wait_ge(dl_ok, h + 1)
                    act.activation(el[:, :], dl[:, :], ACT.Exp).then_inc(el_ok, 1)
                    for c in range(NT):
                        g = h * NT + c
                        act.wait_ge(turned, g + 1)
                        if g >= 2:
                            act.wait_ge(kv_ok, g - 1)
                        act.activation(kr[:, g % 2, :], tps[:, 0:P], ACT.Copy).then_inc(kr_ok, 1)
                        if c == 0 and h >= 2:
                            act.wait_ge(stored[u], 16 * (h // 2))
                        act.wait_ge(o_ok, g + 1)
                        act.activation(ob[:, u, c, :], ops[:, 0:P], ACT.Copy).then_inc(ob_ok, 1)

            @block.gpsimd
            def _(pool):
                for h in range(HH):
                    u = h % 2
                    if h >= 1:
                        pool.wait_ge(s_ok, NT * h)
                        pool.wait_ge(turned, NT * h)
                        pool.wait_ge(o_ok, NT * h)
                    for n, m in enumerate(LEVELS):
                        g = h * NL + n
                        pool.wait_ge(ex_ok, g + 1)
                        pool.wait_ge(k_ok, h + 1)
                        pool.tensor_tensor(split(qk[:, n, :], m)[:, :, 0, :], split(kk[:, :], m)[:, :, 0, :],
                                           split(ex[:, g % 2, :], m)[:, :, 0, :], ALU.mult).then_inc(qk_ok, 1)
                        pool.tensor_tensor(split(qk[:, n, :], m)[:, :, 1, :], split(q[:, u, :], m)[:, :, 1, :],
                                           split(ex[:, g % 2, :], m)[:, :, 1, :], ALU.mult).then_inc(qk_ok, 1)
                    pool.wait_ge(eb_ok, h + 1)
                    pool.tensor_tensor(qb[:, :], q[:, u, :], eb[:, :], ALU.mult).then_inc(qb_ok, 1)
                    pool.wait_ge(el_ok, h + 1)
                    pool.tensor_tensor(kb[:, :], kk[:, :], el[:, :], ALU.mult).then_inc(kb_ok, 1)

            @block.vector
            def _(dve):
                dve.memset(ones[:, :], 1.0).then_inc(ones_ok, 1)
                dve.wait_ge(ones_ok, 1)
                dve.wait_ge(consts_in, 16)
                for h in range(HH):
                    u = h % 2
                    dve.wait_ge(lg_ok, h + 1)
                    dve.scalar_tensor_tensor(out=lf[:, :], in0=f[:, u, :], scalar=0.0, in1=az[:, :], op0=ALU.min,
                                             op1=ALU.subtract).then_inc(lf_ok, 1)
                    dve.wait_ge(lf_ok, h + 1)
                    if h >= 1:
                        dve.wait_ge(eb_ok, h)
                    for c in range(NT):
                        dve.tensor_tensor_scan(b[:, c * P:(c + 1) * P], ones[:, :], lf[:, c * P:(c + 1) * P], 0.0,
                                               ALU.mult, ALU.add).then_inc(b_ok, 1)
                    dve.wait_ge(b_ok, NT * (h + 1))
                    for n, m in enumerate(LEVELS):
                        g = h * NL + n
                        if g >= 2:
                            dve.wait_ge(ex_ok, g - 1)
                        bv, dv = split(b[:, :], m), split(df[:, g % 2, :], m)
                        mid = bv[:, :, 0, m - 1:m].to_broadcast([P, S // (2 * m), m])
                        dve.tensor_tensor(dv[:, :, 0, :], mid, bv[:, :, 0, :], ALU.subtract).then_inc(df_ok, 1)
                        dve.tensor_tensor(dv[:, :, 1, :], bv[:, :, 1, :], mid, ALU.subtract).then_inc(df_ok, 1)
                    bc = b[:, :].rearrange("p (n m) -> p n m", m=P)
                    if h >= 1:
                        dve.wait_ge(el_ok, h)
                    dve.tensor_tensor(dl[:, :].rearrange("p (n m) -> p n m", m=P), bc[:, :, P - 1:P].to_broadcast([P, NT, P]), bc,
                                      ALU.subtract).then_inc(dl_ok, 1)
                    if h >= 1:
                        dve.wait_ge(o_ok, NT * h)
                    dve.memset(state[:, 0, :], 0.0).then_inc(state0, 1)
                    for c in range(NT):
                        g = h * NT + c
                        dve.wait_ge(s_ok, g + 1)
                        dve.tensor_tensor(ms[:, g % 2, :, :].rearrange("p l n -> p (l n)"), sps[g % 2][:, :],
                                          mask[:, :, :].rearrange("p l n -> p (l n)"), ALU.mult).then_inc(ms_ok, 1)
                        dve.wait_ge(ms_ok, g + 1)
                        if g >= 2:
                            dve.wait_ge(o_ok, g - 1)
                        dve.reduce_sum(sT[:, g % 2, :], ms[:, g % 2, :, :].rearrange("p l n -> p n l"), AX.X).then_inc(sT_ok, 1)
                        dve.wait_ge(kv_ok, g + 1)
                        if c == 0:
                            dve.wait_ge(state0, h + 1)
                        else:
                            dve.wait_ge(state_ok, g)
                            dve.wait_ge(o_ok, g)
                        dve.wait_ge(eb_ok, h + 1)
                        dve.scalar_tensor_tensor(out=state[:, (c + 1) % 2, :], in0=state[:, c % 2, :],
                                                 scalar=eb[:, c * P + P - 1:c * P + P], in1=kvs[:, 0:P],
                                                 op0=ALU.mult, op1=ALU.add).then_inc(state_ok, 1)

            @block.tensor
            def _(pe):
                for h in range(HH):
                    u = h % 2
                    pe.wait_ge(qk_ok, 2 * NL * (h + 1))
                    pe.wait_ge(kb_ok, h + 1)
                    pe.wait_ge(qb_ok, h + 1)
                    for c in range(NT):
                        g = h * NT + c
                        cc = slice(c * P, (c + 1) * P)
                        if g >= 2:
                            pe.wait_ge(ms_ok, g - 1)
                        for n in range(NL):
                            pe.matmul(sps[g % 2][:, n * P:(n + 1) * P], qk[:, n, cc], qk[:, n, cc], start=True, stop=True)
                        pe.matmul(sps[g % 2][:, NL * P:(NL + 1) * P], kk[:, cc], q[:, u, cc], start=True, stop=True).then_inc(s_ok, 1)
                        if g >= 1:
                            pe.wait_ge(kr_ok, g)
                        pe.transpose(tps[:, 0:P], kb[:, cc], ident[:, :]).then_inc(turned, 1)
                        pe.wait_ge(kr_ok, g + 1)
                        if g >= 1:
                            pe.wait_ge(state_ok, g)
                        pe.matmul(kvs[:, 0:P], kr[:, g % 2, :], vv[:, u, c, :], start=True, stop=True).then_inc(kv_ok, 1)
                        pe.wait_ge(sT_ok, g + 1)
                        if c == 0:
                            pe.wait_ge(state0, h + 1)
                        if g >= 1:
                            pe.wait_ge(ob_ok, g)
                        pe.matmul(ops[:, 0:P], sT[:, g % 2, :], vv[:, u, c, :], start=True, stop=False)
                        pe.matmul(ops[:, 0:P], qb[:, cc], state[:, c % 2, :], start=False, stop=True).then_inc(o_ok, 1)



def rg_lru(nc, xT_in, A, hT):
    NTI = 4
    with stage(nc) as st:
        x = st.sb("lr_x", [P, 2, S + 4])
        gt = st.sb("lr_gt", [P, 2, S])
        cva, cvb = st.sb("lr_cva", [P, 2, S]), st.sb("lr_cvb", [P, 2, S])
        wa, wx = st.sb("lr_wa", [P, NTI, P]), st.sb("lr_wx", [P, NTI, P])
        cw, cb = st.sb("lr_cw", [P, NTI, 4]), st.sb("lr_cb", [P, NTI])
        ba, bx, lam = st.sb("lr_ba", [P, NTI]), st.sb("lr_bx", [P, NTI]), st.sb("lr_lam", [P, NTI])
        sm = [st.sb(f"lr_sm{i}", [P, NTI]) for i in range(12)]
        r, ig, y, a, th, a2, m2, mu, u1, u2, hs, sg, gs, hg = (
            st.sb("lr_" + n, [P, S]) for n in ("r", "ig", "y", "a", "th", "a2", "m2", "mu", "u1", "u2", "hs", "sg", "gs", "hg"))
        pa, px = st.ps("lr_pa", [P, S]), st.ps("lr_px", [P, S])
        consts_in, cleared, e_ok, c8_ok, d, conv, mm, r_ok, ig_ok, y_ok, a_ok, th_ok, m2_ok, mu_ok, sg_ok, h_ok, lam_ok, pads = (
            st.sem("lr_" + n) for n in ("consts", "cleared", "e_ok", "c8_ok", "step", "conv", "mm", "r_ok", "ig_ok", "y_ok", "a_ok",
                                        "th_ok", "m2_ok", "mu_ok", "sg_ok", "h_ok", "lam_ok", "pads"))
        wab_in = st.sem("lr_wab_in")
        hg_ok, hi_ok, lo_ok = (st.sem("lr_" + n) for n in ("hg_ok", "hi_ok", "lo_ok"))
        x_in = [st.sem(f"lr_x_in{u}") for u in range(2)]
        with nc.Block() as block:
            @block.sync
            def _(sp):
                slow = dict(allow_slow_non_contiguous=True)
                for j in range(4):
                    sp.dma_start(cw[:, :, j], A["conv_w_2"][0, j, :].rearrange("(t p) -> p t", p=P), **slow).then_inc(consts_in, 16)
                for dst, name in ((cb, "conv_b_2"), (ba, "lru_b_a_2"), (bx, "lru_b_x_2"), (lam, "lru_lambda_2")):
                    sp.dma_start(dst[:, :], A[name][0].rearrange("(t p) -> p t", p=P), **slow).then_inc(consts_in, 16)
                sp.wait_ge(cleared, 2)
                for dst, name in ((wa, "lru_w_a_2"), (wx, "lru_w_x_2")):
                    for b in range(2):
                        sp.dma_start(dst[64 * b:64 * b + 64, :, 64 * b:64 * b + 64],
                                     A[name][0].rearrange("(t b) i j -> b i t j", b=2)[b]).then_inc(wab_in, 16)
                sp.wait_ge(pads, 1)
                for t in range(NTI):
                    if t >= 2:
                        sp.wait_ge(h_ok, t - 1)
                    sp.dma_start(x[:, t % 2, 4:S + 4], xT_in[t * P:(t + 1) * P, :]).then_inc(x_in[t % 2], 16)
                    sp.dma_start(gt[:, t % 2, :], xT_in[512 + t * P:512 + (t + 1) * P, :]).then_inc(x_in[t % 2], 16)

            @block.gpsimd
            def _(pool):
                pool.memset(wa[:, :, :], 0.0).then_inc(cleared, 1)
                pool.memset(wx[:, :, :], 0.0).then_inc(cleared, 1)
                for t in range(NTI):
                    u = t % 2
                    pool.wait_ge(sg_ok, t + 1)
                    if t >= 1:
                        pool.wait_ge(h_ok, t)
                    pool.tensor_tensor(gs[:, :], gt[:, u, :], sg[:, :], ALU.mult).then_inc(lam_ok, 1)
                    pool.wait_ge(hg_ok, t + 1)
                    pool.tensor_copy(hT[:, HI, 4 + t, :], hg[:, :]).then_inc(hi_ok, 1)
                    pool.wait_ge(hi_ok, t + 1)
                    pool.tensor_tensor(hT[:, LO, 4 + t, :], hg[:, :], hT[:, HI, 4 + t, :].bitcast(F32), ALU.subtract).then_inc(lo_ok, 1)

            @block.tensor
            def _(pe):
                pe.wait_ge(wab_in, 16 * 4)
                for t in range(NTI):
                    pe.wait_ge(conv, 4 * (t + 1))
                    if t >= 1:
                        pe.wait_ge(ig_ok, t)
                        pe.wait_ge(r_ok, t)
                    for dst, w in ((pa, wa), (px, wx)):
                        for n in range(2):
                            m = pe.matmul(dst[:, n * BANK:(n + 1) * BANK], w[:, t, :], cvb[:, t % 2, n * BANK:(n + 1) * BANK],
                                          start=True, stop=True)
                    m.then_inc(mm, 1)

            @block.scalar
            def _(act):
                act.wait_ge(e_ok, 1)
                act.activation(sm[1][:, :], sm[0][:, :], ACT.Exp, scale=-1.0).then_inc(e_ok, 1)
                act.wait_ge(consts_in, 16 * 8)
                for t in range(NTI):
                    u = t % 2
                    act.wait_ge(x_in[u], 32 * (t // 2 + 1))
                    if t >= 1:
                        act.wait_ge(lam_ok, t)
                        act.wait_ge(h_ok, t)
                    act.activation(sg[:, :], gt[:, u, :], ACT.Sigmoid).then_inc(sg_ok, 1)
                    act.wait_ge(mm, t + 1)
                    act.activation(r[:, :], pa[:, :], ACT.Sigmoid, bias=ba[:, t:t + 1]).then_inc(r_ok, 1)
                    act.activation(ig[:, :], px[:, :], ACT.Sigmoid, bias=bx[:, t:t + 1]).then_inc(ig_ok, 1)
                    act.wait_ge(y_ok, t + 1)
                    act.activation(a[:, :], y[:, :], ACT.Exp, scale=-1.0).then_inc(a_ok, 1)
                    act.activation(th[:, :], y[:, :], ACT.Tanh).then_inc(th_ok, 1)
                    act.wait_ge(m2_ok, t + 1)
                    act.activation(mu[:, :], m2[:, :], ACT.Sqrt).then_inc(mu_ok, 1)

            @block.vector
            def _(dve):
                n = [0]

                def step(ins):
                    n[0] += 1
                    ins.then_inc(d, 1)
                    dve.wait_ge(d, n[0])

                dve.memset(x[:, :, 0:4], 0.0).then_inc(pads, 1)
                dve.wait_ge(consts_in, 16 * 8)
                step(dve.scalar_tensor_tensor(out=sm[0][:, :], in0=lam[:, :], scalar=-1.0, in1=lam[:, :], op0=ALU.mult, op1=ALU.max))
                dve.sem_inc(e_ok, 1)
                dve.wait_ge(e_ok, 2)
                step(dve.tensor_scalar(sm[2][:, :], sm[1][:, :], 2.0, None, ALU.add))
                step(dve.reciprocal(sm[3][:, :], sm[2][:, :]))
                step(dve.tensor_tensor(sm[4][:, :], sm[1][:, :], sm[3][:, :], ALU.mult))
                step(dve.tensor_tensor(sm[5][:, :], sm[4][:, :], sm[4][:, :], ALU.mult))
                step(dve.tensor_scalar(sm[6][:, :], sm[5][:, :], 1.0 / 17, 1.0 / 15, ALU.mult, ALU.add))
                for k in (13, 11, 9, 7, 5, 3, 1):
                    step(dve.tensor_tensor(sm[7][:, :], sm[6][:, :], sm[5][:, :], ALU.mult))
                    step(dve.tensor_scalar(sm[6][:, :], sm[7][:, :], 1.0 / k, None, ALU.add))
                step(dve.tensor_tensor(sm[8][:, :], sm[6][:, :], sm[4][:, :], ALU.mult))
                step(dve.tensor_scalar(sm[9][:, :], lam[:, :], -1.0, 0.0, ALU.mult, ALU.max))
                step(dve.scalar_tensor_tensor(out=sm[10][:, :], in0=sm[8][:, :], scalar=2.0, in1=sm[9][:, :], op0=ALU.mult, op1=ALU.add))
                step(dve.tensor_scalar(sm[11][:, :], sm[10][:, :], 8.0, None, ALU.mult))
                for t in range(NTI):
                    u = t % 2
                    dve.wait_ge(x_in[u], 32 * (t // 2 + 1))
                    if t == 0:
                        dve.wait_ge(pads, 1)
                    src = [x[:, u, 1 + j:1 + j + S] for j in range(4)]
                    if t >= 2:
                        dve.wait_ge(mm, t - 1)
                    dve.tensor_scalar(cva[:, u, :], src[0], cw[:, t, 0:1], cb[:, t:t + 1], ALU.mult, ALU.add).then_inc(conv, 1)
                    for j, (o, i) in enumerate(((cvb, cva), (cva, cvb), (cvb, cva)), 1):
                        dve.wait_ge(conv, 4 * t + j)
                        dve.scalar_tensor_tensor(out=o[:, u, :], in0=src[j], scalar=cw[:, t, j:j + 1], in1=i[:, u, :],
                                                 op0=ALU.mult, op1=ALU.add).then_inc(conv, 1)
                    xc = cvb[:, u, :]
                    dve.wait_ge(r_ok, t + 1)
                    step(dve.tensor_scalar(y[:, :], r[:, :], sm[11][:, t:t + 1], None, ALU.mult))
                    dve.sem_inc(y_ok, 1)
                    dve.wait_ge(ig_ok, t + 1)
                    dve.wait_ge(conv, 4 * t + 4)
                    step(dve.tensor_tensor(u1[:, :], ig[:, :], xc, ALU.mult))
                    dve.wait_ge(a_ok, t + 1)
                    step(dve.tensor_tensor(a2[:, :], a[:, :], a[:, :], ALU.mult))
                    dve.wait_ge(th_ok, t + 1)
                    dve.scalar_tensor_tensor(out=m2[:, :], in0=a2[:, :], scalar=1.0, in1=th[:, :], op0=ALU.add,
                                             op1=ALU.mult).then_inc(m2_ok, 1)
                    dve.wait_ge(mu_ok, t + 1)
                    step(dve.memset(mu[:, 0:1], 1.0))
                    step(dve.tensor_tensor(u2[:, :], mu[:, :], u1[:, :], ALU.mult))
                    step(dve.tensor_tensor_scan(hs[:, :], a[:, :], u2[:, :], 0.0, ALU.mult, ALU.add))
                    dve.wait_ge(lam_ok, t + 1)
                    if t >= 1:
                        dve.wait_ge(lo_ok, t)
                    dve.tensor_tensor(hg[:, :], hs[:, :], gs[:, :], ALU.mult).then_inc(hg_ok, 1)
                    dve.sem_inc(h_ok, 1)


def second(nc, A, C, scr, ident, hT, out):
    we = A["even_w_in_2"][0]
    row_chunk = lambda w, c, dst, c0: dict(kind="row", width=512, load=columns(w, c, 512), dst=to_rows(dst, c0, 512))
    T_chunk = lambda w, c, dst, r0: dict(kind="T", width=512, load=columns(w, c, 512), dst=to_T(dst, r0, 512))
    project(nc, "pe", hT, 8, [row_chunk(we, c, scr["erows"], c) for c in (0, 512, 1024)] +
            [T_chunk(we, 1536 + c, scr["sqkT"], c) for c in (0, 512)] +
            [row_chunk(we, 2560 + c, scr["srows"], c) for c in (0, 512)], gain=[(0, A["pre_norm_w_2"][0])])
    retention(nc, ident, scr["erows"], C, scr["ret"])
    stick_breaking(nc, ident, 8, scr["sqkT"], scr["srows"], C, scr["stick"])
    mix_out(nc, "em", ident, hT, A["even_w_out_2"][0], None,
            dict(width=D, loads=[(0, 512, lambda t: rows(scr["ret"], t)), (512, 512, lambda t: rows(scr["stick"], t))],
                 groups=[(128 * h, 128) for h in range(4)], hT=hT,
                 gate=[(0, 512, lambda t: rows(scr["erows"][:, 1024:1536], t)), (512, 512, lambda t: rows(scr["srows"][:, 512:1024], t))]),
            dict(width=D, loads=[(0, D, lambda t: rows(scr["x2"], t))], groups=[(0, D)], hT=hT, post=A["post_norm_w_2"][0],
                 keep=scr["x3"]))
    wo = A["odd_w_in_2"][0]
    project(nc, "pg", hT, 8, [T_chunk(wo, c, scr["oT"], c) for c in (0, 512)] +
            [row_chunk(wo, 1024 + c, scr["orows"], c) for c in (0, 512)] +
            [T_chunk(wo, 2048 + c, scr["oT"], 1024 + c) for c in (0, 512)], gain=[(0, A["pre_norm_w_2"][1])])
    hgrn2(nc, ident, scr["oT"], scr["orows"], C, scr["hc"])
    rg_lru(nc, scr["oT"][1024:2048, :], A, hT)
    mix_out(nc, "om", ident, hT, A["odd_w_out_2"][0], None,
            dict(width=512, loads=[(0, 512, lambda t: rows(scr["hc"], t))], groups=[(128 * h, 128) for h in range(4)], hT=hT,
                 gate=[(0, 512, lambda t: rows(scr["orows"][:, 512:1024], t))]),
            dict(width=D, loads=[(0, D, lambda t: rows(scr["x3"], t))], groups=[], post=A["post_norm_w_2"][1], keep=out))


SCRATCH.update(erows=(S, 1536), sqkT=(1024, S), srows=(S, 1024), ret=(S, 512), stick=(S, 512), x3=(S, D),
               oT=(2048, S), orows=(S, 1024), hc=(S, 512))


def build(nc, A, C, out):
    scr = {n: nc.dram_tensor("scr_" + n, s, F32, kind="Internal").ap() for n, s in SCRATCH.items()}
    with ExitStack() as ctx:
        ident = ctx.enter_context(nc.sbuf_tensor("ident", [P, P], F32))
        hT = ctx.enter_context(nc.sbuf_tensor("hT", [P, 2, 8, S], F32R))
        identity(nc, ident)
        first_attention(nc, A, C, scr, ident, hT)
        moe(nc, A, C, scr, ident, hT)
        second(nc, A, C, scr, ident, hT, out.rearrange("b s d -> (b s) d"))


def kernel(**inputs):
    import concourse.bacc as _bacc
    from concourse.bass_utils import run_bass_kernel_spmd as _run
    nc = _bacc.Bacc("TRN2", target_bir_lowering=False, num_devices=1)
    arrays, A, C = {}, {}, {}
    for name, v in inputs.items():
        if name == "hgrn_lb_logits_2":
            continue
        v = np.ascontiguousarray(v)
        arrays["in_" + name] = v
        A[name] = nc.dram_tensor("in_" + name, v.shape, F32, kind="ExternalInput").ap()
    for name, v in constants().items():
        arrays["const_" + name] = v
        C[name] = nc.dram_tensor("const_" + name, v.shape, F32, kind="ExternalInput").ap()
    out = nc.dram_tensor("out", (1, S, D), F32, kind="ExternalOutput").ap()
    build(nc, A, C, out)
    r = _run(nc, [arrays], core_ids=[0])
    return r.results[0]["out"]
```

```python
import math
from contextlib import ExitStack, contextmanager

import numpy as np
import concourse.bass as bass
from concourse import mybir

F32 = mybir.dt.float32
F32R = mybir.dt.float32r
U32 = mybir.dt.uint32
ALU = mybir.AluOpType
ACT = mybir.ActivationFunctionType
AX = mybir.AxisListType

P = 128
D = 1024
S = 1024
NT = S // P
BANK = 512
EPS = 1e-6
NEG = -1e30


class Stage:

    def __init__(self, nc):
        self.nc, self.ctx, self.sems = nc, ExitStack(), []

    def sb(self, name, shape, dt=F32):
        return self.ctx.enter_context(self.nc.sbuf_tensor(name, shape, dt))

    def ps(self, name, shape, dt=F32):
        return self.ctx.enter_context(self.nc.psum_tensor(name, shape, dt))

    def sem(self, name):
        s = self.nc.alloc_semaphore(name)
        self.sems.append(s)
        return s


@contextmanager
def stage(nc):
    st = Stage(nc)
    yield st
    nc.clear_and_free_semaphores(st.sems)
    nc.all_engine_barrier()
    st.ctx.close()


def tiled(ap):
    return ap.rearrange("(k p) n -> p k n", p=P)


def rows(ap, t):
    return ap[bass.ds(t * P, P), :]


def along(eng, count, step, body):
    if count == step:
        for i in range(count):
            body(i, i)
        return
    with eng.Fori(0, count // step) as r:
        for u in range(step):
            body(r * step + u, u)



HI, LO = 0, 1
PARTS = ((HI, HI), (HI, LO), (LO, HI))


def product(pe, out, n, a, b, before=None):
    for k in range(n):
        if before:
            before(k)
        for i, (p, q) in enumerate(PARTS):
            mm = pe.matmul(out, a(p, k), b(q, k), start=(k == 0 and i == 0), stop=(k == n - 1 and i == 2))
    return mm


def project(nc, name, hT, nk, chunks, gain=None):
    N = len(chunks)

    def groups(ch):
        return NT if ch["kind"] == "row" else 2 * max(1, ch["width"] // P)

    def size(ch):
        return (P, ch["width"]) if ch["kind"] == "row" else (min(P, ch["width"]), BANK)

    uses = [[sum(groups(c) > j for c in chunks[:g]) for j in range(groups(ch))] for g, ch in enumerate(chunks)]
    loads = [len(ch["load"]) for ch in chunks]
    by_k = loads[0] == 1 and nk == 8
    if by_k:
        loads[0] = 0
    nst = [[16 * uses[g][j] for j in range(groups(ch))] for g, ch in enumerate(chunks)]

    with stage(nc) as st:
        raw = st.sb(name + "_raw", [P, 2, nk, BANK])
        w = st.sb(name + "_w", [P, 2, 2, nk, BANK], F32R)
        obuf = st.sb(name + "_o", [P, NT, BANK])
        gcol = st.sb(name + "_g", [P, nk]) if gain is not None else None
        acc = [st.ps(f"{name}_acc{j}", [P, BANK]) for j in range(NT)]
        gain_in = st.sem(name + "_gain_in")
        raw_in = [st.sem(f"{name}_raw_in{s}") for s in range(2)]
        k_in = [st.sem(f"{name}_k_in{k}") for k in range(nk)] if by_k else None
        hi_ok, lo_ok = st.sem(name + "_hi_ok"), st.sem(name + "_lo_ok")
        mm_done = [st.sem(f"{name}_mm{j}") for j in range(NT)]
        copied = [st.sem(f"{name}_copied{j}") for j in range(NT)]
        stored = [st.sem(f"{name}_stored{j}") for j in range(NT)]

        with nc.Block() as block:
            @block.sync
            def _(sp):
                if gain is not None:
                    for k0, v in gain:
                        sp.dma_start(gcol[:, k0:k0 + v.shape[0] // P], v.rearrange("(k p) -> p k", p=P),
                                     allow_slow_non_contiguous=True).then_inc(gain_in, 16)
                for g, ch in enumerate(chunks):
                    if g >= 2:
                        sp.wait_ge(lo_ok, nk * (g - 1))
                    if g == 0 and by_k:
                        (dst, src), = ch["load"]
                        for k in range(nk):
                            sp.dma_start(raw[:, 0, k, dst], src[:, k, :]).then_inc(k_in[k], 16)
                        continue
                    for dst, src in ch["load"]:
                        sp.dma_start(raw[:, g % 2, :, dst], src).then_inc(raw_in[g % 2], 16)

            @block.tensor
            def _(pe):
                for g, ch in enumerate(chunks):
                    m, n = size(ch)
                    s = g % 2
                    if g > 0:
                        pe.wait_ge(lo_ok, nk * (g + 1))
                    for j in range(groups(ch)):
                        if uses[g][j]:
                            pe.wait_ge(copied[j], uses[g][j])
                        before = (lambda k: pe.wait_ge(lo_ok, k + 1)) if g == 0 and j == 0 else None
                        if ch["kind"] == "row":
                            mm = product(pe, acc[j][0:m, 0:n], nk, lambda p, k: hT[:, p, k, j * P:(j + 1) * P],
                                         lambda q, k: w[:, s, q, k, 0:n], before)
                        else:
                            c0 = (j // 2) * P
                            mm = product(pe, acc[j][0:m, 0:n], nk, lambda p, k: w[:, s, p, k, c0:c0 + m],
                                         lambda q, k: hT[:, q, k, (j % 2) * BANK:(j % 2 + 1) * BANK], before)
                        mm.then_inc(mm_done[j], 1)

            def split_hi(act, g):
                n = chunks[g]["width"]
                if loads[g]:
                    act.wait_ge(raw_in[g % 2], 16 * sum(loads[g % 2:g + 1:2]))
                if g >= 2:
                    last = groups(chunks[g - 2]) - 1
                    act.wait_ge(mm_done[last], uses[g - 2][last] + 1)
                for k in range(nk):
                    if not loads[g]:
                        act.wait_ge(k_in[k], 16)
                    act.activation(w[:, g % 2, HI, k, 0:n], raw[:, g % 2, k, 0:n], ACT.Copy,
                                   scale=1.0 if gain is None else gcol[:, k:k + 1]).then_inc(hi_ok, 1)

            def split_lo(dve, g):
                n = chunks[g]["width"]
                if loads[g]:
                    dve.wait_ge(raw_in[g % 2], 16 * sum(loads[g % 2:g + 1:2]))
                for k in range(nk):
                    if not loads[g]:
                        dve.wait_ge(k_in[k], 16)
                    dve.wait_ge(hi_ok, nk * g + k + 1)
                    dve.scalar_tensor_tensor(out=w[:, g % 2, LO, k, 0:n], in0=raw[:, g % 2, k, 0:n],
                                             scalar=1.0 if gain is None else gcol[:, k:k + 1],
                                             in1=w[:, g % 2, HI, k, 0:n].bitcast(F32), op0=ALU.mult,
                                             op1=ALU.subtract).then_inc(lo_ok, 1)

            @block.scalar
            def _(act):
                if gain is not None:
                    act.wait_ge(gain_in, 16 * len(gain))
                split_hi(act, 0)
                for g, ch in enumerate(chunks):
                    m, n = size(ch)
                    if g + 1 < N:
                        split_hi(act, g + 1)
                    for j in range(groups(ch)):
                        dst = ch["dst"]
                        if j % 2 == 0:
                            act.wait_ge(mm_done[j], uses[g][j] + 1)
                            if nst[g][j]:
                                act.wait_ge(stored[j], nst[g][j])
                            act.activation(obuf[0:m, j, 0:n], acc[j][0:m, 0:n], ACT.Copy).then_inc(copied[j], 1)
                        act.wait_ge(copied[j], uses[g][j] + 1)
                        act.dma_start(dst(j), obuf[0:m, j, 0:n]).then_inc(stored[j], 16)
                for j in range(NT):
                    total = 16 * sum(groups(c) > j for c in chunks)
                    if total:
                        act.wait_ge(stored[j], total)

            @block.vector
            def _(dve):
                if gain is not None:
                    dve.wait_ge(gain_in, 16 * len(gain))
                split_lo(dve, 0)
                for g, ch in enumerate(chunks):
                    m, n = size(ch)
                    if g + 1 < N:
                        split_lo(dve, g + 1)
                    for j in range(groups(ch)):
                        if j % 2 == 1:
                            dve.wait_ge(mm_done[j], uses[g][j] + 1)
                            if nst[g][j]:
                                dve.wait_ge(stored[j], nst[g][j])
                            dve.tensor_copy(obuf[0:m, j, 0:n], acc[j][0:m, 0:n]).then_inc(copied[j], 1)


def columns(w, c0, width):
    return [(slice(0, width), tiled(w)[:, :, c0:c0 + width])]


def to_rows(dst, c0, width):
    return lambda j: dst[j * P:(j + 1) * P, c0:c0 + width]


def to_T(dst, r0, width):
    m = min(P, width)

    return lambda j: dst[r0 + (j // 2) * P:r0 + (j // 2) * P + m, (j % 2) * BANK:(j % 2 + 1) * BANK]



class Rows:

    def __init__(self, nc, st, name, ident, width, loads, groups, hT=None, y_psum=None, post=None,
                 gate=None, expert_rows=None, keep=None, keep_normed=None, ns=2):
        self.ident, self.width, self.loads, self.groups, self.hT, self.ns = ident, width, loads, groups, hT, ns
        self.y_psum, self.post, self.gate, self.expert_rows = y_psum, post, gate, expert_rows
        self.keep, self.keep_normed = keep, keep_normed
        self.nk, self.ng = width // P, len(groups)
        self.nl = len(loads) + len(gate or [])
        self.has_y = y_psum is not None or expert_rows is not None
        sb = lambda n, shape=(P, ns, width), dt=F32: st.sb(name + n, list(shape), dt)
        self.x = sb("_x")
        self.junk = sb("_junk", (P, width))
        self.y = sb("_y") if expert_rows else None
        self.e = [sb(f"_e{c}", (P, 2, width)) for c in range(2)] if expert_rows else None
        self.xe = sb("_xe", (P, width)) if expert_rows else None
        self.xs = sb("_xs") if self.has_y else self.x
        self.z = sb("_z", (P, 1 if gate else 2, width)) if self.ng else None
        self.gt = sb("_gt") if gate else None
        self.sg = sb("_sg", (P, width)) if gate else None
        self.zg = sb("_zg", (P, 2, width)) if gate else self.z
        self.ss, self.ms, self.rs = (sb(n, (P, ns, 8)) for n in ("_ss", "_ms", "_rs"))
        self.half = sb("_half", (P, 1))
        self.prow = sb("_prow", (P, width)) if post is not None else None
        self.tp = st.ps(name + "_tp", [P, width]) if hT is not None else None
        sem = lambda n: st.sem(name + n)
        self.post_in, self.half_ok = sem("_post_in"), sem("_half_ok")
        self.tile_in = [sem(f"_tile_in{u}") for u in range(ns)]
        self.rows_in = [sem(f"_rows_in{u}") for u in range(2)] if expert_rows else None
        self.summed1, self.summed, self.x_ok, self.y_sq, self.y_ms, self.y_rs, self.yn_ok = (
            sem(n) for n in ("_summed1", "_summed", "_x_ok", "_y_sq", "_y_ms", "_y_rs", "_yn_ok"))
        self.sq, self.ms_ok, self.rs_ok, self.z_ok, self.sig, self.silu, self.zg_ok = (
            sem(n) for n in ("_sq", "_ms_ok", "_rs_ok", "_z_ok", "_sig", "_silu", "_zg_ok"))
        self.turned, self.hi_ok, self.lo_ok = sem("_turned"), sem("_hi_ok"), sem("_lo_ok")
        self.kept = [sem(f"_kept{u}") for u in range(ns)]
        self.kept_z = [sem(f"_kept_z{u}") for u in range(2)]
        end = max([c0 + w for c0, w in groups], default=0)
        self.rest = (end, width) if self.ng and end < width else None
        self.nz = self.ng + (self.rest is not None)

    def loaded(self, eng, t):
        if self.nl:
            eng.wait_ge(self.tile_in[t % self.ns], 16 * self.nl * (t // self.ns + 1))

    def x_done(self, eng, t):
        if self.xs is not self.x:
            eng.wait_ge(self.x_ok, t + 1)
        else:
            self.loaded(eng, t)

    def z_done(self, eng, t):
        if self.gate:
            eng.wait_ge(self.zg_ok, t + 1)
        else:
            eng.wait_ge(self.z_ok, self.nz * (t + 1))

    def load(self, sp, t):
        u = t % self.ns
        if t == 0 and self.post is not None:
            sp.dma_start(self.prow[:, :], self.post.partition_broadcast(P)).then_inc(self.post_in, 16)
        if t >= self.ns:
            if self.expert_rows:
                sp.wait_ge(self.summed, t - self.ns + 1)
            elif self.xs is not self.x:
                sp.wait_ge(self.x_ok, t - self.ns + 1)
            else:
                self.z_done(sp, t - self.ns)
        for c0, w, src in self.loads:
            sp.dma_start(self.x[:, u, c0:c0 + w], src(t)).then_inc(self.tile_in[u], 16)
        for c0, w, src in self.gate or []:
            sp.dma_start(self.gt[:, u, c0:c0 + w], src(t)).then_inc(self.tile_in[u], 16)


    def pool_gather(self, pool, t):
        slot_out, gates, slots = self.expert_rows
        if t >= 2:
            pool.wait_ge(self.summed, t - 1)
        for c in range(2):
            pool.indirect_dma_start(self.e[c][:, t % 2, :], None, slot_out,
                                    bass.IndirectOffsetOnAxis(ap=slots[:, t, c:c + 1], axis=0)).then_inc(self.rows_in[t % 2], 16)

    def pool_begin(self, pool):
        pool.memset(self.half[:, :], -0.5).then_inc(self.half_ok, 1)
        pool.wait_ge(self.half_ok, 1)

    def pool_y(self, pool, t):
        u = t % self.ns
        if self.post is not None:
            pool.wait_ge(self.y_sq, t + 1)
            pool.tensor_scalar(self.ms[:, u, 7:8], self.ss[:, u, 7:8], 1.0 / self.width, EPS, ALU.mult, ALU.add).then_inc(self.y_ms, 1)
            pool.wait_ge(self.y_ms, t + 1)
            pool.tensor_tensor(self.rs[:, u, 7:8], self.ms[:, u, 7:8], self.half[:, :], ALU.pow).then_inc(self.y_rs, 1)

    def pool_x(self, pool, t):
        u = t % self.ns
        if self.ng:
            pool.wait_ge(self.sq, self.ng * (t + 1))
            for n, (c0, w) in enumerate(self.groups):
                pool.tensor_scalar(self.ms[:, u, n:n + 1], self.ss[:, u, n:n + 1], 1.0 / w, EPS, ALU.mult,
                                   ALU.add).then_inc(self.ms_ok, 1)
            pool.wait_ge(self.ms_ok, self.ng * (t + 1))
            if t >= self.ns:
                pool.wait_ge(self.z_ok, self.nz * (t - self.ns + 1))
            pool.tensor_tensor(self.rs[:, u, 0:self.ng], self.ms[:, u, 0:self.ng], self.half[:, :].to_broadcast([P, self.ng]),
                               ALU.pow).then_inc(self.rs_ok, 1)


    def act_y(self, act, t):
        if self.post is not None:
            if self.y_psum is not None:
                src, done, _ = self.y_psum
                act.wait_ge(done, t + 1)
                src = src(t)
            else:
                act.wait_ge(self.summed, t + 1)
                src = self.y[:, t % self.ns, :]
            if t >= 1:
                act.wait_ge(self.sq if self.ng else self.y_sq, max(1, self.ng) * t)
            act.activation(self.junk[:, :], src, ACT.Square, accum_out=self.ss[:, t % self.ns, 7:8]).then_inc(self.y_sq, 1)

    def act_x(self, act, t):
        u = t % self.ns
        if self.gate:
            self.loaded(act, t)
            if t >= 1:
                act.wait_ge(self.zg_ok, t)
            act.activation(self.sg[:, :], self.gt[:, u, :], ACT.Sigmoid).then_inc(self.sig, 1)
        if self.ng or self.keep is not None:
            self.x_done(act, t)
        if self.keep is not None:
            act.dma_start(rows(self.keep, t), self.xs[:, u, :]).then_inc(self.kept[u], 16)
        if self.ng and self.post is not None:
            act.wait_ge(self.y_sq, t + 1)
        elif self.ng and t >= 1:
            act.wait_ge(self.sq, self.ng * t)
        for n, (c0, w) in enumerate(self.groups):
            act.activation(self.junk[:, c0:c0 + w], self.xs[:, u, c0:c0 + w], ACT.Square,
                           accum_out=self.ss[:, u, n:n + 1]).then_inc(self.sq, 1)

    def act_turn(self, act, t):
        if self.keep_normed is not None:
            self.z_done(act, t)
            act.dma_start(rows(self.keep_normed, t), self.zg[:, t % 2, :]).then_inc(self.kept_z[t % 2], 16)
        if self.hT is not None:
            act.wait_ge(self.turned, t + 1)
            act.activation(self.hT[:, HI, 0:self.nk, t * P:(t + 1) * P], self.tp[:, :].rearrange("p (k n) -> p k n", n=P),
                           ACT.Copy).then_inc(self.hi_ok, 1)

    def act_end(self, act):
        for u in range(self.ns):
            if self.keep is not None:
                act.wait_ge(self.kept[u], 16 * NT // self.ns)
        for u in range(2):
            if self.keep_normed is not None:
                act.wait_ge(self.kept_z[u], 16 * NT // 2)


    def dve_y(self, dve, t):
        if self.expert_rows:
            u = t % self.ns
            _, gates, _ = self.expert_rows
            self.loaded(dve, t)
            dve.wait_ge(self.rows_in[t % 2], 32 * (t // 2 + 1))
            dve.scalar_tensor_tensor(out=self.xe[:, :], in0=self.e[0][:, t % 2, :], scalar=gates[:, t, 0:1], in1=self.x[:, u, :],
                                     op0=ALU.mult, op1=ALU.add).then_inc(self.summed1, 1)
            dve.wait_ge(self.summed1, t + 1)
            dve.scalar_tensor_tensor(out=self.y[:, u, :], in0=self.e[1][:, t % 2, :], scalar=gates[:, t, 1:2], in1=self.xe[:, :],
                                     op0=ALU.mult, op1=ALU.add).then_inc(self.summed, 1)

    def dve_x(self, dve, t):
        if not self.has_y:
            return
        u = t % self.ns
        if t == 0 and self.post is not None:
            dve.wait_ge(self.post_in, 16)
        self.loaded(dve, t)
        if self.keep is not None and t >= self.ns:
            dve.wait_ge(self.kept[u], 16 * (t // self.ns))
        if self.y_psum is not None:
            y, done, free = self.y_psum
            dve.wait_ge(done, t + 1)
            y = y(t)
        else:
            y, free = self.y[:, u, :], None
        if self.post is not None:
            dve.wait_ge(self.y_rs, t + 1)
            add_x = self.loads and not self.expert_rows
            ok = self.yn_ok if add_x else self.x_ok
            dve.scalar_tensor_tensor(out=self.xs[:, u, :], in0=y, scalar=self.rs[:, u, 7:8], in1=self.prow[:, :],
                                     op0=ALU.mult, op1=ALU.mult).then_inc(ok, 1)
            dve.wait_ge(ok, t + 1)
            if free is not None:
                dve.sem_inc(free, 1)
            if add_x:
                dve.tensor_tensor(self.xs[:, u, :], self.x[:, u, :], self.xs[:, u, :], ALU.add).then_inc(self.x_ok, 1)
        else:
            dve.tensor_tensor(self.xs[:, u, :], y, self.x[:, u, :], ALU.add).then_inc(self.x_ok, 1)
            if free is not None:
                dve.wait_ge(self.x_ok, t + 1)
                dve.sem_inc(free, 1)

    def dve_z(self, dve, t):
        u, zu = t % self.ns, 0 if self.gate else t % 2
        if self.gate:
            dve.wait_ge(self.sig, t + 1)
            dve.tensor_tensor(self.sg[:, :], self.sg[:, :], self.gt[:, u, :], ALU.mult).then_inc(self.silu, 1)
        if self.ng:
            dve.wait_ge(self.rs_ok, t + 1)
            self.x_done(dve, t)
            if t >= 2 and not self.gate:
                if self.hT is not None:
                    dve.wait_ge(self.turned, t - 1)
                if self.keep_normed is not None:
                    dve.wait_ge(self.kept_z[t % 2], 16 * (t // 2))
            for n, (c0, w) in enumerate(self.groups):
                dve.tensor_scalar(self.z[:, zu, c0:c0 + w], self.xs[:, u, c0:c0 + w], self.rs[:, u, n:n + 1], None,
                                  ALU.mult).then_inc(self.z_ok, 1)
            if self.rest:
                a, b = self.rest
                dve.tensor_copy(self.z[:, zu, a:b], self.xs[:, u, a:b]).then_inc(self.z_ok, 1)
        if self.gate:
            dve.wait_ge(self.z_ok, self.nz * (t + 1))
            dve.wait_ge(self.silu, t + 1)
            if t >= 2:
                dve.wait_ge(self.turned, t - 1)
            dve.tensor_tensor(self.zg[:, t % 2, :], self.z[:, 0, :], self.sg[:, :], ALU.mult).then_inc(self.zg_ok, 1)

    def dve_turn(self, dve, t):
        if self.hT is not None:
            dve.wait_ge(self.hi_ok, t + 1)
            at = (slice(0, self.nk), slice(t * P, (t + 1) * P))
            dve.tensor_tensor(self.hT[:, LO, at[0], at[1]], self.tp[:, :].rearrange("p (k n) -> p k n", n=P),
                              self.hT[:, HI, at[0], at[1]].bitcast(F32), ALU.subtract).then_inc(self.lo_ok, 1)


    def pe_turn(self, pe, t):
        if self.hT is not None:
            self.z_done(pe, t)
            if t >= 1:
                pe.wait_ge(self.lo_ok, t)
            for k in range(self.nk):
                mm = pe.transpose(self.tp[:, k * P:(k + 1) * P], self.zg[:, t % 2, k * P:(k + 1) * P], self.ident[:, :])
            mm.then_inc(self.turned, 1)


def at_step(s, *calls):
    for f, lag, eng in calls:
        if 0 <= s - lag < NT:
            f(eng, s - lag)


def norm_rows(nc, name, ident, width, loads, groups, also=None, **options):
    with stage(nc) as st:
        r = Rows(nc, st, name, ident, width, loads, groups, ns=4, **options)
        lx = 1 if r.has_y else 0
        small = also(st) if also else None
        with nc.Block() as block:
            @block.sync
            def _(sp):
                for t in range(NT):
                    r.load(sp, t)
                    if t == 1 and small:
                        small.load(sp)
                if small:
                    small.store(sp)

            @block.gpsimd
            def _(pool):
                r.pool_begin(pool)
                if r.expert_rows:
                    r.pool_gather(pool, 0)
                for s in range(NT + lx):
                    if r.expert_rows:
                        at_step(s, (r.pool_gather, -1, pool))
                    at_step(s, (r.pool_x, lx, pool), (r.pool_y, 0, pool))

            @block.scalar
            def _(act):
                for s in range(NT + lx + 2):
                    at_step(s, (r.act_turn, lx + 2, act), (r.act_x, lx, act), (r.act_y, 0, act))
                r.act_end(act)

            @block.vector
            def _(dve):
                for s in range(NT + lx + 2):
                    at_step(s, (r.dve_z, lx + 1, dve), (r.dve_turn, lx + 2, dve), (r.dve_x, lx, dve), (r.dve_y, 0, dve))
                    if s == 5 and small:
                        small.vector(dve)

            @block.tensor
            def _(pe):
                for t in range(NT):
                    r.pe_turn(pe, t)
                    if t == 2 and small:
                        small.tensor(pe)


def mix_out(nc, name, ident, hT, w_out, gain, front, back):
    with stage(nc) as st:
        raw = st.sb(name + "_raw", [P, 2, D])
        w = st.sb(name + "_w", [P, 2, 8, D], F32R)
        gcol = st.sb(name + "_g", [P, 8]) if gain is not None else None
        acc = [st.ps(f"{name}_acc{u}", [P, D]) for u in range(2)]
        gain_in, hi_ok, lo_ok, y_done, y_free = (st.sem(name + n) for n in ("_gain_in", "_whi_ok", "_wlo_ok", "_y_done", "_y_free"))
        raw_in = [st.sem(f"{name}_raw_in{u}") for u in range(2)]
        f = Rows(nc, st, name + "f", ident, **front)
        b = Rows(nc, st, name + "b", ident, y_psum=(lambda t: acc[t % 2][:, :], y_done, y_free), **back)
        wv = tiled(w_out)
        STEPS = NT + 5

        with nc.Block() as block:
            @block.sync
            def _(sp):
                f.load(sp, 0)
                f.load(sp, 1)
                if gain is not None:
                    for k0, v in gain:
                        sp.dma_start(gcol[:, k0:k0 + v.shape[0] // P], v.rearrange("(k p) -> p k", p=P),
                                     allow_slow_non_contiguous=True).then_inc(gain_in, 16)
                for k in range(8):
                    if k >= 2:
                        sp.wait_ge(lo_ok, k - 1)
                    sp.dma_start(raw[:, k % 2, :], wv[:, k, :]).then_inc(raw_in[k % 2], 16)
                b.load(sp, 0)
                b.load(sp, 1)
                for t in range(2, NT + 2):
                    if t < NT:
                        f.load(sp, t)
                    if t >= 4:
                        b.load(sp, t - 2)

            @block.gpsimd
            def _(pool):
                f.pool_begin(pool)
                b.pool_begin(pool)
                for s in range(STEPS):
                    at_step(s, (b.pool_y, 3, pool), (f.pool_x, 0, pool), (b.pool_x, 3, pool))

            def scale(k):
                return 1.0 if gain is None else gcol[:, k:k + 1]

            @block.scalar
            def _(act):
                for s in range(STEPS):
                    at_step(s, (b.act_y, 3, act), (f.act_turn, 1, act), (b.act_turn, 5, act), (f.act_x, 0, act), (b.act_x, 3, act))
                    if s == 0:
                        if gain is not None:
                            act.wait_ge(gain_in, 16 * len(gain))
                        for k in range(8):
                            act.wait_ge(raw_in[k % 2], 16 * (k // 2 + 1))
                            act.activation(w[:, HI, k, :], raw[:, k % 2, :], ACT.Copy, scale=scale(k)).then_inc(hi_ok, 1)
                b.act_end(act)

            @block.vector
            def _(dve):
                for s in range(STEPS):
                    at_step(s, (f.dve_z, 1, dve))
                    if s == 1:
                        if gain is not None:
                            dve.wait_ge(gain_in, 16 * len(gain))
                        for k in range(8):
                            dve.wait_ge(hi_ok, k + 1)
                            dve.scalar_tensor_tensor(out=w[:, LO, k, :], in0=raw[:, k % 2, :], scalar=scale(k),
                                                     in1=w[:, HI, k, :].bitcast(F32), op0=ALU.mult, op1=ALU.subtract).then_inc(lo_ok, 1)
                    at_step(s, (b.dve_z, 4, dve), (b.dve_x, 3, dve), (f.dve_turn, 1, dve), (b.dve_turn, 5, dve))

            @block.tensor
            def _(pe):
                def multiply(pe, t):
                    pe.wait_ge(f.lo_ok, t + 1)
                    if t >= 2:
                        pe.wait_ge(y_free, t - 1)
                    for n in range(2):
                        nn = slice(n * BANK, (n + 1) * BANK)
                        for k in range(8):
                            if t == 0 and n == 0:
                                pe.wait_ge(lo_ok, k + 1)
                            for i, (p, q) in enumerate(PARTS):
                                mm = pe.matmul(acc[t % 2][:, nn], hT[:, p, k, t * P:(t + 1) * P], w[:, q, k, nn],
                                               start=(k == 0 and i == 0), stop=(k == 7 and i == 2))
                    mm.then_inc(y_done, 1)

                for s in range(STEPS):
                    at_step(s, (f.pe_turn, 1, pe), (b.pe_turn, 5, pe), (multiply, 2, pe))



class BiasTable:

    def __init__(self, st, rel_bias, onehot, log_count, table):
        self.W = 2 * S
        self.srcs = rel_bias, onehot, log_count
        self.table = table
        self.oh = st.sb("bt_oh", [32, self.W])
        self.rb = st.sb("bt_rb", [32, 8])
        self.lc = st.sb("bt_lc", [8, self.W])
        self.out = st.sb("bt_out", [8, self.W])
        self.out8 = st.sb("bt_out8", [8, self.W])
        self.ps = st.ps("bt_ps", [P, self.W])
        self.consts_in, self.mm, self.added, self.scaled, self.stored = (
            st.sem("bt_" + n) for n in ("in", "mm", "added", "scaled", "stored"))

    def load(self, sp):
        rel_bias, onehot, log_count = self.srcs
        sp.dma_start(self.oh[:, :], onehot).then_inc(self.consts_in, 16)
        sp.dma_start(self.rb[:, :], rel_bias).then_inc(self.consts_in, 16)
        sp.dma_start(self.lc[:, :], log_count.partition_broadcast(8)).then_inc(self.consts_in, 16)

    def store(self, sp):
        sp.wait_ge(self.scaled, 1)
        sp.dma_start(self.table, self.out8[:, :]).then_inc(self.stored, 16)
        sp.wait_ge(self.stored, 16)

    def tensor(self, pe):
        pe.wait_ge(self.consts_in, 48)
        for c in range(self.W // BANK):
            m = pe.matmul(self.ps[0:8, c * BANK:(c + 1) * BANK], self.rb[:, :], self.oh[:, c * BANK:(c + 1) * BANK],
                          start=True, stop=True)
        m.then_inc(self.mm, 1)

    def vector(self, dve):
        dve.wait_ge(self.consts_in, 48)
        dve.wait_ge(self.mm, 1)
        dve.tensor_tensor(self.out[:, :], self.ps[0:8, :], self.lc[:, :], ALU.add).then_inc(self.added, 1)
        dve.wait_ge(self.added, 1)
        dve.tensor_scalar(self.out8[:, :], self.out[:, :], 8.0, None, ALU.mult).then_inc(self.scaled, 1)


TURN = 16


def tiles(eng, total, peel, lag, body):
    for T in range(peel):
        body(T % TURN, T)
    with eng.Fori(0, total // TURN - 1) as r:
        for l in range(peel, peel + TURN):
            body(l % TURN, r * TURN + l)
    for T in range(total - TURN + peel, total + lag):
        body(T % TURN, T)


def active(T, k, total):
    return not isinstance(T, int) or 0 <= T - k < total


def reached(eng, sem, n):
    if not isinstance(n, int) or n > 0:
        eng.wait_ge(sem, n)



def softmax_attention(nc, name, ident, heads, scale, q_src, k_src, v_src, out, table=None, rope=None):
    DV, T8 = 64, NT
    total = heads * T8
    WB = 2 * S - P
    nraw = 4 + (4 if rope else 0)
    nv = 1 + (table is not None)
    H = T8 // 2 * P
    nhi = 3 if rope else 2

    with stage(nc) as st:
        qraw, kraw = (st.sb(name + n, [P, 2, S]) for n in ("_qraw", "_kraw"))
        qs, kh, kl = (st.sb(name + n, [P, 2, S], F32R) for n in ("_qs", "_kh", "_kl"))
        if rope:
            rqraw, krraw = st.sb(name + "_rqraw", [P, 2, S]), st.sb(name + "_krraw", [P, S])
            rqs, krs = st.sb(name + "_rqs", [P, 2, S], F32R), st.sb(name + "_krs", [P, S], F32R)
        v = st.sb(name + "_v", [P, 2, NT, DV])
        wb = st.sb(name + "_wb", [P, 2, WB]) if table is not None else None
        sc = st.sb(name + "_sc", [P, 2, S]) if table is not None else None
        p = st.sb(name + "_p", [P, 4, S])
        pT = st.sb(name + "_pT", [P, 2, S])
        mx, nm, rs, ri = (st.sb(name + n, [P, TURN]) for n in ("_mx", "_nm", "_rs", "_ri"))
        o = st.sb(name + "_ob", [P, 2, NT, DV])
        sps = [st.ps(f"{name}_s{s}", [P, S]) for s in range(2)]
        tps = st.ps(name + "_t", [P, S])
        ops = [st.ps(f"{name}_op{s}", [P, BANK]) for s in range(2)]
        raw_in = [st.sem(f"{name}_raw_in{s}") for s in range(2)]
        v_in = [st.sem(f"{name}_v_in{s}") for s in range(2)]
        kr_in, kr_ok, hi_ok, lo_ok, s_done, s_free, max_done, nm_done, p_done = (
            st.sem(name + n) for n in ("_kr_in", "_kr_ok", "_hi_ok", "_lo_ok", "_s_done", "_s_free", "_max", "_nm_done", "_p_done"))
        turned_a, turned_b, pT_a, pT_b = (st.sem(name + n) for n in ("_turned_a", "_turned_b", "_pT_a", "_pT_b"))
        pv_done, ri_done, o_done = (st.sem(name + n) for n in ("_pv_done", "_ri_done", "_o_done"))
        passed = st.sem(name + "_passed")
        stored = [st.sem(f"{name}_stored{s}") for s in range(2)]

        with nc.Block() as block:
            @block.sync
            def _(sp):
                def load_raw(h, u):
                    for b in range(2):
                        sp.dma_start(qraw[64 * b:64 * b + 64, u, :], q_src(h)).then_inc(raw_in[u], 16)
                        sp.dma_start(kraw[64 * b:64 * b + 64, u, :], k_src(h)).then_inc(raw_in[u], 16)
                    if rope:
                        for b in range(4):
                            sp.dma_start(rqraw[32 * b:32 * b + 32, u, :], rope(h)).then_inc(raw_in[u], 16)

                def load_v(h, u):
                    sp.dma_start(v[:, u, :, :], v_src(h)).then_inc(v_in[u], 16)
                    if table is not None:
                        src = bass.AP(table.tensor, h * (2 * S), [[1, P], [1, WB]])
                        sp.dma_start(wb[:, u, :], src).then_inc(v_in[u], 16)

                def store(h, u):
                    sp.wait_ge(o_done, h * T8 + T8)
                    sp.sem_inc(passed, 1)
                    sp.dma_start(out[:, bass.ds(h * DV, DV)].rearrange("(t p) d -> p t d", p=P),
                                 o[:, u, :, :]).then_inc(stored[u], 16)

                sp.sem_inc(stored[0], 16)
                sp.sem_inc(stored[1], 16)
                load_raw(0, 0)
                if rope:
                    for b in range(4):
                        sp.dma_start(krraw[32 * b:32 * b + 32, :], rope(None)).then_inc(kr_in, 16)
                load_v(0, 0)
                load_raw(1, 1)
                load_v(1, 1)
                with sp.Fori(0, heads // 2 - 1) as r:
                    for u in range(2):
                        h = r * 2 + u
                        sp.wait_ge(lo_ok, h * 8 + 8)
                        sp.sem_inc(passed, 1)
                        load_raw(h + 2, u)
                        store(h, u)
                        sp.wait_ge(pv_done, h * T8 + T8)
                        sp.sem_inc(passed, 1)
                        load_v(h + 2, u)
                for u in range(2):
                    store(heads - 2 + u, u)
                for u in range(2):
                    sp.wait_ge(stored[u], 16 * (heads // 2 + 1))

            @block.gpsimd
            def _(pool):
                def split_lo(u, done, hi):
                    def lo(dst, raw, n, total):
                        pool.tensor_tensor(dst, raw, dst.bitcast(F32), ALU.subtract).then_inc(lo_ok, n)
                        done(total)
                    hi(1)
                    lo(qs[64:P, u, :], qraw[64:P, u, :], 4, 4)
                    hi(2)
                    pool.tensor_tensor(kl[:, u, :], kraw[:, u, :], kh[:, u, :].bitcast(F32),
                                       ALU.subtract).then_inc(lo_ok, 2 if rope else 4)
                    done(6 if rope else 8)
                    if rope:
                        hi(3)
                        lo(rqs[64:P, u, :], rqraw[64:P, u, :], 2, 8)

                split_lo(1, lambda n: pool.wait_ge(lo_ok, 8 + n), lambda n: pool.wait_ge(hi_ok, nhi + n))
                with pool.Fori(0, heads // 2 - 1) as r:
                    for u in range(2):
                        split_lo(u, lambda n: pool.wait_ge(lo_ok, r * 16 + (8 * (u + 2) + n)),
                                 lambda n: pool.wait_ge(hi_ok, r * (2 * nhi) + (nhi * (u + 2) + n)))

            @block.tensor
            def _(pe):
                if rope:
                    pe.wait_ge(kr_ok, 3)

                def body(l, T):
                    if active(T, 0, total):
                        u, i = l // T8, l % T8
                        if i == 0:
                            pe.wait_ge(lo_ok, T + 8)
                        reached(pe, s_free if table is not None else p_done, T - 1)
                        ii = slice(i * P, (i + 1) * P)
                        for c in range(2):
                            cc = slice(c * BANK, (c + 1) * BANK)
                            pe.matmul(sps[l % 2][:, cc], qs[:, u, ii], kh[:, u, cc], start=True, stop=False)
                            mm = pe.matmul(sps[l % 2][:, cc], qs[:, u, ii], kl[:, u, cc], start=False, stop=not rope)
                            if rope:
                                mm = pe.matmul(sps[l % 2][:, cc], rqs[:, u, ii], krs[:, cc], start=False, stop=True)
                        mm.then_inc(s_done, 1)
                    if active(T, 2, total):
                        m = (l - 2) % TURN
                        reached(pe, p_done, T - 1)
                        reached(pe, pT_a, T - 2)
                        for k in range(NT):
                            if k == NT // 2:
                                reached(pe, pT_b, T - 2)
                            mm = pe.transpose(tps[:, k * P:(k + 1) * P], p[:, m % 4, k * P:(k + 1) * P], ident[:, :])
                            if k == NT // 2 - 1:
                                mm.then_inc(turned_a, 1)
                        mm.then_inc(turned_b, 1)
                    if active(T, 3, total):
                        m = (l - 3) % TURN
                        u, i = m // T8, m % T8
                        if i == 0:
                            pe.wait_ge(v_in[u], (T - 3 - 8 * u) * nv + 16 * nv)
                        reached(pe, o_done, T - 4)
                        reached(pe, pT_a, T - 2)
                        reached(pe, pT_b, T - 2)
                        for k in range(NT):
                            mm = pe.matmul(ops[m % 2][:, 0:DV], pT[:, m % 2, k * P:(k + 1) * P], v[:, u, k, :],
                                           start=(k == 0), stop=(k == NT - 1))
                        mm.then_inc(pv_done, 1)
                tiles(pe, total, 5, 3, body)

            @block.vector
            def _(dve):
                def body(l, T):
                    if active(T, 0, total):
                        u, i = l // T8, l % T8
                        dve.wait_ge(s_done, T + 1)
                        if table is not None:
                            if i == 0:
                                dve.wait_ge(v_in[u], (T - 8 * u) * nv + 16 * nv)
                            reached(dve, p_done, T - 1)
                            dve.sem_inc(passed, 1)
                            dve.tensor_tensor_reduce(out=sc[:, l % 2, :], in0=sps[l % 2][:, :], in1=wb[:, u, i * P:i * P + S][:, ::-1],
                                                     scale=1.0, scalar=-3e38, op0=ALU.add, op1=ALU.max,
                                                     accum_out=mx[:, l:l + 1]).then_inc(s_free, 1)
                            dve.wait_ge(s_free, T + 1)
                        else:
                            dve.reduce_max(mx[:, l:l + 1], sps[l % 2][:, :], AX.X).then_inc(max_done, 1)
                            dve.wait_ge(max_done, T + 1)
                        dve.tensor_scalar(nm[:, l:l + 1], mx[:, l:l + 1], -scale, None, ALU.mult).then_inc(nm_done, 1)
                    if active(T, 2, total):
                        m = (l - 2) % TURN
                        reached(dve, turned_a, T - 1)
                        reached(dve, pv_done, T - 3)
                        dve.tensor_copy(pT[:, m % 2, 0:H], tps[:, 0:H]).then_inc(pT_a, 1)
                    if active(T, 3, total):
                        m = (l - 3) % TURN
                        u, i = m // T8, m % T8
                        reached(dve, p_done, T - 2)
                        dve.reciprocal(ri[:, m:m + 1], rs[:, m:m + 1]).then_inc(ri_done, 1)
                        reached(dve, pv_done, T - 2)
                        reached(dve, ri_done, T - 2)
                        if i == 0:
                            dve.wait_ge(stored[u], T - 3 - 8 * u + 16)
                        dve.tensor_scalar(o[:, u, i, :], ops[m % 2][:, 0:DV], ri[:, m:m + 1], None,
                                          ALU.mult).then_inc(o_done, 1)
                def lo(dst, raw):
                    return dve.tensor_tensor(dst, raw, dst.bitcast(F32), ALU.subtract)
                dve.wait_ge(hi_ok, 1)
                lo(qs[64:P, 0, :], qraw[64:P, 0, :]).then_inc(lo_ok, 4)
                dve.wait_ge(hi_ok, 2)
                dve.tensor_tensor(kl[:, 0, :], kraw[:, 0, :], kh[:, 0, :].bitcast(F32), ALU.subtract).then_inc(lo_ok, 2 if rope else 4)
                if rope:
                    dve.wait_ge(hi_ok, 3)
                    lo(rqs[64:P, 0, :], rqraw[64:P, 0, :]).then_inc(lo_ok, 2)
                    dve.wait_ge(kr_ok, 1)
                    for b in (1, 3):
                        rows_ = slice(32 * b, 32 * b + 32)
                        lo(krs[rows_, :], krraw[rows_, :]).then_inc(kr_ok, 1)
                tiles(dve, total, 5, 3, body)

            @block.scalar
            def _(act):
                def split_hi(u, n):
                    dst, raw = ((qs, qraw), (kh, kraw), (rqs, rqraw) if rope else None)[n]
                    act.activation(dst[:, u, :], raw[:, u, :], ACT.Copy).then_inc(hi_ok, 1)

                act.wait_ge(raw_in[0], 16 * nraw)
                for n in range(nhi):
                    split_hi(0, n)
                if rope:
                    act.wait_ge(kr_in, 64)
                    act.activation(krs[:, :], krraw[:, :], ACT.Copy).then_inc(kr_ok, 1)

                def body(l, T):
                    if active(T, 2, total):
                        m = (l - 2) % TURN
                        reached(act, turned_b, T - 1)
                        reached(act, pv_done, T - 3)
                        act.activation(pT[:, m % 2, H:S], tps[:, H:S], ACT.Copy).then_inc(pT_b, 1)
                    if active(T, 0, total):
                        act.wait_ge(nm_done, T + 1)
                        reached(act, turned_b, T - 3)
                        src = sc[:, l % 2, :] if table is not None else sps[l % 2][:, :]
                        act.activation(p[:, l % 4, :], src, ACT.Exp, bias=nm[:, l:l + 1], scale=scale,
                                       accum_out=rs[:, l:l + 1]).then_inc(p_done, 1)
                        n, ahead = l % T8 - 1, 9 - l % T8
                        if 0 <= n < nhi and active(T + ahead - 1, 0, total):
                            u = 1 - l // T8
                            if n == 0:
                                act.wait_ge(s_done, T + 1)
                                act.wait_ge(raw_in[u], (T + 7 - 8 * u) * nraw + 16 * nraw)
                            split_hi(u, n)
                tiles(act, total, 5, 3, body)


def rope_keys_queries(nc, qlT, cosT, sinT, qrT_out, krT_src, krT_out):
    with stage(nc) as st:
        c = st.sb("rk_c", [P, S])
        s = st.sb("rk_s", [P, S])
        a = st.sb("rk_a", [P, 3, S])
        b = st.sb("rk_b", [P, 3, S])
        o = st.sb("rk_o", [P, 3, S])
        loaded, ma, mb, added, stored = (st.sem("rk_" + n) for n in ("in", "ma", "mb", "added", "stored"))
        n = [P, P, 32]
        with nc.Block() as block:
            @block.sync
            def _(sp):
                sp.dma_start(c[:, :], cosT).then_inc(loaded, 16)
                sp.dma_start(s[:, :], sinT).then_inc(loaded, 16)
                for j in range(2):
                    sp.dma_start(a[:, j, :], qlT[512 + j * P:512 + (j + 1) * P, :]).then_inc(loaded, 16)
                    sp.dma_start(b[:, j, :], qlT[768 + j * P:768 + (j + 1) * P, :]).then_inc(loaded, 16)
                sp.dma_start(a[0:32, 2, :], krT_src[0:32, :]).then_inc(loaded, 16)
                sp.dma_start(b[0:32, 2, :], krT_src[32:64, :]).then_inc(loaded, 16)
                for j in range(3):
                    sp.wait_ge(added, j + 1)
                    dst = qrT_out[j * P:(j + 1) * P, :] if j < 2 else krT_out
                    sp.dma_start(dst, o[0:n[j], j, :]).then_inc(stored, 16)
                sp.wait_ge(stored, 48)

            @block.gpsimd
            def _(pool):
                pool.wait_ge(loaded, 128)
                for j in range(3):
                    pool.tensor_tensor(b[0:n[j], j, :], b[0:n[j], j, :], s[0:n[j], :], ALU.mult).then_inc(mb, 1)

            @block.vector
            def _(dve):
                dve.wait_ge(loaded, 128)
                for j in range(3):
                    dve.tensor_tensor(a[0:n[j], j, :], a[0:n[j], j, :], c[0:n[j], :], ALU.mult).then_inc(ma, 1)
                    dve.wait_ge(ma, j + 1)
                    dve.wait_ge(mb, j + 1)
                    dve.tensor_tensor(o[0:n[j], j, :], a[0:n[j], j, :], b[0:n[j], j, :], ALU.add).then_inc(added, 1)


def first_attention(nc, A, C, scr, ident, hT):
    x0 = A["x"].rearrange("b s d -> (b s) d")
    norm_rows(nc, "n0", ident, D, [(0, D, lambda t: rows(x0, t))], [(0, D)], hT=hT,
              also=lambda st: BiasTable(st, A["rel_bias"], C["onehot"], C["log_count"], scr["table"]))
    w_in = A["w_in"][0]
    kr0 = 3 * 512 + 384
    krv = tiled(w_in)
    project(nc, "pa", hT, 8, [
        *(dict(kind="T", width=512, load=columns(w_in, c, 512), dst=to_T(scr["qkT"], c, 512)) for c in (0, 512)),
        dict(kind="row", width=512, load=columns(w_in, 1024, 512), dst=to_rows(scr["va"], 0, 512)),
        dict(kind="row", width=384, load=columns(w_in, 1536, 384), dst=to_rows(scr["lat"], 0, 384)),
        dict(kind="T", width=64, dst=to_T(scr["krT"], 0, 64),
             load=[(slice(0, 32), krv[:, :, kr0:kr0 + 32]), (slice(32, 48), krv[:, :, kr0 + 16:kr0 + 32]),
                             (slice(48, 64), krv[:, :, kr0:kr0 + 16])]),
    ], gain=[(0, A["g_attn_norm"][0])])
    qk = scr["qkT"]
    heads_of = lambda src, h0=0: lambda h: src[bass.ds(h * 64 + h0, 64), :]
    values_of = lambda src: lambda h: src[:, bass.ds(h * 64, 64)].rearrange("(t p) d -> p t d", p=P)
    softmax_attention(nc, "aa", ident, 8, 64 ** -0.5, heads_of(qk), heads_of(qk, 512), values_of(scr["va"]), scr["oa"],
                      table=scr["table"])
    norm_rows(nc, "nl", ident, 384, [(0, 384, lambda t: rows(scr["lat"], t))], [(0, 256), (256, 128)], hT=hT)
    wq = tiled(A["w_q_up"][0])
    q_nope = [(slice(64 * h, 64 * h + 64), wq[:, :, 96 * h:96 * h + 64]) for h in range(8)]
    q_rope = []
    for h in range(8):
        r0 = 96 * h + 64
        q_rope += [(slice(32 * h, 32 * h + 32), wq[:, :, r0:r0 + 32]),
                   (slice(256 + 32 * h, 256 + 32 * h + 16), wq[:, :, r0 + 16:r0 + 32]),
                   (slice(256 + 32 * h + 16, 256 + 32 * h + 32), wq[:, :, r0:r0 + 16])]
    project(nc, "pq", hT[:, :, 0:2, :], 2, [
        dict(kind="T", width=512, load=q_nope, dst=to_T(scr["qlT"], 0, 512)),
        dict(kind="T", width=512, load=q_rope, dst=to_T(scr["qlT"], 512, 512)),
    ], gain=[(0, A["g_q_latent"][0])])
    kvw = tiled(A["w_kv_up"][0])
    project(nc, "pk", hT[:, :, 2:3, :], 1, [
        dict(kind="T", width=512, dst=to_T(scr["knT"], 0, 512),
             load=[(slice(64 * h, 64 * h + 64), kvw[:, :, 128 * h:128 * h + 64]) for h in range(8)]),
        dict(kind="row", width=512, dst=to_rows(scr["vb"], 0, 512),
             load=[(slice(64 * h, 64 * h + 64), kvw[:, :, 128 * h + 64:128 * h + 128]) for h in range(8)]),
    ], gain=[(0, A["g_kv_latent"][0])])
    rope_keys_queries(nc, scr["qlT"], C["mla_cosT"], C["mla_sinT"], scr["qrT"], scr["krT"], scr["krT2"])
    softmax_attention(nc, "ab", ident, 8, 96 ** -0.5, heads_of(scr["qlT"]), heads_of(scr["knT"]), values_of(scr["vb"]), scr["ob"],
                      rope=lambda h: scr["krT2"] if h is None else scr["qrT"][bass.ds(h * 32, 32), :])
    mix_out(nc, "am", ident, hT, A["w_out"][0], [(0, A["g_out_a"][0]), (4, A["g_out_b"][0])],
            dict(width=D, loads=[(0, 512, lambda t: rows(scr["oa"], t)), (512, 512, lambda t: rows(scr["ob"], t))],
                 groups=[(0, 512), (512, 512)], hT=hT),
            dict(width=D, loads=[(0, D, lambda t: rows(x0, t))], groups=[(0, D)], hT=hT, keep=scr["x1"], keep_normed=scr["xn"]))


def identity(nc, ident, diag=1):
    with stage(nc) as st:
        zero, done = st.sem("id_zero"), st.sem("id_done")
        with nc.Block() as block:
            @block.gpsimd
            def _(pool):
                pool.memset(ident[:, :], 0.0).then_inc(zero, 1)
                pool.wait_ge(zero, 1)
                pool.affine_select(out=ident[:, :], in_=ident[:, :], compare_op=ALU.not_equal, fill=1.0, base=0,
                                   pattern=[[-1, P]], channel_multiplier=1).then_inc(done, 1)
                pool.wait_ge(done, 1)


SCRATCH = dict(
    qkT=(1024, S), va=(S, 512), lat=(S, 384), krT=(64, S), krT2=(32, S), table=(8, 2 * S), oa=(S, 512),
    qlT=(1024, S), qrT=(256, S), knT=(512, S), vb=(S, 512), ob=(S, 512),
)


def constants():
    rel = (S - 1) - np.arange(2 * S)
    half, exact = 16, 8
    n = np.abs(rel)
    large = exact + (np.log(np.maximum(n, 1) / exact) / math.log(1024 / exact) * (half - exact)).astype(np.int32)
    bucket = np.where(rel > 0, half, 0) + np.where(n < exact, n, np.minimum(large, half - 1))
    count = np.zeros(2 * S)
    for window, dilation in ((128, 1), (512, 4), (2048, 16)):
        steps = window // (2 * dilation)
        count += (rel % dilation == 0) & (n <= steps * dilation)
    c = {
        "onehot": (bucket[None, :] == np.arange(32)[:, None]).astype(np.float32),
        "log_count": np.where(count > 0, np.log(np.maximum(count, 1)), NEG).astype(np.float32),
    }
    inv = (10000.0 ** (-(np.arange(16, dtype=np.float32) / np.float32(16)))).astype(np.float32)
    ang = (np.arange(S, dtype=np.float32)[:, None] * inv[None, :]).astype(np.float32)
    c["mla_cosT"] = np.tile(np.cos(ang).T, (8, 1)).astype(np.float32)
    c["mla_sinT"] = np.tile(np.concatenate([-np.sin(ang).T, np.sin(ang).T], 0), (4, 1)).astype(np.float32)
    e = np.arange(32)
    c["router"] = np.concatenate([e, 32 - e, np.arange(15)]).astype(np.float32)
    c["before"] = np.triu(np.ones((P, P)), 1).astype(np.float32)
    pos = np.arange(P, dtype=np.float64)
    inv = (10000.0 ** (-(np.arange(32, dtype=np.float32) / np.float32(32)))).astype(np.float32)
    ang = (np.arange(S, dtype=np.float32)[:, None] * inv[None, :]).astype(np.float32)
    c["ret_cs"] = np.concatenate([np.cos(ang), np.sin(ang)], 1).astype(np.float32)
    g = np.log(1.0 - 2.0 ** (-5.0 - np.arange(4)))
    scale = 64 ** -0.5
    dist = pos[None, :] - pos[:, None]
    c["ret_decay"] = np.concatenate([np.where(dist >= 0, np.exp(gh * np.maximum(dist, 0)), 0) * scale for gh in g],
                                    1).astype(np.float32)
    c["ret_rowdec"] = np.concatenate([np.exp(g[None, :] * (pos + 1)[:, None]),
                                      np.exp(g[None, :] * (P - 1 - pos)[:, None]) * scale], 1).astype(np.float32)
    c["ret_gchunk"] = np.exp(P * np.stack([np.repeat(g[2 * j:2 * j + 2], 64) for j in range(2)], 1)).astype(np.float32)
    strict = pos[None, :] < pos[:, None]
    c["strict"] = np.stack([strict, ~strict], 1).astype(np.float32)
    s, t = np.arange(P)[:, None], np.arange(P)[None, :]
    c["levels"] = np.stack([(s // (2 * m) == t // (2 * m)) & (s % (2 * m) < m) & (t % (2 * m) >= m)
                            for m in (64, 32, 16, 8, 4, 2, 1)] + [s == t], 1).astype(np.float32)
    return c



NG, NE, FF = 4, 32, 256
EG = NE // NG
NOV = 2 * S // P - 1
NB = 48


def route(nc, ident, hT, A, C, tok_of_slot, slot_out, gates, slots, over, weights):
    with stage(nc) as st:
        wr = st.sb("ro_wr", [P, 8, NG + NE])
        wg = st.sb("ro_wg", [P, 8, NG + NE])
        ws = st.sb("ro_ws", [P, 2, 8, NG + NE], F32R)
        gcol = st.sb("ro_g", [P, 8])
        br = st.sb("ro_br", [P, NG + NE])
        cst = st.sb("ro_cst", [P, 2 * NE + NOV])
        ltm = st.sb("ro_lt", [P, P])
        ones = st.sb("ro_ones", [P, P])
        L = st.sb("ro_L", [P, NT, NG + NE])
        g4 = [st.sb(f"ro_g4{i}", [P, NT, NG]) for i in range(6)]
        c1 = [st.sb(f"ro_c1{i}", [P, NT]) for i in range(14)]
        e32 = [st.sb(f"ro_e{i}", [P, NT, NE]) for i in range(14)]
        M = st.sb("ro_M", [P, NT, NE])
        cum = st.sb("ro_cum", [P, NT + 1, NE])
        rank = st.sb("ro_rank", [P, NT, NE])
        kk = st.sb("ro_kk", [P, 8, NT, NE])
        cnt = st.sb("ro_cnt", [P, 12, NE])
        ovb = st.sb("ro_ovb", [P, NOV, NE])
        ovs = st.sb("ro_ovs", [P, 2 * NB])
        posf = st.sb("ro_posf", [P, NT, 2])
        zero = st.sb("ro_zero", [P, NB], U32)
        tok = st.sb("ro_tok", [P, NT], U32)
        blank = st.sb("ro_blank", [P, D])
        blanked = st.sem("ro_blanked")
        lt = st.sb("ro_ltT", [NG + NE, S])
        pt = st.ps("ro_pt", [P, S])
        pl = st.ps("ro_pl", [P, BANK])
        pr = st.ps("ro_pr", [P, BANK])
        pc = st.ps("ro_pc", [P, BANK])
        ins, cleared, lg, exps, e_ready, m_ready, ranks, d, tok_ready, slots_ready, scattered, e2_ready, e2s, split_ok, lgT, lt_ok = (
            st.sem("ro_" + n) for n in ("in", "cleared", "logits", "exps", "e_ready", "m_ready", "ranks", "step", "tok", "slots",
                                        "scattered", "e2_ready", "e2", "split_ok", "logitsT", "lt_ok"))
        G8, E8 = [P, NT, NG], [P, NT, NE]
        with nc.Block() as block:
            @block.sync
            def _(sp):
                sp.dma_start(wr[:, :, 0:NG], tiled(A["w_router_group"][0])).then_inc(ins, 16)
                sp.dma_start(wr[:, :, NG:], tiled(A["w_router_expert"][0])).then_inc(ins, 16)
                sp.dma_start(br[:, 0:NG], A["b_router_group"][0].partition_broadcast(P)).then_inc(ins, 16)
                sp.dma_start(br[:, NG:], A["b_router_expert"][0].partition_broadcast(P)).then_inc(ins, 16)
                sp.dma_start(cst[:, :], C["router"].partition_broadcast(P)).then_inc(ins, 16)
                sp.dma_start(ltm[:, :], C["before"]).then_inc(ins, 16)
                sp.dma_start(gcol[:, :], A["g_ffn_norm"][0].rearrange("(k p) -> p k", p=P),
                             allow_slow_non_contiguous=True).then_inc(ins, 16)
                sp.wait_ge(ins, 112)
                for e in range(NW):
                    weights.load(sp, slice(e, e + 1), e)

            @block.tensor
            def _(pe):
                pe.wait_ge(ins, 112)
                pe.wait_ge(split_ok, 1)
                for n in range(2):
                    mm = product(pe, pt[0:NG + NE, n * BANK:(n + 1) * BANK], 8, lambda p, k: ws[:, p, k, :],
                                 lambda q, k: hT[:, q, k, n * BANK:(n + 1) * BANK])
                    mm.then_inc(lgT, 1)
                for n in range(2):
                    pe.wait_ge(lt_ok, n + 1)
                    for t in range(n * NT // 2, (n + 1) * NT // 2):
                        mm = pe.transpose(pl[:, t * 36:(t + 1) * 36], lt[:, t * P:(t + 1) * P], ident[0:NG + NE, 0:NG + NE])
                mm.then_inc(lg, 1)
                pe.wait_ge(m_ready, 1)
                pe.matmul(pr[:, 0:NT * NE], ltm[:, :], M[:, :, :].rearrange("p t e -> p (t e)"), start=True, stop=False)
                pe.matmul(pr[:, 0:NT * NE], ones[:, :], cum[:, 0:NT, :].rearrange("p t e -> p (t e)"), start=False, stop=True)
                pe.matmul(pc[:, 0:NE], ones[:, :], cum[:, NT, :], start=True, stop=True).then_inc(ranks, 1)

            @block.scalar
            def _(act):
                act.wait_ge(tok_ready, 3)
                act.wait_ge(ins, 112)
                act.dma_start(slot_out.rearrange("(p b) n -> p b n", b=NB)[:, NE:, :],
                              blank[:, :].unsqueeze(1).to_broadcast([P, NB - NE, D])).then_inc(blanked, 16)
                for n in range(2):
                    act.wait_ge(lgT, n + 1)
                    act.activation(lt[:, n * BANK:(n + 1) * BANK], pt[0:NG + NE, n * BANK:(n + 1) * BANK], ACT.Copy).then_inc(lt_ok, 1)
                act.wait_ge(e_ready, 1)
                act.activation(g4[3][:, :, :], g4[2][:, :, :], ACT.Exp).then_inc(exps, 1)
                act.wait_ge(e2_ready, 1)
                act.activation(c1[7][:, :], c1[6][:, :], ACT.Exp).then_inc(e2s, 1)
                act.wait_ge(blanked, 16)

            @block.vector
            def _(dve):
                n = [0]

                def step(ins_):
                    n[0] += 1
                    ins_.then_inc(d, 1)
                    dve.wait_ge(d, n[0])

                step(dve.memset(ones[:, :], 1.0))
                dve.wait_ge(ins, 112)
                step(dve.tensor_tensor(wg[:, :, :], wr[:, :, :], gcol[:, :].unsqueeze(2).to_broadcast([P, 8, NG + NE]), ALU.mult))
                step(dve.tensor_copy(ws[:, HI, :, :], wg[:, :, :]))
                dve.tensor_tensor(ws[:, LO, :, :], wg[:, :, :], ws[:, HI, :, :].bitcast(F32), ALU.subtract).then_inc(split_ok, 1)
                dve.wait_ge(lg, 1)
                step(dve.tensor_tensor(L[:, :, :], pl[:, 0:NT * 36].rearrange("p (t n) -> p t n", t=NT),
                                       br[:, :].unsqueeze(1).to_broadcast([P, NT, 36]), ALU.add))
                Lg, Le = L[:, :, 0:NG], L[:, :, NG:]
                step(dve.reduce_max(c1[0][:, :], Lg, AX.X))
                gm = c1[0][:, :].unsqueeze(2).to_broadcast(G8)
                dve.tensor_tensor(g4[2][:, :, :], Lg, gm, ALU.subtract).then_inc(e_ready, 1)
                step(dve.tensor_tensor(g4[0][:, :, :], Lg, gm, ALU.is_equal))
                step(dve.tensor_tensor(g4[1][:, :, :], g4[0][:, :, :],
                                       cst[:, 2 * NE - NG:2 * NE].unsqueeze(1).to_broadcast(G8), ALU.mult))
                step(dve.reduce_max(c1[1][:, :], g4[1][:, :, :], AX.X))
                step(dve.tensor_tensor(g4[4][:, :, :], g4[1][:, :, :], c1[1][:, :].unsqueeze(2).to_broadcast(G8), ALU.is_equal))
                step(dve.tensor_scalar(g4[5][:, :, :], g4[4][:, :, :], -1.0, 1e30, ALU.add, ALU.mult))
                E4 = [P, NT, NG, EG]
                v4 = lambda x: x.rearrange("p t (g e) -> p t g e", g=NG)
                step(dve.tensor_tensor(v4(e32[0][:, :, :]), v4(Le), g4[4][:, :, :].unsqueeze(3).to_broadcast(E4), ALU.mult))
                step(dve.tensor_tensor(v4(e32[1][:, :, :]), v4(e32[0][:, :, :]), g4[5][:, :, :].unsqueeze(3).to_broadcast(E4), ALU.add))
                prio = cst[:, NE:2 * NE].unsqueeze(1).to_broadcast(E8)

                def pick(src, mx, pm, eq, pri, oh):
                    step(dve.reduce_max(mx[:, :], src[:, :, :], AX.X))
                    step(dve.tensor_tensor(eq[:, :, :], src[:, :, :], mx[:, :].unsqueeze(2).to_broadcast(E8), ALU.is_equal))
                    step(dve.tensor_tensor(pri[:, :, :], eq[:, :, :], prio, ALU.mult))
                    step(dve.reduce_max(pm[:, :], pri[:, :, :], AX.X))
                    step(dve.tensor_tensor(oh[:, :, :], pri[:, :, :], pm[:, :].unsqueeze(2).to_broadcast(E8), ALU.is_equal))

                oh1, oh2 = e32[4], e32[8]
                pick(e32[1], c1[2], c1[3], e32[2], e32[3], oh1)
                step(dve.scalar_tensor_tensor(out=e32[5][:, :, :], in0=oh1[:, :, :], scalar=-4e30, in1=e32[1][:, :, :],
                                              op0=ALU.mult, op1=ALU.add))
                pick(e32[5], c1[4], c1[5], e32[6], e32[7], oh2)
                dve.tensor_tensor(c1[6][:, :], c1[4][:, :], c1[2][:, :], ALU.subtract).then_inc(e2_ready, 1)
                step(dve.tensor_tensor(M[:, :, :], oh1[:, :, :], oh2[:, :, :], ALU.add))
                step(dve.memset(cum[:, 0, :], 0.0))
                for t in range(NT):
                    ins_ = dve.tensor_tensor(cum[:, t + 1, :], cum[:, t, :], M[:, t, :], ALU.add)
                    if t == NT - 1:
                        dve_last = ins_
                        ins_.then_inc(m_ready, 1)
                        dve.wait_ge(m_ready, 1)
                    else:
                        step(ins_)
                dve.wait_ge(exps, 1)
                step(dve.reduce_sum(c1[8][:, :], g4[3][:, :, :], AX.X))
                dve.wait_ge(e2s, 1)
                step(dve.tensor_scalar(c1[9][:, :], c1[7][:, :], 1.0, None, ALU.add))
                step(dve.tensor_tensor(c1[10][:, :], c1[9][:, :], c1[8][:, :], ALU.mult))
                step(dve.reciprocal(gates[:, :, 0], c1[10][:, :]))
                step(dve.tensor_tensor(gates[:, :, 1], gates[:, :, 0], c1[7][:, :], ALU.mult))
                dve.wait_ge(ranks, 1)
                step(dve.tensor_copy(cnt[:, 0, :], pc[:, 0:NE]))
                step(dve.memset(cnt[:, 1, :], 0.0))
                for j in range(1, 8):
                    step(dve.scalar_tensor_tensor(out=cnt[:, 1 + j, :], in0=cnt[:, 0, :], scalar=float(P * j), in1=cnt[:, j, :],
                                                  op0=ALU.is_gt, op1=ALU.add))
                nov, oend, obase = cnt[:, 8, :], cnt[:, 9, :], cnt[:, 10, :]
                step(dve.tensor_tensor_scan(oend, ones[:, 0:NE], nov, 0.0, ALU.mult, ALU.add))
                step(dve.tensor_tensor(cnt[:, 11, :], oend, nov, ALU.subtract))
                step(dve.tensor_tensor(obase, cnt[:, 11, :], cst[:, 0:NE], ALU.subtract))
                step(dve.tensor_tensor(ovb[:, :, :], oend.unsqueeze(1).to_broadcast([P, NOV, NE]),
                                       cst[:, 2 * NE:].unsqueeze(2).to_broadcast([P, NOV, NE]), ALU.is_le))
                step(dve.reduce_sum(ovs[:, 0:NOV], ovb[:, :, :], AX.X))
                step(dve.tensor_scalar(ovs[:, NB:NB + NOV], ovs[:, 0:NOV], float(NE - 1), None, ALU.min))
                step(dve.tensor_copy(over[:, 0:NOV], ovs[:, NB:NB + NOV]))
                step(dve.tensor_copy(over[:, NOV:NOV + 1], cnt[:, 9, NE - 1:NE]))
                step(dve.tensor_copy(rank[:, :, :], pr[:, 0:NT * NE].rearrange("p (t e) -> p t e", t=NT)))
                step(dve.tensor_scalar(kk[:, 1, :, :], rank[:, :, :], float(P), None, ALU.is_ge))
                for j in range(2, 8):
                    step(dve.scalar_tensor_tensor(out=kk[:, j, :, :], in0=rank[:, :, :], scalar=float(P * j), in1=kk[:, j - 1, :, :],
                                                  op0=ALU.is_ge, op1=ALU.add))
                step(dve.tensor_scalar(e32[9][:, :, :], rank[:, :, :], float(NB), None, ALU.mult))
                step(dve.scalar_tensor_tensor(out=e32[10][:, :, :], in0=kk[:, 7, :, :], scalar=float(1 - NB * P), in1=e32[9][:, :, :],
                                              op0=ALU.mult, op1=ALU.add))
                step(dve.tensor_scalar(cnt[:, 1, :], obase, float(NE - 1), None, ALU.add))
                step(dve.tensor_tensor(e32[11][:, :, :], kk[:, 1, :, :], cnt[:, 1, :].unsqueeze(1).to_broadcast(E8), ALU.mult))
                step(dve.tensor_tensor(e32[12][:, :, :], e32[10][:, :, :], e32[11][:, :, :], ALU.add))
                step(dve.tensor_tensor(e32[13][:, :, :], e32[12][:, :, :], cst[:, 0:NE].unsqueeze(1).to_broadcast(E8), ALU.add))
                step(dve.tensor_tensor(e32[9][:, :, :], e32[13][:, :, :], oh1[:, :, :], ALU.mult))
                step(dve.tensor_tensor(e32[10][:, :, :], e32[13][:, :, :], oh2[:, :, :], ALU.mult))
                step(dve.reduce_sum(posf[:, :, 0], e32[9][:, :, :], AX.X))
                step(dve.reduce_sum(posf[:, :, 1], e32[10][:, :, :], AX.X))
                dve.tensor_copy(slots[:, :, :], posf[:, :, :]).then_inc(slots_ready, 1)

            @block.gpsimd
            def _(pool):
                pool.memset(zero[:, :], 0).then_inc(tok_ready, 1)
                pool.iota(tok[:, :], pattern=[[P, NT]], base=0, channel_multiplier=1).then_inc(tok_ready, 1)
                pool.memset(blank[:, :], 0.0).then_inc(tok_ready, 1)
                pool.wait_ge(tok_ready, 3)
                pool.dma_start(tok_of_slot.rearrange("(p b) n -> p (b n)", p=P), zero[:, :]).then_inc(cleared, 16)
                pool.wait_ge(cleared, 16)
                pool.wait_ge(slots_ready, 1)
                for t in range(NT):
                    for c in range(2):
                        pool.indirect_dma_start(tok_of_slot, bass.IndirectOffsetOnAxis(ap=slots[:, t, c:c + 1], axis=0),
                                                tok[:, t:t + 1], None).then_inc(scattered, 16)
                pool.wait_ge(scattered, 16 * 2 * NT)


NW = 3


class ExpertWeights:

    def __init__(self, st, A):
        self.w_gate, self.w_up = (A[n][0].rearrange("e (k p) n -> p e k n", p=P) for n in ("w_gate", "w_up"))
        self.w_down = A["w_down"][0].rearrange("e (k p) n -> p e k n", p=P)
        self.wgu = st.sb("ex_wgu", [P, NW, 8, 2 * FF])
        self.wd = st.sb("ex_wd", [P, NW, 2, D])
        self.w_in = [st.sem(f"ex_w_in{s}") for s in range(NW)]

    def load(self, sp, e, slot):
        sp.dma_start(self.wgu[:, slot, :, 0:FF], self.w_gate[:, e]).then_inc(self.w_in[slot], 16)
        sp.dma_start(self.wgu[:, slot, :, FF:], self.w_up[:, e]).then_inc(self.w_in[slot], 16)
        sp.dma_start(self.wd[:, slot, :, :], self.w_down[:, e]).then_inc(self.w_in[slot], 16)


def experts(nc, ident, xn, A, tok_of_slot, slot_out, weights):
    out_v = slot_out.rearrange("(p b) n -> p b n", b=NB)
    wgu, wd, w_in = weights.wgu, weights.wd, weights.w_in
    with stage(nc) as st:
        idx = st.sb("ex_idx", [P, NB], U32)
        idc = st.sb("ex_idc", [P, 2], U32)
        gain = st.sb("ex_gain", [P, 8])
        xg = st.sb("ex_xg", [P, 2, D])
        xT = st.sb("ex_xT", [P, 2, 8, P])
        sg = st.sb("ex_sg", [P, 2, FF])
        hh = st.sb("ex_hh", [P, 2, FF])
        h2 = st.sb("ex_h2", [P, 2, FF])
        hTs = st.sb("ex_hT", [P, 2, 2, P])
        ob = st.sb("ex_ob", [P, 2, D])
        tp = st.ps("ex_tp", [P, D])
        gu = [st.ps(f"ex_gu{s}", [P, BANK]) for s in range(2)]
        tph = st.ps("ex_tph", [P, BANK])
        dn = st.ps("ex_dn", [P, D])
        consts_in, idx_in = st.sem("ex_consts"), st.sem("ex_idx_in")
        w_used = st.sem("ex_w_used")
        idx_ok, passed = st.sem("ex_idx_ok"), st.sem("ex_passed")
        x_in = [st.sem(f"ex_x_in{s}") for s in range(2)]
        turned, xT_ok, gu_ok, sig_ok, hh_ok, h2_ok, hturned, hT_ok, dn_ok, ob_a, ob_b = (
            st.sem("ex_" + n) for n in ("turned", "xT_ok", "gu_ok", "sig_ok", "hh_ok", "h2_ok", "hturned", "hT_ok", "dn_ok", "ob_a", "ob_b"))
        stored = [st.sem(f"ex_stored{s}") for s in range(2)]

        def steps(eng, lags, body):
            first, loops = 8, 3
            for s in range(first):
                body(s, s, True)
            with eng.Fori(0, loops) as r:
                for v in range(6):
                    body(r * 6 + (first + v), first + v, False)
            for s in range(first + 6 * loops, NE + lags):
                body(s, s, True)

        def gather(pool, b, slot):
            pool.indirect_dma_start(xg[:, slot, :], None, xn, bass.IndirectOffsetOnAxis(ap=idc[:, slot:slot + 1], axis=0)
                                    ).then_inc(x_in[slot], 16)

        with nc.Block() as block:
            @block.sync
            def _(sp):
                sp.dma_start(idx[:, :], tok_of_slot.rearrange("(p b) n -> p (b n)", p=P)).then_inc(idx_in, 16)
                sp.dma_start(gain[:, :], A["g_ffn_norm"][0].rearrange("(k p) -> p k", p=P),
                             allow_slow_non_contiguous=True).then_inc(consts_in, 16)

                def body(b, c, fixed):
                    if fixed and (c >= NE or c < NW):
                        return
                    sp.wait_ge(w_used, b - (NW - 1))
                    e = b
                    weights.load(sp, slice(e, e + 1) if fixed else bass.ds(e, 1), c % NW)
                steps(sp, 0, body)

            @block.gpsimd
            def _(pool):
                pool.wait_ge(idx_in, 16)

                def body(b, c, fixed):
                    if fixed and c >= NE:
                        return
                    if c >= 2:
                        pool.wait_ge(turned, b - 1)
                    pool.tensor_copy(idc[:, c % 2:c % 2 + 1], idx[:, bass.ds(b, 1)]).then_inc(idx_ok, 1)
                    pool.wait_ge(idx_ok, b + 1)
                    pool.sem_inc(passed, 1)
                    gather(pool, b, c % 2)
                steps(pool, 0, body)

            @block.tensor
            def _(pe):
                def body(s, c, fixed):
                    if not fixed or c < NE:
                        pe.wait_ge(x_in[c % 2], (s - c % 2) * 8 + 16)
                        if c >= 1:
                            pe.wait_ge(xT_ok, s)
                        for k in range(8):
                            mm = pe.transpose(tp[:, k * P:(k + 1) * P], xg[:, c % 2, k * P:(k + 1) * P], ident[:, :])
                        mm.then_inc(turned, 1)
                    b, c1 = s - 1, c - 1
                    if c1 >= 0 and (not fixed or c1 < NE):
                        pe.wait_ge(w_in[c1 % NW], (b - c1 % NW) * 16 + 48)
                        pe.wait_ge(xT_ok, b + 1)
                        if c1 >= 2:
                            pe.wait_ge(h2_ok, b - 1)
                        for k in range(8):
                            mm = pe.matmul(gu[c1 % 2][:, :], xT[:, c1 % 2, k, :], wgu[:, c1 % NW, k, :], start=(k == 0), stop=(k == 7))
                        mm.then_inc(gu_ok, 1)
                    b, c2 = s - 2, c - 2
                    if c2 >= 0 and (not fixed or c2 < NE):
                        pe.wait_ge(h2_ok, b + 1)
                        if c2 >= 1:
                            pe.wait_ge(hT_ok, b)
                        for k in range(2):
                            mm = pe.transpose(tph[:, k * P:(k + 1) * P], h2[:, c2 % 2, k * P:(k + 1) * P], ident[:, :])
                        mm.then_inc(hturned, 1)
                        pe.wait_ge(hT_ok, b + 1)
                        if c2 >= 1:
                            pe.wait_ge(ob_a, b)
                            pe.wait_ge(ob_b, b)
                        for n in range(2):
                            for k in range(2):
                                mm = pe.matmul(dn[:, n * BANK:(n + 1) * BANK], hTs[:, c2 % 2, k, :],
                                               wd[:, c2 % NW, k, n * BANK:(n + 1) * BANK], start=(k == 0), stop=(k == 1))
                        mm.then_inc(dn_ok, 1)
                        pe.wait_ge(dn_ok, b + 1)
                        pe.sem_inc(w_used, 1)
                steps(pe, 2, body)

            @block.scalar
            def _(act):
                def body(s, c, fixed):
                    b, c1 = s - 1, c - 1
                    if c1 >= 0 and (not fixed or c1 < NE):
                        act.wait_ge(gu_ok, b + 1)
                        act.activation(sg[:, c1 % 2, :], gu[c1 % 2][:, 0:FF], ACT.Sigmoid).then_inc(sig_ok, 1)
                    b, c2 = s - 2, c - 2
                    if c2 >= 0 and (not fixed or c2 < NE):
                        act.wait_ge(hturned, b + 1)
                        act.activation(hTs[:, c2 % 2, :, :].rearrange("p k n -> p (k n)"), tph[:, 0:2 * P], ACT.Copy).then_inc(hT_ok, 1)
                        act.wait_ge(dn_ok, b + 1)
                        if c2 >= 2:
                            act.wait_ge(stored[c2 % 2], (b - c2 % 2) * 8)
                        act.activation(ob[:, c2 % 2, 0:BANK], dn[:, 0:BANK], ACT.Copy).then_inc(ob_a, 1)
                        act.wait_ge(ob_a, b + 1)
                        act.wait_ge(ob_b, b + 1)
                        act.dma_start(out_v[:, bass.ds(b, 1), :].rearrange("p b n -> p (b n)"), ob[:, c2 % 2, :]).then_inc(stored[c2 % 2], 16)
                steps(act, 2, body)
                act.wait_ge(stored[0], 8 * NE)
                act.wait_ge(stored[1], 8 * NE)

            @block.vector
            def _(dve):
                dve.wait_ge(consts_in, 16)

                def body(s, c, fixed):
                    if not fixed or c < NE:
                        dve.wait_ge(turned, s + 1)
                        if c >= 2:
                            dve.wait_ge(gu_ok, s - 1)
                        dve.tensor_tensor(xT[:, c % 2, :, :], tp[:, :].rearrange("p (k n) -> p k n", k=8),
                                          gain[:, :].unsqueeze(2).to_broadcast([P, 8, P]), ALU.mult).then_inc(xT_ok, 1)
                    b, c1 = s - 1, c - 1
                    if c1 >= 0 and (not fixed or c1 < NE):
                        dve.wait_ge(sig_ok, b + 1)
                        dve.tensor_tensor(hh[:, c1 % 2, :], gu[c1 % 2][:, 0:FF], sg[:, c1 % 2, :], ALU.mult).then_inc(hh_ok, 1)
                        dve.wait_ge(hh_ok, b + 1)
                        if c1 >= 2:
                            dve.wait_ge(hturned, b - 1)
                        dve.tensor_tensor(h2[:, c1 % 2, :], hh[:, c1 % 2, :], gu[c1 % 2][:, FF:], ALU.mult).then_inc(h2_ok, 1)
                    b, c2 = s - 2, c - 2
                    if c2 >= 0 and (not fixed or c2 < NE):
                        dve.wait_ge(dn_ok, b + 1)
                        if c2 >= 2:
                            dve.wait_ge(stored[c2 % 2], (b - c2 % 2) * 8)
                        dve.tensor_copy(ob[:, c2 % 2, BANK:], dn[:, BANK:]).then_inc(ob_b, 1)
                steps(dve, 2, body)


def further_blocks(nc, ident, xn, A, tok_of_slot, slot_out, over):
    out_v = slot_out.rearrange("(p b) n -> p b n", b=NB)
    wg_d = A["w_gate"][0].rearrange("e (k p) n -> p e k n", p=P)
    wu_d = A["w_up"][0].rearrange("e (k p) n -> p e k n", p=P)
    wd_d = A["w_down"][0].rearrange("e (k p) n -> p e k n", p=P)
    with stage(nc) as st:
        idx = st.sb("fx_idx", [P, NB], U32)
        idc = st.sb("fx_idc", [P, 1], U32)
        gain = st.sb("fx_gain", [P, 8])
        wgu = st.sb("fx_wgu", [P, 8, 2 * FF])
        wd = st.sb("fx_wd", [P, 2, D])
        xg = st.sb("fx_xg", [P, D])
        xT = st.sb("fx_xT", [P, 8, P])
        sg, hh, h2 = (st.sb("fx_" + n, [P, FF]) for n in ("sg", "hh", "h2"))
        hTs = st.sb("fx_hT", [P, 2 * P])
        ob = st.sb("fx_ob", [P, D])
        tp, dn = st.ps("fx_tp", [P, D]), st.ps("fx_dn", [P, D])
        gu, tph = st.ps("fx_gu", [P, BANK]), st.ps("fx_tph", [P, BANK])
        consts_in, w_in, idx_ok, x_in, turned, xT_ok, gu_ok, sig_ok, hh_ok, h2_ok, hturned, hT_ok, dn_ok, ob_ok, stored = (
            st.sem("fx_" + n) for n in ("consts", "w_in", "idx_ok", "x_in", "turned", "xT_ok", "gu_ok", "sig_ok", "hh_ok",
                                        "h2_ok", "hturned", "hT_ok", "dn_ok", "ob_ok", "stored"))

        passed = st.sem("fx_passed")

        def each(eng, body):
            n = eng.value_load(over[0:1, NOV:NOV + 1], min_val=0, max_val=NOV)
            with eng.Fori(0, NOV) as j:
                with eng.If(n > j):
                    body(j)

        with nc.Block() as block:
            @block.sync
            def _(sp):
                sp.dma_start(idx[:, :], tok_of_slot.rearrange("(p b) n -> p (b n)", p=P)).then_inc(consts_in, 16)
                sp.dma_start(gain[:, :], A["g_ffn_norm"][0].rearrange("(k p) -> p k", p=P),
                             allow_slow_non_contiguous=True).then_inc(consts_in, 16)
                sp.wait_ge(consts_in, 32)
                sp.sem_inc(stored, 16)

                def body(j):
                    e = sp.value_load(over[0:1, bass.ds(j, 1)], min_val=0, max_val=NE - 1)
                    sp.wait_ge(stored, j * 16 + 16)
                    sp.dma_start(wgu[:, :, 0:FF], wg_d[:, bass.ds(e, 1)]).then_inc(w_in, 16)
                    sp.dma_start(wgu[:, :, FF:], wu_d[:, bass.ds(e, 1)]).then_inc(w_in, 16)
                    sp.dma_start(wd[:, :, :], wd_d[:, bass.ds(e, 1)]).then_inc(w_in, 16)
                    sp.wait_ge(ob_ok, j + 1)
                    sp.dma_start(out_v[:, bass.ds(j + NE, 1), :].rearrange("p b n -> p (b n)"), ob[:, :]).then_inc(stored, 16)
                    sp.wait_ge(stored, j * 16 + 32)
                    sp.sem_inc(passed, 1)
                each(sp, body)

            @block.gpsimd
            def _(pool):
                pool.wait_ge(consts_in, 32)

                def body(j):
                    pool.wait_ge(stored, j * 16 + 16)
                    pool.tensor_copy(idc[:, :], idx[:, bass.ds(j + NE, 1)]).then_inc(idx_ok, 1)
                    pool.wait_ge(idx_ok, j + 1)
                    pool.sem_inc(passed, 1)
                    pool.indirect_dma_start(xg[:, :], None, xn, bass.IndirectOffsetOnAxis(ap=idc[:, :], axis=0)).then_inc(x_in, 16)
                each(pool, body)

            @block.tensor
            def _(pe):
                def body(j):
                    pe.wait_ge(x_in, j * 16 + 16)
                    for k in range(8):
                        mm = pe.transpose(tp[:, k * P:(k + 1) * P], xg[:, k * P:(k + 1) * P], ident[:, :])
                    mm.then_inc(turned, 1)
                    pe.wait_ge(w_in, j * 48 + 48)
                    pe.wait_ge(xT_ok, j + 1)
                    for k in range(8):
                        mm = pe.matmul(gu[:, :], xT[:, k, :], wgu[:, k, :], start=(k == 0), stop=(k == 7))
                    mm.then_inc(gu_ok, 1)
                    pe.wait_ge(h2_ok, j + 1)
                    for k in range(2):
                        mm = pe.transpose(tph[:, k * P:(k + 1) * P], h2[:, k * P:(k + 1) * P], ident[:, :])
                    mm.then_inc(hturned, 1)
                    pe.wait_ge(hT_ok, j + 1)
                    for n in range(2):
                        for k in range(2):
                            mm = pe.matmul(dn[:, n * BANK:(n + 1) * BANK], hTs[:, k * P:(k + 1) * P],
                                           wd[:, k, n * BANK:(n + 1) * BANK], start=(k == 0), stop=(k == 1))
                    mm.then_inc(dn_ok, 1)
                each(pe, body)

            @block.scalar
            def _(act):
                def body(j):
                    act.wait_ge(gu_ok, j + 1)
                    act.activation(sg[:, :], gu[:, 0:FF], ACT.Sigmoid).then_inc(sig_ok, 1)
                    act.wait_ge(hturned, j + 1)
                    act.activation(hTs[:, :], tph[:, 0:2 * P], ACT.Copy).then_inc(hT_ok, 1)
                each(act, body)

            @block.vector
            def _(dve):
                dve.wait_ge(consts_in, 32)

                def body(j):
                    dve.wait_ge(turned, j + 1)
                    dve.tensor_tensor(xT[:, :, :], tp[:, :].rearrange("p (k n) -> p k n", k=8),
                                      gain[:, :].unsqueeze(2).to_broadcast([P, 8, P]), ALU.mult).then_inc(xT_ok, 1)
                    dve.wait_ge(sig_ok, j + 1)
                    dve.tensor_tensor(hh[:, :], gu[:, 0:FF], sg[:, :], ALU.mult).then_inc(hh_ok, 1)
                    dve.wait_ge(hh_ok, j + 1)
                    dve.tensor_tensor(h2[:, :], hh[:, :], gu[:, FF:], ALU.mult).then_inc(h2_ok, 1)
                    dve.wait_ge(dn_ok, j + 1)
                    dve.tensor_copy(ob[:, :], dn[:, :]).then_inc(ob_ok, 1)
                each(dve, body)


def moe(nc, A, C, scr, ident, hT):
    with ExitStack() as ctx:
        gates = ctx.enter_context(nc.sbuf_tensor("gates", [P, NT, 2], F32))
        slots = ctx.enter_context(nc.sbuf_tensor("slots", [P, NT, 2], U32))
        over = ctx.enter_context(nc.sbuf_tensor("over", [P, NOV + 1], U32))
        tok_of_slot = nc.dram_tensor("tok_of_slot", (P * NB, 1), U32, kind="Internal").ap()
        with stage(nc) as st:
            weights = ExpertWeights(st, A)
            route(nc, ident, hT, A, C, tok_of_slot, scr["slot_out"], gates, slots, over, weights)
            experts(nc, ident, scr["xn"], A, tok_of_slot, scr["slot_out"], weights)
        further_blocks(nc, ident, scr["xn"], A, tok_of_slot, scr["slot_out"], over)
        norm_rows(nc, "e0", ident, D, [(0, D, lambda t: rows(scr["x1"], t))], [(0, D)], hT=hT,
                  expert_rows=(scr["slot_out"], gates, slots), post=A["g_final"], keep=scr["x2"])


SCRATCH.update(x1=(S, D), xn=(S, D), slot_out=(P * NB, D), x2=(S, D))



RH, RDK, RDV = 4, 64, 128


def retention(nc, ident, rows_in, C, out):
    QK = 2 * RH

    def by_parity(ap, q):
        return ap.rearrange("p (j q n) -> p j q n", q=2, n=P)[:, :, q, :]

    with stage(nc) as st:
        x = st.sb("re_x", [P, 2, 1024])
        cs = st.sb("re_cs", [P, NT, 64])
        t1, t2, t3, t4 = (st.sb(f"re_t{i}", [P, 2, QK, 32]) for i in range(4))
        rot = st.sb("re_rot", [P, 2, QK, 64])
        dec = st.sb("re_dec", [P, 2, QK, 64])
        rowdec = st.sb("re_rowdec", [P, QK])
        dmat = st.sb("re_dmat", [P, RH * P])
        gch = st.sb("re_gch", [P, 2])
        qkT = st.sb("re_qkT", [P, 2, 6, P])
        sc = st.sb("re_sc", [P, 2, RH * P])
        state = st.sb("re_state", [P, 2, 2, RDV])
        ob = st.sb("re_ob", [P, 2, RH * RDV])
        tp = [st.ps(f"re_tp{i}", [P, BANK]) for i in range(2)]
        sps = [st.ps(f"re_s{i}", [P, BANK]) for i in range(2)]
        ops = [st.ps(f"re_o{i}", [P, BANK]) for i in range(2)]
        kv = st.ps("re_kv", [P, BANK])
        consts_in, m1, rotated, decayed, turned, T_ok, s_ok, sc_ok, o_ok, kv_ok, state_ok, ob_ok = (
            st.sem("re_" + n) for n in ("consts", "m1", "rotated", "decayed", "turned", "T_ok", "s_ok", "sc_ok", "o_ok", "kv_ok",
                                        "state_ok", "ob_ok"))
        x_in = [st.sem(f"re_x_in{u}") for u in range(2)]
        stored = [st.sem(f"re_stored{u}") for u in range(2)]
        with nc.Block() as block:
            @block.sync
            def _(sp):
                sp.dma_start(cs[:, :, :], C["ret_cs"].rearrange("(t p) n -> p t n", p=P)).then_inc(consts_in, 16)
                sp.dma_start(rowdec[:, :], C["ret_rowdec"]).then_inc(consts_in, 16)
                sp.dma_start(dmat[:, :], C["ret_decay"]).then_inc(consts_in, 16)
                sp.dma_start(gch[:, :], C["ret_gchunk"]).then_inc(consts_in, 16)
                for t in range(NT):
                    u = t % 2
                    if t >= 2:
                        sp.wait_ge(kv_ok, t - 1)
                        sp.wait_ge(o_ok, t - 1)
                        sp.wait_ge(m1, 4 * (t - 1))
                    sp.dma_start(x[:, u, :], rows_in[t * P:(t + 1) * P, 0:1024]).then_inc(x_in[u], 16)

            @block.gpsimd
            def _(pool):
                pool.wait_ge(consts_in, 64)
                for t in range(NT):
                    u = t % 2
                    pool.wait_ge(x_in[u], 16 * (t // 2 + 1))
                    if t >= 2:
                        pool.wait_ge(turned, t - 1)
                        pool.wait_ge(kv_ok, t - 1)
                    xv = x[:, u, 0:512].rearrange("p (h d) -> p h d", d=64)
                    c = cs[:, t, 0:32].unsqueeze(1).to_broadcast([P, QK, 32])
                    s = cs[:, t, 32:64].unsqueeze(1).to_broadcast([P, QK, 32])
                    for o, a, b in ((t1, 0, c), (t2, 1, s), (t3, 0, s), (t4, 1, c)):
                        pool.tensor_tensor(o[:, u, :, :], xv[:, :, 32 * a:32 * a + 32], b, ALU.mult).then_inc(m1, 1)
                    pool.wait_ge(m1, 4 * (t + 1))
                    pool.tensor_tensor(rot[:, u, :, 0:32], t1[:, u, :, :], t2[:, u, :, :], ALU.subtract).then_inc(rotated, 1)
                    pool.tensor_tensor(rot[:, u, :, 32:64], t3[:, u, :, :], t4[:, u, :, :], ALU.add).then_inc(rotated, 1)
                    pool.wait_ge(rotated, 2 * (t + 1))
                    pool.tensor_tensor(dec[:, u, :, :], rot[:, u, :, :], rowdec[:, :].unsqueeze(2).to_broadcast([P, QK, 64]),
                                       ALU.mult).then_inc(decayed, 1)

            @block.tensor
            def _(pe):
                for t in range(NT):
                    u = t % 2
                    pe.wait_ge(decayed, t + 1)
                    if t >= 1:
                        pe.wait_ge(T_ok, 2 * t)
                    r = rot[:, u, :, :].rearrange("p h d -> p (h d)")
                    d = dec[:, u, :, :].rearrange("p h d -> p (h d)")
                    for j in range(4):
                        pe.transpose(tp[0][:, j * P:(j + 1) * P], r[:, j * P:(j + 1) * P], ident[:, :])
                    for j in range(2):
                        mm = pe.transpose(tp[1][:, j * P:(j + 1) * P], d[:, j * P:(j + 1) * P], ident[:, :])
                    mm.then_inc(turned, 1)
                    pe.wait_ge(T_ok, 2 * (t + 1))
                    if t >= 1:
                        pe.wait_ge(sc_ok, 2 * t)
                    for h in range(RH):
                        p0, j = 64 * (h % 2), h // 2
                        mm = pe.matmul(sps[h % 2][:, j * P:(j + 1) * P], qkT[p0:p0 + 64, u, 2 + j, :], qkT[p0:p0 + 64, u, j, :],
                                       start=True, stop=True)
                    mm.then_inc(s_ok, 1)
                    if t >= 1:
                        pe.wait_ge(state_ok, 2 * t + 1)
                    for h in range(RH):
                        p0, j = 64 * (h % 2), h // 2
                        mm = pe.matmul(kv[p0:p0 + 64, j * RDV:(j + 1) * RDV], dec[:, u, RH + h, :],
                                       x[:, u, 512 + h * RDV:512 + (h + 1) * RDV], start=True, stop=True, skip_group_check=True)
                    mm.then_inc(kv_ok, 1)
                    pe.wait_ge(sc_ok, 2 * (t + 1))
                    pe.wait_ge(state_ok, 2 * t + 1)
                    if t >= 1:
                        pe.wait_ge(ob_ok, 2 * t)
                    for h in range(RH):
                        p0, j = 64 * (h % 2), h // 2
                        o = ops[h % 2][:, j * RDV:(j + 1) * RDV]
                        pe.matmul(o, sc[:, u, h * P:(h + 1) * P], x[:, u, 512 + h * RDV:512 + (h + 1) * RDV], start=True, stop=False)
                        mm = pe.matmul(o, qkT[p0:p0 + 64, u, 4 + j, :], state[p0:p0 + 64, u, j, :], start=False, stop=True)
                    mm.then_inc(o_ok, 1)

            @block.vector
            def _(dve):
                dve.memset(state[:, 0, :, :], 0.0).then_inc(state_ok, 1)
                dve.wait_ge(consts_in, 64)
                for t in range(NT):
                    u = t % 2
                    dve.wait_ge(turned, t + 1)
                    if t >= 2:
                        dve.wait_ge(o_ok, t - 1)
                    dve.tensor_copy(qkT[:, u, 0:4, :].rearrange("p j n -> p (j n)"), tp[0][:, :]).then_inc(T_ok, 1)
                    dve.tensor_copy(qkT[:, u, 4:6, :].rearrange("p j n -> p (j n)"), tp[1][:, 0:2 * P]).then_inc(T_ok, 1)
                    dve.wait_ge(s_ok, t + 1)
                    for q in range(2):
                        dve.tensor_tensor(by_parity(sc[:, u, :], q), sps[q][:, 0:2 * P].rearrange("p (j n) -> p j n", j=2),
                                          by_parity(dmat[:, :], q), ALU.mult).then_inc(sc_ok, 1)
                    dve.wait_ge(kv_ok, t + 1)
                    dve.wait_ge(state_ok, 2 * t + 1)
                    if t >= 1:
                        dve.wait_ge(o_ok, t)
                    for j in range(2):
                        dve.scalar_tensor_tensor(out=state[:, 1 - u, j, :], in0=state[:, u, j, :], scalar=gch[:, j:j + 1],
                                                 in1=kv[:, j * RDV:(j + 1) * RDV], op0=ALU.mult, op1=ALU.add).then_inc(state_ok, 1)

            @block.scalar
            def _(act):
                for t in range(NT):
                    u = t % 2
                    act.wait_ge(o_ok, t + 1)
                    if t >= 2:
                        act.wait_ge(stored[u], 16 * (t // 2))
                    for q in range(2):
                        act.activation(by_parity(ob[:, u, :], q), ops[q][:, 0:2 * P].rearrange("p (j n) -> p j n", j=2),
                                       ACT.Copy).then_inc(ob_ok, 1)
                    act.wait_ge(ob_ok, 2 * (t + 1))
                    act.dma_start(rows(out, t), ob[:, u, :]).then_inc(stored[u], 16)
                act.wait_ge(stored[0], 64)
                act.wait_ge(stored[1], 64)



def stick_breaking(nc, ident, heads, qkT_in, v_in_d, C, out):
    T8, DV = NT, 64
    total = heads * T8
    widths = [(i + 1) * P for i in range(T8)]
    with stage(nc) as st:
        qraw, kraw = (st.sb("sb_" + n, [P, 2, S]) for n in ("qraw", "kraw"))
        qs, kh, kl = (st.sb("sb_" + n, [P, 2, S], F32R) for n in ("qs", "kh", "kl"))
        v = st.sb("sb_v", [P, 2, NT, DV])
        om = st.sb("sb_om", [P, 2, S])
        be = st.sb("sb_be", [P, 4, S])
        pr = st.sb("sb_pr", [P, 2, S + 1])
        w = st.sb("sb_w", [P, 4, S])
        wT = st.sb("sb_wT", [P, 2, S])
        ones = st.sb("sb_ones", [P, S])
        masks = st.sb("sb_masks", [P, 2, P])
        o = st.sb("sb_ob", [P, 2, NT, DV])
        sps = [st.ps(f"sb_s{s}", [P, S]) for s in range(2)]
        tps = st.ps("sb_t", [P, S])
        ops = [st.ps(f"sb_op{s}", [P, BANK]) for s in range(2)]
        raw_in = [st.sem(f"sb_raw_in{s}") for s in range(2)]
        v_in = [st.sem(f"sb_v_in{s}") for s in range(2)]
        stored = [st.sem(f"sb_stored{s}") for s in range(2)]
        (consts_in, ones_ok, hi_ok, lo_ok, z_ok, om_ok, be_ok, om_masked, be_masked, pr_ok, w_ok, turned_a, turned_b,
         wT_a, wT_b, pv_done, o_done) = (
            st.sem("sb_" + n) for n in ("consts", "ones_ok", "hi_ok", "lo_ok", "z_ok", "om_ok", "be_ok", "om_masked", "be_masked",
                                        "pr_ok", "w_ok", "turned_a", "turned_b", "wT_a", "wT_b", "pv_done", "o_done"))

        passed = st.sem("sb_passed")

        def halves(i):
            return min(i + 1, BANK // P), i + 1

        with nc.Block() as block:
            @block.sync
            def _(sp):
                def load_raw(h, u):
                    for b in range(2):
                        sp.dma_start(qraw[64 * b:64 * b + 64, u, :], qkT_in[bass.ds(h * 64, 64), :]).then_inc(raw_in[u], 16)
                        sp.dma_start(kraw[64 * b:64 * b + 64, u, :], qkT_in[bass.ds(h * 64 + 512, 64), :]).then_inc(raw_in[u], 16)

                def load_v(h, u):
                    sp.dma_start(v[:, u, :, :], v_in_d[:, bass.ds(h * 64, 64)].rearrange("(t p) d -> p t d", p=P)).then_inc(v_in[u], 16)

                def store(h, u):
                    sp.wait_ge(o_done, h * T8 + T8)
                    sp.sem_inc(passed, 1)
                    sp.dma_start(out[:, bass.ds(h * DV, DV)].rearrange("(t p) d -> p t d", p=P),
                                 o[:, u, :, :]).then_inc(stored[u], 16)

                sp.sem_inc(stored[0], 16)
                sp.sem_inc(stored[1], 16)
                load_raw(0, 0)
                sp.dma_start(masks[:, :, :], C["strict"]).then_inc(consts_in, 16)
                load_v(0, 0)
                load_raw(1, 1)
                load_v(1, 1)
                with sp.Fori(0, heads // 2 - 1) as r:
                    for u in range(2):
                        h = r * 2 + u
                        sp.wait_ge(lo_ok, h * 8 + 8)
                        sp.sem_inc(passed, 1)
                        load_raw(h + 2, u)
                        store(h, u)
                        sp.wait_ge(pv_done, h * T8 + T8)
                        sp.sem_inc(passed, 1)
                        load_v(h + 2, u)
                for u in range(2):
                    store(heads - 2 + u, u)
                for u in range(2):
                    sp.wait_ge(stored[u], 16 * (heads // 2 + 1))

            @block.tensor
            def _(pe):
                def body(l, T):
                    if active(T, 0, total):
                        u, i = l // T8, l % T8
                        if i == 0:
                            pe.wait_ge(lo_ok, T + 8)
                        reached(pe, be_ok, T - 1)
                        for c0 in range(0, widths[i], BANK):
                            cc = slice(c0, min(widths[i], c0 + BANK))
                            pe.matmul(sps[l % 2][:, cc], qs[:, u, i * P:(i + 1) * P], kh[:, u, cc], start=True, stop=False)
                            mm = pe.matmul(sps[l % 2][:, cc], qs[:, u, i * P:(i + 1) * P], kl[:, u, cc], start=False, stop=True)
                        mm.then_inc(z_ok, 1)
                    if active(T, 3, total):
                        m = (l - 3) % TURN
                        a, b = halves(m % T8)
                        reached(pe, w_ok, T - 2)
                        reached(pe, wT_a, T - 3)
                        reached(pe, wT_b, T - 3)
                        for k in range(b):
                            mm = pe.transpose(tps[:, k * P:(k + 1) * P], w[:, m % 4, k * P:(k + 1) * P], ident[:, :])
                            if k == a - 1 and b > a:
                                mm.then_inc(turned_a, 1)
                        if b > a:
                            mm.then_inc(turned_b, 1)
                        else:
                            mm.then_inc(turned_a, 1)
                            pe.wait_ge(turned_a, T - 2)
                            pe.sem_inc(turned_b, 1)
                    if active(T, 4, total):
                        m = (l - 4) % TURN
                        u, i = m // T8, m % T8
                        if i == 0:
                            pe.wait_ge(v_in[u], T - 4 - 8 * u + 16)
                        reached(pe, o_done, T - 5)
                        reached(pe, wT_a, T - 3)
                        reached(pe, wT_b, T - 3)
                        for k in range(i + 1):
                            mm = pe.matmul(ops[m % 2][:, 0:DV], wT[:, m % 2, k * P:(k + 1) * P], v[:, u, k, :],
                                           start=(k == 0), stop=(k == i))
                        mm.then_inc(pv_done, 1)
                tiles(pe, total, 8, 4, body)

            @block.scalar
            def _(act):
                def split_hi(u, n_in):
                    act.wait_ge(raw_in[u], n_in)
                    act.activation(qs[:, u, :], qraw[:, u, :], ACT.Copy).then_inc(hi_ok, 4)
                    act.activation(kh[:, u, :], kraw[:, u, :], ACT.Copy).then_inc(hi_ok, 4)

                split_hi(0, 64)

                def body(l, T):
                    if active(T, 0, total):
                        n = widths[l % T8]
                        act.wait_ge(z_ok, T + 1)
                        reached(act, pr_ok, T - 1)
                        act.activation(om[:, l % 2, 0:n], sps[l % 2][:, 0:n], ACT.Sigmoid, scale=-0.125).then_inc(om_ok, 1)
                    if active(T, 3, total):
                        m = (l - 3) % TURN
                        a, b = halves(m % T8)
                        reached(act, turned_b, T - 2)
                        if b > a:
                            reached(act, pv_done, T - 4)
                            act.activation(wT[:, m % 2, a * P:b * P], tps[:, a * P:b * P], ACT.Copy).then_inc(wT_b, 1)
                        else:
                            act.sem_inc(wT_b, 1)
                    if active(T, 0, total):
                        n = widths[l % T8]
                        reached(act, w_ok, T - 3)
                        act.activation(be[:, l % 4, 0:n], sps[l % 2][:, 0:n], ACT.Sigmoid, scale=0.125).then_inc(be_ok, 1)
                        if l % T8 == 3 and active(T + 5, 0, total):
                            u = 1 - l // T8
                            split_hi(u, (T + 5 - 8 * u) * 4 + 64)
                tiles(act, total, 8, 4, body)

            @block.vector
            def _(dve):
                def split_lo(u, n_hi):
                    dve.wait_ge(hi_ok, n_hi)
                    dve.tensor_tensor(qs[64:P, u, :], qraw[64:P, u, :], qs[64:P, u, :].bitcast(F32), ALU.subtract).then_inc(lo_ok, 4)
                    dve.tensor_tensor(kl[:, u, :], kraw[:, u, :], kh[:, u, :].bitcast(F32), ALU.subtract).then_inc(lo_ok, 4)

                dve.memset(ones[:, :], 1.0).then_inc(ones_ok, 1)
                dve.memset(pr[:, :, S:S + 1], 1.0).then_inc(ones_ok, 1)
                split_lo(0, 8)
                dve.wait_ge(ones_ok, 2)
                dve.wait_ge(consts_in, 16)

                def body(l, T):
                    if active(T, 3, total):
                        m = (l - 3) % TURN
                        a, _ = halves(m % T8)
                        reached(dve, turned_a, T - 2)
                        reached(dve, pv_done, T - 4)
                        dve.tensor_copy(wT[:, m % 2, 0:a * P], tps[:, 0:a * P]).then_inc(wT_a, 1)
                    if active(T, 0, total):
                        n = widths[l % T8]
                        dve.wait_ge(om_ok, T + 1)
                        d = om[:, l % 2, n - P:n]
                        dve.tensor_tensor(d, d, masks[:, 1, :], ALU.max).then_inc(om_masked, 1)
                        dve.wait_ge(om_masked, T + 1)
                        reached(dve, w_ok, T - 1)
                        dve.tensor_tensor_scan(pr[:, l % 2, S - n:S][:, ::-1], om[:, l % 2, 0:n][:, ::-1], ones[:, 0:n], 1.0,
                                               ALU.mult, ALU.mult).then_inc(pr_ok, 1)
                        dve.wait_ge(be_ok, T + 1)
                        d = be[:, l % 4, n - P:n]
                        dve.tensor_tensor(d, d, masks[:, 0, :], ALU.mult).then_inc(be_masked, 1)
                        if l % T8 == 4 and active(T + 4, 0, total):
                            split_lo(1 - l // T8, T + 4 + 8)
                    if active(T, 4, total):
                        m = (l - 4) % TURN
                        u, i = m // T8, m % T8
                        reached(dve, pv_done, T - 3)
                        if i == 0:
                            dve.wait_ge(stored[u], T - 4 - 8 * u + 16)
                        dve.tensor_copy(o[:, u, i, :], ops[m % 2][:, 0:DV]).then_inc(o_done, 1)
                tiles(dve, total, 8, 4, body)

            @block.gpsimd
            def _(pool):
                def body(l, T):
                    if active(T, 0, total):
                        n = widths[l % T8]
                        pool.wait_ge(be_masked, T + 1)
                        pool.wait_ge(pr_ok, T + 1)
                        reached(pool, turned_b, T - 3)
                        pool.tensor_tensor(w[:, l % 4, 0:n], be[:, l % 4, 0:n], pr[:, l % 2, S - n + 1:S + 1],
                                           ALU.mult).then_inc(w_ok, 1)
                tiles(pool, total, 8, 0, body)



HH = 4
LEVELS = [64, 32, 16, 8, 4, 2, 1]


def hgrn2(nc, ident, fT_in, v_in, C, out):
    NL = len(LEVELS)
    UC = NT // 2
    U = UC * P
    NU = HH * 2
    NG_ = HH * NT
    LEVELS_OF = ((0,), (1, 2), (3, 4), (5, 6))
    with stage(nc) as st:
        q = st.sb("hg_q", [P, 2, S])
        f = st.sb("hg_f", [P, 2, S])
        vv = st.sb("hg_v", [P, 2, NT, P])
        kk = st.sb("hg_k", [P, 4, U])
        az, ez, ln, lf, b, dl, el = (st.sb("hg_" + n, [P, U]) for n in ("az", "ez", "ln", "lf", "b", "dl", "el"))
        df, ex, eb, qb, kb = (st.sb("hg_" + n, [P, 2, U]) for n in ("df", "ex", "eb", "qb", "kb"))
        qk = st.sb("hg_qk", [P, 2, NL, U])
        ones = st.sb("hg_ones", [P, P])
        mask = st.sb("hg_mask", [P, NL + 1, P])
        ms = st.sb("hg_ms", [P, 2, NL + 1, P])
        sT = st.sb("hg_sT", [P, 2, P])
        kr = st.sb("hg_kr", [P, 2, P])
        state = st.sb("hg_state", [P, 2, P])
        ob = st.sb("hg_ob", [P, 2, NT, P])
        sps = [st.ps(f"hg_s{i}", [P, 2 * BANK]) for i in range(2)]
        tps, ops, kvs = st.ps("hg_t", [P, BANK]), st.ps("hg_o", [P, BANK]), st.ps("hg_kv", [P, BANK])
        f_in = [st.sem(f"hg_f_in{u}") for u in range(2)]
        qv_in = [st.sem(f"hg_qv_in{u}") for u in range(2)]
        stored = [st.sem(f"hg_stored{u}") for u in range(2)]
        (consts_in, ones_ok, k_ok, az_ok, ez_ok, ln_ok, lf_ok, b_ok, df_ok, ex_ok, qk_ok, dl_ok, eb_ok, el_ok, qb_ok, kb_ok,
         s_ok, ms_ok, sT_ok, turned, kr_ok, o_ok, kv_ok, state_ok, ob_ok, state0) = (
            st.sem("hg_" + n) for n in ("consts", "ones_ok", "k_ok", "az_ok", "ez_ok", "ln_ok", "lf_ok", "b_ok", "df_ok", "ex_ok",
                                        "qk_ok", "dl_ok", "eb_ok", "el_ok", "qb_ok", "kb_ok", "s_ok", "ms_ok", "sT_ok", "turned",
                                        "kr_ok", "o_ok", "kv_ok", "state_ok", "ob_ok", "state0"))

        def split(x, m):
            return x.rearrange("p (n h m) -> p n h m", h=2, m=m)

        def of_unit(buf, n):
            return buf[:, (n // 2) % 2, (n % 2) * U:(n % 2 + 1) * U]

        def chunk(G):
            return G // UC, G // NT, G % NT, slice(G % UC * P, (G % UC + 1) * P)

        def schedule(step, prep):
            for part in range(4):
                prep(0, part)
            prep(1, 0)
            for G in range(NG_ + 1):
                step(G)
                n, part = (G + 1) // UC + 1, (G + 1) % UC
                if G + 1 >= 1 and n < NU:
                    prep(n, part)

        with nc.Block() as block:
            @block.sync
            def _(sp):
                def load_f(h):
                    u = h % 2
                    if h >= 2:
                        sp.wait_ge(lf_ok, 2 * (h - 1))
                        sp.wait_ge(k_ok, 2 * (h - 1))
                    sp.dma_start(f[:, u, :], fT_in[512 + h * P:512 + (h + 1) * P, :]).then_inc(f_in[u], 16)

                def load_qv(h):
                    u = h % 2
                    if h >= 2:
                        sp.wait_ge(o_ok, NT * (h - 1))
                        sp.wait_ge(kv_ok, NT * (h - 1))
                        sp.wait_ge(qb_ok, 2 * (h - 1))
                    sp.dma_start(q[:, u, :], fT_in[h * P:(h + 1) * P, :]).then_inc(qv_in[u], 16)
                    sp.dma_start(vv[:, u, :, :], v_in[:, h * P:(h + 1) * P].rearrange("(t p) d -> p t d", p=P)).then_inc(qv_in[u], 16)

                load_f(0)
                load_qv(0)
                sp.dma_start(mask[:, :, :], C["levels"]).then_inc(consts_in, 16)
                load_f(1)
                load_qv(1)
                for h in range(HH):
                    if h + 2 < HH:
                        load_f(h + 2)
                        load_qv(h + 2)
                    sp.wait_ge(ob_ok, NT * (h + 1))
                    sp.dma_start(out[:, h * P:(h + 1) * P].rearrange("(t p) d -> p t d", p=P), ob[:, h % 2, :, :]).then_inc(stored[h % 2], 16)
                sp.wait_ge(stored[0], 32)
                sp.wait_ge(stored[1], 32)

            @block.scalar
            def _(act):
                def logs(n):
                    h = n // 2
                    act.wait_ge(f_in[h % 2], 16 * (h // 2 + 1))
                    if n >= 4:
                        act.wait_ge(s_ok, UC * (n - 3))
                        act.wait_ge(qk_ok, 2 * NL * (n - 3))
                        act.wait_ge(kb_ok, n - 3)
                    act.activation(kk[:, n % 4, :], of_unit(f, n), ACT.Sigmoid, scale=-1.0).then_inc(k_ok, 1)
                    act.activation(az[:, :], of_unit(f, n), ACT.Abs).then_inc(az_ok, 1)
                    act.wait_ge(az_ok, n + 1)
                    act.activation(ez[:, :], az[:, :], ACT.Exp, scale=-1.0).then_inc(ez_ok, 1)
                    act.wait_ge(ez_ok, n + 1)
                    if n >= 1:
                        act.wait_ge(lf_ok, n)
                    act.activation(ln[:, :], ez[:, :], ACT.Ln, bias=1.0).then_inc(ln_ok, 1)

                def prep(n, part):
                    for l in LEVELS_OF[part]:
                        g = n * NL + l
                        act.wait_ge(df_ok, 2 * (g + 1))
                        if g >= 2:
                            act.wait_ge(qk_ok, 2 * (g - 1))
                        act.activation(ex[:, g % 2, :], df[:, g % 2, :], ACT.Exp).then_inc(ex_ok, 1)
                    if part == 3:
                        act.wait_ge(b_ok, UC * (n + 1))
                        if n >= 2:
                            act.wait_ge(state_ok, UC * (n - 1))
                            act.wait_ge(qb_ok, n - 1)
                        act.activation(eb[:, n % 2, :], b[:, :], ACT.Exp).then_inc(eb_ok, 1)
                        act.wait_ge(dl_ok, n + 1)
                        if n >= 1:
                            act.wait_ge(kb_ok, n)
                        act.activation(el[:, :], dl[:, :], ACT.Exp).then_inc(el_ok, 1)

                def step(G):
                    if G < NG_:
                        act.wait_ge(turned, G + 1)
                        if G >= 2:
                            act.wait_ge(kv_ok, G - 1)
                        act.activation(kr[:, G % 2, :], tps[:, 0:P], ACT.Copy).then_inc(kr_ok, 1)
                    if G >= 1:
                        _, h, c, _ = chunk(G - 1)
                        if c == 0 and h >= 2:
                            act.wait_ge(stored[h % 2], 16 * (h // 2))
                        act.wait_ge(o_ok, G)
                        act.activation(ob[:, h % 2, c, :], ops[:, 0:P], ACT.Copy).then_inc(ob_ok, 1)
                    if (G + 2) % UC == 0 and (G + 2) // UC + 1 < NU:
                        logs((G + 2) // UC + 1)

                logs(0)
                logs(1)
                schedule(step, prep)

            @block.gpsimd
            def _(pool):
                def prep(n, part):
                    if part == 0:
                        pool.wait_ge(qv_in[n // 2 % 2], 32 * (n // 4 + 1))
                        pool.wait_ge(k_ok, n + 1)
                        if n >= 2:
                            pool.wait_ge(s_ok, UC * (n - 1))
                    for l in LEVELS_OF[part]:
                        g, m = n * NL + l, LEVELS[l]
                        pool.wait_ge(ex_ok, g + 1)
                        for half, src in enumerate((kk[:, n % 4, :], of_unit(q, n))):
                            pool.tensor_tensor(split(qk[:, n % 2, l, :], m)[:, :, half, :], split(src, m)[:, :, half, :],
                                               split(ex[:, g % 2, :], m)[:, :, half, :], ALU.mult).then_inc(qk_ok, 1)
                    if part == 3:
                        if n >= 2:
                            pool.wait_ge(o_ok, UC * (n - 1))
                            pool.wait_ge(turned, UC * (n - 1))
                        pool.wait_ge(eb_ok, n + 1)
                        pool.tensor_tensor(qb[:, n % 2, :], of_unit(q, n), eb[:, n % 2, :], ALU.mult).then_inc(qb_ok, 1)
                        pool.wait_ge(el_ok, n + 1)
                        pool.tensor_tensor(kb[:, n % 2, :], kk[:, n % 4, :], el[:, :], ALU.mult).then_inc(kb_ok, 1)

                schedule(lambda G: None, prep)

            @block.vector
            def _(dve):
                dve.memset(ones[:, :], 1.0).then_inc(ones_ok, 1)
                dve.wait_ge(ones_ok, 1)

                def prep(n, part):
                    if part == 0:
                        dve.wait_ge(ln_ok, n + 1)
                        dve.scalar_tensor_tensor(out=lf[:, :], in0=of_unit(f, n), scalar=0.0, in1=ln[:, :], op0=ALU.min,
                                                 op1=ALU.subtract).then_inc(lf_ok, 1)
                        dve.wait_ge(lf_ok, n + 1)
                        if n >= 1:
                            dve.wait_ge(eb_ok, n)
                        for c in range(UC):
                            cc = slice(c * P, (c + 1) * P)
                            dve.tensor_tensor_scan(b[:, cc], ones[:, :], lf[:, cc], 0.0, ALU.mult, ALU.add).then_inc(b_ok, 1)
                        dve.wait_ge(b_ok, UC * (n + 1))
                    for l in LEVELS_OF[part]:
                        g, m = n * NL + l, LEVELS[l]
                        if g >= 2:
                            dve.wait_ge(ex_ok, g - 1)
                        bv, dv = split(b[:, :], m), split(df[:, g % 2, :], m)
                        mid = bv[:, :, 0, m - 1:m].to_broadcast([P, U // (2 * m), m])
                        dve.tensor_tensor(dv[:, :, 0, :], mid, bv[:, :, 0, :], ALU.subtract).then_inc(df_ok, 1)
                        dve.tensor_tensor(dv[:, :, 1, :], bv[:, :, 1, :], mid, ALU.subtract).then_inc(df_ok, 1)
                    if part == 3:
                        bc = b[:, :].rearrange("p (n m) -> p n m", m=P)
                        if n >= 1:
                            dve.wait_ge(el_ok, n)
                        dve.tensor_tensor(dl[:, :].rearrange("p (n m) -> p n m", m=P), bc[:, :, P - 1:P].to_broadcast([P, UC, P]), bc,
                                          ALU.subtract).then_inc(dl_ok, 1)

                def step(G):
                    if G == 0:
                        dve.wait_ge(consts_in, 16)
                    if G < NG_:
                        dve.wait_ge(s_ok, G + 1)
                        dve.tensor_tensor(ms[:, G % 2, :, :].rearrange("p l n -> p (l n)"), sps[G % 2][:, :],
                                          mask[:, :, :].rearrange("p l n -> p (l n)"), ALU.mult).then_inc(ms_ok, 1)
                        dve.wait_ge(ms_ok, G + 1)
                        if G >= 2:
                            dve.wait_ge(o_ok, G - 1)
                        dve.reduce_sum(sT[:, G % 2, :], ms[:, G % 2, :, :].rearrange("p l n -> p n l"), AX.X).then_inc(sT_ok, 1)
                    if G >= 1:
                        n, h, c, cc = chunk(G - 1)
                        dve.wait_ge(kv_ok, G)
                        if c == 0:
                            dve.wait_ge(state0, h + 1)
                        if G >= 2:
                            dve.wait_ge(state_ok, G - 1)
                            dve.wait_ge(o_ok, G - 1)
                        dve.wait_ge(eb_ok, n + 1)
                        dve.scalar_tensor_tensor(out=state[:, (c + 1) % 2, :], in0=state[:, c % 2, :],
                                                 scalar=eb[:, n % 2, cc.stop - 1:cc.stop], in1=kvs[:, 0:P],
                                                 op0=ALU.mult, op1=ALU.add).then_inc(state_ok, 1)
                    if G % NT == 0 and G < NG_:
                        if G:
                            dve.wait_ge(state_ok, G)
                        dve.memset(state[:, 0, :], 0.0).then_inc(state0, 1)

                schedule(step, prep)

            @block.tensor
            def _(pe):
                for G in range(NG_ + 1):
                    if G < NG_:
                        n, h, c, cc = chunk(G)
                        if G % UC == 0:
                            pe.wait_ge(qk_ok, 2 * NL * (n + 1))
                            pe.wait_ge(kb_ok, n + 1)
                            pe.wait_ge(qb_ok, n + 1)
                        if G >= 2:
                            pe.wait_ge(ms_ok, G - 1)
                        for l in range(NL):
                            pe.matmul(sps[G % 2][:, l * P:(l + 1) * P], qk[:, n % 2, l, cc], qk[:, n % 2, l, cc], start=True, stop=True)
                        pe.matmul(sps[G % 2][:, NL * P:(NL + 1) * P], kk[:, n % 4, cc], q[:, h % 2, c * P:(c + 1) * P],
                                  start=True, stop=True).then_inc(s_ok, 1)
                        if G >= 1:
                            pe.wait_ge(kr_ok, G)
                        pe.transpose(tps[:, 0:P], kb[:, n % 2, cc], ident[:, :]).then_inc(turned, 1)
                    if G >= 1:
                        n, h, c, cc = chunk(G - 1)
                        pe.wait_ge(kr_ok, G)
                        if G >= 2:
                            pe.wait_ge(state_ok, G - 1)
                        pe.matmul(kvs[:, 0:P], kr[:, (G - 1) % 2, :], vv[:, h % 2, c, :], start=True, stop=True).then_inc(kv_ok, 1)
                        pe.wait_ge(sT_ok, G)
                        if c == 0:
                            pe.wait_ge(state0, h + 1)
                        if G >= 2:
                            pe.wait_ge(ob_ok, G - 1)
                        pe.matmul(ops[:, 0:P], sT[:, (G - 1) % 2, :], vv[:, h % 2, c, :], start=True, stop=False)
                        pe.matmul(ops[:, 0:P], qb[:, n % 2, cc], state[:, c % 2, :], start=False, stop=True).then_inc(o_ok, 1)



def rg_lru(nc, xT_in, A, hT):
    NTI = 4
    with stage(nc) as st:
        x = st.sb("lr_x", [P, 2, S + 4])
        gt = st.sb("lr_gt", [P, 2, S])
        cv = st.sb("lr_cv", [P, S])
        wa, wx = st.sb("lr_wa", [P, NTI, P]), st.sb("lr_wx", [P, NTI, P])
        cw, cb = st.sb("lr_cw", [P, NTI, 4]), st.sb("lr_cb", [P, NTI])
        ba, bx, lam = st.sb("lr_ba", [P, NTI]), st.sb("lr_bx", [P, NTI]), st.sb("lr_lam", [P, NTI])
        sm = [st.sb(f"lr_sm{i}", [P, NTI]) for i in range(13)]
        xc, r, ig, a, sg = (st.sb("lr_" + n, [P, NTI, S]) for n in ("xc", "r", "ig", "a", "sg"))
        a2, u2, hs = (st.sb("lr_" + n, [P, S]) for n in ("a2", "u2", "hs"))
        hg = st.sb("lr_hg", [P, 2, S])
        pa, px = st.ps("lr_pa", [P, S]), st.ps("lr_px", [P, S])
        consts_in, cleared, e_ok, d, conv, mm, r_ok, ig_ok, u1_ok, c8_ok, a_ok, th_ok, m2_ok, mu_ok, sg_ok, gs_ok, pads = (
            st.sem("lr_" + n) for n in ("consts", "cleared", "e_ok", "step", "conv", "mm", "r_ok", "ig_ok", "u1_ok", "c8_ok", "a_ok",
                                        "th_ok", "m2_ok", "mu_ok", "sg_ok", "gs_ok", "pads"))
        wab_in, hg_ok, hi_ok, lo_ok = (st.sem("lr_" + n) for n in ("wab_in", "hg_ok", "hi_ok", "lo_ok"))
        x_in = [st.sem(f"lr_x_in{u}") for u in range(2)]
        g_in = [st.sem(f"lr_g_in{u}") for u in range(2)]
        with nc.Block() as block:
            @block.sync
            def _(sp):
                slow = dict(allow_slow_non_contiguous=True)
                sp.wait_ge(pads, 1)

                def load(t):
                    if t >= 2:
                        sp.wait_ge(conv, 4 * (t - 1))
                        sp.wait_ge(gs_ok, t - 1)
                    sp.dma_start(x[:, t % 2, 4:S + 4], xT_in[t * P:(t + 1) * P, :]).then_inc(x_in[t % 2], 16)
                    sp.dma_start(gt[:, t % 2, :], xT_in[512 + t * P:512 + (t + 1) * P, :]).then_inc(g_in[t % 2], 16)

                load(0)
                for j in range(4):
                    sp.dma_start(cw[:, :, j], A["conv_w_2"][0, j, :].rearrange("(t p) -> p t", p=P), **slow).then_inc(consts_in, 16)
                for dst, name in ((cb, "conv_b_2"), (ba, "lru_b_a_2"), (bx, "lru_b_x_2"), (lam, "lru_lambda_2")):
                    sp.dma_start(dst[:, :], A[name][0].rearrange("(t p) -> p t", p=P), **slow).then_inc(consts_in, 16)
                sp.wait_ge(cleared, 2)
                for dst, name in ((wa, "lru_w_a_2"), (wx, "lru_w_x_2")):
                    for b in range(2):
                        sp.dma_start(dst[64 * b:64 * b + 64, :, 64 * b:64 * b + 64],
                                     A[name][0].rearrange("(t b) i j -> b i t j", b=2)[b]).then_inc(wab_in, 16)
                for t in range(1, NTI):
                    load(t)

            @block.gpsimd
            def _(pool):
                pool.memset(wa[:, :, :], 0.0).then_inc(cleared, 1)
                pool.memset(wx[:, :, :], 0.0).then_inc(cleared, 1)
                for t in range(NTI):
                    pool.wait_ge(sg_ok, t + 1)
                    pool.tensor_tensor(sg[:, t, :], gt[:, t % 2, :], sg[:, t, :], ALU.mult).then_inc(gs_ok, 1)
                for t in range(NTI):
                    pool.wait_ge(hi_ok, t + 1)
                    pool.tensor_tensor(hT[:, LO, 4 + t, :], hg[:, t % 2, :], hT[:, HI, 4 + t, :].bitcast(F32),
                                       ALU.subtract).then_inc(lo_ok, 1)

            @block.tensor
            def _(pe):
                pe.wait_ge(wab_in, 16 * 4)
                for t in range(NTI):
                    pe.wait_ge(conv, 4 * (t + 1))
                    if t >= 1:
                        pe.wait_ge(ig_ok, t)
                        pe.wait_ge(r_ok, t)
                    for dst, w in ((pa, wa), (px, wx)):
                        for n in range(2):
                            m = pe.matmul(dst[:, n * BANK:(n + 1) * BANK], w[:, t, :], xc[:, t, n * BANK:(n + 1) * BANK],
                                          start=True, stop=True)
                    m.then_inc(mm, 1)

            @block.scalar
            def _(act):
                act.wait_ge(consts_in, 16 * 8)
                for t in range(NTI):
                    act.wait_ge(g_in[t % 2], 16 * (t // 2 + 1))
                    act.activation(sg[:, t, :], gt[:, t % 2, :], ACT.Sigmoid).then_inc(sg_ok, 1)
                    act.wait_ge(mm, t + 1)
                    act.activation(r[:, t, :], pa[:, :], ACT.Sigmoid, bias=ba[:, t:t + 1]).then_inc(r_ok, 1)
                    act.activation(ig[:, t, :], px[:, :], ACT.Sigmoid, bias=bx[:, t:t + 1]).then_inc(ig_ok, 1)
                act.wait_ge(e_ok, 1)
                act.activation(sm[1][:, :], sm[0][:, :], ACT.Exp, scale=-1.0).then_inc(e_ok, 1)
                act.wait_ge(r_ok, NTI)
                act.wait_ge(c8_ok, 1)
                for t in range(NTI):
                    act.activation(a[:, t, :], r[:, t, :], ACT.Exp, scale=sm[12][:, t:t + 1]).then_inc(a_ok, 1)
                for t in range(NTI):
                    act.wait_ge(u1_ok, t + 1)
                    act.activation(xc[:, t, :], r[:, t, :], ACT.Tanh, scale=sm[11][:, t:t + 1]).then_inc(th_ok, 1)
                for t in range(NTI):
                    act.wait_ge(m2_ok, t + 1)
                    act.activation(xc[:, t, :], xc[:, t, :], ACT.Sqrt).then_inc(mu_ok, 1)
                for t in range(NTI):
                    act.wait_ge(hg_ok, t + 1)
                    act.activation(hT[:, HI, 4 + t, :], hg[:, t % 2, :], ACT.Copy).then_inc(hi_ok, 1)

            @block.vector
            def _(dve):
                n = [0]

                def step(ins):
                    n[0] += 1
                    ins.then_inc(d, 1)
                    dve.wait_ge(d, n[0])

                dve.memset(x[:, :, 0:4], 0.0).then_inc(pads, 1)
                dve.wait_ge(consts_in, 16 * 8)
                step(dve.scalar_tensor_tensor(out=sm[0][:, :], in0=lam[:, :], scalar=-1.0, in1=lam[:, :], op0=ALU.mult, op1=ALU.max))
                dve.sem_inc(e_ok, 1)
                for t in range(NTI):
                    u = t % 2
                    dve.wait_ge(x_in[u], 16 * (t // 2 + 1))
                    dve.wait_ge(pads, 1)
                    if t >= 1:
                        dve.wait_ge(conv, 4 * t)
                    src = [x[:, u, 1 + j:1 + j + S] for j in range(4)]
                    dve.tensor_scalar(cv[:, :], src[0], cw[:, t, 0:1], cb[:, t:t + 1], ALU.mult, ALU.add).then_inc(conv, 1)
                    for j, (o, i) in enumerate(((xc[:, t, :], cv[:, :]), (cv[:, :], xc[:, t, :]), (xc[:, t, :], cv[:, :])), 1):
                        dve.wait_ge(conv, 4 * t + j)
                        dve.scalar_tensor_tensor(out=o, in0=src[j], scalar=cw[:, t, j:j + 1], in1=i,
                                                 op0=ALU.mult, op1=ALU.add).then_inc(conv, 1)
                    if t >= 1:
                        dve.wait_ge(ig_ok, t)
                        dve.tensor_tensor(ig[:, t - 1, :], ig[:, t - 1, :], xc[:, t - 1, :], ALU.mult).then_inc(u1_ok, 1)
                dve.wait_ge(e_ok, 2)
                step(dve.tensor_scalar(sm[2][:, :], sm[1][:, :], 2.0, None, ALU.add))
                step(dve.reciprocal(sm[3][:, :], sm[2][:, :]))
                step(dve.tensor_tensor(sm[4][:, :], sm[1][:, :], sm[3][:, :], ALU.mult))
                step(dve.tensor_tensor(sm[5][:, :], sm[4][:, :], sm[4][:, :], ALU.mult))
                step(dve.tensor_scalar(sm[6][:, :], sm[5][:, :], 1.0 / 17, 1.0 / 15, ALU.mult, ALU.add))
                for k in (13, 11, 9, 7, 5, 3, 1):
                    step(dve.tensor_tensor(sm[7][:, :], sm[6][:, :], sm[5][:, :], ALU.mult))
                    step(dve.tensor_scalar(sm[6][:, :], sm[7][:, :], 1.0 / k, None, ALU.add))
                step(dve.tensor_tensor(sm[8][:, :], sm[6][:, :], sm[4][:, :], ALU.mult))
                step(dve.tensor_scalar(sm[9][:, :], lam[:, :], -1.0, 0.0, ALU.mult, ALU.max))
                step(dve.scalar_tensor_tensor(out=sm[10][:, :], in0=sm[8][:, :], scalar=2.0, in1=sm[9][:, :], op0=ALU.mult, op1=ALU.add))
                step(dve.tensor_scalar(sm[11][:, :], sm[10][:, :], 8.0, None, ALU.mult))
                step(dve.tensor_scalar(sm[12][:, :], sm[10][:, :], -8.0, None, ALU.mult))
                dve.sem_inc(c8_ok, 1)
                dve.wait_ge(ig_ok, NTI)
                dve.wait_ge(conv, 4 * NTI)
                dve.tensor_tensor(ig[:, NTI - 1, :], ig[:, NTI - 1, :], xc[:, NTI - 1, :], ALU.mult).then_inc(u1_ok, 1)
                for t in range(NTI):
                    dve.wait_ge(a_ok, t + 1)
                    if t >= 1:
                        dve.wait_ge(m2_ok, t)
                    step(dve.tensor_tensor(a2[:, :], a[:, t, :], a[:, t, :], ALU.mult))
                    dve.wait_ge(th_ok, t + 1)
                    dve.scalar_tensor_tensor(out=xc[:, t, :], in0=a2[:, :], scalar=1.0, in1=xc[:, t, :], op0=ALU.add,
                                             op1=ALU.mult).then_inc(m2_ok, 1)
                dve.wait_ge(u1_ok, NTI)
                for t in range(NTI):
                    dve.wait_ge(mu_ok, t + 1)
                    step(dve.memset(xc[:, t, 0:1], 1.0))
                    step(dve.tensor_tensor(u2[:, :], xc[:, t, :], ig[:, t, :], ALU.mult))
                    if t >= 1:
                        dve.wait_ge(hg_ok, t)
                    step(dve.tensor_tensor_scan(hs[:, :], a[:, t, :], u2[:, :], 0.0, ALU.mult, ALU.add))
                    dve.wait_ge(gs_ok, t + 1)
                    if t >= 2:
                        dve.wait_ge(lo_ok, t - 1)
                    dve.tensor_tensor(hg[:, t % 2, :], hs[:, :], sg[:, t, :], ALU.mult).then_inc(hg_ok, 1)


def second(nc, A, C, scr, ident, hT, out):
    we = A["even_w_in_2"][0]
    row_chunk = lambda w, c, dst, c0: dict(kind="row", width=512, load=columns(w, c, 512), dst=to_rows(dst, c0, 512))
    T_chunk = lambda w, c, dst, r0: dict(kind="T", width=512, load=columns(w, c, 512), dst=to_T(dst, r0, 512))
    project(nc, "pe", hT, 8, [row_chunk(we, c, scr["erows"], c) for c in (0, 512, 1024)] +
            [T_chunk(we, 1536 + c, scr["sqkT"], c) for c in (0, 512)] +
            [row_chunk(we, 2560 + c, scr["srows"], c) for c in (0, 512)], gain=[(0, A["pre_norm_w_2"][0])])
    retention(nc, ident, scr["erows"], C, scr["ret"])
    stick_breaking(nc, ident, 8, scr["sqkT"], scr["srows"], C, scr["stick"])
    mix_out(nc, "em", ident, hT, A["even_w_out_2"][0], None,
            dict(width=D, loads=[(0, 512, lambda t: rows(scr["ret"], t)), (512, 512, lambda t: rows(scr["stick"], t))],
                 groups=[(128 * h, 128) for h in range(4)], hT=hT,
                 gate=[(0, 512, lambda t: rows(scr["erows"][:, 1024:1536], t)), (512, 512, lambda t: rows(scr["srows"][:, 512:1024], t))]),
            dict(width=D, loads=[(0, D, lambda t: rows(scr["x2"], t))], groups=[(0, D)], hT=hT, post=A["post_norm_w_2"][0],
                 keep=scr["x3"]))
    wo = A["odd_w_in_2"][0]
    project(nc, "pg", hT, 8, [T_chunk(wo, c, scr["oT"], c) for c in (0, 512)] +
            [row_chunk(wo, 1024 + c, scr["orows"], c) for c in (0, 512)] +
            [T_chunk(wo, 2048 + c, scr["oT"], 1024 + c) for c in (0, 512)], gain=[(0, A["pre_norm_w_2"][1])])
    hgrn2(nc, ident, scr["oT"], scr["orows"], C, scr["hc"])
    rg_lru(nc, scr["oT"][1024:2048, :], A, hT)
    mix_out(nc, "om", ident, hT, A["odd_w_out_2"][0], None,
            dict(width=512, loads=[(0, 512, lambda t: rows(scr["hc"], t))], groups=[(128 * h, 128) for h in range(4)], hT=hT,
                 gate=[(0, 512, lambda t: rows(scr["orows"][:, 512:1024], t))]),
            dict(width=D, loads=[(0, D, lambda t: rows(scr["x3"], t))], groups=[], post=A["post_norm_w_2"][1], keep=out))


SCRATCH.update(erows=(S, 1536), sqkT=(1024, S), srows=(S, 1024), ret=(S, 512), stick=(S, 512), x3=(S, D),
               oT=(2048, S), orows=(S, 1024), hc=(S, 512))


def build(nc, A, C, out):
    scr = {n: nc.dram_tensor("scr_" + n, s, F32, kind="Internal").ap() for n, s in SCRATCH.items()}
    with ExitStack() as ctx:
        ident = ctx.enter_context(nc.sbuf_tensor("ident", [P, P], F32))
        hT = ctx.enter_context(nc.sbuf_tensor("hT", [P, 2, 8, S], F32R))
        identity(nc, ident)
        first_attention(nc, A, C, scr, ident, hT)
        moe(nc, A, C, scr, ident, hT)
        second(nc, A, C, scr, ident, hT, out.rearrange("b s d -> (b s) d"))


def kernel(**inputs):
    import concourse.bacc as _bacc
    from concourse.bass_utils import run_bass_kernel_spmd as _run
    nc = _bacc.Bacc("TRN2", target_bir_lowering=False, num_devices=1)
    arrays, A, C = {}, {}, {}
    for name, v in inputs.items():
        if name == "hgrn_lb_logits_2":
            continue
        v = np.ascontiguousarray(v)
        arrays["in_" + name] = v
        A[name] = nc.dram_tensor("in_" + name, v.shape, F32, kind="ExternalInput").ap()
    for name, v in constants().items():
        arrays["const_" + name] = v
        C[name] = nc.dram_tensor("const_" + name, v.shape, F32, kind="ExternalInput").ap()
    out = nc.dram_tensor("out", (1, S, D), F32, kind="ExternalOutput").ap()
    build(nc, A, C, out)
    r = _run(nc, [arrays], core_ids=[0])
    return r.results[0]["out"]
```
